# Optimizing a Trainium2 kernel written in Bass

```python
import math
import jax
import jax.numpy as jnp
from jax import lax
import numpy as np
import jax, jax.numpy as jnp

D_MODEL = 1024
BATCH = 1
SEQ = 512
DEPTH = 1

D_HEAD = 64
NSA_HEADS = 8
NSA_KV_HEADS = 2
NSA_GROUP = NSA_HEADS // NSA_KV_HEADS
D_NSA = NSA_HEADS * D_HEAD
D_KV = NSA_KV_HEADS * D_HEAD
N_BRANCH = 3
N_GATES = NSA_HEADS * N_BRANCH
CMP_BLOCK = 32
CMP_STRIDE = 16
CMP_HIDDEN = 256
SEL_BLOCK = 64
SEL_TOPK = 16
WINDOW = 512
Q_BLOCK = 64
GMLP_GROUPS = 8
GMLP_GROUP_DIM = 64
D_GMLP = GMLP_GROUPS * GMLP_GROUP_DIM
CHUNK = 128
D_MIX = D_NSA + D_GMLP
D_PROJ = D_NSA + 6 * D_KV + N_GATES + 2 * D_GMLP
SPLITS = (D_NSA, D_NSA + D_KV, D_NSA + 2 * D_KV, D_NSA + 3 * D_KV, D_NSA + 4 * D_KV, D_NSA + 5 * D_KV, D_NSA + 6 * D_KV, D_NSA + 6 * D_KV + N_GATES)
REL_BUCKETS = 32
REL_MAX_DIST = 128
D_FF = 2816
CONV_WIDTH = 3
EPS = 1e-6
NEG_INF = -1e30
FORCED_SCORE = 1e4


def _rms_norm(x, g):
    xf = x.astype(jnp.float32)
    y = xf * lax.rsqrt(jnp.mean(xf * xf, axis=-1, keepdims=True) + EPS)
    return (y * g.astype(jnp.float32)).astype(x.dtype)

def _rel_bucket(dist):
    max_exact = REL_BUCKETS // 2
    d = jnp.maximum(dist, 1).astype(jnp.float32)
    log_b = max_exact + (jnp.log(d / max_exact) / math.log(REL_MAX_DIST / max_exact) * (REL_BUCKETS - max_exact)).astype(jnp.int32)
    log_b = jnp.clip(log_b, max_exact, REL_BUCKETS - 1)
    return jnp.where(dist < max_exact, jnp.maximum(dist, 0), log_b)

def _bias_shared(dist, rel_bias):
    b = rel_bias[_rel_bucket(dist)]
    return jnp.transpose(b, (2, 0, 1)).reshape(NSA_KV_HEADS, NSA_GROUP, dist.shape[0], dist.shape[1]).astype(jnp.float32)

def _bias_gathered(dist, rel_bias):
    table = rel_bias.T.reshape(NSA_KV_HEADS, NSA_GROUP, REL_BUCKETS)
    gi = jnp.arange(NSA_KV_HEADS)[None, :, None, None, None]
    ri = jnp.arange(NSA_GROUP)[None, None, :, None, None]
    return table[gi, ri, _rel_bucket(dist)[:, :, None]].astype(jnp.float32)

def _heads(t, B, T):
    return jnp.transpose(t.reshape(B, T, NSA_KV_HEADS, D_HEAD), (0, 2, 1, 3))

def _compress(tok, pe, w1, b1, w2):
    B, G, T, D = tok.shape
    nc = (T - CMP_BLOCK) // CMP_STRIDE + 1
    idx = jnp.arange(nc)[:, None] * CMP_STRIDE + jnp.arange(CMP_BLOCK)[None, :]
    blk = (tok[:, :, idx] + pe).reshape(B, G, nc, CMP_BLOCK * D)
    return jax.nn.gelu(blk @ w1 + b1) @ w2

def _nsa(q, k_cmp, v_cmp, k_slc, v_slc, k_win, v_win, gates, rel_bias):
    B, G, R, T, D = q.shape
    nc = k_cmp.shape[2]
    ns = T // SEL_BLOCK
    n_sel = min(SEL_TOPK, ns)
    cmp_end = jnp.arange(nc) * CMP_STRIDE + (CMP_BLOCK - 1)
    cs = jnp.arange(nc)[:, None] * CMP_STRIDE
    ss = jnp.arange(ns)[None, :] * SEL_BLOCK
    overlap = ((cs < ss + SEL_BLOCK) & (cs + CMP_BLOCK > ss)).astype(jnp.float32)
    blk_start = jnp.arange(ns) * SEL_BLOCK
    k_blocks = k_slc.reshape(B, G, ns, SEL_BLOCK, D)
    v_blocks = v_slc.reshape(B, G, ns, SEL_BLOCK, D)
    k_pad = jnp.pad(k_win, ((0, 0), (0, 0), (WINDOW, 0), (0, 0)))
    v_pad = jnp.pad(v_win, ((0, 0), (0, 0), (WINDOW, 0), (0, 0)))
    bi = jnp.arange(B)[:, None, None, None]
    gi = jnp.arange(G)[None, :, None, None]

    def block(qi):
        t0 = qi * Q_BLOCK
        tpos = t0 + jnp.arange(Q_BLOCK)
        qb = lax.dynamic_slice_in_dim(q, t0, Q_BLOCK, axis=3)
        gb = lax.dynamic_slice_in_dim(gates, t0, Q_BLOCK, axis=3)

        dist_c = tpos[:, None] - cmp_end[None, :]
        valid_c = dist_c >= 0
        s_c = jnp.einsum('bgrqd,bgnd->bgrqn', qb, k_cmp).astype(jnp.float32) + _bias_shared(dist_c, rel_bias)
        p_c = jnp.where(valid_c, jax.nn.softmax(jnp.where(valid_c, s_c, NEG_INF), axis=-1), 0.0)
        o_c = jnp.einsum('bgrqn,bgnd->bgrqd', p_c.astype(v_cmp.dtype), v_cmp)

        imp = jnp.einsum('bgrqn,ns->bgqs', p_c, overlap)
        cur = tpos[:, None] // SEL_BLOCK
        j = jnp.arange(ns)[None, :]
        forced = (j == 0) | (j == cur) | (j == cur - 1)
        causal_blk = blk_start[None, :] <= tpos[:, None]
        score = jnp.where(forced, FORCED_SCORE, jnp.where(causal_blk, imp, NEG_INF))
        _, sel = lax.top_k(score, n_sel)

        k_sel = k_blocks[bi, gi, sel].reshape(B, G, Q_BLOCK, n_sel * SEL_BLOCK, D)
        v_sel = v_blocks[bi, gi, sel].reshape(B, G, Q_BLOCK, n_sel * SEL_BLOCK, D)
        kpos = (sel[..., None] * SEL_BLOCK + jnp.arange(SEL_BLOCK)).reshape(B, G, Q_BLOCK, n_sel * SEL_BLOCK)
        dist_s = tpos[None, None, :, None] - kpos
        s_s = jnp.einsum('bgrqd,bgqkd->bgrqk', qb, k_sel).astype(jnp.float32) + _bias_gathered(dist_s, rel_bias)
        p_s = jax.nn.softmax(jnp.where((dist_s >= 0)[:, :, None], s_s, NEG_INF), axis=-1)
        o_s = jnp.einsum('bgrqk,bgqkd->bgrqd', p_s.astype(v_sel.dtype), v_sel)

        kw = lax.dynamic_slice_in_dim(k_pad, t0, Q_BLOCK + WINDOW, axis=2)
        vw = lax.dynamic_slice_in_dim(v_pad, t0, Q_BLOCK + WINDOW, axis=2)
        kpos_w = t0 - WINDOW + jnp.arange(Q_BLOCK + WINDOW)
        dist_w = tpos[:, None] - kpos_w[None, :]
        valid_w = (dist_w >= 0) & (dist_w < WINDOW) & (kpos_w[None, :] >= 0)
        s_w = jnp.einsum('bgrqd,bgkd->bgrqk', qb, kw).astype(jnp.float32) + _bias_shared(dist_w, rel_bias)
        p_w = jax.nn.softmax(jnp.where(valid_w, s_w, NEG_INF), axis=-1)
        o_w = jnp.einsum('bgrqk,bgkd->bgrqd', p_w.astype(vw.dtype), vw)

        return gb[..., 0:1] * o_c + gb[..., 1:2] * o_s + gb[..., 2:3] * o_w

    o = lax.map(block, jnp.arange(T // Q_BLOCK))
    return jnp.transpose(o, (1, 0, 4, 2, 3, 5)).reshape(B, T, G * R * D)

def _sgu(uv, sgu_norm, sgu_w, sgu_b):
    B, T, _ = uv.shape
    u, v = jnp.split(jax.nn.gelu(uv), 2, axis=-1)
    v = _rms_norm(v, sgu_norm).reshape(B, T // CHUNK, CHUNK, GMLP_GROUPS, GMLP_GROUP_DIM)
    w = sgu_w * jnp.tril(jnp.ones((CHUNK, CHUNK), sgu_w.dtype))
    z = jnp.einsum('gij,bcjge->bcige', w, v) + sgu_b.T[:, :, None]
    return u * z.reshape(B, T, D_GMLP)

def _conv_ffn(h, w_up, conv_w, conv_b, w_down):
    up = h @ w_up
    up = lax.conv_general_dilated(up, conv_w[:, None, :], (1,), [(CONV_WIDTH - 1, 0)], dimension_numbers=('NWC', 'WIO', 'NWC'), feature_group_count=up.shape[-1]) + conv_b
    a, g = jnp.split(up, 2, axis=-1)
    return (jax.nn.silu(g) * a) @ w_down

def first_inputs(seed: int = 0) -> dict:
    key = jax.random.key(seed)
    ks = jax.random.split(key, 32)
    L = DEPTH

    def nrm(k, shape, scale):
        return jax.random.normal(k, shape, jnp.float32) * scale

    def gain(k, shape):
        return 1.0 + 0.01 * jax.random.normal(k, shape, jnp.float32)

    return {
        "x": nrm(ks[0], (BATCH, SEQ, D_MODEL), 1.0),
        "rel_bias": nrm(ks[1], (REL_BUCKETS, NSA_HEADS), 0.5),
        "attn_norm": gain(ks[2], (L, D_MODEL)),
        "w_in": nrm(ks[3], (L, D_MODEL, D_PROJ), D_MODEL ** -0.5),
        "q_norm": gain(ks[4], (L, D_HEAD)),
        "k_norm_cmp": gain(ks[5], (L, D_HEAD)),
        "k_norm_slc": gain(ks[6], (L, D_HEAD)),
        "k_norm_win": gain(ks[7], (L, D_HEAD)),
        "cmp_pe_k": nrm(ks[8], (L, CMP_BLOCK, D_HEAD), 0.1),
        "cmp_w1_k": nrm(ks[9], (L, CMP_BLOCK * D_HEAD, CMP_HIDDEN), (CMP_BLOCK * D_HEAD) ** -0.5),
        "cmp_b1_k": nrm(ks[10], (L, CMP_HIDDEN), 0.01),
        "cmp_w2_k": nrm(ks[11], (L, CMP_HIDDEN, D_HEAD), CMP_HIDDEN ** -0.5),
        "cmp_pe_v": nrm(ks[12], (L, CMP_BLOCK, D_HEAD), 0.1),
        "cmp_w1_v": nrm(ks[13], (L, CMP_BLOCK * D_HEAD, CMP_HIDDEN), (CMP_BLOCK * D_HEAD) ** -0.5),
        "cmp_b1_v": nrm(ks[14], (L, CMP_HIDDEN), 0.01),
        "cmp_w2_v": nrm(ks[15], (L, CMP_HIDDEN, D_HEAD), CMP_HIDDEN ** -0.5),
        "sgu_norm": gain(ks[16], (L, D_GMLP)),
        "sgu_w": nrm(ks[17], (L, GMLP_GROUPS, CHUNK, CHUNK), CHUNK ** -0.5),
        "sgu_b": gain(ks[18], (L, GMLP_GROUPS, CHUNK)),
        "w_out": nrm(ks[19], (L, D_MIX, D_MODEL), D_MIX ** -0.5),
        "ffn_norm": gain(ks[20], (L, D_MODEL)),
        "w_up": nrm(ks[21], (L, D_MODEL, 2 * D_FF), D_MODEL ** -0.5),
        "conv_w": nrm(ks[22], (L, CONV_WIDTH, 2 * D_FF), CONV_WIDTH ** -0.5),
        "conv_b": nrm(ks[23], (L, 2 * D_FF), 0.01),
        "w_down": nrm(ks[24], (L, D_FF, D_MODEL), D_FF ** -0.5),
    }

def first_block(x, rel_bias, attn_norm, w_in, q_norm, k_norm_cmp, k_norm_slc, k_norm_win,
              cmp_pe_k, cmp_w1_k, cmp_b1_k, cmp_w2_k, cmp_pe_v, cmp_w1_v, cmp_b1_v, cmp_w2_v,
              sgu_norm, sgu_w, sgu_b, w_out, ffn_norm, w_up, conv_w, conv_b, w_down):
    B, T, _ = x.shape
    G, R = NSA_KV_HEADS, NSA_GROUP
    for l in range(DEPTH):
        h = _rms_norm(x, attn_norm[l])
        proj = h @ w_in[l]
        q, kc, vc, ks_, vs, kw, vw, gl, uv = jnp.split(proj, SPLITS, axis=-1)
        q = _rms_norm(q.reshape(B, T, G, R, D_HEAD), q_norm[l]) * (D_HEAD ** -0.5)
        q = jnp.transpose(q, (0, 2, 3, 1, 4))
        k_cmp = _rms_norm(_compress(_heads(kc, B, T), cmp_pe_k[l], cmp_w1_k[l], cmp_b1_k[l], cmp_w2_k[l]), k_norm_cmp[l])
        v_cmp = _compress(_heads(vc, B, T), cmp_pe_v[l], cmp_w1_v[l], cmp_b1_v[l], cmp_w2_v[l])
        k_slc = _rms_norm(_heads(ks_, B, T), k_norm_slc[l])
        v_slc = _heads(vs, B, T)
        k_win = _rms_norm(_heads(kw, B, T), k_norm_win[l])
        v_win = _heads(vw, B, T)
        gates = jnp.transpose(jax.nn.sigmoid(gl.reshape(B, T, G, R, N_BRANCH)), (0, 2, 3, 1, 4))
        o_nsa = _nsa(q, k_cmp, v_cmp, k_slc, v_slc, k_win, v_win, gates, rel_bias)
        o_sgu = _sgu(uv, sgu_norm[l], sgu_w[l], sgu_b[l])
        x = x + jnp.concatenate([o_nsa, o_sgu], axis=-1) @ w_out[l]
        x = x + _conv_ffn(_rms_norm(x, ffn_norm[l]), w_up[l], conv_w[l], conv_b[l], w_down[l])
    return x


_first_inputs = first_inputs


def first_inputs(seed=0):
    import zlib

    import numpy as np

    out = dict(_first_inputs(seed))
    spreads = {}
    factors = {}
    for name, (base, spread) in spreads.items():
        noise = np.random.default_rng([zlib.crc32(name.encode()), seed]).standard_normal(out[name].shape)
        drawn = base * np.exp(spread * noise) if base else spread * noise
        out[name] = jnp.asarray(drawn.astype(out[name].dtype))
    for name, factor in factors.items():
        out[name] = (out[name] * factor).astype(out[name].dtype)
    return out


_narrow_inputs = first_inputs


def first_inputs(seed=0):

    out = dict(_narrow_inputs(seed))
    wider = {'attn_norm': 9.2,
     'q_norm': 12.0,
     'k_norm_cmp': 12.0,
     'k_norm_slc': 12.0,
     'k_norm_win': 12.0,
     'cmp_pe_k': 12.0,
     'cmp_b1_k': 12.0,
     'cmp_pe_v': 3.5,
     'cmp_b1_v': 12.0,
     'sgu_norm': 12.0,
     'sgu_b': 12.0,
     'ffn_norm': 9.95,
     'conv_b': 9.92}
    for name, times in wider.items():
        mean = out[name].mean()
        out[name] = (mean + times * (out[name] - mean)).astype(out[name].dtype)
    return out


CHUNK_2 = 64
QBLOCK = 128
PLE_DIM = 256
N_BRANCH_2 = 4
GDN_HEADS = 4
GDN_HEAD_DIM = 128
GDN_WIDTH = GDN_HEADS * GDN_HEAD_DIM
GDN_CONV = 4
CONV_WIDTH_2 = D_MODEL // 2
CONV_K = 31
SB_HEADS = 8
SB_HEAD_DIM = 64
SB_WIDTH = SB_HEADS * SB_HEAD_DIM
FOX_HEADS = 8
FOX_HEAD_DIM = 64
FOX_WIDTH = FOX_HEADS * FOX_HEAD_DIM
BRANCH_WIDTH = 512
ALPHA = (2 * DEPTH) ** 0.25
BETA = (8 * DEPTH) ** -0.25
EPS_2 = 1e-5

SIZES = ([GDN_WIDTH] * 4 + [GDN_HEADS, GDN_HEADS]
         + [2 * CONV_WIDTH_2, CONV_WIDTH_2]
         + [SB_WIDTH] * 4
         + [FOX_WIDTH] * 4 + [FOX_HEADS]
         + [N_BRANCH_2 * D_MODEL])
PROJ_WIDTH = sum(SIZES)
SPLIT_POINTS = [sum(SIZES[:i + 1]) for i in range(len(SIZES) - 1)]


def layer_norm(x, g, b):
    xf = x.astype(jnp.float32)
    mu = jnp.mean(xf, axis=-1, keepdims=True)
    var = jnp.mean(jnp.square(xf - mu), axis=-1, keepdims=True)
    return ((xf - mu) * lax.rsqrt(var + EPS_2) * g.astype(jnp.float32) + b.astype(jnp.float32)).astype(x.dtype)

def rms_norm(x, g):
    xf = x.astype(jnp.float32)
    return xf * lax.rsqrt(jnp.mean(jnp.square(xf), axis=-1, keepdims=True) + EPS_2) * g.astype(jnp.float32)

def l2_normalize(x):
    xf = x.astype(jnp.float32)
    return xf * lax.rsqrt(jnp.sum(jnp.square(xf), axis=-1, keepdims=True) + 1e-6)

def causal_dwconv(x, w):
    k_width, c = w.shape
    xp = jnp.pad(x, ((0, 0), (k_width - 1, 0), (0, 0)))
    return lax.conv_general_dilated(xp, w[:, None, :].astype(x.dtype), window_strides=(1,), padding='VALID',
                                    dimension_numbers=('NWC', 'WIO', 'NWC'), feature_group_count=c)

def gated_delta_rule(q, k, v, g, beta):
    B, T, H, dk = q.shape
    dv = v.shape[-1]
    n = T // CHUNK_2
    f32 = jnp.float32

    def chunks(a):
        a = a.astype(f32).reshape((B, n, CHUNK_2, H) + a.shape[3:])
        return jnp.moveaxis(a, 3, 1)

    qc = chunks(q) * dk ** -0.5
    kc, vc, bc = chunks(k), chunks(v), chunks(beta)
    gc = jnp.cumsum(chunks(g), axis=-1)
    idx = jnp.arange(CHUNK_2)
    incl = idx[:, None] >= idx[None, :]
    strict = idx[:, None] > idx[None, :]
    decay = jnp.where(incl, jnp.exp(jnp.where(incl, gc[..., :, None] - gc[..., None, :], 0.0)), 0.0)
    kb = kc * bc[..., None]
    lower = jnp.where(strict, jnp.einsum('bhncd,bhnsd->bhncs', kb, kc) * decay, 0.0)
    eye = jnp.eye(CHUNK_2, dtype=f32)
    rhs = jnp.concatenate([vc * bc[..., None], kb * jnp.exp(gc)[..., None]], axis=-1)
    sol = lax.linalg.triangular_solve(eye + lower, rhs, left_side=True, lower=True, unit_diagonal=True)
    u, w = sol[..., :dv], sol[..., dv:]
    a_qk = jnp.einsum('bhncd,bhnsd->bhncs', qc, kc) * decay
    q_dec = qc * jnp.exp(gc)[..., None]
    k_dec = kc * jnp.exp(gc[..., -1:] - gc)[..., None]
    g_last = jnp.exp(gc[..., -1])

    def step(S, xs):
        a_i, q_i, u_i, w_i, k_i, gl = xs
        v_new = u_i - jnp.einsum('bhck,bhkv->bhcv', w_i, S)
        o = jnp.einsum('bhck,bhkv->bhcv', q_i, S) + jnp.einsum('bhcs,bhsv->bhcv', a_i, v_new)
        S = S * gl[..., None, None] + jnp.einsum('bhck,bhcv->bhkv', k_i, v_new)
        return S, o

    xs = tuple(jnp.moveaxis(a, 2, 0) for a in (a_qk, q_dec, u, w, k_dec, g_last))
    _, o = lax.scan(step, jnp.zeros((B, H, dk, dv), f32), xs)
    return o.transpose(1, 0, 3, 2, 4).reshape(B, T, H, dv)

def stick_breaking_attention(q, k, v):
    B, T, H, d = q.shape
    nb = T // QBLOCK
    scale = d ** -0.5
    kh = k.transpose(0, 2, 1, 3)
    vh = v.transpose(0, 2, 1, 3)
    qb = q.reshape(B, nb, QBLOCK, H, d).transpose(1, 0, 3, 2, 4)
    kpos = jnp.arange(T)

    def block(args):
        qi, i = args
        qpos = i * QBLOCK + jnp.arange(QBLOCK)
        mask = kpos[None, :] < qpos[:, None]
        z = jnp.einsum('bhqd,bhsd->bhqs', qi, kh).astype(jnp.float32) * scale
        log_beta = jax.nn.log_sigmoid(z)
        log_rest = jnp.where(mask, jax.nn.log_sigmoid(-z), 0.0)
        between = lax.cumsum(log_rest, axis=3, reverse=True) - log_rest
        att = jnp.where(mask, jnp.exp(log_beta + between), 0.0)
        return jnp.einsum('bhqs,bhsd->bhqd', att, vh.astype(jnp.float32)).astype(q.dtype)

    o = lax.map(block, (qb, jnp.arange(nb)))
    return o.transpose(1, 0, 3, 2, 4).reshape(B, T, H, d)

def forgetting_attention(q, k, v, log_f):
    B, T, H, d = q.shape
    nb = T // QBLOCK
    scale = d ** -0.5
    F = jnp.cumsum(log_f.astype(jnp.float32), axis=1).transpose(0, 2, 1)
    kh = k.transpose(0, 2, 1, 3)
    vh = v.transpose(0, 2, 1, 3)
    qb = q.reshape(B, nb, QBLOCK, H, d).transpose(1, 0, 3, 2, 4)
    Fq = F.reshape(B, H, nb, QBLOCK).transpose(2, 0, 1, 3)
    kpos = jnp.arange(T)

    def block(args):
        qi, fi, i = args
        qpos = i * QBLOCK + jnp.arange(QBLOCK)
        z = jnp.einsum('bhqd,bhsd->bhqs', qi, kh).astype(jnp.float32) * scale
        z = z + fi[..., :, None] - F[:, :, None, :]
        z = jnp.where(kpos[None, :] <= qpos[:, None], z, -jnp.inf)
        att = jax.nn.softmax(z, axis=-1)
        return jnp.einsum('bhqs,bhsd->bhqd', att, vh.astype(jnp.float32)).astype(q.dtype)

    o = lax.map(block, (qb, Fq, jnp.arange(nb)))
    return o.transpose(1, 0, 3, 2, 4).reshape(B, T, H, d)

def hybrid_layer(x, p_i, w_in, b_gate, conv_qkv, a_log, dt_bias, gdn_norm, conv_dw, conv_dw_bias,
                 conv_ln_g, conv_ln_b, forget_bias, w_branch, w_out, w_ple, w_ple_gate, b_ple_gate,
                 ln_g, ln_b):
    B, T, _ = x.shape
    dt = x.dtype
    proj = x @ w_in
    (qA, kA, vA, zA, aA, bA, glu, zB, qC, kC, vC, zC,
     qD, kD, vD, zD, fD, gates) = jnp.split(proj, SPLIT_POINTS, axis=-1)

    qkvA = jax.nn.silu(causal_dwconv(jnp.concatenate([qA, kA, vA], axis=-1), conv_qkv))
    qA, kA, vA = jnp.split(qkvA, 3, axis=-1)
    qA = l2_normalize(qA.reshape(B, T, GDN_HEADS, GDN_HEAD_DIM))
    kA = l2_normalize(kA.reshape(B, T, GDN_HEADS, GDN_HEAD_DIM))
    vA = vA.reshape(B, T, GDN_HEADS, GDN_HEAD_DIM)
    gA = -jnp.exp(a_log.astype(jnp.float32)) * jax.nn.softplus(aA.astype(jnp.float32) + dt_bias.astype(jnp.float32))
    betaA = jax.nn.sigmoid(bA.astype(jnp.float32))
    oA = gated_delta_rule(qA, kA, vA, gA, betaA)
    yA = rms_norm(oA, gdn_norm).reshape(B, T, GDN_WIDTH).astype(dt) * jax.nn.silu(zA)

    g_lin, g_gate = jnp.split(glu, 2, axis=-1)
    hB = g_lin * jax.nn.sigmoid(g_gate)
    hB = causal_dwconv(hB, conv_dw) + conv_dw_bias
    hB = jax.nn.silu(layer_norm(hB, conv_ln_g, conv_ln_b))
    yB = hB * jax.nn.silu(zB)

    oC = stick_breaking_attention(qC.reshape(B, T, SB_HEADS, SB_HEAD_DIM),
                                  kC.reshape(B, T, SB_HEADS, SB_HEAD_DIM),
                                  vC.reshape(B, T, SB_HEADS, SB_HEAD_DIM))
    yC = oC.reshape(B, T, SB_WIDTH) * jax.nn.silu(zC)

    log_f = jax.nn.log_sigmoid(fD.astype(jnp.float32) + forget_bias.astype(jnp.float32))
    oD = forgetting_attention(qD.reshape(B, T, FOX_HEADS, FOX_HEAD_DIM),
                              kD.reshape(B, T, FOX_HEADS, FOX_HEAD_DIM),
                              vD.reshape(B, T, FOX_HEADS, FOX_HEAD_DIM), log_f)
    yD = oD.reshape(B, T, FOX_WIDTH) * jax.nn.silu(zD)

    gate = jax.nn.sigmoid(gates + b_gate).reshape(B, T, N_BRANCH_2, D_MODEL)
    merged = gate[:, :, 0] * (yA @ w_branch[0])
    merged = merged + gate[:, :, 1] * (yB @ w_branch[1])
    merged = merged + gate[:, :, 2] * (yC @ w_branch[2])
    merged = merged + gate[:, :, 3] * (yD @ w_branch[3])
    mix = merged @ w_out

    r = ALPHA * x + mix
    r = r + jax.nn.sigmoid(r @ w_ple_gate + b_ple_gate) * (p_i @ w_ple)
    return layer_norm(r, ln_g, ln_b)

def second_inputs(seed: int = 0) -> dict:
    key = jax.random.key(seed)
    ks = jax.random.split(key, 24)
    f32 = jnp.float32

    def nrm(k, shape, s):
        return jax.random.normal(k, shape, f32) * s

    dt_init = jnp.exp(jax.random.uniform(ks[6], (DEPTH, GDN_HEADS), f32, math.log(1e-3), math.log(1e-1)))
    return {
        "x": nrm(ks[0], (BATCH, SEQ, D_MODEL), 1.0),
        "p": nrm(ks[1], (DEPTH, BATCH, SEQ, PLE_DIM), 1.0),
        "w_in": nrm(ks[2], (DEPTH, D_MODEL, PROJ_WIDTH), D_MODEL ** -0.5),
        "b_gate": nrm(ks[3], (DEPTH, N_BRANCH_2 * D_MODEL), 0.02),
        "conv_qkv": nrm(ks[4], (DEPTH, GDN_CONV, 3 * GDN_WIDTH), GDN_CONV ** -0.5),
        "a_log": jnp.log(jax.random.uniform(ks[5], (DEPTH, GDN_HEADS), f32, 1.0, 16.0)),
        "dt_bias": dt_init + jnp.log(-jnp.expm1(-dt_init)),
        "gdn_norm": 1.0 + nrm(ks[7], (DEPTH, GDN_HEAD_DIM), 0.02),
        "conv_dw": nrm(ks[8], (DEPTH, CONV_K, CONV_WIDTH_2), CONV_K ** -0.5),
        "conv_dw_bias": nrm(ks[9], (DEPTH, CONV_WIDTH_2), 0.02),
        "conv_ln_g": 1.0 + nrm(ks[10], (DEPTH, CONV_WIDTH_2), 0.02),
        "conv_ln_b": nrm(ks[11], (DEPTH, CONV_WIDTH_2), 0.02),
        "forget_bias": 2.0 + nrm(ks[12], (DEPTH, FOX_HEADS), 0.5),
        "w_branch": nrm(ks[13], (DEPTH, N_BRANCH_2, BRANCH_WIDTH, D_MODEL), BETA * BRANCH_WIDTH ** -0.5),
        "w_out": nrm(ks[14], (DEPTH, D_MODEL, D_MODEL), BETA * D_MODEL ** -0.5),
        "w_ple": nrm(ks[15], (DEPTH, PLE_DIM, D_MODEL), PLE_DIM ** -0.5),
        "w_ple_gate": nrm(ks[16], (DEPTH, D_MODEL, D_MODEL), D_MODEL ** -0.5),
        "b_ple_gate": nrm(ks[17], (DEPTH, D_MODEL), 0.02),
        "ln_g": 1.0 + nrm(ks[18], (DEPTH, D_MODEL), 0.02),
        "ln_b": nrm(ks[19], (DEPTH, D_MODEL), 0.02),
    }

def second_block(x, p, w_in, b_gate, conv_qkv, a_log, dt_bias, gdn_norm, conv_dw, conv_dw_bias,
              conv_ln_g, conv_ln_b, forget_bias, w_branch, w_out, w_ple, w_ple_gate, b_ple_gate,
              ln_g, ln_b):
    for i in range(DEPTH):
        x = hybrid_layer(x, p[i], w_in[i], b_gate[i], conv_qkv[i], a_log[i], dt_bias[i], gdn_norm[i],
                         conv_dw[i], conv_dw_bias[i], conv_ln_g[i], conv_ln_b[i], forget_bias[i],
                         w_branch[i], w_out[i], w_ple[i], w_ple_gate[i], b_ple_gate[i], ln_g[i], ln_b[i])
    return x


_first_inputs_2 = second_inputs


def second_inputs(seed=0):
    import zlib

    import numpy as np

    out = dict(_first_inputs_2(seed))
    spreads = {}
    factors = {'b_gate': 8.0,
     'a_log': 8.0,
     'gdn_norm': 60.783,
     'conv_dw_bias': 8.0,
     'conv_ln_g': 52.93,
     'conv_ln_b': 52.524,
     'forget_bias': 58.968,
     'b_ple_gate': 23.627,
     'ln_g': 8.487,
     'ln_b': 8.276}
    for name, (base, spread) in spreads.items():
        noise = np.random.default_rng([zlib.crc32(name.encode()), seed]).standard_normal(out[name].shape)
        drawn = base * np.exp(spread * noise) if base else spread * noise
        out[name] = __import__('jax').numpy.asarray(drawn.astype(out[name].dtype))
    for name, factor in factors.items():
        out[name] = (out[name] * factor).astype(out[name].dtype)
    return out


_narrow_inputs_2 = second_inputs


def second_inputs(seed=0):

    out = dict(_narrow_inputs_2(seed))
    wider = {'gdn_norm': 4.62,
     'conv_ln_g': 4.41,
     'conv_ln_b': 4.34,
     'b_ple_gate': 7.55,
     'ln_g': 3.27,
     'ln_b': 3.28}
    for name, times in wider.items():
        mean = out[name].mean()
        out[name] = (mean + times * (out[name] - mean)).astype(out[name].dtype)
    return out


GRID_W = 64
CTX_LEN = 256
ROPE_THETA = 10000.0
Q_BLOCK_3 = 128

DIFF_HEADS = 4
DIFF_HEAD_DIM = 64
DIFF_V_DIM = 2 * DIFF_HEAD_DIM
DIFF_WIDTH = DIFF_HEADS * DIFF_V_DIM
DIFF_SCALE = DIFF_HEAD_DIM ** -0.5

MLA_HEADS = 4
MLA_NOPE = 128
MLA_ROPE = 64
MLA_V = 128
MLA_Q_RANK = 256
MLA_KV_RANK = 128
MLA_WIDTH = MLA_HEADS * MLA_V
MLA_SCALE = (MLA_NOPE + MLA_ROPE) ** -0.5

MIX_WIDTH = DIFF_WIDTH + MLA_WIDTH
ROPE_PAIRS = DIFF_HEAD_DIM // 4

IN_SPLITS = (DIFF_HEADS * 2 * DIFF_HEAD_DIM,
             DIFF_HEADS * 2 * DIFF_HEAD_DIM,
             DIFF_HEADS * DIFF_V_DIM,
             MLA_Q_RANK,
             MLA_KV_RANK,
             MLA_ROPE)
IN_COLS = sum(IN_SPLITS)

N_EXPERTS = 32
TOP_K = 4
D_FF_3 = 1024
SWIGLU_LIMIT = 7.0
SWIGLU_ALPHA = 1.702
MOE_BLOCK = 128


def rmsnorm(x, w):
    xf = x.astype(jnp.float32)
    y = xf * lax.rsqrt(jnp.mean(xf * xf, axis=-1, keepdims=True) + EPS)
    return (y * w.astype(jnp.float32)).astype(x.dtype)

def modulate(h, shift, scale):
    return h * (1 + scale) + shift

def axial_angles(n):
    rows = n // GRID_W
    row = jnp.repeat(jnp.arange(rows, dtype=jnp.float32), GRID_W)
    col = jnp.tile(jnp.arange(GRID_W, dtype=jnp.float32), rows)
    inv = ROPE_THETA ** (-jnp.arange(ROPE_PAIRS, dtype=jnp.float32) / ROPE_PAIRS)
    return jnp.stack([row[:, None] * inv, col[:, None] * inv], axis=1)

def apply_axial_rope(x, ang):
    p = x.shape[-1] // 4
    xf = x.astype(jnp.float32).reshape(*x.shape[:-1], 2, 2, p)
    x1, x2 = xf[..., 0, :], xf[..., 1, :]
    cos, sin = jnp.cos(ang), jnp.sin(ang)
    out = jnp.stack([x1 * cos - x2 * sin, x2 * cos + x1 * sin], axis=-2)
    return out.reshape(x.shape).astype(x.dtype)

def mixer_inputs(h, w_in, q_norm_w, kv_norm_w, w_uq, w_ukv, ang):
    B, n, _ = h.shape
    proj = h @ w_in
    cuts = list(np.cumsum(IN_SPLITS)[:-1])
    dq, dk, dv, cq, ckv, kr = jnp.split(proj, cuts, axis=-1)
    dq = dq.reshape(B, n, DIFF_HEADS, 2, DIFF_HEAD_DIM)
    dk = dk.reshape(B, n, DIFF_HEADS, 2, DIFF_HEAD_DIM)
    dv = dv.reshape(B, n, DIFF_HEADS, DIFF_V_DIM)
    q = (rmsnorm(cq, q_norm_w) @ w_uq).reshape(B, n, MLA_HEADS, MLA_NOPE + MLA_ROPE)
    kv = (rmsnorm(ckv, kv_norm_w) @ w_ukv).reshape(B, n, MLA_HEADS, MLA_NOPE + MLA_V)
    q_nope, q_rope = q[..., :MLA_NOPE], q[..., MLA_NOPE:]
    k_nope, mv = kv[..., :MLA_NOPE], kv[..., MLA_NOPE:]
    if ang is not None:
        dq = apply_axial_rope(dq, ang[:, None, None])
        dk = apply_axial_rope(dk, ang[:, None, None])
        q_rope = apply_axial_rope(q_rope, ang[:, None])
        kr = apply_axial_rope(kr, ang)
    return (dq, dk, dv, q_nope, q_rope, k_nope, kr, mv)

def diff_attend(q, k, v, lam):
    s = jnp.einsum('bqhcd,bkhcd->bchqk', q, k).astype(jnp.float32) * DIFF_SCALE
    p = jax.nn.softmax(s, axis=-1)
    p = p[:, 0] - lam * p[:, 1]
    return jnp.einsum('bhqk,bkhe->bqhe', p.astype(v.dtype), v)

def mla_attend(q_nope, q_rope, k_nope, k_rope, v):
    s = (jnp.einsum('bqhd,bkhd->bhqk', q_nope, k_nope)
         + jnp.einsum('bqhr,bkr->bhqk', q_rope, k_rope)).astype(jnp.float32) * MLA_SCALE
    p = jax.nn.softmax(s, axis=-1)
    return jnp.einsum('bhqk,bkhe->bqhe', p.astype(v.dtype), v)

def to_blocks(t):
    B, n = t.shape[:2]
    return jnp.moveaxis(t.reshape(B, n // Q_BLOCK_3, Q_BLOCK_3, *t.shape[2:]), 1, 0)

def from_blocks(t):
    t = jnp.moveaxis(t, 0, 1)
    return t.reshape(t.shape[0], -1, *t.shape[3:])

def merge_heads(o_diff, o_mla, subln_w, lam_init, w_out):
    B, n = o_diff.shape[:2]
    o_diff = rmsnorm(o_diff, subln_w) * (1.0 - lam_init)
    mix = jnp.concatenate([o_diff.reshape(B, n, DIFF_WIDTH), o_mla.reshape(B, n, MLA_WIDTH)], axis=-1)
    return mix @ w_out

def clamped_swiglu(g, u):
    g = jnp.minimum(g, SWIGLU_LIMIT)
    u = jnp.clip(u, -SWIGLU_LIMIT, SWIGLU_LIMIT)
    return g * jax.nn.sigmoid(SWIGLU_ALPHA * g) * (u + 1)

def moe(h, router_w, router_b, w1, b1, w2, b2):
    T, D = h.shape
    logits = (h @ router_w + router_b).astype(jnp.float32)
    top_v, top_i = lax.top_k(logits, TOP_K)
    gates = jax.nn.softmax(top_v, axis=-1).astype(h.dtype)
    flat_e = top_i.reshape(-1)
    flat_tok = jnp.repeat(jnp.arange(T, dtype=jnp.int32), TOP_K)
    order = jnp.argsort(flat_e)
    e_sorted = flat_e[order]
    tok_sorted = flat_tok[order]
    gate_sorted = gates.reshape(-1)[order]
    counts = jnp.bincount(flat_e, length=N_EXPERTS)
    padded = ((counts + MOE_BLOCK - 1) // MOE_BLOCK) * MOE_BLOCK
    ends = jnp.cumsum(padded)
    pad_start = ends - padded
    grp_start = jnp.cumsum(counts) - counts
    n_assign = T * TOP_K
    rank = jnp.arange(n_assign, dtype=jnp.int32) - grp_start[e_sorted]
    dest = pad_start[e_sorted] + rank
    n_blocks = (n_assign + N_EXPERTS * (MOE_BLOCK - 1) + MOE_BLOCK - 1) // MOE_BLOCK
    row_tok = jnp.full((n_blocks * MOE_BLOCK,), T, jnp.int32).at[dest].set(tok_sorted)
    h_pad = jnp.concatenate([h, jnp.zeros((1, D), h.dtype)], axis=0)
    xs = h_pad[row_tok].reshape(n_blocks, MOE_BLOCK, D)
    blk_e = jnp.minimum(jnp.searchsorted(ends, jnp.arange(n_blocks) * MOE_BLOCK, side='right'),
                        N_EXPERTS - 1)

    def expert_block(args):
        xb, e = args
        hid = xb @ w1[e] + b1[e]
        return clamped_swiglu(hid[:, :D_FF_3], hid[:, D_FF_3:]) @ w2[e] + b2[e]

    ys = lax.map(expert_block, (xs, blk_e)).reshape(-1, D)
    contrib = ys[dest] * gate_sorted[:, None]
    return jax.ops.segment_sum(contrib, tok_sorted, num_segments=T)

def third_inputs(seed: int = 0) -> dict:
    key = jax.random.key(seed)
    ks = jax.random.split(key, 32)
    f32 = jnp.float32
    L = DEPTH

    def nrm(k, shape, scale):
        return jax.random.normal(k, shape, f32) * scale

    def gain(k, shape):
        return 1.0 + 0.05 * jax.random.normal(k, shape, f32)

    return {
        'x': nrm(ks[0], (BATCH, SEQ, D_MODEL), 1.0),
        'c': nrm(ks[1], (BATCH, D_MODEL), 1.0),
        'ctx': nrm(ks[2], (BATCH, CTX_LEN, D_MODEL), 1.0),
        'c_ctx': nrm(ks[3], (D_MODEL,), 1.0),
        'w_ada': nrm(ks[4], (L, D_MODEL, 6 * D_MODEL), 0.5 * D_MODEL ** -0.5),
        'b_ada': nrm(ks[5], (L, 6 * D_MODEL), 0.02),
        'attn_norm_w': gain(ks[6], (L, D_MODEL)),
        'w_in': nrm(ks[7], (L, D_MODEL, IN_COLS), D_MODEL ** -0.5),
        'q_norm_w': gain(ks[8], (L, MLA_Q_RANK)),
        'kv_norm_w': gain(ks[9], (L, MLA_KV_RANK)),
        'w_uq': nrm(ks[10], (L, MLA_Q_RANK, MLA_HEADS * (MLA_NOPE + MLA_ROPE)), MLA_Q_RANK ** -0.5),
        'w_ukv': nrm(ks[11], (L, MLA_KV_RANK, MLA_HEADS * (MLA_NOPE + MLA_V)), MLA_KV_RANK ** -0.5),
        'lambda_q1': nrm(ks[12], (L, DIFF_HEAD_DIM), 0.1),
        'lambda_k1': nrm(ks[13], (L, DIFF_HEAD_DIM), 0.1),
        'lambda_q2': nrm(ks[14], (L, DIFF_HEAD_DIM), 0.1),
        'lambda_k2': nrm(ks[15], (L, DIFF_HEAD_DIM), 0.1),
        'subln_w': gain(ks[16], (L, DIFF_V_DIM)),
        'w_out': nrm(ks[17], (L, MIX_WIDTH, D_MODEL), MIX_WIDTH ** -0.5),
        'ffn_norm_w': gain(ks[18], (L, D_MODEL)),
        'router_w': nrm(ks[19], (L, D_MODEL, N_EXPERTS), D_MODEL ** -0.5),
        'router_b': nrm(ks[20], (L, N_EXPERTS), 0.01),
        'w1': nrm(ks[21], (L, N_EXPERTS, D_MODEL, 2 * D_FF_3), D_MODEL ** -0.5),
        'b1': nrm(ks[22], (L, N_EXPERTS, 2 * D_FF_3), 0.02),
        'w2': nrm(ks[23], (L, N_EXPERTS, D_FF_3, D_MODEL), D_FF_3 ** -0.5),
        'b2': nrm(ks[24], (L, N_EXPERTS, D_MODEL), 0.02),
        'final_norm_w': gain(ks[25], (D_MODEL,)),
    }

def third_block(x, c, ctx, c_ctx, w_ada, b_ada, attn_norm_w, w_in, q_norm_w, kv_norm_w, w_uq, w_ukv,
              lambda_q1, lambda_k1, lambda_q2, lambda_k2, subln_w, w_out, ffn_norm_w,
              router_w, router_b, w1, b1, w2, b2, final_norm_w):
    B, n, D = x.shape
    ang = axial_angles(n)
    for l in range(DEPTH):
        last = l == DEPTH - 1
        lam_init = 0.8 - 0.6 * math.exp(-0.3 * l)
        mod_lat = (jax.nn.silu(c) @ w_ada[l] + b_ada[l])[:, None, :]
        mod_ctx = (jax.nn.silu(c_ctx) @ w_ada[l] + b_ada[l])[None, None, :]
        sa, sca, ga, sf, scf, gf = jnp.split(mod_lat, 6, axis=-1)
        csa, csca, cga, csf, cscf, cgf = jnp.split(mod_ctx, 6, axis=-1)
        lam = (jnp.exp(jnp.sum(lambda_q1[l].astype(jnp.float32) * lambda_k1[l].astype(jnp.float32)))
               - jnp.exp(jnp.sum(lambda_q2[l].astype(jnp.float32) * lambda_k2[l].astype(jnp.float32)))
               + lam_init)
        mp = (w_in[l], q_norm_w[l], kv_norm_w[l], w_uq[l], w_ukv[l])

        l_dq, l_dk, l_dv, l_qn, l_qr, l_kn, l_kr, l_v = mixer_inputs(
            modulate(rmsnorm(x, attn_norm_w[l]), sa, sca), *mp, ang)
        c_dq, c_dk, c_dv, c_qn, c_qr, c_kn, c_kr, c_v = mixer_inputs(
            modulate(rmsnorm(ctx, attn_norm_w[l]), csa, csca), *mp, None)
        dk_all = jnp.concatenate([c_dk, l_dk], axis=1)
        dv_all = jnp.concatenate([c_dv, l_dv], axis=1)
        kn_all = jnp.concatenate([c_kn, l_kn], axis=1)
        kr_all = jnp.concatenate([c_kr, l_kr], axis=1)
        v_all = jnp.concatenate([c_v, l_v], axis=1)
        o_diff = from_blocks(lax.map(lambda qb: diff_attend(qb, dk_all, dv_all, lam), to_blocks(l_dq)))
        o_mla = from_blocks(lax.map(lambda qs: mla_attend(qs[0], qs[1], kn_all, kr_all, v_all),
                                    (to_blocks(l_qn), to_blocks(l_qr))))
        x_new = x + ga * merge_heads(o_diff, o_mla, subln_w[l], lam_init, w_out[l])
        if not last:
            oc_diff = diff_attend(c_dq, c_dk, c_dv, lam)
            oc_mla = mla_attend(c_qn, c_qr, c_kn, c_kr, c_v)
            ctx = ctx + cga * merge_heads(oc_diff, oc_mla, subln_w[l], lam_init, w_out[l])
        x = x_new

        hf = modulate(rmsnorm(x, ffn_norm_w[l]), sf, scf)
        x = x + gf * moe(hf.reshape(B * n, D), router_w[l], router_b[l], w1[l], b1[l], w2[l], b2[l]).reshape(B, n, D)
        if not last:
            hc = modulate(rmsnorm(ctx, ffn_norm_w[l]), csf, cscf)
            ctx = ctx + cgf * moe(hc.reshape(-1, D), router_w[l], router_b[l], w1[l], b1[l], w2[l], b2[l]).reshape(ctx.shape)
    return rmsnorm(x, final_norm_w)


def setup_inputs(seed=0):
    out = dict(first_inputs(seed))
    for name, value in second_inputs(seed + 1).items():
        if name != "x":
            out[name + "_2"] = value
    for name, value in third_inputs(seed + 2).items():
        if name != "x":
            out[name + "_3"] = value
    return out


def reference(
    x, rel_bias, attn_norm, w_in, q_norm, k_norm_cmp, k_norm_slc, k_norm_win, cmp_pe_k,
    cmp_w1_k, cmp_b1_k, cmp_w2_k, cmp_pe_v, cmp_w1_v, cmp_b1_v, cmp_w2_v, sgu_norm, sgu_w,
    sgu_b, w_out, ffn_norm, w_up, conv_w, conv_b, w_down, p_2, w_in_2, b_gate_2, conv_qkv_2,
    a_log_2, dt_bias_2, gdn_norm_2, conv_dw_2, conv_dw_bias_2, conv_ln_g_2, conv_ln_b_2,
    forget_bias_2, w_branch_2, w_out_2, w_ple_2, w_ple_gate_2, b_ple_gate_2, ln_g_2, ln_b_2,
    c_3, ctx_3, c_ctx_3, w_ada_3, b_ada_3, attn_norm_w_3, w_in_3, q_norm_w_3, kv_norm_w_3,
    w_uq_3, w_ukv_3, lambda_q1_3, lambda_k1_3, lambda_q2_3, lambda_k2_3, subln_w_3, w_out_3,
    ffn_norm_w_3, router_w_3, router_b_3, w1_3, b1_3, w2_3, b2_3, final_norm_w_3,
):
    x = first_block(
        x, rel_bias, attn_norm, w_in, q_norm, k_norm_cmp, k_norm_slc, k_norm_win, cmp_pe_k,
        cmp_w1_k, cmp_b1_k, cmp_w2_k, cmp_pe_v, cmp_w1_v, cmp_b1_v, cmp_w2_v, sgu_norm, sgu_w,
        sgu_b, w_out, ffn_norm, w_up, conv_w, conv_b, w_down,
    )
    x = second_block(
        x, p_2, w_in_2, b_gate_2, conv_qkv_2, a_log_2, dt_bias_2, gdn_norm_2, conv_dw_2,
        conv_dw_bias_2, conv_ln_g_2, conv_ln_b_2, forget_bias_2, w_branch_2, w_out_2, w_ple_2,
        w_ple_gate_2, b_ple_gate_2, ln_g_2, ln_b_2,
    )
    return third_block(
        x, c_3, ctx_3, c_ctx_3, w_ada_3, b_ada_3, attn_norm_w_3, w_in_3, q_norm_w_3,
        kv_norm_w_3, w_uq_3, w_ukv_3, lambda_q1_3, lambda_k1_3, lambda_q2_3, lambda_k2_3,
        subln_w_3, w_out_3, ffn_norm_w_3, router_w_3, router_b_3, w1_3, b1_3, w2_3, b2_3,
        final_norm_w_3,
    )


_drawn_inputs = setup_inputs


def setup_inputs(seed=0):
    import zlib

    import numpy as np

    out = dict(_drawn_inputs(seed))
    spreads = {}
    factors = {'q_norm': 3.35,
     'k_norm_cmp': 6.739,
     'k_norm_slc': 4.752,
     'k_norm_win': 4.772,
     'cmp_b1_k': 8.0,
     'dt_bias_2': 3.95,
     'ctx_3': 8.0,
     'c_ctx_3': 6.907,
     'b_ada_3': 8.0,
     'attn_norm_w_3': 8.0,
     'q_norm_w_3': 8.0,
     'kv_norm_w_3': 8.0,
     'w_uq_3': 8.0,
     'w_ukv_3': 8.0,
     'lambda_q1_3': 8.0,
     'lambda_k1_3': 8.0,
     'lambda_q2_3': 8.0,
     'lambda_k2_3': 8.0,
     'subln_w_3': 29.269,
     'w_out_3': 2.673,
     'ffn_norm_w_3': 8.0,
     'router_w_3': 3.185,
     'router_b_3': 56.843,
     'w1_3': 3.167,
     'b1_3': 50.243,
     'w2_3': 3.01,
     'b2_3': 200.0}
    for name, (base, spread) in spreads.items():
        noise = np.random.default_rng([zlib.crc32(name.encode()), seed]).standard_normal(out[name].shape)
        drawn = base * np.exp(spread * noise) if base else spread * noise
        out[name] = jnp.asarray(drawn.astype(out[name].dtype))
    for name, factor in factors.items():
        out[name] = (out[name] * factor).astype(out[name].dtype)
    return out
```

```python
import math
from contextlib import ExitStack, contextmanager

import numpy as np

import concourse.bass as bass
from concourse import mybir

F32 = mybir.dt.float32
I32 = mybir.dt.int32
U32 = mybir.dt.uint32
ALU = mybir.AluOpType
ACT = mybir.ActivationFunctionType
AX_X = mybir.AxisListType.X

P = 128
T = 512
TT = T // P
D = 1024
KD = D // P
BANK = 512
NEG = -1e30
EPS = 1e-6
EPS_2 = 1e-5

NSA_HEADS, NSA_GROUPS, DH = 8, 2, 64
CMP_BLOCK, CMP_STRIDE, CMP_HIDDEN = 32, 16, 256
NCMP = (T - CMP_BLOCK) // CMP_STRIDE + 1
CMP_PAIRS = CMP_BLOCK * DH // P
REL_BUCKETS, REL_MAX_DIST = 32, 128
STRIP = T + 3 * P
SKEW = STRIP + P
D_FF = 2816
FF_CHUNKS = D_FF // P
GDN_HEADS, GDN_CHUNK, GDN_CONV = 4, 64, 4
GDN_QKV = 3 * GDN_HEADS
CONV_K = 31
BRANCHES = 4
PLE = 256
ALPHA = 2 ** 0.25
CTX = 256
TA = T + CTX
DIFF_HEADS, MLA_HEADS = 4, 4
LAM_INIT = 0.8 - 0.6 * math.exp(0.0)
EXPERTS, TOP_K, D_FF_3 = 32, 4, 1024
LIMIT, SWIGLU_ALPHA = 7.0, 1.702
SLOTS_MAX = T * TOP_K // P + EXPERTS - 1


class Core:

    def __init__(self, nc, ctx, dram):
        self.nc, self.ctx, self.dram = nc, ctx, dram
        self.psum = ctx.enter_context(nc.psum_tensor("psum", [P, 8 * BANK], F32))

    def keep(self, name, shape, dtype=F32):
        return self.ctx.enter_context(self.nc.sbuf_tensor(name, shape, dtype))

    def bank(self, n, width=BANK):
        return self.psum[:, n * BANK:n * BANK + width]

    def c(self, name):
        at, n = CONST_AT[name]
        return self.const[:, at:at + n]

    def p(self, name, n=None):
        at, width = PARAM_AT[name]
        return self.param[:, at:at + width] if n is None else self.param[:, at + n:at + n + 1]

    @contextmanager
    def stage(self, name):
        nc, sems = self.nc, []
        with ExitStack() as ctx:
            def sb(what, shape, dtype=F32):
                return ctx.enter_context(nc.sbuf_tensor(f"{name}_{what}", shape, dtype))

            def sem(what):
                sems.append(nc.alloc_semaphore(f"{name}_{what}"))
                return sems[-1]

            yield sb, sem
        nc.clear_and_free_semaphores(sems)
        nc.all_engine_barrier()


class Steps:

    def __init__(self, eng, sem):
        self.eng, self.sem, self.n = eng, sem, 0

    def then(self, instruction):
        self.n = self.n + 1
        instruction.then_inc(self.sem, 1)

    def settle(self):
        self.eng.wait_ge(self.sem, self.n)

    def do(self, instruction):
        self.then(instruction)
        self.settle()


def wait_apart(eng, sem, count, passed):
    eng.wait_ge(sem, count)
    eng.sem_inc(passed, 1)


def at(ap, n):
    if isinstance(n, int):
        return ap[:, n, :]
    return ap[:, bass.ds(n, 1), :].rearrange("p a n -> p (a n)")


def col(ap, n):
    return ap[:, n:n + 1] if isinstance(n, int) else ap[:, bass.ds(n, 1)]



def constants():
    i = np.arange(P)
    row, colm = i[:, None], i[None, :]
    same = row // GDN_CHUNK == colm // GDN_CHUNK
    c = {
        "ident": np.eye(P),
        "ones": np.ones((P, P)),
        "halves": row // DH == colm // DH,
        "upto": np.concatenate([row <= colm, np.ones((P, 3 * P))], 1),
        "before": np.concatenate([row < colm, np.ones((P, 3 * P))], 1),
        "minus_from": -1.0 * (row >= colm),
        "minus_ones": -np.ones((P, P)),
        "not_before": np.where(row >= colm, NEG, 0.0),
        "g_upto": same & (row <= colm),
        "g_after": same & (row > colm),
    }
    for n in range(6):
        k = 1 << n
        c[f"g_level{n}"] = (row // (2 * k) == colm // (2 * k)) & (row % (2 * k) >= k) & (colm % (2 * k) < k)
    m = np.arange(T)
    c["causal"] = np.where(row - m[None, :] + 3 * P >= 0, 0.0, NEG)
    pairs, grid = DH // 4, 64
    inv = 10000.0 ** (-np.arange(pairs, dtype=np.float32) / np.float32(pairs)).astype(np.float32)
    tok = np.arange(T)
    spot = np.stack([tok // grid, tok % grid]).astype(np.float32)
    feat = i % DH
    ang = spot[feat // 32] * inv.astype(np.float32)[feat % pairs][:, None]
    c["rope_cos"], c["rope_sin"] = np.cos(ang), np.sin(ang)
    swap = np.zeros((P, P))
    for f in range(P):
        other = f + pairs if f % 32 < pairs else f - pairs
        swap[other, f] = -1.0 if f % 32 < pairs else 1.0
    c["rope_swap"] = swap
    c["any_cmp"] = (row + P * np.arange(TT)[None, :]) >= CMP_BLOCK - 1
    c["gdn_scale"] = np.full((P, 1), float(P) ** -0.5)
    c["eps"] = np.full((P, 1), EPS)
    c["eps_2"] = np.full((P, 1), EPS_2)
    c["lane"] = row
    c["lanes_on"] = row + P * np.arange(TT)[None, :]
    c["experts"] = np.broadcast_to(np.arange(EXPERTS), (P, EXPERTS))
    c["blocks"] = np.broadcast_to(np.arange(SLOTS_MAX + 1), (P, SLOTS_MAX + 1))
    c["one"] = np.ones((P, 1))
    return {k: np.ascontiguousarray(v, dtype=np.float32) for k, v in c.items()}


def bucket_rows():
    dist = 3 * P + P - 1 - np.arange(SKEW)
    half = REL_BUCKETS // 2
    d = np.maximum(dist, 1).astype(np.float32)
    log_b = half + (np.log(d / np.float32(half)) / np.float32(math.log(REL_MAX_DIST / half))
                    * np.float32(REL_BUCKETS - half)).astype(np.int32)
    bucket = np.where(dist < half, np.maximum(dist, 0), np.clip(log_b, half, REL_BUCKETS - 1))
    rows = np.zeros((REL_BUCKETS + 1, SKEW), np.float32)
    rows[bucket, np.arange(SKEW)] = dist >= 0
    rows[REL_BUCKETS] = dist < 0
    return rows


def places(named):
    found, n = {}, 0
    for name, a in named.items():
        found[name] = (n, a.shape[1])
        n += a.shape[1]
    return found, n


CONST_AT, CONST_N = places(constants())
PARAM_COLUMNS = {
    "attn_norm": 8, "ffn_norm": 8, "q_norm": 1, "k_norm_cmp": 1, "k_norm_slc": 1, "k_norm_win": 1,
    "cmp_pe_k": CMP_PAIRS, "cmp_b1_k": 2, "cmp_pe_v": CMP_PAIRS, "cmp_b1_v": 2,
    "conv_w": 3 * 2 * FF_CHUNKS, "conv_b": 2 * FF_CHUNKS,
    "b_gate": 32, "conv_qkv": GDN_CONV * GDN_QKV, "gdn_norm": 1, "conv_dw": CONV_K * 4,
    "conv_dw_bias": 4, "conv_ln_g": 4, "conv_ln_b": 4, "b_ple_gate": 8, "ln_g": 8, "ln_b": 8,
    "c": 16, "b_ada": 48, "attn_norm_w": 8, "q_norm_w": 2, "kv_norm_w": 1, "subln_w": 1,
    "ffn_norm_w": 8, "final_norm_w": 8, "lambdas": 4,
}
PARAM_AT, PARAM_N = {}, 0
for _name, _n in PARAM_COLUMNS.items():
    PARAM_AT[_name] = (PARAM_N, _n)
    PARAM_N += _n



def feature_norm(k, name, groups, matrix, scale, eps, shift=None):
    nc = k.nc
    results = [o for _, out, _ in groups for o in out]
    flat = [(g, n) for g, (src, _, _) in enumerate(groups) for n in range(len(src))]
    width = [src[0].shape[-1] for src, _, _ in groups]
    with k.stage(name) as (sb, sem):
        sq = sb("sq", [P, 3, T])
        std = sb("std", [P, 2, T])
        rstd = sb("rstd", [P, 2, T])
        squared, summed, rooted, turned, scaled, shifted = (
            sem(x) for x in ("squared", "summed", "rooted", "turned", "scaled", "shifted"))
        with nc.Block() as block:
            @block.scalar
            def _(act):
                done = 0
                for g, (src, _, _) in enumerate(groups):
                    for s in src:
                        if done >= 3:
                            act.wait_ge(summed, done - 2)
                        act.activation(sq[:, done % 3, 0:width[g]], s, ACT.Square).then_inc(squared, 1)
                        done += 1
                    act.wait_ge(summed, done)
                    if g >= 2:
                        act.wait_ge(turned, g - 1)
                    act.activation(std[:, g % 2, 0:width[g]], k.bank(g % 2, width[g]), ACT.Sqrt,
                                   bias=k.c(eps), scale=scale).then_inc(rooted, 1)
                for n, o in enumerate(results if shift else []):
                    act.wait_ge(scaled, n + 1)
                    act.activation(o, o, ACT.Identity, bias=shift[n]).then_inc(shifted, 1)

            @block.tensor
            def _(pe):
                for n, (g, s) in enumerate(flat):
                    pe.wait_ge(squared, n + 1)
                    if s == 0 and g >= 2:
                        pe.wait_ge(rooted, g - 1)
                    pe.matmul(k.bank(g % 2, width[g]), matrix, sq[:, n % 3, 0:width[g]], start=(s == 0),
                              stop=(s == len(groups[g][0]) - 1)).then_inc(summed, 1)

            @block.vector
            def _(dve):
                for g, (src, out, gain) in enumerate(groups):
                    dve.wait_ge(rooted, g + 1)
                    r = rstd[:, g % 2, 0:width[g]]
                    dve.reciprocal(r, std[:, g % 2, 0:width[g]]).then_inc(turned, 1)
                    dve.wait_ge(turned, g + 1)
                    for n, s in enumerate(src):
                        if gain is None:
                            dve.tensor_tensor(out[n], s, r, ALU.mult).then_inc(scaled, 1)
                        else:
                            dve.scalar_tensor_tensor(out[n], s, gain[n], r, ALU.mult,
                                                     ALU.mult).then_inc(scaled, 1)


class Section:

    def __init__(self, weights, units, kc, source, finish, engine, chunks=4, width=T, by_tokens=False, rows=P):
        self.weights, self.units, self.kc, self.source = weights, units, kc, source
        self.finish, self.engine, self.chunks = finish, engine, chunks
        self.width, self.by_tokens, self.rows = width, by_tokens, rows
        self.columns = width if by_tokens else chunks * P


def run_units(eng, units, start, body):
    pairs = units // 2
    if pairs >= 2:
        with eng.Fori(0, pairs) as i:
            for s in range(2):
                body(2 * i + s, (start + s) % 2, i)
    else:
        pairs = 0
    for u in range(2 * pairs, units):
        body(u, (start + u) % 2, u // 2)


def project(k, name, sections, beside=None):
    nc = k.nc
    starts, landed0, done0 = [], [], []
    n, lands, dones = 0, [0, 0], [0, 0]
    for s in sections:
        starts.append(n)
        landed0.append(list(lands))
        done0.append(list(dones))
        for u in range(s.units):
            lands[(n + u) % 2] += 1
            dones[(n + u) % 2] += s.chunks
        n += s.units
    size = max(s.kc * s.columns for s in sections)
    with k.stage(name) as (sb, sem):
        ring = sb("weights", [P, 2, size])
        landed = [sem(f"weights{i}_landed") for i in range(2)]
        ready = [sem(f"sums{i}_ready") for i in range(2)]
        emptied = [sem(f"banks{i}_emptied") for i in range(2)]
        with nc.Block() as block:
            @block.sync
            def _(sp):
                for q, s in enumerate(sections):
                    def load(u, slot, turn, q=q, s=s):
                        sp.wait_ge(emptied[slot], turn * s.chunks + done0[q][slot])
                        src = s.weights[u, :, :] if isinstance(u, int) else \
                            s.weights[bass.ds(u, 1), :, :].rearrange("a p n -> p (a n)")
                        sp.dma_start(ring[:, slot, 0:s.kc * s.columns], src).then_inc(landed[slot], 16)
                    run_units(sp, s.units, starts[q], load)

            @block.tensor
            def _(pe):
                for q, s in enumerate(sections):
                    def products(u, slot, turn, q=q, s=s):
                        w = ring[:, slot, 0:s.kc * s.columns].rearrange("p (k n) -> p k n", k=s.kc)
                        pe.wait_ge(landed[slot], turn * 16 + 16 * landed0[q][slot] + 16)
                        pe.wait_ge(emptied[slot], turn * s.chunks + done0[q][slot])
                        for j in range(s.chunks):
                            out = k.bank(4 * slot + j, s.width)[0:s.rows, :]
                            for kk in range(s.kc):
                                if s.by_tokens:
                                    left, right = s.source[:, kk, j * P:j * P + s.rows], w[:, kk, :]
                                else:
                                    left, right = w[:, kk, j * P:(j + 1) * P], s.source[:, kk, 0:s.width]
                                last = pe.matmul(out, left, right, start=(kk == 0), stop=(kk == s.kc - 1))
                            last.then_inc(ready[slot], 1)
                    run_units(pe, s.units, starts[q], products)

            def empty(eng, engine):
                for q, s in enumerate(sections):
                    def take(u, slot, turn, q=q, s=s):
                        for j in range(s.chunks):
                            eng.wait_ge(ready[slot], turn * s.chunks + done0[q][slot] + j + 1)
                            s.finish(eng, u * s.chunks + j, k.bank(4 * slot + j, s.width)[0:s.rows, :]).then_inc(emptied[slot], 1)
                    if s.engine == engine:
                        run_units(eng, s.units, starts[q], take)

            @block.scalar
            def _(act):
                empty(act, "scalar")

            @block.vector
            def _(dve):
                empty(dve, "vector")
                if beside is not None:
                    beside(dve, sem)


def copies_to(dst):
    return lambda eng, n, ps: eng.tensor_copy(at(dst, n), ps)


def adds_to(dst):
    return lambda eng, n, ps: eng.tensor_tensor(at(dst, n), ps, at(dst, n), ALU.add)


def activates_to(dst, func, bias=None):
    def finish(eng, n, ps):
        if bias is None:
            return eng.activation(at(dst, n), ps, func)
        return eng.activation(at(dst, n), ps, func, bias=col(bias, n))
    return finish


class Unit:

    def __init__(self, products, keys, bias, gate, tiles, out, group, opens, closes):
        self.products, self.keys, self.bias, self.gate = products, keys, bias, gate
        self.tiles, self.out, self.group, self.opens, self.closes = tiles, out, group, opens, closes


def attention(k, name, rounds, copies, units, results, gating=False):
    nc, U = k.nc, len(units)
    wide = max(u.keys for u in units) > BANK
    turn_buffers = 1 if wide else 2
    keys_max = max(u.keys for u in units)
    closing = {u.group: n for n, u in enumerate(units)}
    G = len(closing)
    n_copies = len(copies(0))
    assert U % 2 == 0
    with k.stage(name) as (sb, sem):
        masked_sb = sb("masked", [P, 2, keys_max])
        probs = sb("probs", [P, 2, keys_max])
        top = sb("top", [P, 2])
        total = sb("total", [P, 2])
        inverse = sb("inverse", [P, 2])
        diag = sb("diag", [P, 2, P])
        turned_sb = sb("turned", [P, 2, -(-keys_max // P) * P])
        staged, scored, masked, exped, inverted, weighed, turned, copied, summed, taken, passed = (sem(x) for x in (
            "operands_staged", "scores_ready", "scores_masked", "probs_ready", "sums_inverted", "weights_ready",
            "probs_turned", "probs_copied", "values_summed", "results_taken", "waits_passed"))

        def scores_bank(n):
            return k.psum[:, (n % 2) * 2 * BANK:(n % 2) * 2 * BANK + 2 * BANK]

        def turned_bank(n):
            return k.psum[:, (4 + (n % 2 if not wide else 0)) * BANK:(5 + (n % 2) if not wide else 6) * BANK]

        def out_bank(g, u):
            lo, hi = u.out
            return k.psum[lo:hi, (6 + g % 2) * BANK:(6 + g % 2) * BANK + P]

        def loop(eng, body):
            with eng.Fori(0, rounds) as i:
                body(i)

        with nc.Block() as block:
            @block.gpsimd
            def _(pool):
                def body(i):
                    pool.wait_ge(summed, i * U)
                    pool.wait_ge(weighed, i * U)
                    for dst, src in copies(i):
                        pool.tensor_copy(dst, src).then_inc(staged, 1)
                loop(pool, body)

            @block.tensor
            def _(pe):
                def body(i):
                    pe.wait_ge(staged, i * n_copies + n_copies)
                    for step in range(U + 2):
                        if step < U:
                            u = units[step]
                            if step >= 2:
                                pe.wait_ge(masked, i * U + step - 1)
                            for m, (left, right) in enumerate(u.products):
                                for lo in range(0, u.keys, BANK):
                                    hi = min(lo + BANK, u.keys)
                                    last = pe.matmul(scores_bank(step)[:, lo:hi], left, right[:, lo:hi],
                                                     start=(m == 0), stop=(m == len(u.products) - 1))
                            last.then_inc(scored, 1)
                        v = step - 1
                        if 0 <= v < U:
                            u = units[v]
                            pe.wait_ge(weighed, i * U + v + 1)
                            if v >= turn_buffers:
                                pe.wait_ge(copied, i * U + v + 1 - turn_buffers)
                            for n, (lo, keys, _) in enumerate(u.tiles):
                                last = pe.matmul(turned_bank(v)[0:keys, n * P:(n + 1) * P],
                                                 probs[:, v % 2, lo:lo + keys], diag[:, v % 2, :],
                                                 start=True, stop=True)
                            last.then_inc(turned, 1)
                        w = step - 2
                        if 0 <= w < U:
                            u = units[w]
                            pe.wait_ge(copied, i * U + w + 1)
                            if u.opens and u.group >= 2:
                                pe.wait_ge(taken, i * G + u.group - 1)
                            for n, (_, keys, values) in enumerate(u.tiles):
                                last = pe.matmul(out_bank(u.group, u), values, turned_sb[0:keys, w % 2, n * P:(n + 1) * P],
                                                 start=(u.opens and n == 0), stop=(u.closes and n == len(u.tiles) - 1))
                            last.then_inc(summed, 1)
                loop(pe, body)

            @block.vector
            def _(dve):
                def body(i):
                    dve.wait_ge(staged, i * n_copies + n_copies)
                    for step in range(U + 3):
                        if step < U:
                            u, b = units[step], step % 2
                            if step >= 2:
                                dve.wait_ge(exped, i * U + step - 1)
                            wait_apart(dve, scored, i * U + step + 1, passed)
                            dve.tensor_tensor_reduce(masked_sb[:, b, 0:u.keys], scores_bank(step)[:, 0:u.keys], u.bias,
                                                     -1.0, 3.0e38, ALU.add, ALU.min, top[:, b:b + 1]).then_inc(masked, 1)
                        v = step - 1
                        if 0 <= v < U:
                            u, b = units[v], v % 2
                            dve.wait_ge(exped, i * U + v + 1)
                            dve.reciprocal(inverse[:, b:b + 1], total[:, b:b + 1]).then_inc(inverted, 1)
                            dve.wait_ge(inverted, i * U + v + 1)
                            if v >= 2:
                                dve.wait_ge(turned, i * U + v - 1)
                            dve.tensor_scalar(diag[:, b, :], k.c("ident"), inverse[:, b:b + 1], u.gate,
                                              ALU.mult, ALU.mult).then_inc(weighed, 1)
                        w = step - 3
                        if 0 <= w < U and units[w].closes and closing[units[w].group] == w:
                            dve.wait_ge(summed, i * U + w + 1)
                            g = units[w].group
                            dst = results(i, g)
                            ps = k.psum[:, (6 + g % 2) * BANK:(6 + g % 2) * BANK + P]
                            if gating:
                                dve.tensor_tensor(dst, ps, dst, ALU.mult).then_inc(taken, 1)
                            else:
                                dve.tensor_copy(dst, ps).then_inc(taken, 1)
                loop(dve, body)

            @block.scalar
            def _(act):
                def body(i):
                    for step in range(U + 2):
                        if step < U:
                            u, b = units[step], step % 2
                            act.wait_ge(masked, i * U + step + 1)
                            act.wait_ge(turned, i * U + max(step - 1, 0))
                            act.activation(probs[:, b, 0:u.keys], masked_sb[:, b, 0:u.keys], ACT.Exp, scale=-1.0,
                                           bias=top[:, b:b + 1], accum_out=total[:, b:b + 1]).then_inc(exped, 1)
                        v = step - 2
                        if 0 <= v < U:
                            u, b = units[v], v % 2
                            act.wait_ge(turned, i * U + v + 1)
                            act.wait_ge(summed, i * U + max(v - 1, 0))
                            rows = max(keys for _, keys, _ in u.tiles)
                            act.copy(turned_sb[0:rows, b, 0:len(u.tiles) * P],
                                     turned_bank(v)[0:rows, 0:len(u.tiles) * P]).then_inc(copied, 1)
                loop(act, body)



def load_inputs(k):
    nc = k.nc
    with k.stage("inputs") as (sb, sem):
        landed = sem("inputs_landed")
        with nc.Block() as block:
            @block.sync
            def _(sp):
                sp.dma_start(k.x[:, :, :], k.dram["xT"].rearrange("(k p) t -> p k t", p=P)).then_inc(landed, 16)
                sp.dma_start(k.param[:, :], k.dram["params"]).then_inc(landed, 16)
                sp.wait_ge(landed, 48)

            @block.scalar
            def _(act):
                act.dma_start(k.const[:, :], k.dram["consts"]).then_inc(landed, 16)


def bias_strips(k, strips):
    nc = k.nc
    rows = REL_BUCKETS + 1
    skewed = nc.dram_tensor("bias_skewed", (NSA_HEADS, P * (SKEW + 1)), F32, kind="Internal").ap()
    with k.stage("strips") as (sb, sem):
        bias = sb("rel_bias", [rows, NSA_HEADS])
        hot = sb("buckets", [rows, SKEW])
        spread = sb("spread", [rows, NSA_HEADS, P])
        line = sb("line", [P, 2, SKEW])
        landed, filled, spreaded, ready, copied, written, back = (sem(x) for x in (
            "inputs_landed", "mask_row_set", "bias_spread", "lines_ready", "lines_copied", "lines_written",
            "strips_landed"))
        with nc.Block() as block:
            @block.sync
            def _(sp):
                sp.dma_start(bias[0:REL_BUCKETS, :], k.dram["rel_bias"]).then_inc(landed, 16)
                sp.dma_start(hot[:, :], k.dram["buckets"]).then_inc(landed, 16)
                for h in range(NSA_HEADS):
                    sp.wait_ge(copied, 2 * h + 2)
                    sp.dma_start(skewed[h].rearrange("(p w) -> p w", w=SKEW + 1)[:, 0:SKEW],
                                 line[:, h % 2, :]).then_inc(written, 16)
                    sp.wait_ge(written, 16 * h + 16)
                    sp.dma_start(strips[:, h, :], skewed[h, P - 1:P - 1 + P * SKEW].rearrange("(p w) -> p w", w=SKEW)
                                 [:, 0:STRIP]).then_inc(back, 16)
                sp.wait_ge(back, 16 * NSA_HEADS)

            @block.vector
            def _(dve):
                dve.memset(bias[REL_BUCKETS:rows, :], NEG).then_inc(filled, 1)
                dve.wait_ge(filled, 1)
                dve.wait_ge(landed, 32)
                for h in range(NSA_HEADS):
                    dve.tensor_scalar(spread[:, h, :], k.c("ones")[0:rows, :], bias[:, h:h + 1], None,
                                      ALU.mult).then_inc(spreaded, 1)
                for h in range(NSA_HEADS):
                    if h >= 2:
                        dve.wait_ge(written, 16 * h - 16)
                    for half in range(2):
                        dve.wait_ge(ready, 2 * h + half + 1)
                        dve.tensor_copy(line[:, h % 2, half * BANK:(half + 1) * BANK],
                                        k.bank(2 * (h % 2) + half)).then_inc(copied, 1)

            @block.tensor
            def _(pe):
                for h in range(NSA_HEADS):
                    pe.wait_ge(spreaded, h + 1)
                    if h >= 2:
                        pe.wait_ge(copied, 2 * h - 2)
                    for half in range(2):
                        pe.matmul(k.bank(2 * (h % 2) + half), spread[:, h, :], hot[:, half * BANK:(half + 1) * BANK],
                                  start=True, stop=True).then_inc(ready, 1)


def first_norm(k, src, out, gain, name, eps="eps"):
    feature_norm(k, name, [([src[:, n, :] for n in range(KD)], [out[:, n, :] for n in range(KD)],
                            [k.p(gain, n) for n in range(KD)])], k.c("ones"), 1.0 / D, eps)


def twice(k, name, pairs):
    with k.stage(name) as (sb, sem):
        moved = sem("copies_moved")
        with k.nc.Block() as block:
            @block.sync
            def _(sp):
                for dst, src in pairs:
                    sp.dma_start(dst, src).then_inc(moved, 16)
                sp.wait_ge(moved, 16 * len(pairs))


def compress(k, raw_kc, raw_vc, k_cmp, v_cmp):
    nc = k.nc
    N = NSA_GROUPS * NCMP
    with k.stage("compress") as (sb, sem):
        pairs = [sb(f"pairs_{x}", [P, NSA_GROUPS, T]) for x in "kv"]
        w1 = [sb(f"w1_{x}", [P, CMP_PAIRS, CMP_HIDDEN]) for x in "kv"]
        w2k = sb("w2_k", [P, 2, P])
        w2v = sb("w2_v", [P, 2, DH])
        hid = [sb(f"hidden_{x}", [P, 2, N]) for x in "kv"]
        bias = sb("bias", [P, 4])
        landed, cleared, hidden, based, gelued, outs, copied = (sem(x) for x in (
            "inputs_landed", "ends_cleared", "hidden_ready", "bias_ready", "hidden_gelued", "outputs_ready",
            "outputs_copied"))
        raws = (raw_kc, raw_vc)
        with nc.Block() as block:
            @block.sync
            def _(sp):
                sp.wait_ge(cleared, 2)
                for n in range(2):
                    for g in range(NSA_GROUPS):
                        sp.dma_start(pairs[n][0:DH, g, :], raws[n][g * DH:(g + 1) * DH, :]).then_inc(landed, 16)
                        sp.dma_start(pairs[n][DH:P, g, 0:T - 1],
                                     raws[n][g * DH:(g + 1) * DH, 1:T]).then_inc(landed, 16)
                    sp.dma_start(w1[n][:, :, :], k.dram[f"cmp_w1_{'kv'[n]}"].rearrange("(j p) n -> p j n", p=P)
                                 ).then_inc(landed, 16)
                sp.dma_start(w2k[:, :, :], k.dram["cmp_w2_k"].rearrange("(c p) n -> p c n", p=P)).then_inc(landed, 16)
                sp.dma_start(w2v[:, :, :], k.dram["cmp_w2_v"].rearrange("(c p) n -> p c n", p=P)).then_inc(landed, 16)

            @block.gpsimd
            def _(pool):
                for n in range(2):
                    pool.memset(pairs[n][:, :, T - 1:T], 0.0).then_inc(cleared, 1)

            @block.tensor
            def _(pe):
                pe.wait_ge(landed, 16 * 12)
                for n in range(2):
                    for c in range(2):
                        b = 2 * n + c
                        pe_col = k.p(f"cmp_pe_{'kv'[n]}")
                        for j in range(CMP_PAIRS):
                            pe.matmul(k.bank(b, N), w1[n][:, j, c * P:(c + 1) * P],
                                      pairs[n][:, :, 2 * j:2 * j + CMP_STRIDE * (NCMP - 1) + 1:CMP_STRIDE],
                                      start=(j == 0), stop=(j == CMP_PAIRS - 1))
                        for j in range(CMP_PAIRS):
                            last = pe.matmul(k.psum[:, (4 + b) * BANK:(4 + b) * BANK + 1], w1[n][:, j, c * P:(c + 1) * P],
                                             pe_col[:, j:j + 1], start=(j == 0), stop=(j == CMP_PAIRS - 1))
                        last.then_inc(hidden, 1)
                pe.wait_ge(gelued, 4)
                for c in range(2):
                    last = pe.matmul(k.bank(0, N), w2k[:, c, :], hid[0][:, c, :], start=(c == 0), stop=(c == 1))
                last.then_inc(outs, 1)
                for g in range(NSA_GROUPS):
                    for c in range(2):
                        last = pe.matmul(k.psum[0:NCMP, (1 + g) * BANK:(1 + g) * BANK + DH],
                                         hid[1][:, c, g * NCMP:(g + 1) * NCMP], w2v[:, c, :],
                                         start=(c == 0), stop=(c == 1))
                    last.then_inc(outs, 1)

            @block.vector
            def _(dve):
                for n in range(2):
                    for c in range(2):
                        b = 2 * n + c
                        dve.wait_ge(hidden, b + 1)
                        dve.tensor_tensor(bias[:, b:b + 1], k.psum[:, (4 + b) * BANK:(4 + b) * BANK + 1],
                                          k.p(f"cmp_b1_{'kv'[n]}", c), ALU.add).then_inc(based, 1)
                dve.wait_ge(outs, 1)
                dve.tensor_copy(k_cmp[:, :, :].rearrange("p g n -> p (g n)"), k.bank(0, N)).then_inc(copied, 1)
                for g in range(NSA_GROUPS):
                    dve.wait_ge(outs, 2 + g)
                    dve.tensor_copy(v_cmp[0:NCMP, g, :], k.psum[0:NCMP, (1 + g) * BANK:(1 + g) * BANK + DH]
                                    ).then_inc(copied, 1)

            @block.scalar
            def _(act):
                for n in range(2):
                    for c in range(2):
                        b = 2 * n + c
                        act.wait_ge(based, b + 1)
                        act.activation(hid[n][:, c, :], k.bank(b, N), ACT.Gelu_apprx_tanh,
                                       bias=bias[:, b:b + 1]).then_inc(gelued, 1)


def sparse_attention(k, q, k_cmp, v_cmp, k_slc, k_win, v_both, gates, strips, out):
    for g in range(NSA_GROUPS):
        with ExitStack() as ctx:
            def sb(what, shape):
                return ctx.enter_context(k.nc.sbuf_tensor(f"nsa{g}_{what}", shape, F32))

            qs = sb("q", [P, T])
            strip = sb("strip", [P, 2, STRIP])
            gate = sb("gate", [P, TT, 2, 3])

            def copies(i, g=g):
                h = 4 * g + 2 * i
                pair = 2 * g + i
                return [(qs[:, :], at(q, pair)),
                        (strip[:, :, :], strips[:, h:h + 2, :] if isinstance(i, int) else strips[:, bass.ds(h, 2), :]),
                        (gate[:, :, :, :], gates[:, :, h:h + 2, :] if isinstance(i, int) else gates[:, :, bass.ds(h, 2), :])]

            units = []
            for t in range(TT):
                keys = (t + 1) * P
                lo = 3 * P - t * P
                for h in range(2):
                    half = slice(h * DH, (h + 1) * DH)
                    query = qs[half, t * P:(t + 1) * P]
                    first = lo + CMP_BLOCK - 1
                    units.append(Unit([(query, k_cmp[half, g, :])], NCMP,
                                      strip[:, h, first:first + CMP_STRIDE * (NCMP - 1) + 1:CMP_STRIDE],
                                      gate[:, t, h, 0:1], [(0, NCMP, v_cmp[0:NCMP, g, :])],
                                      (h * DH, (h + 1) * DH), t, True, False))
                    for b, keys_of in ((1, k_slc), (2, k_win)):
                        units.append(Unit([(query, keys_of[half, g, 0:keys])], keys, strip[:, h, lo:lo + keys],
                                          gate[:, t, h, b:b + 1],
                                          [(n * P, P, v_both[:, n, (b - 1) * P + g * DH:(b - 1) * P + (g + 1) * DH])
                                           for n in range(t + 1)],
                                          (h * DH, (h + 1) * DH), t, False, b == 2))

            def results(i, t, g=g):
                return at(out, 2 * g + i)[:, t * P:(t + 1) * P]

            attention(k, f"nsa{g}", 2, copies, units, results)


def spatial_gate(k, u, v, out):
    nc = k.nc
    G, chunks = 8, T // P
    with k.stage("sgu") as (sb, sem):
        w = sb("w", [P, G, P])
        gain = sb("gain", [P, T])
        b = sb("b", [P, G // 2, P])
        junk = sb("squares", [P, T])
        mean = sb("mean", [P, chunks])
        root = sb("root", [P, chunks])
        rstd = sb("rstd", [P, chunks])
        z = sb("z", [P, 2, T])
        landed, masked, squared, rooted, turned, scaled, mixed, biased, gated = (sem(x) for x in (
            "inputs_landed", "w_masked", "v_squared", "v_rooted", "rstd_ready", "v_scaled", "z_ready", "z_biased",
            "results_ready"))
        with nc.Block() as block:
            @block.sync
            def _(sp):
                sp.dma_start(w[:, :, :], k.dram["sgu_wT"].rearrange("j (g i) -> j g i", g=G)).then_inc(landed, 16)
                sp.dma_start(gain[:, :], k.dram["sgu_norm"][0:1, :].broadcast_to([P, T])).then_inc(landed, 16)
                for g in range(G):
                    sp.dma_start(b[(g % 2) * DH:(g % 2 + 1) * DH, g // 2, :],
                                 k.dram["sgu_b"][g:g + 1, :].broadcast_to([DH, P])).then_inc(landed, 16)

            @block.scalar
            def _(act):
                for c in range(chunks):
                    if c:
                        act.wait_ge(squared, c)
                    act.activation(junk[:, :], v[:, c, :], ACT.Square, accum_out=mean[:, c:c + 1]).then_inc(squared, 1)
                act.wait_ge(squared, chunks)
                act.activation(root[:, :], mean[:, :], ACT.Sqrt, bias=k.c("eps"), scale=1.0 / T).then_inc(rooted, 1)

            @block.vector
            def _(dve):
                dve.wait_ge(landed, 16 * (2 + G))
                for g in range(G):
                    dve.tensor_tensor(w[:, g, :], w[:, g, :], k.c("upto")[:, 0:P], ALU.mult).then_inc(masked, 1)
                dve.wait_ge(rooted, 1)
                dve.reciprocal(rstd[:, :], root[:, :]).then_inc(turned, 1)
                dve.wait_ge(turned, 1)
                for c in range(chunks):
                    dve.scalar_tensor_tensor(v[:, c, :], v[:, c, :], rstd[:, c:c + 1], gain[:, :], ALU.mult,
                                             ALU.mult).then_inc(scaled, 1)
                for n in range(G // 2):
                    dve.wait_ge(mixed, n + 1)
                    zn = z[:, n % 2, :]
                    if n >= 2:
                        dve.wait_ge(gated, n - 1)
                    dve.tensor_tensor(zn.rearrange("p (c i) -> p c i", c=chunks),
                                      k.bank(n).rearrange("p (c i) -> p c i", c=chunks),
                                      b[:, n:n + 1, :].broadcast_to([P, chunks, P]), ALU.add).then_inc(biased, 1)
                    dve.wait_ge(biased, n + 1)
                    dve.tensor_tensor(out[:, n, :], zn, u[:, n, :], ALU.mult).then_inc(gated, 1)

            @block.tensor
            def _(pe):
                pe.wait_ge(masked, G)
                pe.wait_ge(scaled, chunks)
                for n in range(G // 2):
                    for h in range(2):
                        g = 2 * n + h
                        for c in range(chunks):
                            last = pe.matmul(k.psum[h * DH:(h + 1) * DH, n * BANK + c * P:n * BANK + (c + 1) * P],
                                             v[:, c, g * DH:(g + 1) * DH], w[:, g, :], start=True, stop=True)
                    last.then_inc(mixed, 1)


def feed_forward_up(k, src, act_out):
    nc = k.nc
    units, taps = FF_CHUNKS, 3
    with k.stage("ff_up") as (sb, sem):
        ring = sb("weights", [P, 2, KD * 2 * P])
        conv = sb("conv", [P, 4, T])
        gate = sb("gate", [P, 2, T])
        landed, ready, based, tapped, silued, done = ([sem(f"{x}{i}") for i in range(2)] for x in (
            "weights_landed", "sums_ready", "last_tap", "taps_added", "gate_ready", "unit_done"))
        own = [sem(f"tap_written{i}") for i in range(2)]

        def pairs(eng, body):
            with eng.Fori(0, units // 2) as i:
                for s in range(2):
                    body(i, s, 2 * i + s)

        with nc.Block() as block:
            @block.sync
            def _(sp):
                def body(i, s, n):
                    sp.wait_ge(ready[s], 2 * i)
                    sp.dma_start(ring[:, s, :], k.dram["w_up"][bass.ds(n, 1), :, :].rearrange("a p n -> p (a n)")
                                 ).then_inc(landed[s], 16)
                pairs(sp, body)

            @block.tensor
            def _(pe):
                def body(i, s, n):
                    w = ring[:, s, :].rearrange("p (k n) -> p k n", k=KD)
                    pe.wait_ge(landed[s], 16 * i + 16)
                    pe.wait_ge(tapped[s], 2 * i)
                    for j in range(2):
                        for kk in range(KD):
                            last = pe.matmul(k.bank(2 * s + j), w[:, kk, j * P:(j + 1) * P], src[:, kk, :],
                                             start=(kk == 0), stop=(kk == KD - 1))
                        last.then_inc(ready[s], 1)
                pairs(pe, body)

            @block.scalar
            def _(act):
                w, b = k.p("conv_w"), k.p("conv_b")

                def body(i, s, n):
                    act.wait_ge(done[s], i)
                    for j in range(2):
                        act.wait_ge(ready[s], 2 * i + j + 1)
                        act.activation(conv[:, 2 * s + j, :], k.bank(2 * s + j), ACT.Identity,
                                       bias=col(b, 2 * n + j), scale=col(w, 2 * 2 * FF_CHUNKS + 2 * n + j)
                                       ).then_inc(based[s], 1)
                    act.wait_ge(tapped[s], 2 * i + 2)
                    act.activation(gate[:, s, :], conv[:, 2 * s + 1, :], ACT.Silu).then_inc(silued[s], 1)
                pairs(act, body)

            @block.vector
            def _(dve):
                w = k.p("conv_w")

                def body(i, s, n):
                    for j in range(2):
                        dve.wait_ge(based[s], 2 * i + j + 1)
                        c, ps = conv[:, 2 * s + j, :], k.bank(2 * s + j)
                        dve.scalar_tensor_tensor(c[:, 1:T], ps[:, 0:T - 1], col(w, 2 * FF_CHUNKS + 2 * n + j), c[:, 1:T],
                                                 ALU.mult, ALU.add).then_inc(own[s], 1)
                        dve.wait_ge(own[s], 2 * i + j + 1)
                        dve.scalar_tensor_tensor(c[:, 2:T], ps[:, 0:T - 2], col(w, 2 * n + j), c[:, 2:T],
                                                 ALU.mult, ALU.add).then_inc(tapped[s], 1)
                    dve.wait_ge(silued[s], i + 1)
                    dve.tensor_tensor(at(act_out, n), gate[:, s, :], conv[:, 2 * s, :], ALU.mult).then_inc(done[s], 1)
                pairs(dve, body)


def first_block(k):
    with ExitStack() as ctx:
        def sb(what, shape):
            return ctx.enter_context(k.nc.sbuf_tensor(what, shape, F32))

        first_norm(k, k.x, k.h, "attn_norm", "attn_norm")
        with ExitStack() as mixers:
            def mx(what, shape):
                return mixers.enter_context(k.nc.sbuf_tensor(what, shape, F32))
            u = mx("sgu_u", [P, 4, T])
            v = mx("sgu_v", [P, TT, T])
            q = mx("nsa_q", [P, 4, T])
            raw = mx("nsa_raw", [P, 4, T])
            v_both = mx("nsa_v", [P, TT, 2 * P])
            gates = mx("nsa_gates", [P, TT, NSA_HEADS, 3])
            k_cmp = mx("nsa_k_cmp", [P, NSA_GROUPS, NCMP])
            v_cmp = mx("nsa_v_cmp", [NCMP, NSA_GROUPS, DH])
            k_slc = mx("nsa_k_slc", [P, NSA_GROUPS, T])
            k_win = mx("nsa_k_win", [P, NSA_GROUPS, T])

            def values_and_gates(eng, n, ps):
                return eng.tensor_copy(v_both[:, n, :], ps)

            def gate(eng, n, ps):
                return eng.activation(gates[:, n, :, :].rearrange("p h b -> p (h b)"), ps, ACT.Sigmoid)

            project(k, "proj1", [
                Section(k.dram["w_in_q"], 1, KD, k.h, copies_to(q), "vector"),
                Section(k.dram["w_in_k"], 1, KD, k.h, copies_to(raw), "vector"),
                Section(k.dram["w_in_v"], 1, KD, k.h, values_and_gates, "vector", chunks=TT, width=2 * P, by_tokens=True),
                Section(k.dram["w_in_g"], 1, KD, k.h, gate, "scalar", chunks=TT, width=3 * NSA_HEADS, by_tokens=True),
                Section(k.dram["w_in_u"], 1, KD, k.h, activates_to(u, ACT.Gelu_apprx_tanh), "scalar"),
                Section(k.dram["w_in_sv"], 1, KD, k.h, activates_to(v, ACT.Gelu_apprx_tanh), "scalar", chunks=TT,
                        by_tokens=True),
            ])
            spatial_gate(k, u, v, k.h[:, 4:8, :])
            compress(k, raw[:, 0, :], raw[:, 1, :], k_cmp, v_cmp)
            with k.stage("nsa_gains") as (sb2, sem):
                made = sem("gains_made")
                q_gain = mx("nsa_q_gain", [P, 1])
                with k.nc.Block() as block:
                    @block.vector
                    def _(dve):
                        dve.tensor_scalar(q_gain[:, :], k.p("q_norm"), DH ** -0.5, None, ALU.mult).then_inc(made, 1)
                        first = gates[:, 0, :, 0:1]
                        dve.tensor_scalar(first, first, k.c("any_cmp")[:, 0:1], None, ALU.mult).then_inc(made, 1)
                        dve.wait_ge(made, 2)
            cmp_flat = k_cmp[:, :, :].rearrange("p g n -> p (g n)")
            feature_norm(k, "nsa_norm",
                         [([q[:, n, :]], [q[:, n, :]], [q_gain[:, :]]) for n in range(4)]
                         + [([raw[:, 2, :]], [raw[:, 2, :]], [k.p("k_norm_slc")]),
                            ([raw[:, 3, :]], [raw[:, 3, :]], [k.p("k_norm_win")]),
                            ([cmp_flat], [cmp_flat], [k.p("k_norm_cmp")])],
                         k.c("halves"), 1.0 / DH, "eps")
            twice(k, "nsa_keys", [(dst[h * DH:(h + 1) * DH, g, :], raw[g * DH:(g + 1) * DH, n, :])
                                  for dst, n in ((k_slc, 2), (k_win, 3)) for g in range(2) for h in range(2)])
            strips = mx("nsa_strips", [P, NSA_HEADS, STRIP])
            bias_strips(k, strips)
            sparse_attention(k, q, k_cmp, v_cmp, k_slc, k_win, v_both, gates, strips, k.h)
        project(k, "out1", [Section(k.dram["w_out"], 2, KD, k.h, adds_to(k.x), "vector")])
        first_norm(k, k.x, k.h, "ffn_norm", "ffn_norm")
        hidden = sb("ff_hidden", [P, FF_CHUNKS, T])
        feed_forward_up(k, k.h, hidden)
        project(k, "down1", [Section(k.dram["w_down"], KD, FF_CHUNKS, hidden, adds_to(k.x), "vector", chunks=1)])



def feature_center(k, name, srcs):
    n = len(srcs)
    with k.stage(name) as (sb, sem):
        summed, centered = sem("summed"), sem("centered")
        with k.nc.Block() as block:
            @block.tensor
            def _(pe):
                for m, s in enumerate(srcs):
                    last = pe.matmul(k.bank(0), k.c("ones"), s, start=(m == 0), stop=(m == n - 1))
                last.then_inc(summed, 1)

            @block.vector
            def _(dve):
                dve.wait_ge(summed, 1)
                for s in srcs:
                    dve.scalar_tensor_tensor(s, k.bank(0), -1.0 / (n * P), s, ALU.mult, ALU.add).then_inc(centered, 1)


def gated_products(k, name, weights, loops, kc_gate, source_gate, bias, kc, source, base, out):
    nc, N = k.nc, KD
    size = (kc_gate + kc) * P
    with k.stage(name) as (sb, sem):
        ring = sb("weights", [P, 2, size])
        gate = sb("gate", [P, 2, T])
        part = sb("part", [P, 2, T])
        landed, ready, opened, timed, added = ([sem(f"{x}{i}") for i in range(2)] for x in (
            "weights_landed", "sums_ready", "gate_ready", "gated", "added"))

        def each(eng, body):
            for q in range(loops):
                with eng.Fori(0, N // 2) as i:
                    for s in range(2):
                        body(q, s, 2 * i + s, i + q * (N // 2))

        with nc.Block() as block:
            @block.sync
            def _(sp):
                def body(q, s, n, m):
                    sp.wait_ge(ready[s], 2 * m)
                    sp.dma_start(ring[:, s, :], weights[bass.ds(n + q * N, 1), :, :].rearrange("a p n -> p (a n)")
                                 ).then_inc(landed[s], 16)
                each(sp, body)

            @block.tensor
            def _(pe):
                def body(q, s, n, m):
                    w = ring[:, s, :].rearrange("p (k n) -> p k n", n=P)
                    pe.wait_ge(landed[s], 16 * m + 16)
                    pe.wait_ge(timed[s], m)
                    for j, (first, count, src) in enumerate(((0, kc_gate, source_gate), (kc_gate, kc, source(q)))):
                        for kk in range(count):
                            last = pe.matmul(k.bank(2 * s + j), w[:, first + kk, :], src[:, kk, :],
                                             start=(kk == 0), stop=(kk == count - 1))
                        last.then_inc(ready[s], 1)
                each(pe, body)

            @block.scalar
            def _(act):
                def body(q, s, n, m):
                    act.wait_ge(ready[s], 2 * m + 1)
                    act.wait_ge(timed[s], m)
                    act.activation(gate[:, s, :], k.bank(2 * s), ACT.Sigmoid, bias=col(bias, n + q * N)
                                   ).then_inc(opened[s], 1)
                each(act, body)

            @block.vector
            def _(dve):
                def body(q, s, n, m):
                    dve.wait_ge(opened[s], m + 1)
                    dve.wait_ge(ready[s], 2 * m + 2)
                    dve.tensor_tensor(part[:, s, :], k.bank(2 * s + 1), gate[:, s, :], ALU.mult).then_inc(timed[s], 1)
                    dve.wait_ge(timed[s], m + 1)
                    dve.wait_ge(added[s], m)
                    dve.tensor_tensor(at(out, n), part[:, s, :], at(base, n), ALU.add).then_inc(added[s], 1)
                each(dve, body)


def rates(k, raw, g, beta, log_f):
    nc = k.nc
    H, F = GDN_HEADS, 8
    W = H + F
    with k.stage("rates") as (sb, sem):
        bias = sb("bias", [P, 2 * H + F])
        y, mag, e, s, s2, p = (sb(x, [P, TT, W]) for x in ("y", "mag", "e", "s", "s2", "p"))
        rate = sb("rate", [P, H])
        landed, biased, exped, own, other = (sem(x) for x in (
            "biases_landed", "y_ready", "exp_ready", "vector_steps", "scalar_steps"))
        with nc.Block() as block:
            @block.sync
            def _(sp):
                sp.dma_start(bias[:, :], k.dram["rate_biases"][0:1, :].broadcast_to([P, 2 * H + F])).then_inc(landed, 16)

            @block.scalar
            def _(act):
                act.wait_ge(landed, 16)
                act.activation(rate[:, :], bias[:, W:W + H], ACT.Exp).then_inc(exped, 1)
                act.wait_ge(biased, 1)
                act.activation(mag[:, :, :], y[:, :, :], ACT.Abs).then_inc(other, 1)
                act.wait_ge(other, 1)
                act.activation(e[:, :, :], mag[:, :, :], ACT.Exp, scale=-1.0).then_inc(exped, 1)
                act.activation(beta[:, :, :], raw[:, :, H:2 * H], ACT.Sigmoid).then_inc(exped, 1)

            @block.vector
            def _(dve):
                step = Steps(dve, own)
                dve.wait_ge(landed, 16)
                step.then(dve.tensor_tensor(y[:, :, 0:H], raw[:, :, 0:H],
                                            bias[:, 0:H].unsqueeze(1).broadcast_to([P, TT, H]), ALU.add))
                step.do(dve.tensor_tensor(y[:, :, H:W], raw[:, :, 2 * H:2 * H + F],
                                          bias[:, H:W].unsqueeze(1).broadcast_to([P, TT, F]), ALU.add))
                dve.tensor_scalar(y[:, :, H:W], y[:, :, H:W], -1.0, None, ALU.mult).then_inc(biased, 1)
                dve.wait_ge(exped, 3)
                step.do(dve.tensor_scalar(s[:, :, :], e[:, :, :], 2.0, None, ALU.add))
                step.do(dve.reciprocal(s[:, :, :], s[:, :, :]))
                step.do(dve.tensor_tensor(s[:, :, :], s[:, :, :], e[:, :, :], ALU.mult))
                step.do(dve.tensor_tensor(s2[:, :, :], s[:, :, :], s[:, :, :], ALU.mult))
                step.do(dve.tensor_scalar(p[:, :, :], s2[:, :, :], 1.0 / 15, None, ALU.mult))
                for n in (13, 11, 9, 7, 5, 3):
                    step.do(dve.scalar_tensor_tensor(p[:, :, :], p[:, :, :], 1.0 / n, s2[:, :, :], ALU.add, ALU.mult))
                step.do(dve.scalar_tensor_tensor(p[:, :, :], p[:, :, :], 1.0, s[:, :, :], ALU.add, ALU.mult))
                step.do(dve.tensor_scalar(p[:, :, :], p[:, :, :], 2.0, None, ALU.mult))
                step.do(dve.scalar_tensor_tensor(p[:, :, :], y[:, :, :], 0.0, p[:, :, :], ALU.max, ALU.add))
                step.then(dve.tensor_scalar(log_f[:, :, :], p[:, :, H:W], -1.0, None, ALU.mult))
                step.do(dve.scalar_tensor_tensor(g[:, :, :], p[:, :, 0:H], -1.0,
                                                 rate[:, :].unsqueeze(1).broadcast_to([P, TT, H]), ALU.mult, ALU.mult))


def forget_rows(k, log_f, f_query, f_key):
    nc, H = k.nc, 8
    with k.stage("forget") as (sb, sem):
        row = sb("row", [H, 2, T])
        summed, copied, moved, filled = (sem(x) for x in ("sums_ready", "rows_copied", "rows_moved", "ones_filled"))
        with nc.Block() as block:
            @block.tensor
            def _(pe):
                for n in range(TT):
                    last = pe.matmul(k.psum[0:H, n * P:T], log_f[:, n, :], k.c("upto")[:, 0:T - n * P],
                                     start=(n == 0), stop=(n == TT - 1))
                last.then_inc(summed, 1)

            @block.vector
            def _(dve):
                dve.wait_ge(summed, 1)
                dve.tensor_copy(row[:, 0, :], k.psum[0:H, 0:T]).then_inc(copied, 1)
                dve.tensor_scalar(row[:, 1, :], k.psum[0:H, 0:T], -1.0, None, ALU.mult).then_inc(copied, 1)

            @block.gpsimd
            def _(pool):
                pool.memset(f_query[:, :, :], 1.0).then_inc(filled, 1)
                pool.memset(f_key[:, :, :], 1.0).then_inc(filled, 1)

            @block.sync
            def _(sp):
                sp.wait_ge(copied, 2)
                sp.wait_ge(filled, 2)
                sp.dma_start(f_query[0:1, :, :], row[:, 0, :]).then_inc(moved, 16)
                sp.dma_start(f_key[1:2, :, :], row[:, 1, :]).then_inc(moved, 16)
                sp.wait_ge(moved, 32)


def stick_breaking(k, q, keys, v, out):
    nc, pairs = k.nc, 4
    U = 2 * TT
    with k.stage("stick") as (sb, sem):
        qs, ks, vs = sb("q", [P, T]), sb("k", [P, T]), sb("v", [P, TT, P])
        mag = sb("mag", [P, 2, T])
        soft = sb("softplus", [P, 2, TT, T])
        att = sb("att", [P, 2, T])
        staged, scored, absed, exped, logged, soft_ready, summed, weighed, valued, taken, own = (sem(x) for x in (
            "operands_staged", "scores_ready", "magnitudes", "exps", "logs", "softplus_ready", "sums_ready",
            "weights_ready", "values_summed", "results_taken", "softplus_masked"))

        def cols(n):
            return slice(n * P, T)

        def loop(eng, body):
            with eng.Fori(0, pairs) as i:
                body(i)

        with nc.Block() as block:
            @block.gpsimd
            def _(pool):
                def body(i):
                    pool.wait_ge(valued, i * U)
                    pool.tensor_copy(qs[:, :], at(q, i)).then_inc(staged, 1)
                    pool.tensor_copy(ks[:, :], at(keys, i)).then_inc(staged, 1)
                    pool.tensor_copy(vs[:, :, :], v[:, :, bass.ds(i * P, P)]).then_inc(staged, 1)
                loop(pool, body)

            @block.tensor
            def _(pe):
                def body(i):
                    pe.wait_ge(staged, 3 * i + 3)

                    def scores(h):
                        half = slice(h * DH, (h + 1) * DH)
                        for n in range(TT):
                            pe.wait_ge(weighed, i * U + (n + 1 if h else 0))
                            pe.matmul(k.psum[:, n * BANK:n * BANK + T - n * P], ks[half, n * P:(n + 1) * P], qs[half, cols(n)],
                                      start=True, stop=True, skip_group_check=True).then_inc(scored, 1)

                    for h in range(2):
                        scores(h)
                        half = slice(h * DH, (h + 1) * DH)
                        pe.wait_ge(soft_ready, i * U + (h + 1) * TT)
                        for n in range(TT):
                            pe.matmul(k.psum[:, n * BANK:n * BANK + T - n * P], k.c("minus_from"), soft[:, h, n, cols(n)],
                                      start=False, stop=False, skip_group_check=True)
                            for m in range(n + 1, TT):
                                pe.matmul(k.psum[:, n * BANK + (m - n) * P:n * BANK + T - n * P], k.c("minus_ones"),
                                          soft[:, h, m, cols(m)], start=False, stop=False, skip_group_check=True)
                            pe.matmul(k.psum[:, n * BANK:n * BANK + P], k.c("ident"), k.c("not_before"),
                                      start=False, stop=True, skip_group_check=True).then_inc(summed, 1)
                        if h == 0:
                            pe.wait_ge(taken, i)
                        for n in range(TT):
                            pe.wait_ge(weighed, i * U + h * TT + n + 1)
                            pe.matmul(k.psum[half, 4 * BANK + n * P:4 * BANK + T], vs[:, n, half], att[:, n % 2, cols(n)],
                                      start=(n == 0), stop=(n == TT - 1), skip_group_check=True).then_inc(valued, 1)
                loop(pe, body)

            @block.scalar
            def _(act):
                def body(i):
                    for h in range(2):
                        for n in range(TT):
                            m, b = h * TT + n, n % 2
                            act.wait_ge(scored, i * U + m + 1)
                            act.wait_ge(soft_ready, i * U + max(m - 1, 0))
                            z = k.psum[:, n * BANK:n * BANK + T - n * P]
                            act.activation(mag[:, b, cols(n)], z, ACT.Abs).then_inc(absed, 1)
                            act.wait_ge(absed, i * U + m + 1)
                            act.activation(mag[:, b, cols(n)], mag[:, b, cols(n)], ACT.Exp, scale=-1.0).then_inc(exped, 1)
                            act.wait_ge(exped, i * U + m + 1)
                            act.activation(mag[:, b, cols(n)], mag[:, b, cols(n)], ACT.Ln, bias=k.c("one")
                                           ).then_inc(logged, 1)
                        for n in range(TT):
                            m = h * TT + n
                            act.wait_ge(summed, i * U + m + 1)
                            act.wait_ge(valued, i * U + max(m - 1, 0))
                            act.activation(att[:, n % 2, cols(n)], k.psum[:, n * BANK:n * BANK + T - n * P], ACT.Exp
                                           ).then_inc(weighed, 1)
                loop(act, body)

            @block.vector
            def _(dve):
                def body(i):
                    for h in range(2):
                        for n in range(TT):
                            m, b = h * TT + n, n % 2
                            s = soft[:, h, n, :]
                            dve.wait_ge(logged, i * U + m + 1)
                            dve.scalar_tensor_tensor(s[:, cols(n)], k.psum[:, n * BANK:n * BANK + T - n * P], 0.0,
                                                     mag[:, b, cols(n)], ALU.max, ALU.add).then_inc(own, 1)
                            dve.wait_ge(own, i * U + m + 1)
                            dve.tensor_tensor(s[:, n * P:(n + 1) * P], s[:, n * P:(n + 1) * P], k.c("before")[:, 0:P],
                                              ALU.mult).then_inc(soft_ready, 1)
                    dve.wait_ge(valued, i * U + U)
                    dve.tensor_tensor(at(out, i), k.bank(4), at(out, i), ALU.mult).then_inc(taken, 1)
                loop(dve, body)


def forgetting(k, q, keys, v, f_query, f_key, out):
    with ExitStack() as ctx:
        def sb(what, shape):
            return ctx.enter_context(k.nc.sbuf_tensor(f"fox_{what}", shape, F32))

        qs, ks, vs = sb("q", [P, T]), sb("k", [P, T]), sb("v", [P, TT, P])
        fq, fk = sb("f_query", [2, 2, T]), sb("f_key", [2, 2, T])

        def copies(i):
            heads = slice(2 * i, 2 * i + 2) if isinstance(i, int) else bass.ds(2 * i, 2)
            pair = slice(i * P, (i + 1) * P) if isinstance(i, int) else bass.ds(i * P, P)
            return [(qs[:, :], at(q, i)), (ks[:, :], at(keys, i)), (vs[:, :, :], v[:, :, pair]),
                    (fq[:, :, :], f_query[:, heads, :]), (fk[:, :, :], f_key[:, heads, :])]

        units = []
        for t in range(TT):
            n = (t + 1) * P
            lo = 3 * P - t * P
            for h in range(2):
                half = slice(h * DH, (h + 1) * DH)
                here = slice(t * P, (t + 1) * P)
                units.append(Unit([(qs[half, here], ks[half, 0:n]), (fq[:, h, here], fk[:, h, 0:n])], n,
                                  k.c("causal")[:, lo:lo + n], 1.0,
                                  [(m * P, P, vs[:, m, half]) for m in range(t + 1)], (h * DH, (h + 1) * DH), t, True, True))
        attention(k, "fox", 4, copies, units, lambda i, t: at(out, i)[:, t * P:(t + 1) * P], gating=True)


def delta_rule(k, qkv, g, beta, out):
    nc, H, C = k.nc, GDN_HEADS, GDN_CHUNK
    W = H * P
    with k.stage("delta_prepare") as (sb, sem):
        def kept(what, shape):
            return k.gdn.enter_context(nc.sbuf_tensor(f"delta_{what}", shape, F32))

        u = kept("u", [P, TT, W])
        wT = kept("w", [P, TT, W])
        q_dec = kept("q_dec", [P, H, T])
        k_dec = kept("k_dec", [P, TT, W])
        a_qk = kept("a_qk", [P, TT, W])
        g_end = kept("g_end", [P, H, T])
        with ExitStack() as inner:
            def tmp(what, shape):
                return inner.enter_context(nc.sbuf_tensor(f"delta_{what}", shape, F32))
            kv = tmp("kv", [P, 2, W])
            kb = tmp("kb", [P, W])
            vb = tmp("vb", [P, W])
            ga = tmp("ga", [P, W])
            gb = tmp("gb", [P, W])
            ex = tmp("ex", [P, 3, H])
            dec = tmp("decay", [P, 2, W])
            low = tmp("lower", [P, W])
            lev = tmp("level", [P, W])
            inv = tmp("inverse", [P, 2, W])
            mid = tmp("middle", [P, W])
            vs, ss, ps_ = sem("vector_steps"), sem("scalar_steps"), sem("tensor_steps")

            def heads(ap):
                return ap.rearrange("p (h c) -> p h c", h=H)

            def mask(name):
                return k.c(name)[:, 0:P].unsqueeze(1).broadcast_to([P, H, P])

            with nc.Block() as block:
                V_TILE, S_TILE, E_TILE = 31, 12, 21

                @block.tensor
                def _(pe):
                    for t in range(TT):
                        v0, s0 = V_TILE * t, S_TILE * t
                        here = slice(t * P, (t + 1) * P)
                        if t:
                            pe.wait_ge(vs, v0)
                            pe.wait_ge(ss, s0)
                        for n, first in ((0, GDN_HEADS), (1, 2 * GDN_HEADS)):
                            for h in range(H):
                                last = pe.transpose(k.bank(n)[:, h * P:(h + 1) * P], qkv[:, first + h, here], k.c("ident"))
                            last.then_inc(ps_, 1)
                        pe.matmul(k.psum[:, 2 * BANK:2 * BANK + H], k.c("g_upto"), g[:, t, :], start=True, stop=True)
                        pe.matmul(k.psum[:, 2 * BANK + H:2 * BANK + 2 * H], k.c("g_after"), g[:, t, :], start=True,
                                  stop=True).then_inc(ps_, 1)
                        pe.wait_ge(vs, v0 + 2)
                        for n, (left, right) in enumerate(((lambda h: k.c("g_upto"), lambda h: ga[:, h * P:(h + 1) * P]),
                                                           (lambda h: ga[:, h * P:(h + 1) * P], lambda h: k.c("g_upto")),
                                                           (lambda h: gb[:, h * P:(h + 1) * P], lambda h: k.c("g_upto")))):
                            for h in range(H):
                                last = pe.matmul(k.bank(3 + n)[:, h * P:(h + 1) * P], left(h), right(h), start=True, stop=True)
                            last.then_inc(ps_, 1)
                        for n, (left, right) in enumerate(((H, H), (H, 0))):
                            for h in range(H):
                                last = pe.matmul(k.bank(6 + n)[:, h * P:(h + 1) * P], qkv[:, left + h, here],
                                                 qkv[:, right + h, here], start=True, stop=True)
                            last.then_inc(ps_, 1)
                        for lv in range(6):
                            last_level = lv == 5
                            pe.wait_ge(vs, v0 + 13 + 3 * lv)
                            for h in range(H):
                                hs = slice(h * P, (h + 1) * P)
                                last = pe.matmul(k.bank(0)[:, hs], lev[:, hs], inv[:, 1, hs], start=True, stop=True)
                            last.then_inc(ps_, 1)
                            pe.wait_ge(ss, s0 + 7 + lv)
                            for h in range(H):
                                hs = slice(h * P, (h + 1) * P)
                                last = pe.matmul(k.bank(1)[:, hs], inv[:, 0, hs], mid[:, hs], start=True, stop=True)
                            if not last_level:
                                for h in range(H):
                                    hs = slice(h * P, (h + 1) * P)
                                    last = pe.matmul(k.bank(2)[:, hs], mid[:, hs], inv[:, 0, hs], start=True, stop=True)
                            last.then_inc(ps_, 1)
                        pe.wait_ge(vs, v0 + 29)
                        for n in range(2):
                            for h in range(H):
                                hs = slice(h * P, (h + 1) * P)
                                left, right = (inv[:, 1, hs], vb[:, hs]) if n == 0 else (kb[:, hs], inv[:, 1, hs])
                                last = pe.matmul(k.bank(3 + n)[:, hs], left, right, start=True, stop=True)
                        last.then_inc(ps_, 1)

                @block.scalar
                def _(act):
                    for t in range(TT):
                        s, e0, v0 = Steps(act, ss), E_TILE * t, V_TILE * t
                        s.n = S_TILE * t
                        if t:
                            act.wait_ge(vs, v0)
                        act.wait_ge(ps_, e0 + 3)
                        s.then(act.activation(ex[:, 0:2, :].rearrange("p a h -> p (a h)"),
                                              k.psum[:, 2 * BANK:2 * BANK + 2 * H], ACT.Exp))
                        for n in range(2):
                            act.wait_ge(ps_, e0 + 4 + n)
                            s.then(act.activation(dec[:, n, :], k.bank(3 + n), ACT.Exp))
                        act.wait_ge(ps_, e0 + 6)
                        s.then(act.activation(g_end[:, :, t * P:(t + 1) * P], heads(k.bank(5)), ACT.Exp))
                        act.wait_ge(ps_, e0 + 2)
                        s.then(act.copy(kv[:, 0, :], k.bank(0)))
                        s.then(act.copy(kv[:, 1, :], k.bank(1)))
                        for lv in range(6):
                            act.wait_ge(ps_, e0 + 9 + 2 * lv)
                            s.then(act.copy(mid[:, :], k.bank(0)))

                @block.vector
                def _(dve):
                    for t in range(TT):
                        v, e0, s0 = Steps(dve, vs), E_TILE * t, S_TILE * t
                        v.n = V_TILE * t
                        here = slice(t * P, (t + 1) * P)
                        if t:
                            dve.wait_ge(ps_, e0)
                        gt = g[:, t, :].unsqueeze(2).broadcast_to([P, H, P])
                        bt = beta[:, t, :].unsqueeze(2).broadcast_to([P, H, P])
                        v.then(dve.tensor_tensor(heads(ga[:, :]), mask("g_after"), gt, ALU.mult))
                        v.then(dve.tensor_tensor(heads(gb[:, :]), mask("ones"), gt, ALU.mult))
                        dve.wait_ge(ss, s0 + 1)
                        v.do(dve.tensor_tensor(ex[:, 2, :], ex[:, 0, :], beta[:, t, :], ALU.mult))
                        dve.wait_ge(ss, s0 + 6)
                        v.then(dve.tensor_tensor(heads(vb[:, :]), heads(kv[:, 1, :]), bt, ALU.mult))
                        v.then(dve.tensor_tensor(heads(kb[:, :]), heads(kv[:, 0, :]),
                                                 ex[:, 2, :].unsqueeze(2).broadcast_to([P, H, P]), ALU.mult))
                        v.then(dve.tensor_tensor(heads(k_dec[:, t, :]), heads(kv[:, 0, :]),
                                                 ex[:, 1, :].unsqueeze(2).broadcast_to([P, H, P]), ALU.mult))
                        v.then(dve.tensor_tensor(q_dec[:, :, here], qkv[:, 0:H, here], g_end[:, :, here], ALU.mult))
                        dve.wait_ge(ps_, e0 + 8)
                        v.do(dve.tensor_tensor(low[:, :], k.bank(6), dec[:, 0, :], ALU.mult))
                        v.then(dve.tensor_tensor(heads(low[:, :]), heads(low[:, :]), bt, ALU.mult))
                        v.do(dve.tensor_tensor(a_qk[:, t, :], k.bank(7), dec[:, 1, :], ALU.mult))
                        v.then(dve.tensor_tensor(heads(a_qk[:, t, :]), heads(a_qk[:, t, :]), mask("g_upto"), ALU.mult))
                        v.then(dve.tensor_copy(inv[:, :, :].rearrange("p a (h c) -> p (a h) c", h=H),
                                               k.c("ident").unsqueeze(1).broadcast_to([P, 2 * H, P])))
                        for lv in range(6):
                            v.settle()
                            v.then(dve.tensor_tensor(heads(lev[:, :]), heads(low[:, :]), mask(f"g_level{lv}"), ALU.mult))
                            dve.wait_ge(ps_, e0 + 10 + 2 * lv)
                            v.then(dve.tensor_tensor(inv[:, 1, :], inv[:, 1, :], k.bank(1), ALU.subtract))
                            if lv < 5:
                                v.then(dve.tensor_tensor(inv[:, 0, :], inv[:, 0, :], k.bank(2), ALU.subtract))
                        dve.wait_ge(ps_, e0 + 21)
                        v.then(dve.tensor_copy(u[:, t, :], k.bank(3)))
                        v.then(dve.tensor_copy(wT[:, t, :], k.bank(4)))
    with k.stage("delta_scan") as (sb, sem):
        state = sb("state", [P, H, P])
        fresh = sb("v_new", [P, 2, W])
        cleared, guessed, corrected, answered, learned, kept_, taken = (sem(x) for x in (
            "state_cleared", "predictions_ready", "v_new_ready", "answers_ready", "updates_ready", "state_updated",
            "answers_taken"))
        N = T // C
        with nc.Block() as block:
            @block.gpsimd
            def _(pool):
                pool.memset(state[:, :, :], 0.0).then_inc(cleared, 1)

            @block.tensor
            def _(pe):
                pe.wait_ge(cleared, 1)
                for n in range(N):
                    t, rows = n // 2, slice((n % 2) * C, (n % 2 + 1) * C)
                    tok = slice(n * C, (n + 1) * C)
                    pe.wait_ge(kept_, H * n)
                    for h in range(H):
                        hs = slice(h * P, (h + 1) * P)
                        last = pe.matmul(k.psum[rows, (n % 2) * BANK + h * P:(n % 2) * BANK + (h + 1) * P],
                                         wT[:, t, h * P + rows.start:h * P + rows.stop], state[:, h, :], start=True, stop=True)
                    last.then_inc(guessed, 1)
                    pe.wait_ge(corrected, n + 1)
                    if n >= 2:
                        pe.wait_ge(taken, n - 1)
                    for h in range(H):
                        hs = slice(h * P, (h + 1) * P)
                        o = k.psum[:, (2 + n % 2) * BANK + h * C:(2 + n % 2) * BANK + (h + 1) * C]
                        pe.matmul(o, state[:, h, :], q_dec[:, h, tok], start=True, stop=False)
                        last = pe.matmul(o, fresh[rows, n % 2, hs], a_qk[rows, t, h * P + rows.start:h * P + rows.stop],
                                         start=False, stop=True)
                    last.then_inc(answered, 1)
                    for h in range(H):
                        hs = slice(h * P, (h + 1) * P)
                        last = pe.matmul(k.bank(4 + n % 2)[:, hs], k_dec[rows, t, hs], fresh[rows, n % 2, hs],
                                         start=True, stop=True)
                    last.then_inc(learned, 1)

            @block.vector
            def _(dve):
                for n in range(N):
                    t, rows = n // 2, slice((n % 2) * C, (n % 2 + 1) * C)
                    dve.wait_ge(guessed, n + 1)
                    dve.tensor_tensor(fresh[rows, n % 2, :], u[rows, t, :], k.psum[rows, (n % 2) * BANK:(n % 2 + 1) * BANK],
                                      ALU.subtract).then_inc(corrected, 1)
                    dve.wait_ge(learned, n + 1)
                    if n:
                        dve.wait_ge(kept_, H * n)
                    for h in range(H):
                        end = (n + 1) * C - 1
                        dve.scalar_tensor_tensor(state[:, h, :], state[:, h, :], g_end[:, h, end:end + 1],
                                                 k.bank(4 + n % 2)[:, h * P:(h + 1) * P], ALU.mult, ALU.add).then_inc(kept_, 1)

            @block.scalar
            def _(act):
                for n in range(N):
                    act.wait_ge(answered, n + 1)
                    act.copy(out[:, :, n * C:(n + 1) * C],
                             k.psum[:, (2 + n % 2) * BANK:(2 + n % 2) * BANK + H * C].rearrange("p (h c) -> p h c", h=H)
                             ).then_inc(taken, 1)


def convolutions(k, qkv, wide, acc, short):
    def beside(dve, sem):
        step = Steps(dve, sem("convolution_steps"))
        w, b = k.p("conv_dw"), k.p("conv_dw_bias")
        for tap in range(CONV_K):
            step.settle()
            for n in range(4):
                x = wide[:, n, tap:tap + T]
                if tap == 0:
                    step.then(dve.tensor_scalar(acc[:, n, :], x, w[:, n:n + 1], b[:, n:n + 1], ALU.mult, ALU.add))
                else:
                    step.then(dve.scalar_tensor_tensor(acc[:, n, :], x, w[:, 4 * tap + n:4 * tap + n + 1], acc[:, n, :],
                                                       ALU.mult, ALU.add))
        w = k.p("conv_qkv")
        for tap in range(GDN_CONV):
            back = tap
            step.settle()
            for n in range(GDN_QKV):
                c = w[:, GDN_QKV * (GDN_CONV - 1 - tap) + n:GDN_QKV * (GDN_CONV - 1 - tap) + n + 1]
                if tap == 0:
                    step.then(dve.tensor_scalar(short[:, n, :], qkv[:, n, :], c, None, ALU.mult))
                else:
                    step.then(dve.scalar_tensor_tensor(short[:, n, back:T], qkv[:, n, 0:T - back], c, short[:, n, back:T],
                                                       ALU.mult, ALU.add))
        step.settle()
    return beside


def activate(k, name, func, pairs):
    with k.stage(name) as (sb, sem):
        done = sem("activated")
        with k.nc.Block() as block:
            @block.scalar
            def _(act):
                for out, src, bias in pairs:
                    if bias is None:
                        act.activation(out, src, func).then_inc(done, 1)
                    else:
                        act.activation(out, src, func, bias=bias).then_inc(done, 1)


def multiply(k, name, triples):
    with k.stage(name) as (sb, sem):
        done = sem("multiplied")
        with k.nc.Block() as block:
            @block.vector
            def _(dve):
                for out, a, b in triples:
                    dve.tensor_tensor(out, a, b, ALU.mult).then_inc(done, 1)


def second_block(k):
    nc = k.nc
    with ExitStack() as ctx:
        def sb(what, shape, stack=ctx):
            return stack.enter_context(nc.sbuf_tensor(f"second_{what}", shape, F32))

        y = sb("branches", [P, 4 * BRANCHES, T])
        g, beta, log_f = sb("g", [P, TT, GDN_HEADS]), sb("beta", [P, TT, GDN_HEADS]), sb("log_f", [P, TT, 8])
        with ExitStack() as branch_a:
            short = sb("qkv", [P, GDN_QKV, T], branch_a)
            with ExitStack() as branch_d:
                q_d, k_d, v_d = (sb(f"{x}_fox", [P, 4, T], branch_d) for x in "qkv")
                with ExitStack() as branch_c:
                    q_c, k_c, v_c = (sb(f"{x}_stick", [P, 4, T], branch_c) for x in "qkv")
                    second_projections(k, y, short, q_d, k_d, v_d, q_c, k_c, v_c, g, beta, log_f)
                    stick_breaking(k, q_c, k_c, v_c, y[:, 8:12, :])
                f_query, f_key = sb("f_query", [2, 8, T], branch_d), sb("f_key", [2, 8, T], branch_d)
                forget_rows(k, log_f, f_query, f_key)
                forgetting(k, q_d, k_d, v_d, f_query, f_key, y[:, 12:16, :])
            feature_norm(k, "delta_unit", [([short[:, n, :]], [short[:, n, :]], [k.c("gdn_scale")] if n < GDN_HEADS else None)
                                           for n in range(2 * GDN_HEADS)], k.c("ones"), 1.0, "eps")
            with ExitStack() as k.gdn:
                answers = k.h[:, 0:GDN_HEADS, :]
                delta_rule(k, short, g, beta, answers)
            feature_norm(k, "delta_norm", [([answers[:, n, :]], [answers[:, n, :]], [k.p("gdn_norm")])
                                           for n in range(GDN_HEADS)], k.c("ones"), 1.0 / P, "eps_2")
            multiply(k, "delta_gate", [(y[:, n, :], y[:, n, :], answers[:, n, :]) for n in range(GDN_HEADS)])
        merged = k.h
        with k.stage("merged") as (sb2, sem):
            cleared = sem("merged_cleared")
            with nc.Block() as block:
                @block.gpsimd
                def _(pool):
                    pool.memset(merged[:, :, :], 0.0).then_inc(cleared, 1)
        gated_products(k, "merge", k.dram["w_merge"], BRANCHES, KD, k.x, k.p("b_gate"), 4,
                       lambda q: y[:, 4 * q:4 * q + 4, :], merged, merged)

    def residual(eng, n, ps):
        return eng.scalar_tensor_tensor(at(k.x, n), at(k.x, n), ALPHA, ps, ALU.mult, ALU.add)

    project(k, "out2", [Section(k.dram["w_out_2"], 2, KD, k.h, residual, "vector")])
    with k.stage("ple_in") as (sb, sem):
        per_layer = sb("p", [P, PLE // P, T])
        landed = sem("p_landed")
        with nc.Block() as block:
            @block.sync
            def _(sp):
                sp.dma_start(per_layer[:, :, :], k.dram["pT"].rearrange("(c p) t -> p c t", p=P)).then_inc(landed, 16)
                sp.wait_ge(landed, 16)
        gated_products(k, "ple", k.dram["w_ple"], 1, KD, k.x, k.p("b_ple_gate"), PLE // P, lambda q: per_layer, k.x, k.h)
    chunks = [k.h[:, n, :] for n in range(KD)]
    feature_center(k, "ln2_center", chunks)
    feature_norm(k, "ln2", [(chunks, [k.x[:, n, :] for n in range(KD)], [k.p("ln_g", n) for n in range(KD)])],
                 k.c("ones"), 1.0 / D, "eps_2", shift=[k.p("ln_b", n) for n in range(KD)])


def second_projections(k, y, short, q_d, k_d, v_d, q_c, k_c, v_c, g, beta, log_f):
    nc = k.nc
    pad = CONV_K - 1
    acc = k.h[:, 0:4, :]
    with ExitStack() as ctx:
        def sb(what, shape):
            return ctx.enter_context(nc.sbuf_tensor(f"second_{what}", shape, F32))

        wide = sb("wide", [P, 4, pad + T])
        rate = sb("rates", [P, TT, 2 * GDN_HEADS + 8])
        lin = k.h[:, 4:8, :]

        def scaled(dst, scale):
            return lambda eng, n, ps: eng.activation(at(dst, n), ps, ACT.Copy, scale=scale)

        def plain(dst):
            return scaled(dst, 1.0)

        def silu_of(first):
            return activates_to(y[:, first:first + 4, :], ACT.Silu)

        def opened(eng, n, ps):
            return eng.activation(at(wide, n)[:, pad:pad + T], ps, ACT.Sigmoid)

        d = k.dram
        raw = [q_c, k_c, v_c]
        project(k, "proj2a", [
            Section(d["w2_glu_gate"], 1, KD, k.x, opened, "scalar"),
            Section(d["w2_glu_lin"], 1, KD, k.x, plain(lin), "scalar"),
            *[Section(d["w2_qkv_a"][n:n + 1], 1, KD, k.x, plain(raw[n]), "scalar") for n in range(3)],
        ])
        with k.stage("glu") as (sb2, sem):
            opened_, cleared = sem("glu_opened"), sem("pad_cleared")
            with nc.Block() as block:
                @block.vector
                def _(dve):
                    for n in range(4):
                        dve.tensor_tensor(wide[:, n, pad:pad + T], wide[:, n, pad:pad + T], lin[:, n, :],
                                          ALU.mult).then_inc(opened_, 1)

                @block.gpsimd
                def _(pool):
                    pool.memset(wide[:, :, 0:pad], 0.0).then_inc(cleared, 1)

        def raw_chunk(n):
            return raw[n // 4][:, n % 4, :]

        class Raw:
            def __getitem__(self, key):
                return raw_chunk(key[1])[:, key[2]]

        project(k, "proj2b", [
            Section(d["w2_z_a"], 1, KD, k.x, silu_of(0), "scalar"),
            Section(d["w2_z_b"], 1, KD, k.x, silu_of(4), "scalar"),
            Section(d["w2_z_c"], 1, KD, k.x, silu_of(8), "scalar"),
            Section(d["w2_z_d"], 1, KD, k.x, silu_of(12), "scalar"),
            Section(d["w2_q_d"], 1, KD, k.x, scaled(q_d, DH ** -0.5), "scalar"),
            Section(d["w2_k_d"], 1, KD, k.x, plain(k_d), "scalar"),
            Section(d["w2_v_d"], 1, KD, k.x, plain(v_d), "scalar", by_tokens=True),
            Section(d["w2_rates"], 1, KD, k.x, lambda eng, n, ps: eng.activation(rate[:, n, :], ps, ACT.Copy), "scalar",
                    width=2 * GDN_HEADS + 8, by_tokens=True),
        ], beside=convolutions(k, Raw(), wide, acc, short))
        rates(k, rate, g, beta, log_f)
        activate(k, "qkv_silu", ACT.Silu, [(short[:, n, :], short[:, n, :], None) for n in range(GDN_QKV)])
        chunks = [acc[:, n, :] for n in range(4)]
        feature_center(k, "conv_center", chunks)
        feature_norm(k, "conv_ln", [(chunks, chunks, [k.p("conv_ln_g", n) for n in range(4)])], k.c("ones"), 1.0 / 512,
                     "eps_2")
        activate(k, "conv_silu", ACT.Silu, [(acc[:, n, :], acc[:, n, :], k.p("conv_ln_b", n)) for n in range(4)])
        multiply(k, "conv_gate", [(y[:, 4 + n, :], y[:, 4 + n, :], acc[:, n, :]) for n in range(4)])
    project(k, "proj2c", [
        Section(d["w2_q_c"], 1, KD, k.x, scaled(q_c, DH ** -0.5), "scalar"),
        Section(d["w2_k_c"], 1, KD, k.x, plain(k_c), "scalar"),
        Section(d["w2_v_c"], 1, KD, k.x, plain(v_c), "scalar", by_tokens=True),
    ])


def lay_out_second(i, a, p):
    w = i["w_in_2"][0]
    at_col = {"qkv_a": (0, 1536), "z_a": (1536, 512), "glu_lin": (2056, 512), "glu_gate": (2568, 512), "z_b": (3080, 512),
              "q_c": (3592, 512), "k_c": (4104, 512), "z_c": (5128, 512), "q_d": (5640, 512), "k_d": (6152, 512),
              "z_d": (7176, 512)}
    for n, (lo, width) in at_col.items():
        a[f"w2_{n}"] = units_of(w[:, lo:lo + width], 4)
    a["w2_v_c"], a["w2_v_d"] = whole(w[:, 4616:5128]), whole(w[:, 6664:7176])
    a["w2_rates"] = whole(np.concatenate([w[:, 2048:2056], w[:, 7688:7696]], 1))
    a["rate_biases"] = np.concatenate([i["dt_bias_2"], i["forget_bias_2"], i["a_log_2"]], 1)
    gates = units_of(w[:, 7696:], 1)
    branch = np.concatenate([units_of(b, 1) for b in i["w_branch_2"][0]])
    a["w_merge"] = np.concatenate([gates, branch], 2)
    a["w_out_2"] = units_of(i["w_out_2"][0], 4)
    a["pT"] = i["p_2"][0, 0].T
    a["w_ple"] = np.concatenate([units_of(i["w_ple_gate_2"][0], 1), units_of(i["w_ple_2"][0], 1)], 2)
    for n in ("b_gate", "gdn_norm", "conv_dw_bias", "conv_ln_g", "conv_ln_b", "b_ple_gate", "ln_g", "ln_b"):
        p[n] = columns(i[n + "_2"][0])
    p["conv_qkv"] = columns(i["conv_qkv_2"][0].reshape(-1))
    p["conv_dw"] = columns(i["conv_dw_2"][0].reshape(-1))



def modulation(k, mod):
    nc = k.nc
    with ExitStack() as ctx:
        silu = ctx.enter_context(nc.sbuf_tensor("ada_silu", [P, KD, 2], F32))
        rows = ctx.enter_context(nc.sbuf_tensor("ada_rows", [2, 6 * D], F32))
        activate(k, "ada_silu_c", ACT.Silu, [(silu[:, :, :].rearrange("p a b -> p (a b)"), k.p("c"), None)])

        def row(eng, n, ps):
            at_n = slice(n * BANK, (n + 1) * BANK) if isinstance(n, int) else bass.ds(n * BANK, BANK)
            return eng.tensor_copy(rows[:, at_n], ps)

        project(k, "ada", [Section(k.dram["w_ada"], 12, KD, silu, row, "vector", chunks=1, by_tokens=True, rows=2)])
        with k.stage("ada_turn") as (sb, sem):
            turned, biased = sem("turned"), sem("biased")
            with nc.Block() as block:
                @block.tensor
                def _(pe):
                    for n in range(6 * KD):
                        last = pe.transpose(k.psum[:, 2 * n:2 * n + 2], rows[:, n * P:(n + 1) * P], k.c("ident")[0:2, 0:2])
                    last.then_inc(turned, 1)

                @block.vector
                def _(dve):
                    dve.wait_ge(turned, 1)
                    dve.tensor_tensor(mod[:, :, :], k.psum[:, 0:12 * KD].rearrange("p (n c) -> p n c", c=2),
                                      k.p("b_ada").unsqueeze(2).broadcast_to([P, 6 * KD, 2]), ALU.add).then_inc(biased, 1)


def third_columns(k, mod, gains, subln, minus_lam):
    nc = k.nc
    with k.stage("third_columns") as (sb, sem):
        prod, exps, diff = sb("products", [P, 2]), sb("exps", [P, 2]), sb("difference", [P, 1])
        own, summed, exped = sem("vector_steps"), sem("sums_ready"), sem("exps_ready")
        lam = k.p("lambdas")
        with nc.Block() as block:
            @block.vector
            def _(dve):
                step = Steps(dve, own)
                step.then(dve.tensor_tensor(prod[:, 0:1], lam[:, 0:1], lam[:, 1:2], ALU.mult))
                step.then(dve.tensor_tensor(prod[:, 1:2], lam[:, 2:3], lam[:, 3:4], ALU.mult))
                for n, (part, stream, weight) in enumerate(((1, 0, "attn_norm_w"), (1, 1, "attn_norm_w"), (4, 0, "ffn_norm_w"))):
                    step.then(dve.scalar_tensor_tensor(gains[:, n, :], mod[:, part * KD:(part + 1) * KD, stream], 1.0,
                                                       k.p(weight), ALU.add, ALU.mult))
                step.then(dve.tensor_scalar(subln[:, :], k.p("subln_w"), 1.0 - LAM_INIT, None, ALU.mult))
                dve.wait_ge(exped, 1)
                step.do(dve.tensor_tensor(diff[:, :], exps[:, 1:2], exps[:, 0:1], ALU.subtract))
                step.do(dve.tensor_scalar(minus_lam[:, :], diff[:, :], -LAM_INIT, None, ALU.add))

            @block.tensor
            def _(pe):
                pe.wait_ge(own, 2)
                pe.matmul(k.bank(0, 2), k.c("ones"), prod[:, :], start=True, stop=True).then_inc(summed, 1)

            @block.scalar
            def _(act):
                act.wait_ge(summed, 1)
                act.activation(exps[:, :], k.bank(0, 2), ACT.Exp).then_inc(exped, 1)


def rotate(k, name, pairs):
    nc = k.nc
    with k.stage(name) as (sb, sem):
        turn, keep = sb("turned", [P, 2, T]), sb("kept", [P, 2, T])
        swapped, own, done = sem("swapped"), sem("vector_steps"), sem("rotated")
        with nc.Block() as block:
            @block.tensor
            def _(pe):
                for n, (_, x) in enumerate(pairs):
                    if n >= 2:
                        pe.wait_ge(own, 2 * (n - 1))
                    pe.matmul(k.bank(n % 2), k.c("rope_swap"), x, start=True, stop=True).then_inc(swapped, 1)

            @block.vector
            def _(dve):
                for n, (out, x) in enumerate(pairs):
                    dve.wait_ge(swapped, n + 1)
                    if n >= 2:
                        dve.wait_ge(done, n - 1)
                    dve.tensor_tensor(turn[:, n % 2, :], k.bank(n % 2), k.c("rope_sin"), ALU.mult).then_inc(own, 1)
                    dve.tensor_tensor(keep[:, n % 2, :], x, k.c("rope_cos"), ALU.mult).then_inc(own, 1)
                    dve.wait_ge(own, 2 * n + 2)
                    dve.tensor_tensor(out, turn[:, n % 2, :], keep[:, n % 2, :], ALU.add).then_inc(done, 1)


def mixers(k, mod, gains, subln, minus_lam, mix):
    nc, d = k.nc, k.dram
    with ExitStack() as ctx:
        def sb(what, shape, stack=ctx):
            return stack.enter_context(nc.sbuf_tensor(f"third_{what}", shape, F32))

        dq, dk, dv = sb("dq", [P, 4, T]), sb("dk", [P, 4, TA]), sb("dv", [P, TA // P, 4 * P])
        cq, ckv, kr = sb("cq", [P, 2, T]), sb("ckv", [P, 1, TA]), sb("kr", [P, 1, TA])
        zeros = sb("zeros", [P, TA])
        with ExitStack() as inputs:
            hc = sb("ctx_normed", [P, KD, CTX], inputs)
            with ExitStack() as raw:
                cx = sb("ctx", [P, KD, CTX], raw)
                with k.stage("ctx_in") as (sb2, sem):
                    landed, cleared = sem("ctx_landed"), sem("zeros_cleared")
                    with nc.Block() as block:
                        @block.sync
                        def _(sp):
                            sp.dma_start(cx[:, :, :], d["ctxT"].rearrange("(k p) t -> p k t", p=P)).then_inc(landed, 16)
                            sp.wait_ge(landed, 16)

                        @block.gpsimd
                        def _(pool):
                            pool.memset(zeros[:, :], 0.0).then_inc(cleared, 1)
                for stream, (src, dst) in enumerate(((k.x, k.h), (cx, hc))):
                    feature_norm(k, f"third_norm{stream}",
                                 [([src[:, n, :] for n in range(KD)], [dst[:, n, :] for n in range(KD)],
                                   [gains[:, stream, n:n + 1] for n in range(KD)])], k.c("ones"), 1.0 / D, "eps",
                                 shift=[mod[:, n, stream:stream + 1] for n in range(KD)])

            def into(dst, lo, n_tokens, scale=1.0):
                return lambda eng, n, ps: eng.activation(at(dst, n)[:, lo:lo + n_tokens], ps, ACT.Copy, scale=scale)

            def tokens(dst, first):
                return lambda eng, n, ps: eng.activation(dst[:, first + n, :], ps, ACT.Copy)

            def misc(lo, n_tokens, first):
                def finish(eng, n, ps):
                    dst = [cq[:, 0, :], cq[:, 1, :], ckv[:, 0, lo:lo + n_tokens], kr[:, 0, lo:lo + n_tokens]][first + n]
                    return eng.activation(dst, ps, ACT.Copy)
                return finish

            project(k, "proj3", [
                Section(d["w3_dq"], 1, KD, k.h, into(dq, 0, T, DH ** -0.5), "scalar"),
                Section(d["w3_dk"], 1, KD, k.h, into(dk, CTX, T), "scalar"),
                Section(d["w3_dk"], 1, KD, hc, into(dk, 0, CTX), "scalar", width=CTX),
                Section(d["w3_dv"], 1, KD, k.h, tokens(dv, CTX // P), "scalar", by_tokens=True),
                Section(d["w3_dv"], 1, KD, hc, tokens(dv, 0), "scalar", chunks=CTX // P, by_tokens=True),
                Section(d["w3_misc"], 1, KD, k.h, misc(CTX, T, 0), "scalar"),
                Section(d["w3_misc_ctx"], 1, KD, hc, misc(0, CTX, 2), "scalar", chunks=2, width=CTX),
            ])
        rotate(k, "rope_diff", [(dq[:, n, :], dq[:, n, :]) for n in range(4)]
               + [(dk[:, n, CTX:TA], dk[:, n, CTX:TA]) for n in range(4)] + [(kr[:, 0, CTX:TA], kr[:, 0, CTX:TA])])
        halves = [(0, BANK), (BANK, TA)]
        feature_norm(k, "latent_norm", [([cq[:, n, :] for n in range(2)], [cq[:, n, :] for n in range(2)],
                                         [k.p("q_norm_w", n) for n in range(2)])], k.c("ones"), 1.0 / 256, "eps")
        feature_norm(k, "latent_kv_norm", [([ckv[:, 0, a:b]], [ckv[:, 0, a:b]], [k.p("kv_norm_w")]) for a, b in halves],
                     k.c("ones"), 1.0 / P, "eps")

        with ExitStack() as heads:
            qs, ks, vs = sb("diff_q", [P, T], heads), sb("diff_k", [P, TA], heads), sb("diff_v", [P, TA // P, P], heads)

            def copies(i):
                head = slice(i * P, (i + 1) * P) if isinstance(i, int) else bass.ds(i * P, P)
                return [(qs[:, :], at(dq, i)), (ks[:, :], at(dk, i)), (vs[:, :, :], dv[:, :, head])]

            units = []
            for t in range(TT):
                for m in range(2):
                    half = slice(m * DH, (m + 1) * DH)
                    units.append(Unit([(qs[half, t * P:(t + 1) * P], ks[half, :])], TA, zeros[:, :],
                                      minus_lam[:, :] if m else 1.0, [(n * P, P, vs[:, n, :]) for n in range(TA // P)],
                                      (0, P), t, m == 0, m == 1))
            attention(k, "diff", DIFF_HEADS, copies, units, lambda i, t: at(mix, i)[:, t * P:(t + 1) * P])
        feature_norm(k, "diff_norm", [([mix[:, n, :]], [mix[:, n, :]], [subln[:, :]]) for n in range(DIFF_HEADS)],
                     k.c("ones"), 1.0 / P, "eps")

        scale = (P + DH) ** -0.5
        qn, qr = sb("mla_qn", [P, 4, T]), sb("mla_qr", [P, 2, T])
        kn, mv = dk, dv

        def queries(eng, n, ps):
            return eng.activation(qn[:, n, :] if n < 4 else qr[:, n - 4, :], ps, ACT.Copy, scale=scale)

        def shifted(finish, first):
            return lambda eng, n, ps: finish(eng, n + first, ps)

        project(k, "proj3b", [
            Section(d["w3_uq"][0:1], 1, 2, cq, shifted(queries, 0), "scalar", chunks=3),
            Section(d["w3_uq"][1:2], 1, 2, cq, shifted(queries, 3), "scalar", chunks=3),
            Section(d["w3_uk"], 1, 1, ckv[:, :, 0:CTX], lambda eng, n, ps: eng.activation(kn[:, n, 0:CTX], ps, ACT.Copy),
                    "scalar", width=CTX),
            Section(d["w3_uk"], 1, 1, ckv[:, :, CTX:TA], lambda eng, n, ps: eng.activation(kn[:, n, CTX:TA], ps, ACT.Copy),
                    "scalar"),
            Section(d["w3_uv"], 1, 1, ckv, lambda eng, n, ps: eng.activation(mv[:, n, :], ps, ACT.Copy), "scalar",
                    chunks=3, by_tokens=True),
            Section(d["w3_uv"], 1, 1, ckv[:, :, 3 * P:TA], lambda eng, n, ps: eng.activation(mv[:, 3 + n, :], ps, ACT.Copy),
                    "scalar", chunks=3, by_tokens=True),
        ])
        rotate(k, "rope_mla", [(qr[:, n, :], qr[:, n, :]) for n in range(2)])
        with ExitStack() as heads:
            qns, qrs = sb("mla_qns", [P, 2, T], heads), sb("mla_qrs", [P, T], heads)
            kns, vs = sb("mla_kns", [P, 2, TA], heads), sb("mla_vs", [P, TA // P, 2 * P], heads)

            def copies(i):
                pair = slice(2 * i, 2 * i + 2) if isinstance(i, int) else bass.ds(2 * i, 2)
                wide = slice(2 * i * P, 2 * (i + 1) * P) if isinstance(i, int) else bass.ds(2 * i * P, 2 * P)
                return [(qns[:, :, :], qn[:, pair, :]), (qrs[:, :], at(qr, i)), (kns[:, :, :], kn[:, pair, :]),
                        (vs[:, :, :], mv[:, :, wide])]

            units = []
            for t in range(TT):
                here = slice(t * P, (t + 1) * P)
                for h in range(2):
                    half = slice(h * DH, (h + 1) * DH)
                    units.append(Unit([(qns[:, h, here], kns[:, h, :]), (qrs[half, here], kr[half, 0, :])], TA, zeros[:, :], 1.0,
                                      [(n * P, P, vs[:, n, h * P:(h + 1) * P]) for n in range(TA // P)],
                                      (0, P), 2 * t + h, True, True))
            attention(k, "mla", 2, copies, units,
                      lambda i, g: at(mix, 4 + 2 * i + g % 2)[:, (g // 2) * P:(g // 2 + 1) * P])


def route(k, logits, gate, dest, row_of, block_expert, gate_by_expert):
    nc, E, K, B = k.nc, EXPERTS, TOP_K, SLOTS_MAX + 1
    table = nc.dram_tensor("row_tokens", (B * P, 1), I32, kind="Internal").ap()
    with k.stage("route") as (sb, sem):
        top, ids = sb("top", [P, TT, 8]), sb("ids", [P, TT, 8], U32)
        idf, neg = sb("ids_f", [P, TT, 8]), sb("neg", [P, TT])
        ex, total, inv = sb("exps", [P, TT, K]), sb("total", [P, TT]), sb("inverse", [P, TT])
        hot, part = sb("hot", [P, TT, K, E]), sb("part", [P, K, E])
        chosen, slot, spread = sb("chosen", [P, TT, E]), sb("slots", [P, TT, E]), sb("spread", [P, TT, E])
        start, blocks, ends = sb("start", [P, E]), sb("blocks", [E, P]), sb("ends", [E, 1])
        past, count_t = sb("past", [E, B]), sb("counts", [E, P])
        dest_f, toks, fill = sb("dest_f", [P, TT, K]), sb("tokens", [P, TT], I32), sb("fill", [B, P], I32)
        row_i, row_f = sb("row_i", [B, P], I32), sb("row_f", [B, P])
        own, exped, ranked, started, ended, mapped, filled, scattered, loaded, cast, turned = (sem(x) for x in (
            "vector_steps", "exps_ready", "ranks_ready", "starts_ready", "ends_ready", "map_ready", "table_filled",
            "tokens_scattered", "table_loaded", "table_cast", "table_turned"))
        with nc.Block() as block:
            @block.vector
            def _(dve):
                v = Steps(dve, own)
                for t in range(TT):
                    v.do(dve.max(top[:, t, :], logits[:, t, :]))
                    v.then(dve.max_index(ids[:, t, :], top[:, t, :], logits[:, t, :]))
                v.settle()
                v.then(dve.tensor_copy(idf[:, :, :], ids[:, :, :]))
                v.then(dve.tensor_copy(toks[:, :], k.c("lanes_on")))
                v.then(dve.memset(fill[:, :], T))
                v.do(dve.tensor_scalar(neg[:, :], top[:, :, 0], -1.0, None, ALU.mult))
                for t in range(TT):
                    v.do(dve.tensor_tensor(hot[:, t, :, :], k.c("experts").unsqueeze(1).broadcast_to([P, K, E]),
                                           idf[:, t, 0:K].unsqueeze(2).broadcast_to([P, K, E]), ALU.is_equal))
                    v.then(dve.tensor_reduce(chosen[:, t, :], hot[:, t, :, :].rearrange("p k e -> p e k"), AX_X, ALU.add))
                v.settle()
                dve.wait_ge(ranked, 3)
                v.do(dve.tensor_copy(count_t[:, :], k.psum[0:E, 2 * BANK:2 * BANK + P]))
                v.do(dve.tensor_scalar(blocks[:, :], count_t[:, :], 0.0, None, ALU.is_gt))
                for n in range(1, T // P):
                    v.do(dve.scalar_tensor_tensor(blocks[:, :], count_t[:, :], float(n * P), blocks[:, :], ALU.is_gt, ALU.add))
                dve.wait_ge(started, 1)
                v.do(dve.tensor_scalar(start[:, :], k.bank(3, E), float(P), None, ALU.mult))
                v.do(dve.tensor_tensor(slot[:, :, :], k.psum[:, 0:TT * E].rearrange("p (t e) -> p t e", e=E),
                                       start[:, :].unsqueeze(1).broadcast_to([P, TT, E]), ALU.add))
                for t in range(TT):
                    v.do(dve.tensor_tensor(part[:, :, :], hot[:, t, :, :], slot[:, t, :].unsqueeze(1).broadcast_to([P, K, E]),
                                           ALU.mult))
                    v.do(dve.tensor_reduce(dest_f[:, t, :], part[:, :, :], AX_X, ALU.add))
                v.do(dve.tensor_copy(dest[:, :, :], dest_f[:, :, :]))
                dve.wait_ge(ended, 1)
                v.do(dve.tensor_copy(ends[:, :], k.psum[0:E, 4 * BANK:4 * BANK + 1]))
                v.then(dve.tensor_scalar(past[:, :], k.c("blocks")[0:E, :], ends[:, 0:1], None, ALU.is_ge))
                dve.wait_ge(mapped, 1)
                v.then(dve.tensor_copy(block_expert[:, 0:B + 1], k.psum[0:1, 5 * BANK:5 * BANK + B + 1]))
                v.then(dve.tensor_scalar(block_expert[:, B + 1:B + 2], k.psum[0:1, 5 * BANK + B:5 * BANK + B + 1], -1.0, float(B),
                                         ALU.mult, ALU.add))
                dve.wait_ge(exped, TT)
                v.do(dve.reciprocal(inv[:, :], total[:, :]))
                v.do(dve.tensor_tensor(gate[:, :, :], ex[:, :, :], inv[:, :].unsqueeze(2).broadcast_to([P, TT, K]), ALU.mult))
                for t in range(TT):
                    v.do(dve.tensor_tensor(part[:, :, :], hot[:, t, :, :], gate[:, t, :].unsqueeze(2).broadcast_to([P, K, E]),
                                           ALU.mult))
                    v.do(dve.tensor_reduce(spread[:, t, :], part[:, :, :].rearrange("p k e -> p e k"), AX_X, ALU.add))
                dve.wait_ge(loaded, 16)
                dve.tensor_copy(row_f[:, :], row_i[:, :]).then_inc(cast, 1)
                dve.wait_ge(turned, 1)
                v.then(dve.tensor_copy(row_of[:, :], k.psum[:, 6 * BANK:6 * BANK + B]))
                v.then(dve.tensor_copy(gate_by_expert[:, :], k.psum[0:E, 7 * BANK:7 * BANK + T]))

            @block.scalar
            def _(act):
                act.wait_ge(own, 12)
                for t in range(TT):
                    act.activation(ex[:, t, :], top[:, t, 0:K], ACT.Exp, bias=neg[:, t:t + 1],
                                   accum_out=total[:, t:t + 1]).then_inc(exped, 1)

            @block.tensor
            def _(pe):
                pe.wait_ge(own, 20)
                for t in range(TT):
                    out = k.psum[:, t * E:(t + 1) * E]
                    for n in range(t + 1):
                        last = pe.matmul(out, k.c("before")[:, 0:P] if n == t else k.c("ones"), chosen[:, n, :],
                                         start=(n == 0), stop=(n == t))
                last.then_inc(ranked, 2)
                for n in range(TT):
                    last = pe.matmul(k.psum[0:E, 2 * BANK:2 * BANK + P], chosen[:, n, :], k.c("ones"), start=(n == 0),
                                     stop=(n == TT - 1))
                last.then_inc(ranked, 1)
                pe.wait_ge(own, 25)
                pe.matmul(k.bank(3, E), blocks[:, :], k.c("before")[0:E, 0:E], start=True, stop=True).then_inc(started, 1)
                pe.matmul(k.psum[0:E, 4 * BANK:4 * BANK + P], k.c("upto")[0:E, 0:E], blocks[:, :], start=True,
                          stop=True).then_inc(ended, 1)
                pe.wait_ge(own, 38)
                pe.matmul(k.psum[0:1, 5 * BANK:5 * BANK + B], k.c("one")[0:E, :], past[:, :], start=True, stop=True)
                pe.matmul(k.psum[0:1, 5 * BANK + B:5 * BANK + B + 1], blocks[:, 0:1], k.c("one")[0:E, :], start=True,
                          stop=True).then_inc(mapped, 1)
                pe.wait_ge(own, 50)
                for t in range(TT):
                    pe.transpose(k.psum[0:E, 7 * BANK + t * P:7 * BANK + (t + 1) * P], spread[:, t, :], k.c("ident"))
                pe.wait_ge(cast, 1)
                pe.transpose(k.psum[:, 6 * BANK:6 * BANK + B], row_f[:, :], k.c("ident")[0:B, 0:B]).then_inc(turned, 1)

            @block.gpsimd
            def _(pool):
                pool.wait_ge(own, 36)
                pool.wait_ge(filled, 16)
                for t in range(TT):
                    for n in range(K):
                        pool.indirect_dma_start(out=table, out_offset=bass.IndirectOffsetOnAxis(ap=dest[:, t, n:n + 1], axis=0),
                                                in_=toks[:, t:t + 1], in_offset=None).then_inc(scattered, 16)

            @block.sync
            def _(sp):
                sp.wait_ge(own, 12)
                sp.dma_start(table.rearrange("(b p) one -> b (p one)", p=P), fill[:, :]).then_inc(filled, 16)
                sp.wait_ge(scattered, 16 * TT * K)
                sp.dma_start(row_i[:, :], table.rearrange("(b p) one -> b (p one)", p=P)).then_inc(loaded, 16)


def experts(k, rows, row_of, block_expert, results):
    nc, d = k.nc, k.dram
    UP, DOWN, CH = 4, 2, 4
    HALF = 2 * P
    with k.stage("experts") as (sb, sem):
        ring_up = sb("up", [P, UP, KD * CH * P + CH])
        ring_down = sb("down", [P, DOWN, KD * BANK])
        index = sb("index", [P, 2], I32)
        x_rows, x_t = sb("x", [P, 2, D]), sb("xT", [P, 2, KD, P])
        gate, lin, sig = sb("gate", [P, 2, HALF]), sb("lin", [P, 2, HALF]), sb("sig", [P, 2, HALF])
        hidden, y = sb("hidden", [P, KD, P]), sb("y", [P, DOWN, BANK])

        def sems(what, n):
            return [sem(f"{what}{i}") for i in range(n)]

        up_landed, down_landed, up_ready, gated, sigged, hid_done = (sems(x, UP) for x in (
            "up_landed", "down_landed", "up_ready", "gate_ready", "sigmoid_ready", "hidden_done"))
        down_ready, y_copied, y_stored = (sems(x, DOWN) for x in ("down_ready", "y_copied", "y_stored"))
        indexed, gathered, x_turned, x_copied = (sems(x, 2) for x in ("indexed", "gathered", "x_turned", "x_copied"))
        own, cleared, zeroed, passed = (sem(x) for x in ("vector_steps", "zero_cleared", "empty_blocks_zeroed", "waits_passed"))
        zero = sb("zero", [P, D])
        OWN = 4

        def blocks(eng, body, empty=None):
            with eng.Fori(0, (SLOTS_MAX + 1) // 2) as i:
                for s in range(2):
                    b = 2 * i + s
                    e = eng.value_load(block_expert[0:1, bass.ds(b, 1)], min_val=0, max_val=EXPERTS)
                    with eng.If(e < EXPERTS):
                        body(i, s, b, nc.s_assert_within(
                            e, 0, EXPERTS - 1, skip_runtime_bounds_check_because="inside the branch for e < EXPERTS"))
                    if empty:
                        with eng.Else():
                            empty(b)

        with nc.Block() as block:
            @block.sync
            def _(sp):
                def body(i, s, b, e):
                    for u in range(UP):
                        sp.wait_ge(hid_done[u], b)
                        sp.dma_start(ring_up[:, u, :], d["w_up_3"][bass.ds(e, 1), u, :, :].rearrange("a p n -> p (a n)")
                                     ).then_inc(up_landed[u], 16)
                    for u in range(DOWN):
                        sp.wait_ge(y_copied[u], b)
                        sp.dma_start(ring_down[:, u, :], d["w_down_3"][bass.ds(e, 1), u, :, :].rearrange("a p n -> p (a n)")
                                     ).then_inc(down_landed[u], 16)

                def empty(b):
                    sp.dma_start(results[bass.ds(b * P, P), :], zero[:, :]).then_inc(zeroed, 16)

                sp.wait_ge(cleared, 1)
                blocks(sp, body, empty)
                count = SLOTS_MAX + 1
                empties = sp.value_load(block_expert[0:1, count + 1:count + 2], min_val=0, max_val=count)
                wait_apart(sp, zeroed, empties * 16, passed)

            @block.gpsimd
            def _(pool):
                pool.memset(zero[:, :], 0.0).then_inc(cleared, 1)

                def body(i, s, b, e):
                    pool.wait_ge(gathered[s], i * 16)
                    pool.tensor_copy(index[:, s:s + 1], row_of[:, bass.ds(b, 1)]).then_inc(indexed[s], 1)
                    pool.wait_ge(x_turned[s], i)
                    wait_apart(pool, indexed[s], i + 1, passed)
                    pool.indirect_dma_start(out=x_rows[:, s, :], out_offset=None, in_=rows,
                                            in_offset=bass.IndirectOffsetOnAxis(ap=index[:, s:s + 1], axis=0)
                                            ).then_inc(gathered[s], 16)
                blocks(pool, body)

            @block.tensor
            def _(pe):
                def body(i, s, b, e):
                    pe.wait_ge(gathered[s], i * 16 + 16)
                    pe.wait_ge(x_copied[1 - s], i + s)
                    for n in range(KD):
                        last = pe.transpose(k.psum[:, 6 * BANK + n * P:6 * BANK + (n + 1) * P], x_rows[:, s, n * P:(n + 1) * P],
                                            k.c("ident"))
                    last.then_inc(x_turned[s], 1)
                    pe.wait_ge(x_copied[s], i + 1)
                    for u in range(UP):
                        w = ring_up[:, u, 0:KD * CH * P].rearrange("p (k n) -> p k n", k=KD)
                        pe.wait_ge(up_landed[u], b * 16 + 16)
                        pe.wait_ge(hid_done[(u + 2) % UP], b + 1 if u >= 2 else b)
                        for c in range(CH):
                            for kk in range(KD):
                                last = pe.matmul(k.bank(u % 2)[:, c * P:(c + 1) * P], w[:, kk, c * P:(c + 1) * P],
                                                 x_t[:, s, kk, :], start=(kk == 0), stop=(kk == KD - 1))
                        last.then_inc(up_ready[u], 1)
                    for u in range(UP):
                        pe.wait_ge(hid_done[u], b + 1)
                    for u in range(DOWN):
                        w = ring_down[:, u, :].rearrange("p (k n) -> p k n", k=KD)
                        pe.wait_ge(down_landed[u], b * 16 + 16)
                        pe.wait_ge(y_copied[u], b)
                        for kk in range(KD):
                            last = pe.matmul(k.bank(2 + u), hidden[:, kk, :], w[:, kk, :], start=(kk == 0), stop=(kk == KD - 1))
                        last.then_inc(down_ready[u], 1)
                blocks(pe, body)

            @block.scalar
            def _(act):
                def body(i, s, b, e):
                    act.wait_ge(x_turned[s], i + 1)
                    act.wait_ge(up_ready[UP - 1], b)
                    act.copy(x_t[:, s, :, :].rearrange("p k n -> p (k n)"), k.psum[:, 6 * BANK:8 * BANK]
                             ).then_inc(x_copied[s], 1)
                    for u in range(UP):
                        act.wait_ge(gated[u], 2 * b + 2)
                        act.activation(sig[:, u % 2, :], gate[:, u % 2, :], ACT.Sigmoid, scale=SWIGLU_ALPHA
                                       ).then_inc(sigged[u], 1)
                    for u in range(DOWN):
                        act.wait_ge(down_ready[u], b + 1)
                        act.wait_ge(y_stored[u], b * 16)
                        act.copy(y[:, u, :], k.bank(2 + u)).then_inc(y_copied[u], 1)
                        act.wait_ge(y_copied[u], b + 1)
                        act.dma_start(results[bass.ds(b * P, P), u * BANK:(u + 1) * BANK], y[:, u, :]).then_inc(y_stored[u], 16)
                blocks(act, body)
                filled = act.value_load(block_expert[0:1, SLOTS_MAX + 1:SLOTS_MAX + 2], min_val=1, max_val=SLOTS_MAX + 1)
                for u in range(DOWN):
                    wait_apart(act, y_stored[u], filled * 16, passed)

            @block.vector
            def _(dve):
                def body(i, s, b, e):
                    dve.wait_ge(down_ready[DOWN - 1], b)
                    for u in range(UP):
                        n = u % 2
                        bias = ring_up[:, u, KD * CH * P:KD * CH * P + CH]
                        v = Steps(dve, own)
                        v.n = b * (OWN * UP) + u * OWN
                        ps = k.bank(u % 2)
                        dve.wait_ge(up_ready[u], b + 1)
                        for c in range(2):
                            dve.tensor_scalar(gate[:, n, c * P:(c + 1) * P], ps[:, c * P:(c + 1) * P], bias[:, c:c + 1], LIMIT,
                                              ALU.add, ALU.min).then_inc(gated[u], 1)
                        for c in range(2):
                            v.then(dve.tensor_scalar(lin[:, n, c * P:(c + 1) * P], ps[:, (2 + c) * P:(3 + c) * P],
                                                     bias[:, 2 + c:3 + c], -LIMIT, ALU.add, ALU.max))
                        v.settle()
                        v.do(dve.tensor_scalar(lin[:, n, :], lin[:, n, :], LIMIT, 1.0, ALU.min, ALU.add))
                        dve.wait_ge(gated[u], 2 * b + 2)
                        v.do(dve.tensor_tensor(lin[:, n, :], lin[:, n, :], gate[:, n, :], ALU.mult))
                        dve.wait_ge(sigged[u], b + 1)
                        dve.tensor_tensor(hidden[:, 2 * u:2 * u + 2, :].rearrange("p k n -> p (k n)"), lin[:, n, :], sig[:, n, :],
                                          ALU.mult).then_inc(hid_done[u], 1)
                blocks(dve, body)


def third_block(k):
    nc, d = k.nc, k.dram
    with ExitStack() as ctx:
        def sb(what, shape, dtype=F32, stack=ctx):
            return stack.enter_context(nc.sbuf_tensor(f"third_{what}", shape, dtype))

        mod, gains = sb("mod", [P, 6 * KD, 2]), sb("gains", [P, 3, KD])
        subln, minus_lam = sb("subln", [P, 1]), sb("minus_lam", [P, 1])
        modulation(k, mod)
        third_columns(k, mod, gains, subln, minus_lam)
        with ExitStack() as attend:
            mix = sb("mix", [P, KD, T], F32, attend)
            mixers(k, mod, gains, subln, minus_lam, mix)

            def gated_residual(first):
                def finish(eng, n, ps):
                    g = mod[:, first + n, 0:1] if isinstance(n, int) else \
                        mod[:, bass.ds(n + first, 1), 0:1].rearrange("p a b -> p (a b)")
                    return eng.scalar_tensor_tensor(at(k.x, n), ps, g, at(k.x, n), ALU.mult, ALU.add)
                return finish

            project(k, "out3", [Section(d["w_out_3"], 2, KD, mix, gated_residual(2 * KD), "vector")])
        feature_norm(k, "moe_norm", [([k.x[:, n, :] for n in range(KD)], [k.h[:, n, :] for n in range(KD)],
                                      [gains[:, 2, n:n + 1] for n in range(KD)])], k.c("ones"), 1.0 / D, "eps",
                     shift=[mod[:, 3 * KD + n, 0:1] for n in range(KD)])
        gate = sb("gate", [P, TT, TOP_K])
        dest = sb("dest", [P, TT, TOP_K], I32)
        by_expert = sb("gate_by_expert", [EXPERTS, T])
        rows = nc.dram_tensor("token_rows", (T + 1, D), F32, kind="Internal").ap()
        results = nc.dram_tensor("expert_rows", ((SLOTS_MAX + 1) * P, D), F32, kind="Internal").ap()
        with ExitStack() as routing:
            row_of = sb("row_of", [P, SLOTS_MAX + 1], I32, routing)
            block_expert = sb("block_expert", [1, SLOTS_MAX + 3], I32, routing)
            with ExitStack() as deciding:
                logits, bias = sb("logits", [P, TT, EXPERTS], F32, deciding), sb("router_b", [P, EXPERTS], F32, deciding)
                token_rows(k, rows, bias)
                project(k, "router", [Section(d["router_w"], 1, KD, k.h,
                                              lambda eng, n, ps: eng.tensor_tensor(logits[:, n, :], ps, bias[:, :], ALU.add),
                                              "vector", width=EXPERTS, by_tokens=True)])
                route(k, logits, gate, dest, row_of, block_expert, by_expert)
            experts(k, rows, row_of, block_expert, results)
        combine(k, results, gate, dest, by_expert, mod)
    chunks = [k.x[:, n, :] for n in range(KD)]
    feature_norm(k, "final_norm", [(chunks, chunks, [k.p("final_norm_w", n) for n in range(KD)])], k.c("ones"), 1.0 / D, "eps")
    store_stream(k)


def token_rows(k, rows, bias):
    nc = k.nc
    with k.stage("token_rows") as (sb, sem):
        by_token, zero = sb("by_token", [P, TT, D]), sb("zero", [1, D])
        turned, copied, cleared, stored = (sem(x) for x in ("turned", "copied", "zero_cleared", "rows_stored"))
        with nc.Block() as block:
            @block.tensor
            def _(pe):
                for t in range(TT):
                    for half in range(2):
                        for n in range(4):
                            last = pe.transpose(k.bank(2 * t + half)[:, n * P:(n + 1) * P],
                                                k.h[:, 4 * half + n, t * P:(t + 1) * P], k.c("ident"))
                        last.then_inc(turned, 1)

            @block.vector
            def _(dve):
                dve.memset(zero[:, :], 0.0).then_inc(cleared, 1)
                for n in range(2 * TT):
                    dve.wait_ge(turned, n + 1)
                    dve.tensor_copy(by_token[:, n // 2, (n % 2) * BANK:(n % 2 + 1) * BANK], k.bank(n)).then_inc(copied, 1)

            @block.sync
            def _(sp):
                sp.dma_start(bias[:, :], k.dram["router_b"][0:1, :].broadcast_to([P, EXPERTS])).then_inc(stored, 16)
                sp.wait_ge(cleared, 1)
                sp.dma_start(rows[T:T + 1, :], zero[:, :]).then_inc(stored, 16)
                for t in range(TT):
                    sp.wait_ge(copied, 2 * t + 2)
                    sp.dma_start(rows[t * P:(t + 1) * P, :], by_token[:, t, :]).then_inc(stored, 16)
                sp.wait_ge(stored, 16 * (TT + 2))


def combine(k, results, gate, dest, by_expert, mod):
    nc = k.nc
    with k.stage("combine") as (sb, sem):
        b2 = sb("b2", [EXPERTS, D])
        got, acc = sb("got", [P, 4, D]), sb("acc", [P, TT, D])
        landed, gathered, weighed, summed, added = sem("b2_landed"), [sem(f"rows{i}_gathered") for i in range(4)], sem("rows_weighed"), \
            sem("sums_ready"), sem("residual_added")
        N = TT * TOP_K
        with nc.Block() as block:
            @block.sync
            def _(sp):
                sp.dma_start(b2[:, :], k.dram["b2_3"]).then_inc(landed, 16)

            @block.gpsimd
            def _(pool):
                for n in range(N):
                    t, c = n // TOP_K, n % TOP_K
                    if n >= 4:
                        pool.wait_ge(weighed, n - 3)
                    pool.indirect_dma_start(out=got[:, n % 4, :], out_offset=None, in_=results,
                                            in_offset=bass.IndirectOffsetOnAxis(ap=dest[:, t, c:c + 1], axis=0)
                                            ).then_inc(gathered[n % 4], 16)

            @block.vector
            def _(dve):
                for n in range(N):
                    t, c = n // TOP_K, n % TOP_K
                    dve.wait_ge(gathered[n % 4], 16 * (n // 4) + 16)
                    g = gate[:, t, c:c + 1]
                    if c == 0:
                        dve.tensor_scalar(acc[:, t, :], got[:, n % 4, :], g, None, ALU.mult).then_inc(weighed, 1)
                    else:
                        dve.wait_ge(weighed, n)
                        dve.scalar_tensor_tensor(acc[:, t, :], got[:, n % 4, :], g, acc[:, t, :], ALU.mult,
                                                 ALU.add).then_inc(weighed, 1)
                for n in range(KD):
                    dve.wait_ge(summed, n + 1)
                    dve.scalar_tensor_tensor(k.x[:, n, :], k.bank(n), mod[:, 5 * KD + n, 0:1], k.x[:, n, :], ALU.mult,
                                             ALU.add).then_inc(added, 1)

            @block.tensor
            def _(pe):
                pe.wait_ge(landed, 16)
                pe.wait_ge(weighed, N)
                for n in range(KD):
                    pe.matmul(k.bank(n), b2[:, n * P:(n + 1) * P], by_expert[:, :], start=True, stop=False)
                    for t in range(TT):
                        last = pe.matmul(k.bank(n)[:, t * P:(t + 1) * P], acc[:, t, n * P:(n + 1) * P], k.c("ident"),
                                         start=False, stop=(t == TT - 1))
                    last.then_inc(summed, 1)


def lay_out_third(i, a, p):
    a["ctxT"] = i["ctx_3"][0].T
    p["c"] = np.stack([columns(i["c_3"][0]), columns(i["c_ctx_3"])], 2).reshape(P, -1)
    for n in ("b_ada", "attn_norm_w", "q_norm_w", "kv_norm_w", "subln_w", "ffn_norm_w"):
        p[n] = columns(i[n + "_3"][0])
    p["final_norm_w"] = columns(i["final_norm_w_3"])
    lam = np.zeros((P, 4), np.float32)
    for n, name in enumerate(("q1", "k1", "q2", "k2")):
        lam[0:DH, n] = i[f"lambda_{name}_3"][0]
    p["lambdas"] = lam
    a["w_ada"] = units_of(i["w_ada_3"][0], 4)
    w = i["w_in_3"][0]
    kr = np.concatenate([w[:, 1920:1984]] * 2, 1)
    a["w3_dq"], a["w3_dk"], a["w3_dv"] = units_of(w[:, 0:512], 4), units_of(w[:, 512:1024], 4), whole(w[:, 1024:1536])
    a["w3_misc"] = units_of(np.concatenate([w[:, 1536:1920], kr], 1), 4)
    a["w3_misc_ctx"] = units_of(np.concatenate([w[:, 1792:1920], kr], 1), 2)
    uq = i["w_uq_3"][0].reshape(256, MLA_HEADS, P + DH)
    a["w3_uq"] = units_of(np.concatenate([uq[:, :, 0:P].reshape(256, -1), uq[:, :, P:].reshape(256, -1)], 1), 3)
    ukv = i["w_ukv_3"][0].reshape(P, MLA_HEADS, 2, P)
    a["w3_uk"], a["w3_uv"] = units_of(ukv[:, :, 0].reshape(P, -1), 4), whole(ukv[:, :, 1].reshape(P, -1))
    a["w_out_3"] = units_of(i["w_out_3"][0], 4)
    a["router_w"], a["router_b"] = whole(i["router_w_3"][0]), i["router_b_3"]
    w1 = i["w1_3"][0].reshape(EXPERTS, KD, P, 2, 4, 2 * P).transpose(0, 4, 2, 1, 3, 5).reshape(EXPERTS, 4, P, -1)
    b1 = i["b1_3"][0].reshape(EXPERTS, 2, 4, 2, P).transpose(0, 2, 4, 1, 3).reshape(EXPERTS, 4, P, 4)
    a["w_up_3"] = np.concatenate([w1, b1], 3)
    a["w_down_3"] = i["w2_3"][0].reshape(EXPERTS, KD, P, 2, BANK).transpose(0, 3, 2, 1, 4).reshape(EXPERTS, 2, P, -1)
    a["b2_3"] = i["b2_3"][0]



def program(nc, dram):
    with ExitStack() as ctx:
        k = Core(nc, ctx, dram)
        k.x = k.keep("residual", [P, KD, T])
        k.h = k.keep("normed", [P, KD, T])
        k.const = k.keep("constants", [P, CONST_N])
        k.param = k.keep("parameters", [P, PARAM_N])
        load_inputs(k)
        first_block(k)
        second_block(k)
        third_block(k)


def store_stream(k):
    with k.stage("store") as (sb, sem):
        stored = sem("result_stored")
        with k.nc.Block() as block:
            @block.sync
            def _(sp):
                sp.dma_start(k.dram["out"].rearrange("(k p) t -> p k t", p=P), k.x[:, :, :]).then_inc(stored, 16)
                sp.wait_ge(stored, 16)


def units_of(w, chunks):
    kc = w.shape[0] // P
    return w.reshape(kc, P, -1, chunks * P).transpose(2, 1, 0, 3).reshape(-1, P, kc * chunks * P)


def whole(w):
    return w.reshape(w.shape[0] // P, P, -1).transpose(1, 0, 2).reshape(1, P, -1)


def columns(v):
    return v.reshape(-1, P).T


def lay_out(i):
    a = {"consts": np.concatenate(list(constants().values()), 1), "buckets": bucket_rows()}
    a["xT"] = i["x"][0].T
    a["rel_bias"] = i["rel_bias"]
    w = i["w_in"][0]
    a["w_in_q"] = units_of(w[:, 0:512], 4)
    a["w_in_k"] = units_of(np.concatenate([w[:, 512:640], w[:, 640:768], w[:, 768:896], w[:, 1024:1152]], 1), 4)
    a["w_in_v"] = whole(np.concatenate([w[:, 896:1024], w[:, 1152:1280]], 1))
    a["w_in_g"] = whole(w[:, 1280:1304])
    a["w_in_u"] = units_of(w[:, 1304:1816], 4)
    a["w_in_sv"] = whole(w[:, 1816:2328])
    for x in "kv":
        a[f"cmp_w1_{x}"] = i[f"cmp_w1_{x}"][0]
    a["cmp_w2_k"] = np.concatenate([i["cmp_w2_k"][0]] * 2, 1)
    a["cmp_w2_v"] = i["cmp_w2_v"][0]
    a["sgu_wT"] = i["sgu_w"][0].transpose(2, 0, 1).reshape(P, -1)
    a["sgu_norm"] = i["sgu_norm"]
    a["sgu_b"] = i["sgu_b"][0]
    a["w_out"] = units_of(i["w_out"][0], 4)
    up = units_of(i["w_up"][0], 1).reshape(2, FF_CHUNKS, P, KD, P)
    a["w_up"] = up.transpose(1, 2, 3, 0, 4).reshape(FF_CHUNKS, P, KD * 2 * P)
    a["w_down"] = units_of(i["w_down"][0], 1)

    def interleaved(v):
        return v.reshape(-1, 2, FF_CHUNKS, P).transpose(0, 2, 1, 3).reshape(-1)

    p = {n: columns(i[n][0]) for n in ("attn_norm", "ffn_norm", "cmp_b1_k", "cmp_b1_v")}
    p["cmp_pe_k"], p["cmp_pe_v"] = columns(i["cmp_pe_k"][0].reshape(-1)), columns(i["cmp_pe_v"][0].reshape(-1))
    for n in ("q_norm", "k_norm_cmp", "k_norm_slc", "k_norm_win"):
        p[n] = columns(np.concatenate([i[n][0]] * 2))
    p["conv_w"], p["conv_b"] = columns(interleaved(i["conv_w"][0])), columns(interleaved(i["conv_b"][0]))
    lay_out_second(i, a, p)
    lay_out_third(i, a, p)
    a["params"] = np.concatenate([p[n] for n in PARAM_COLUMNS], 1)
    return {n: np.ascontiguousarray(v) for n, v in a.items()}


def kernel(**inputs):
    from concourse import bacc
    from concourse.bass_utils import run_bass_kernel_spmd

    arrays = lay_out({n: np.asarray(v) for n, v in inputs.items()})
    nc = bacc.Bacc("TRN2", target_bir_lowering=False, num_devices=1)
    dram = {n: nc.dram_tensor(f"in_{n}", v.shape, F32, kind="ExternalInput").ap() for n, v in arrays.items()}
    dram["out"] = nc.dram_tensor("out", (D, T), F32, kind="ExternalOutput").ap()
    program(nc, dram)
    run = run_bass_kernel_spmd(nc, [{f"in_{n}": v for n, v in arrays.items()}], core_ids=[0])
    return run.results[0]["out"].T[None]
```

```python
import math
from contextlib import ExitStack, contextmanager

import numpy as np

import concourse.bass as bass
from concourse import mybir

F32 = mybir.dt.float32
F32R = mybir.dt.float32r
I32 = mybir.dt.int32
U32 = mybir.dt.uint32
ALU = mybir.AluOpType
ACT = mybir.ActivationFunctionType
AX_X = mybir.AxisListType.X

P = 128
T = 512
TT = T // P
D = 1024
KD = D // P
BANK = 512
NEG = -1e30
EPS = 1e-6
EPS_2 = 1e-5

NSA_HEADS, NSA_GROUPS, DH = 8, 2, 64
CMP_BLOCK, CMP_STRIDE, CMP_HIDDEN = 32, 16, 256
NCMP = (T - CMP_BLOCK) // CMP_STRIDE + 1
CMP_PAIRS = CMP_BLOCK * DH // P
REL_BUCKETS, REL_MAX_DIST = 32, 128
STRIP = T + 3 * P
SKEW = STRIP + P
D_FF = 2816
FF_CHUNKS = D_FF // P
GDN_HEADS, GDN_CHUNK, GDN_CONV = 4, 64, 4
GDN_QKV = 3 * GDN_HEADS
CONV_K = 31
BRANCHES = 4
PLE = 256
ALPHA = 2 ** 0.25
CTX = 256
TA = T + CTX
DIFF_HEADS, MLA_HEADS = 4, 4
LAM_INIT = 0.8 - 0.6 * math.exp(0.0)
EXPERTS, TOP_K, D_FF_3 = 32, 4, 1024
LIMIT, SWIGLU_ALPHA = 7.0, 1.702
SLOTS_MAX = T * TOP_K // P + EXPERTS - 1


class Core:

    def __init__(self, nc, ctx, dram):
        self.nc, self.ctx, self.dram = nc, ctx, dram
        self.psum = ctx.enter_context(nc.psum_tensor("psum", [P, 8 * BANK], F32))
        self.byte_of = {}

    @contextmanager
    def tensor(self, name, shape, dtype=F32):
        with self.nc.sbuf_tensor(name, shape, dtype) as t:
            self.byte_of[t.name] = self.nc.sbuf_base - 4 * math.prod(shape[1:])
            yield t

    def keep(self, name, shape, dtype=F32):
        return self.ctx.enter_context(self.tensor(name, shape, dtype))

    def over(self, name, ap, shape):
        at = self.byte_of[ap.tensor.name] + 4 * ap.offset
        return self.nc.alloc_sbuf_tensor_at(name, shape, F32R, offset=at)

    def bank(self, n, width=BANK):
        return self.psum[:, n * BANK:n * BANK + width]

    def c(self, name):
        at, n = CONST_AT[name]
        return self.const[:, at:at + n]

    def p(self, name, n=None):
        at, width = PARAM_AT[name]
        return self.param[:, at:at + width] if n is None else self.param[:, at + n:at + n + 1]

    @contextmanager
    def stage(self, name):
        nc, sems = self.nc, []
        with ExitStack() as ctx:
            def sb(what, shape, dtype=F32):
                return ctx.enter_context(self.tensor(f"{name}_{what}", shape, dtype))

            def sem(what):
                sems.append(nc.alloc_semaphore(f"{name}_{what}"))
                return sems[-1]

            yield sb, sem
        nc.clear_and_free_semaphores(sems)
        nc.all_engine_barrier()


class Steps:

    def __init__(self, eng, sem):
        self.eng, self.sem, self.n = eng, sem, 0

    def then(self, instruction):
        self.n = self.n + 1
        instruction.then_inc(self.sem, 1)

    def settle(self):
        self.eng.wait_ge(self.sem, self.n)

    def do(self, instruction):
        self.then(instruction)
        self.settle()


def wait_apart(eng, sem, count, passed):
    eng.wait_ge(sem, count)
    eng.sem_inc(passed, 1)


def at(ap, n):
    if isinstance(n, int):
        return ap[:, n, :]
    return ap[:, bass.ds(n, 1), :].rearrange("p a n -> p (a n)")


def col(ap, n):
    return ap[:, n:n + 1] if isinstance(n, int) else ap[:, bass.ds(n, 1)]



def constants():
    i = np.arange(P)
    row, colm = i[:, None], i[None, :]
    same = row // GDN_CHUNK == colm // GDN_CHUNK
    c = {
        "ident": np.eye(P),
        "ones": np.ones((P, P)),
        "halves": row // DH == colm // DH,
        "upto": np.concatenate([row <= colm, np.ones((P, 3 * P))], 1),
        "before": np.concatenate([row < colm, np.ones((P, 3 * P))], 1),
        "minus_from": -1.0 * (row >= colm),
        "minus_ones": -np.ones((P, P)),
        "not_before": np.where(row >= colm, NEG, 0.0),
        "g_upto": same & (row <= colm),
        "g_after": same & (row > colm),
    }
    for n in range(6):
        k = 1 << n
        c[f"g_level{n}"] = (row // (2 * k) == colm // (2 * k)) & (row % (2 * k) >= k) & (colm % (2 * k) < k)
    m = np.arange(T)
    c["causal"] = np.where(row - m[None, :] + 3 * P >= 0, 0.0, NEG)
    pairs, grid = DH // 4, 64
    inv = 10000.0 ** (-np.arange(pairs, dtype=np.float32) / np.float32(pairs)).astype(np.float32)
    tok = np.arange(T)
    spot = np.stack([tok // grid, tok % grid]).astype(np.float32)
    feat = i % DH
    ang = spot[feat // 32] * inv.astype(np.float32)[feat % pairs][:, None]
    c["rope_cos"], c["rope_sin"] = np.cos(ang), np.sin(ang)
    swap = np.zeros((P, P))
    for f in range(P):
        other = f + pairs if f % 32 < pairs else f - pairs
        swap[other, f] = -1.0 if f % 32 < pairs else 1.0
    c["rope_swap"] = swap
    c["any_cmp"] = (row + P * np.arange(TT)[None, :]) >= CMP_BLOCK - 1
    c["gdn_scale"] = np.full((P, 1), float(P) ** -0.5)
    c["eps"] = np.full((P, 1), EPS)
    c["eps_2"] = np.full((P, 1), EPS_2)
    c["lane"] = row
    c["lanes_on"] = row + P * np.arange(TT)[None, :]
    c["experts"] = np.broadcast_to(np.arange(EXPERTS), (P, EXPERTS))
    c["blocks"] = np.broadcast_to(np.arange(SLOTS_MAX + 1), (P, SLOTS_MAX + 1))
    c["one"] = np.ones((P, 1))
    return {k: np.ascontiguousarray(v, dtype=np.float32) for k, v in c.items()}


def bucket_rows():
    dist = 3 * P + P - 1 - np.arange(SKEW)
    half = REL_BUCKETS // 2
    d = np.maximum(dist, 1).astype(np.float32)
    log_b = half + (np.log(d / np.float32(half)) / np.float32(math.log(REL_MAX_DIST / half))
                    * np.float32(REL_BUCKETS - half)).astype(np.int32)
    bucket = np.where(dist < half, np.maximum(dist, 0), np.clip(log_b, half, REL_BUCKETS - 1))
    rows = np.zeros((REL_BUCKETS + 1, SKEW), np.float32)
    rows[bucket, np.arange(SKEW)] = dist >= 0
    rows[REL_BUCKETS] = dist < 0
    return rows


def places(named):
    found, n = {}, 0
    for name, a in named.items():
        found[name] = (n, a.shape[1])
        n += a.shape[1]
    return found, n


CONST_AT, CONST_N = places(constants())
PARAM_COLUMNS = {
    "attn_norm": 8, "ffn_norm": 8, "q_norm": 1, "k_norm_cmp": 1, "k_norm_slc": 1, "k_norm_win": 1,
    "cmp_pe_k": CMP_PAIRS, "cmp_b1_k": 2, "cmp_pe_v": CMP_PAIRS, "cmp_b1_v": 2,
    "conv_w": 3 * 2 * FF_CHUNKS, "conv_b": 2 * FF_CHUNKS,
    "b_gate": 32, "conv_qkv": GDN_CONV * GDN_QKV, "gdn_norm": 1, "conv_dw": CONV_K * 4,
    "conv_dw_bias": 4, "conv_ln_g": 4, "conv_ln_b": 4, "b_ple_gate": 8, "ln_g": 8, "ln_b": 8,
    "c": 16, "b_ada": 48, "attn_norm_w": 8, "q_norm_w": 2, "kv_norm_w": 1, "subln_w": 1,
    "ffn_norm_w": 8, "final_norm_w": 8, "lambdas": 4,
}
PARAM_AT, PARAM_N = {}, 0
for _name, _n in PARAM_COLUMNS.items():
    PARAM_AT[_name] = (PARAM_N, _n)
    PARAM_N += _n



def feature_norm(k, name, groups, matrix, scale, eps, shift=None):
    nc = k.nc
    results = [o for _, out, _ in groups for o in out]
    flat = [(g, n) for g, (src, _, _) in enumerate(groups) for n in range(len(src))]
    width = [src[0].shape[-1] for src, _, _ in groups]
    with k.stage(name) as (sb, sem):
        sq = sb("sq", [P, 3, T])
        std = sb("std", [P, 2, T])
        rstd = sb("rstd", [P, 2, T])
        squared, summed, rooted, turned, scaled, shifted = (
            sem(x) for x in ("squared", "summed", "rooted", "turned", "scaled", "shifted"))
        with nc.Block() as block:
            @block.scalar
            def _(act):
                done = 0
                for g, (src, _, _) in enumerate(groups):
                    for s in src:
                        if done >= 3:
                            act.wait_ge(summed, done - 2)
                        act.activation(sq[:, done % 3, 0:width[g]], s, ACT.Square).then_inc(squared, 1)
                        done += 1
                    act.wait_ge(summed, done)
                    if g >= 2:
                        act.wait_ge(turned, g - 1)
                    act.activation(std[:, g % 2, 0:width[g]], k.bank(g % 2, width[g]), ACT.Sqrt,
                                   bias=k.c(eps), scale=scale).then_inc(rooted, 1)
                for n, o in enumerate(results if shift else []):
                    act.wait_ge(scaled, n + 1)
                    act.activation(o, o, ACT.Identity, bias=shift[n]).then_inc(shifted, 1)

            @block.tensor
            def _(pe):
                for n, (g, s) in enumerate(flat):
                    pe.wait_ge(squared, n + 1)
                    if s == 0 and g >= 2:
                        pe.wait_ge(rooted, g - 1)
                    pe.matmul(k.bank(g % 2, width[g]), matrix, sq[:, n % 3, 0:width[g]], start=(s == 0),
                              stop=(s == len(groups[g][0]) - 1)).then_inc(summed, 1)

            @block.vector
            def _(dve):
                for g, (src, out, gain) in enumerate(groups):
                    dve.wait_ge(rooted, g + 1)
                    r = rstd[:, g % 2, 0:width[g]]
                    dve.reciprocal(r, std[:, g % 2, 0:width[g]]).then_inc(turned, 1)
                    dve.wait_ge(turned, g + 1)
                    for n, s in enumerate(src):
                        if gain is None:
                            dve.tensor_tensor(out[n], s, r, ALU.mult).then_inc(scaled, 1)
                        else:
                            dve.scalar_tensor_tensor(out[n], s, gain[n], r, ALU.mult,
                                                     ALU.mult).then_inc(scaled, 1)



def leading_bits(dve, out, src):
    return dve.tensor_copy(out, src)


def rest_bits(dve, out, src, leading):
    return dve.tensor_tensor(out, src, leading.bitcast(F32), ALU.subtract)


def three_passes(pe, out, left, right, start, stop):
    (lh, ll), (rh, rl) = left, right
    pe.matmul(out, lh, rh, start=start, stop=False)
    pe.matmul(out, lh, rl, start=False, stop=False)
    return pe.matmul(out, ll, rh, start=False, stop=stop)


class Parts:

    def __init__(self, leading, rest):
        self.leading, self.rest = leading, rest


class Section:

    def __init__(self, weights, units, kc, source, finish, engine, chunks=4, width=T, by_tokens=False, rows=P, spent=False, split=True):
        self.weights, self.units, self.kc, self.source = weights, units, kc, source
        self.finish, self.engine, self.chunks = finish, engine, chunks
        self.width, self.by_tokens, self.rows, self.spent = width, by_tokens, rows, spent
        self.columns = width if by_tokens else chunks * P
        self.pieces = 1 if by_tokens else chunks
        self.split = split and width >= 2 * P


def run_units(eng, units, start, body):
    pairs = (units - 1) // 2
    if pairs >= 2:
        with eng.Fori(0, pairs) as i:
            for s in range(2):
                body(2 * i + s, (start + s) % 2, i)
    else:
        pairs = 0
    for u in range(2 * pairs, units):
        body(u, (start + u) % 2, u // 2)


def project(k, name, sections, beside=None, room={}):
    nc = k.nc
    starts, landed0, done0, split0 = [], [], [], []
    n, lands, dones, splits = 0, [0, 0], [0, 0], [0, 0]
    for s in sections:
        if beside is not None:
            s.split = False
        starts.append(n)
        landed0.append(list(lands))
        done0.append(list(dones))
        split0.append(list(splits))
        for u in range(s.units):
            lands[(n + u) % 2] += 1
            dones[(n + u) % 2] += s.chunks
            splits[(n + u) % 2] += s.split
        n += s.units
    pieces = max([s.pieces for s in sections if s.split], default=1)
    size = max(s.kc * s.columns for s in sections)
    with k.stage(name) as (sb, sem):
        ring = sb("weights", [P, 2, size])
        landed = [sem(f"weights{i}_landed") for i in range(2)]
        ready = [sem(f"sums{i}_ready") for i in range(2)]
        emptied = [sem(f"banks{i}_emptied") for i in range(2)]
        apart = {}
        if any(s.split for s in sections):
            widest = max(s.kc * s.columns for s in sections if s.split)
            if "leading" in room:
                leading = [k.over(f"{name}_leading{i}", a, [P, widest]) for i, a in enumerate(room["leading"])]
            else:
                leading = [sb(f"leading{i}", [P, widest], F32R) for i in range(2)]
            rest = [k.over(f"{name}_rest{i}", ring[:, i, :], [P, widest]) for i in range(2)]
            masked = [sem(f"weights{i}_masked") for i in range(2)]
            split = [sem(f"weights{i}_split") for i in range(2)]
            source_masked, source_split = sem("source_masked"), sem("source_split")
        to_split = []
        for s in sections:
            if s.split and isinstance(s.source, Parts):
                apart[id(s.source)] = (s.source, 0)
            elif s.split and id(s.source) not in apart:
                shape = [P, s.kc, s.source.shape[-1]]
                free = list(room.get("parts", [])) if not apart else []
                places = [free.pop(0) if free else None, s.source if s.spent else free.pop(0) if free else None]
                high, low = (k.over(f"{name}_{x}{len(apart)}", a[:, :, :], shape) if a is not None else sb(f"{x}{len(apart)}", shape, F32R)
                             for x, a in zip(("source_leading", "source_rest"), places))
                apart[id(s.source)] = (Parts(high, low), sum(x.kc for x, _ in to_split) + s.kc)
                to_split.append((s, apart[id(s.source)][0]))

        with nc.Block() as block:
            @block.sync
            def _(sp):
                for q, s in enumerate(sections):
                    def load(u, slot, turn, q=q, s=s):
                        sp.wait_ge(emptied[slot], turn * s.chunks + done0[q][slot])
                        src = s.weights[u, :, :] if isinstance(u, int) else \
                            s.weights[bass.ds(u, 1), :, :].rearrange("a p n -> p (a n)")
                        sp.dma_start(ring[:, slot, 0:s.kc * s.columns], src).then_inc(landed[slot], 16)
                    run_units(sp, s.units, starts[q], load)

            @block.tensor
            def _(pe):
                for q, s in enumerate(sections):
                    if s.split and apart[id(s.source)][1]:
                        pe.wait_ge(source_split, apart[id(s.source)][1])

                    def products(u, slot, turn, q=q, s=s):
                        w = ring[:, slot, 0:s.kc * s.columns].rearrange("p (k n) -> p k n", k=s.kc)
                        if s.split:
                            high, low = (x[slot][:, 0:s.kc * s.columns].rearrange("p (k n) -> p k n", k=s.kc)
                                         for x in (leading, rest))
                            source = apart[id(s.source)][0]
                        else:
                            pe.wait_ge(landed[slot], turn * 16 + 16 * landed0[q][slot] + 16)
                        pe.wait_ge(emptied[slot], turn * s.chunks + done0[q][slot])
                        for j in range(s.chunks):
                            if s.split and j < s.pieces:
                                first = pieces - s.pieces
                                pe.wait_ge(split[slot], (turn + split0[q][slot]) * pieces + first + j + 1)
                            out = k.bank(4 * slot + j, s.width)[0:s.rows, :]
                            for kk in range(s.kc):
                                def both(x):
                                    tok = x[:, kk, j * P:j * P + s.rows] if s.by_tokens else x[:, kk, 0:s.width]
                                    return tok

                                def of(x):
                                    return x[:, kk, :] if s.by_tokens else x[:, kk, j * P:(j + 1) * P]
                                ends = {"start": kk == 0, "stop": kk == s.kc - 1}
                                if s.split:
                                    pair = (both(source.leading), both(source.rest)), (of(high), of(low))
                                    left, right = pair if s.by_tokens else pair[::-1]
                                    last = three_passes(pe, out, left, right, **ends)
                                else:
                                    left, right = (both(s.source), of(w)) if s.by_tokens else (of(w), both(s.source))
                                    last = pe.matmul(out, left, right, **ends)
                            last.then_inc(ready[slot], 1)
                    run_units(pe, s.units, starts[q], products)

            def take(eng, q, s, u, slot, turn):
                for j in range(s.chunks):
                    eng.wait_ge(ready[slot], turn * s.chunks + done0[q][slot] + j + 1)
                    s.finish(eng, u * s.chunks + j, k.bank(4 * slot + j, s.width)[0:s.rows, :]).then_inc(emptied[slot], 1)

            @block.scalar
            def _(act):
                for q, s in enumerate(sections):
                    if s.engine == "scalar":
                        run_units(act, s.units, starts[q], lambda u, slot, turn, q=q, s=s: take(act, q, s, u, slot, turn))

            @block.vector
            def _(dve):
                def split_unit(q, u, slot, turn):
                    s = sections[q]
                    if not s.split:
                        return
                    w, high = ring[:, slot, 0:s.kc * s.columns], leading[slot][:, 0:s.kc * s.columns]
                    dve.wait_ge(landed[slot], turn * 16 + 16 * landed0[q][slot] + 16)
                    leading_bits(dve, high, w).then_inc(masked[slot], 1)
                    dve.wait_ge(masked[slot], turn + split0[q][slot] + 1)
                    w, high, low = (x.rearrange("p (k n) -> p k n", k=s.kc) for x in (w, high, rest[slot][:, 0:s.kc * s.columns]))
                    n = s.columns // s.pieces
                    for j in range(s.pieces):
                        here = slice(j * n, (j + 1) * n)
                        rest_bits(dve, low[:, :, here], w[:, :, here], high[:, :, here]
                                  ).then_inc(split[slot], 1 if j else pieces - s.pieces + 1)

                n = 0
                for s, parts in to_split:
                    for kk in range(s.kc):
                        leading_bits(dve, parts.leading[:, kk, :], s.source[:, kk, :]).then_inc(source_masked, 1)
                    for kk in range(s.kc):
                        n += 1
                        dve.wait_ge(source_masked, n)
                        rest_bits(dve, parts.rest[:, kk, :], s.source[:, kk, :], parts.leading[:, kk, :]
                                  ).then_inc(source_split, 1)
                split_unit(0, 0, starts[0] % 2, 0)
                for q, s in enumerate(sections):
                    def step(u, slot, turn, q=q, s=s):
                        if isinstance(u, int) and u + 1 == s.units:
                            if q + 1 < len(sections):
                                split_unit(q + 1, 0, starts[q + 1] % 2, 0)
                        else:
                            split_unit(q, u + 1, 1 - slot, turn + (slot != starts[q] % 2))
                        if s.engine == "vector":
                            take(dve, q, s, u, slot, turn)
                    if s.split or s.engine == "vector" or q + 1 < len(sections):
                        run_units(dve, s.units, starts[q], step)
                if beside is not None:
                    beside(dve, sem)


def copies_to(dst):
    return lambda eng, n, ps: eng.tensor_copy(at(dst, n), ps)


def adds_to(dst):
    return lambda eng, n, ps: eng.tensor_tensor(at(dst, n), ps, at(dst, n), ALU.add)


def activates_to(dst, func, bias=None):
    def finish(eng, n, ps):
        if bias is None:
            return eng.activation(at(dst, n), ps, func)
        return eng.activation(at(dst, n), ps, func, bias=col(bias, n))
    return finish


def head_copies(dst, src):
    return [(dst[h * DH:(h + 1) * DH, h, :], src[h * DH:(h + 1) * DH, :]) for h in range(2)]


class Unit:

    def __init__(self, products, keys, bias, gate, tiles, out, group, opens, closes):
        self.products, self.keys, self.bias, self.gate = products, keys, bias, gate
        self.tiles, self.out, self.group, self.opens, self.closes = tiles, out, group, opens, closes


def attention(k, name, rounds, copies, units, results, padded=(), gating=False):
    nc = k.nc
    sequence = [u for slot in range(2) for u in units(slot)]
    N = len(sequence)
    U = N // 2
    wide = max(u.keys for u in sequence) > BANK
    score_buffers, turn_buffers = (2, 1) if wide else (4, 2)
    keys_max = max(u.keys for u in sequence)
    G = max(u.group for u in sequence) + 1
    n_copies = len(copies(0, 0))
    AHEAD = 3

    def group(n):
        return (n // U) * G + sequence[n].group

    closing = {group(n): n for n in range(N)}
    with k.stage(name) as (sb, sem):
        masked_sb = sb("masked", [P, AHEAD, keys_max])
        probs = sb("probs", [P, AHEAD, keys_max])
        top, total, inverse = (sb(x, [P, AHEAD]) for x in ("top", "total", "inverse"))
        diag = sb("diag", [P, AHEAD, P])
        turned_sb = sb("turned", [P, 2, -(-keys_max // P) * P])
        scored, masked, exped, inverted, weighed, turned, copied, taken, passed, cleared = (sem(x) for x in (
            "scores_ready", "scores_masked", "probs_ready", "sums_inverted", "weights_ready",
            "probs_turned", "probs_copied", "results_taken", "waits_passed", "padding_cleared"))
        staged, summed = ([sem(f"{x}{slot}") for slot in range(2)] for x in ("operands_staged", "values_summed"))

        def scores_bank(n, keys):
            at = n % score_buffers * (4 // score_buffers) * BANK
            return k.psum[:, at:at + keys]

        def turned_bank(n):
            return k.psum[:, (4 + n % turn_buffers) * BANK:(6 if wide else 5 + n % turn_buffers) * BANK]

        def out_bank(g):
            return k.psum[:, (6 + g % 2) * BANK:(6 + g % 2) * BANK + P]

        def loop(eng, body):
            if rounds == 2:
                body(0)
            else:
                with eng.Fori(0, rounds // 2) as i:
                    body(i)

        with nc.Block() as block:
            @block.gpsimd
            def _(pool):
                for place in padded:
                    pool.memset(place, 0.0).then_inc(cleared, 1)

            @block.sync
            def _(sp):
                if padded:
                    sp.wait_ge(cleared, len(padded))

                def body(i):
                    for slot in range(2):
                        if rounds > 2:
                            sp.wait_ge(summed[slot], i * U)
                        for dst, src in copies(i, slot):
                            sp.dma_start(dst, src).then_inc(staged[slot], 16)
                loop(sp, body)

            @block.tensor
            def _(pe):
                def body(i):
                    for step in range(N + 3):
                        if step < N:
                            u = sequence[step]
                            if step % U == 0:
                                pe.wait_ge(staged[step // U], i * 16 * n_copies + 16 * n_copies)
                            if step >= score_buffers:
                                pe.wait_ge(masked, i * N + step - score_buffers + 1)
                            for lo in range(0, u.keys, BANK):
                                hi = min(lo + BANK, u.keys)
                                for m, (left, right) in enumerate(u.products):
                                    last = pe.matmul(scores_bank(step, u.keys)[:, lo:hi], left, right[:, lo:hi],
                                                     start=(m == 0), stop=(m == len(u.products) - 1))
                            last.then_inc(scored, 1)
                        v = step - 2
                        if 0 <= v < N:
                            u = sequence[v]
                            pe.wait_ge(weighed, i * N + v + 1)
                            if v >= turn_buffers:
                                pe.wait_ge(copied, i * N + v + 1 - turn_buffers)
                            for n, (lo, keys, _) in enumerate(u.tiles):
                                last = pe.matmul(turned_bank(v)[0:keys, n * P:(n + 1) * P],
                                                 probs[:, v % AHEAD, lo:lo + keys], diag[:, v % AHEAD, :],
                                                 start=True, stop=True)
                            last.then_inc(turned, 1)
                        w = step - 3
                        if 0 <= w < N:
                            u = sequence[w]
                            pe.wait_ge(copied, i * N + w + 1)
                            if u.opens and group(w) >= 2:
                                pe.wait_ge(taken, i * 2 * G + group(w) - 1)
                            for n, (_, keys, values) in enumerate(u.tiles):
                                last = pe.matmul(out_bank(group(w))[u.out[0]:u.out[1], :], values,
                                                 turned_sb[0:keys, w % 2, n * P:(n + 1) * P],
                                                 start=(u.opens and n == 0), stop=(u.closes and n == len(u.tiles) - 1))
                            last.then_inc(summed[w // U], 1)
                loop(pe, body)

            @block.vector
            def _(dve):
                def body(i):
                    for step in range(N + 4):
                        if step < N:
                            u, b = sequence[step], step % AHEAD
                            if step % U == 0:
                                dve.wait_ge(staged[step // U], i * 16 * n_copies + 16 * n_copies)
                            if step >= AHEAD:
                                dve.wait_ge(exped, i * N + step - AHEAD + 1)
                            wait_apart(dve, scored, i * N + step + 1, passed)
                            dve.tensor_tensor_reduce(masked_sb[:, b, 0:u.keys], scores_bank(step, u.keys), u.bias,
                                                     -1.0, 3.0e38, ALU.add, ALU.min, top[:, b:b + 1]).then_inc(masked, 1)
                        v = step - 1
                        if 0 <= v < N:
                            u, b = sequence[v], v % AHEAD
                            dve.wait_ge(exped, i * N + v + 1)
                            dve.reciprocal(inverse[:, b:b + 1], total[:, b:b + 1]).then_inc(inverted, 1)
                            if v >= AHEAD:
                                dve.wait_ge(turned, i * N + v - AHEAD + 1)
                            dve.wait_ge(inverted, i * N + v + 1)
                            dve.tensor_scalar(diag[:, b, :], k.c("ident"), inverse[:, b:b + 1], u.gate,
                                              ALU.mult, ALU.mult).then_inc(weighed, 1)
                        w = step - 4
                        if 0 <= w < N and closing[group(w)] == w:
                            dve.wait_ge(summed[w // U], i * U + w % U + 1)
                            g = group(w)
                            dst = results(2 * i + g // G, g % G)
                            if gating:
                                dve.tensor_tensor(dst, out_bank(g), dst, ALU.mult).then_inc(taken, 1)
                            else:
                                dve.tensor_copy(dst, out_bank(g)).then_inc(taken, 1)
                loop(dve, body)

            @block.scalar
            def _(act):
                def body(i):
                    for step in range(N + 2):
                        if step < N:
                            u, b = sequence[step], step % AHEAD
                            if step >= AHEAD:
                                act.wait_ge(turned, i * N + step - AHEAD + 1)
                            act.wait_ge(masked, i * N + step + 1)
                            act.activation(probs[:, b, 0:u.keys], masked_sb[:, b, 0:u.keys], ACT.Exp, scale=-1.0,
                                           bias=top[:, b:b + 1], accum_out=total[:, b:b + 1]).then_inc(exped, 1)
                        v = step - 2
                        if 0 <= v < N:
                            u, b = sequence[v], v % 2
                            if v >= 2:
                                act.wait_ge(summed[(v - 2) // U], i * U + (v - 2) % U + 1)
                            act.wait_ge(turned, i * N + v + 1)
                            rows = max(keys for _, keys, _ in u.tiles)
                            act.copy(turned_sb[0:rows, b, 0:len(u.tiles) * P],
                                     turned_bank(v)[0:rows, 0:len(u.tiles) * P]).then_inc(copied, 1)
                loop(act, body)



def load_inputs(k):
    nc = k.nc
    with k.stage("inputs") as (sb, sem):
        landed = sem("inputs_landed")
        with nc.Block() as block:
            @block.sync
            def _(sp):
                sp.dma_start(k.x[:, :, :], k.dram["xT"].rearrange("(k p) t -> p k t", p=P)).then_inc(landed, 16)
                sp.dma_start(k.param[:, :], k.dram["params"]).then_inc(landed, 16)
                sp.wait_ge(landed, 48)

            @block.scalar
            def _(act):
                act.dma_start(k.const[:, :], k.dram["consts"]).then_inc(landed, 16)


def bias_strips(k, strips):
    nc = k.nc
    rows = REL_BUCKETS + 1
    skewed = nc.dram_tensor("bias_skewed", (NSA_HEADS, P * (SKEW + 1)), F32, kind="Internal").ap()
    with k.stage("strips") as (sb, sem):
        bias = sb("rel_bias", [rows, NSA_HEADS])
        hot = sb("buckets", [rows, SKEW])
        spread = sb("spread", [rows, NSA_HEADS, P])
        line = sb("line", [P, 2, SKEW])
        landed, filled, spreaded, ready, copied, written, back = (sem(x) for x in (
            "inputs_landed", "mask_row_set", "bias_spread", "lines_ready", "lines_copied", "lines_written",
            "strips_landed"))
        with nc.Block() as block:
            @block.sync
            def _(sp):
                sp.dma_start(bias[0:REL_BUCKETS, :], k.dram["rel_bias"]).then_inc(landed, 16)
                sp.dma_start(hot[:, :], k.dram["buckets"]).then_inc(landed, 16)
                for h in range(NSA_HEADS):
                    sp.wait_ge(copied, 2 * h + 2)
                    sp.dma_start(skewed[h].rearrange("(p w) -> p w", w=SKEW + 1)[:, 0:SKEW],
                                 line[:, h % 2, :]).then_inc(written, 16)
                    sp.wait_ge(written, 16 * h + 16)
                    sp.dma_start(strips[:, h, :], skewed[h, P - 1:P - 1 + P * SKEW].rearrange("(p w) -> p w", w=SKEW)
                                 [:, 0:STRIP]).then_inc(back, 16)
                sp.wait_ge(back, 16 * NSA_HEADS)

            @block.vector
            def _(dve):
                dve.memset(bias[REL_BUCKETS:rows, :], NEG).then_inc(filled, 1)
                dve.wait_ge(filled, 1)
                dve.wait_ge(landed, 32)
                for h in range(NSA_HEADS):
                    dve.tensor_scalar(spread[:, h, :], k.c("ones")[0:rows, :], bias[:, h:h + 1], None,
                                      ALU.mult).then_inc(spreaded, 1)
                for h in range(NSA_HEADS):
                    if h >= 2:
                        dve.wait_ge(written, 16 * h - 16)
                    for half in range(2):
                        dve.wait_ge(ready, 2 * h + half + 1)
                        dve.tensor_copy(line[:, h % 2, half * BANK:(half + 1) * BANK],
                                        k.bank(2 * (h % 2) + half)).then_inc(copied, 1)

            @block.tensor
            def _(pe):
                for h in range(NSA_HEADS):
                    pe.wait_ge(spreaded, h + 1)
                    if h >= 2:
                        pe.wait_ge(copied, 2 * h - 2)
                    for half in range(2):
                        pe.matmul(k.bank(2 * (h % 2) + half), spread[:, h, :], hot[:, half * BANK:(half + 1) * BANK],
                                  start=True, stop=True).then_inc(ready, 1)


def first_norm(k, src, out, gain, name, eps="eps"):
    feature_norm(k, name, [([src[:, n, :] for n in range(KD)], [out[:, n, :] for n in range(KD)],
                            [k.p(gain, n) for n in range(KD)])], k.c("ones"), 1.0 / D, eps)


def twice(k, name, pairs):
    with k.stage(name) as (sb, sem):
        moved = sem("copies_moved")
        with k.nc.Block() as block:
            @block.sync
            def _(sp):
                for dst, src in pairs:
                    sp.dma_start(dst, src).then_inc(moved, 16)
                sp.wait_ge(moved, 16 * len(pairs))


def compress(k, raw_kc, raw_vc, k_cmp, v_cmp):
    nc = k.nc
    N = NSA_GROUPS * NCMP
    with k.stage("compress") as (sb, sem):
        pairs = [sb(f"pairs_{x}", [P, NSA_GROUPS, T]) for x in "kv"]
        w1 = [sb(f"w1_{x}", [P, CMP_PAIRS, CMP_HIDDEN]) for x in "kv"]
        w2k = sb("w2_k", [P, 2, P])
        w2v = sb("w2_v", [P, 2, DH])
        hid = [sb(f"hidden_{x}", [P, 2, N]) for x in "kv"]
        bias = sb("bias", [P, 4])
        landed, cleared, hidden, based, gelued, outs, copied = (sem(x) for x in (
            "inputs_landed", "ends_cleared", "hidden_ready", "bias_ready", "hidden_gelued", "outputs_ready",
            "outputs_copied"))
        raws = (raw_kc, raw_vc)
        with nc.Block() as block:
            @block.sync
            def _(sp):
                sp.wait_ge(cleared, 2)
                for n in range(2):
                    for g in range(NSA_GROUPS):
                        sp.dma_start(pairs[n][0:DH, g, :], raws[n][g * DH:(g + 1) * DH, :]).then_inc(landed, 16)
                        sp.dma_start(pairs[n][DH:P, g, 0:T - 1],
                                     raws[n][g * DH:(g + 1) * DH, 1:T]).then_inc(landed, 16)
                    sp.dma_start(w1[n][:, :, :], k.dram[f"cmp_w1_{'kv'[n]}"].rearrange("(j p) n -> p j n", p=P)
                                 ).then_inc(landed, 16)
                sp.dma_start(w2k[:, :, :], k.dram["cmp_w2_k"].rearrange("(c p) n -> p c n", p=P)).then_inc(landed, 16)
                sp.dma_start(w2v[:, :, :], k.dram["cmp_w2_v"].rearrange("(c p) n -> p c n", p=P)).then_inc(landed, 16)

            @block.gpsimd
            def _(pool):
                for n in range(2):
                    pool.memset(pairs[n][:, :, T - 1:T], 0.0).then_inc(cleared, 1)

            @block.tensor
            def _(pe):
                pe.wait_ge(landed, 16 * 12)
                for n in range(2):
                    for c in range(2):
                        b = 2 * n + c
                        pe_col = k.p(f"cmp_pe_{'kv'[n]}")
                        for j in range(CMP_PAIRS):
                            pe.matmul(k.bank(b, N), w1[n][:, j, c * P:(c + 1) * P],
                                      pairs[n][:, :, 2 * j:2 * j + CMP_STRIDE * (NCMP - 1) + 1:CMP_STRIDE],
                                      start=(j == 0), stop=(j == CMP_PAIRS - 1))
                        for j in range(CMP_PAIRS):
                            last = pe.matmul(k.psum[:, (4 + b) * BANK:(4 + b) * BANK + 1], w1[n][:, j, c * P:(c + 1) * P],
                                             pe_col[:, j:j + 1], start=(j == 0), stop=(j == CMP_PAIRS - 1))
                        last.then_inc(hidden, 1)
                pe.wait_ge(gelued, 4)
                for c in range(2):
                    last = pe.matmul(k.bank(0, N), w2k[:, c, :], hid[0][:, c, :], start=(c == 0), stop=(c == 1))
                last.then_inc(outs, 1)
                for g in range(NSA_GROUPS):
                    for c in range(2):
                        last = pe.matmul(k.psum[0:NCMP, (1 + g) * BANK:(1 + g) * BANK + DH],
                                         hid[1][:, c, g * NCMP:(g + 1) * NCMP], w2v[:, c, :],
                                         start=(c == 0), stop=(c == 1))
                    last.then_inc(outs, 1)

            @block.vector
            def _(dve):
                for n in range(2):
                    for c in range(2):
                        b = 2 * n + c
                        dve.wait_ge(hidden, b + 1)
                        dve.tensor_tensor(bias[:, b:b + 1], k.psum[:, (4 + b) * BANK:(4 + b) * BANK + 1],
                                          k.p(f"cmp_b1_{'kv'[n]}", c), ALU.add).then_inc(based, 1)
                dve.wait_ge(outs, 1)
                dve.tensor_copy(k_cmp[:, :, :].rearrange("p g n -> p (g n)"), k.bank(0, N)).then_inc(copied, 1)
                for g in range(NSA_GROUPS):
                    dve.wait_ge(outs, 2 + g)
                    dve.tensor_copy(v_cmp[0:NCMP, g, :], k.psum[0:NCMP, (1 + g) * BANK:(1 + g) * BANK + DH]
                                    ).then_inc(copied, 1)

            @block.scalar
            def _(act):
                for n in range(2):
                    for c in range(2):
                        b = 2 * n + c
                        act.wait_ge(based, b + 1)
                        act.activation(hid[n][:, c, :], k.bank(b, N), ACT.Gelu_apprx_tanh,
                                       bias=bias[:, b:b + 1]).then_inc(gelued, 1)


def sparse_attention(k, q, k_cmp, v_cmp, k_slc, k_win, v_both, gates, strips, out):
    for g in range(NSA_GROUPS):
        with ExitStack() as ctx:
            def sb(what, shape):
                return ctx.enter_context(k.tensor(f"nsa{g}_{what}", shape, F32))

            qs = sb("q", [P, 2, 2, T])
            strip = sb("strip", [P, 2, 2, STRIP])

            def copies(i, slot, g=g):
                pair, h = 2 * g + slot, 4 * g + 2 * slot
                return [*head_copies(qs[:, slot, :, :], at(q, pair)), (strip[:, slot, :, :], strips[:, h:h + 2, :])]

            def units(slot, g=g):
                found = []
                for t in range(TT):
                    keys = (t + 1) * P
                    lo = 3 * P - t * P
                    for h in range(2):
                        query = qs[:, slot, h, t * P:(t + 1) * P]
                        gate = gates[:, t, 4 * g + 2 * slot + h, :]
                        first = lo + CMP_BLOCK - 1
                        found.append(Unit([(query, k_cmp[:, g, :])], NCMP,
                                          strip[:, slot, h, first:first + CMP_STRIDE * (NCMP - 1) + 1:CMP_STRIDE],
                                          gate[:, 0:1], [(0, NCMP, v_cmp[0:NCMP, g, :])],
                                          (h * DH, (h + 1) * DH), t, True, False))
                        for b, keys_of in ((1, k_slc), (2, k_win)):
                            found.append(Unit([(query, keys_of[:, g, 0:keys])], keys, strip[:, slot, h, lo:lo + keys],
                                              gate[:, b:b + 1],
                                              [(n * P, P, v_both[:, n, (b - 1) * P + g * DH:(b - 1) * P + (g + 1) * DH])
                                               for n in range(t + 1)],
                                              (h * DH, (h + 1) * DH), t, False, b == 2))
                return found

            def results(i, t, g=g):
                return at(out, 2 * g + i)[:, t * P:(t + 1) * P]

            attention(k, f"nsa{g}", 2, copies, units, results, padded=[qs[:, :, :, :]])


def spatial_gate(k, u, v, out):
    nc = k.nc
    G, chunks = 8, T // P
    with k.stage("sgu") as (sb, sem):
        w = sb("w", [P, G, P])
        gain = sb("gain", [P, T])
        b = sb("b", [P, G // 2, P])
        junk = sb("squares", [P, T])
        mean = sb("mean", [P, chunks])
        root = sb("root", [P, chunks])
        rstd = sb("rstd", [P, chunks])
        z = sb("z", [P, 2, T])
        landed, masked, squared, rooted, turned, scaled, mixed, biased, gated = (sem(x) for x in (
            "inputs_landed", "w_masked", "v_squared", "v_rooted", "rstd_ready", "v_scaled", "z_ready", "z_biased",
            "results_ready"))
        with nc.Block() as block:
            @block.sync
            def _(sp):
                sp.dma_start(w[:, :, :], k.dram["sgu_wT"].rearrange("j (g i) -> j g i", g=G)).then_inc(landed, 16)
                sp.dma_start(gain[:, :], k.dram["sgu_norm"][0:1, :].broadcast_to([P, T])).then_inc(landed, 16)
                for g in range(G):
                    sp.dma_start(b[(g % 2) * DH:(g % 2 + 1) * DH, g // 2, :],
                                 k.dram["sgu_b"][g:g + 1, :].broadcast_to([DH, P])).then_inc(landed, 16)

            @block.scalar
            def _(act):
                for c in range(chunks):
                    if c:
                        act.wait_ge(squared, c)
                    act.activation(junk[:, :], v[:, c, :], ACT.Square, accum_out=mean[:, c:c + 1]).then_inc(squared, 1)
                act.wait_ge(squared, chunks)
                act.activation(root[:, :], mean[:, :], ACT.Sqrt, bias=k.c("eps"), scale=1.0 / T).then_inc(rooted, 1)

            @block.vector
            def _(dve):
                dve.wait_ge(landed, 16 * (2 + G))
                for g in range(G):
                    dve.tensor_tensor(w[:, g, :], w[:, g, :], k.c("upto")[:, 0:P], ALU.mult).then_inc(masked, 1)
                dve.wait_ge(rooted, 1)
                dve.reciprocal(rstd[:, :], root[:, :]).then_inc(turned, 1)
                dve.wait_ge(turned, 1)
                for c in range(chunks):
                    dve.scalar_tensor_tensor(v[:, c, :], v[:, c, :], rstd[:, c:c + 1], gain[:, :], ALU.mult,
                                             ALU.mult).then_inc(scaled, 1)
                for n in range(G // 2):
                    dve.wait_ge(mixed, n + 1)
                    zn = z[:, n % 2, :]
                    if n >= 2:
                        dve.wait_ge(gated, n - 1)
                    dve.tensor_tensor(zn.rearrange("p (c i) -> p c i", c=chunks),
                                      k.bank(n).rearrange("p (c i) -> p c i", c=chunks),
                                      b[:, n:n + 1, :].broadcast_to([P, chunks, P]), ALU.add).then_inc(biased, 1)
                    dve.wait_ge(biased, n + 1)
                    dve.tensor_tensor(out[:, n, :], zn, u[:, n, :], ALU.mult).then_inc(gated, 1)

            @block.tensor
            def _(pe):
                pe.wait_ge(masked, G)
                pe.wait_ge(scaled, chunks)
                for n in range(G // 2):
                    for h in range(2):
                        g = 2 * n + h
                        for c in range(chunks):
                            last = pe.matmul(k.psum[h * DH:(h + 1) * DH, n * BANK + c * P:n * BANK + (c + 1) * P],
                                             v[:, c, g * DH:(g + 1) * DH], w[:, g, :], start=True, stop=True)
                    last.then_inc(mixed, 1)


def feed_forward_up(k, src, out):
    nc = k.nc
    units = FF_CHUNKS
    width = KD * 2 * P
    with k.stage("ff_up") as (sb, sem):
        ring = sb("weights", [P, 2, width])
        leading = sb("leading", [P, 2, width], F32R)
        rest = k.over("ff_up_rest", ring[:, :, :], [P, 2, width])
        source = Parts(sb("source_leading", [P, KD, T], F32R), k.over("ff_up_source_rest", src[:, :, :], [P, KD, T]))
        conv = sb("conv", [P, 4, T])
        gate = sb("gate", [P, 2, T])
        hidden = sb("hidden", [P, 2, T])
        landed, masked, split, ready, based, tapped, silued, timed, kept, done = ([sem(f"{x}{i}") for i in range(2)] for x in (
            "weights_landed", "weights_masked", "weights_split", "sums_ready", "last_tap", "taps_added", "gate_ready",
            "hidden_ready", "hidden_masked", "unit_done"))
        own = [sem(f"tap_written{i}") for i in range(2)]
        source_masked, source_split = sem("source_masked"), sem("source_split")

        def pairs(eng, body):
            with eng.Fori(0, units // 2 - 1) as i:
                for s in range(2):
                    body(i, s, 2 * i + s)
            for s in range(2):
                body(units // 2 - 1, s, units - 2 + s)

        with nc.Block() as block:
            @block.sync
            def _(sp):
                def body(i, s, n):
                    sp.wait_ge(ready[s], 2 * i)
                    unit = k.dram["w_up"][n, :, :] if isinstance(n, int) else \
                        k.dram["w_up"][bass.ds(n, 1), :, :].rearrange("a p n -> p (a n)")
                    sp.dma_start(ring[:, s, :], unit).then_inc(landed[s], 16)
                pairs(sp, body)

            @block.tensor
            def _(pe):
                def body(i, s, n):
                    high, low = (w[:, s, :].rearrange("p (k n) -> p k n", k=KD) for w in (leading, rest))
                    pe.wait_ge(split[s], i + 1)
                    pe.wait_ge(tapped[s], 2 * i)
                    for j in range(2):
                        here = slice(j * P, (j + 1) * P)
                        for kk in range(KD):
                            last = three_passes(pe, k.bank(2 * s + j), (high[:, kk, here], low[:, kk, here]),
                                                (source.leading[:, kk, :], source.rest[:, kk, :]), kk == 0, kk == KD - 1)
                        last.then_inc(ready[s], 1)
                pe.wait_ge(source_split, KD)
                pairs(pe, body)

            @block.scalar
            def _(act):
                w, b = k.p("conv_w"), k.p("conv_b")

                def body(i, s, n):
                    act.wait_ge(timed[s], i)
                    for j in range(2):
                        act.wait_ge(ready[s], 2 * i + j + 1)
                        act.activation(conv[:, 2 * s + j, :], k.bank(2 * s + j), ACT.Identity,
                                       bias=col(b, 2 * n + j), scale=col(w, 2 * 2 * FF_CHUNKS + 2 * n + j)
                                       ).then_inc(based[s], 1)
                    act.wait_ge(tapped[s], 2 * i + 2)
                    act.activation(gate[:, s, :], conv[:, 2 * s + 1, :], ACT.Silu).then_inc(silued[s], 1)
                    act.wait_ge(timed[s], i + 1)
                    act.activation(at(out.leading, n), hidden[:, s, :], ACT.Copy).then_inc(kept[s], 1)
                pairs(act, body)

            @block.vector
            def _(dve):
                w = k.p("conv_w")

                def split_unit(s, i):
                    dve.wait_ge(landed[s], 16 * i + 16)
                    leading_bits(dve, leading[:, s, :], ring[:, s, :]).then_inc(masked[s], 1)
                    dve.wait_ge(masked[s], i + 1)
                    rest_bits(dve, rest[:, s, :], ring[:, s, :], leading[:, s, :]).then_inc(split[s], 1)

                def body(i, s, n):
                    if not (isinstance(n, int) and n == units - 1):
                        split_unit(1 - s, i + s)
                    for j in range(2):
                        dve.wait_ge(based[s], 2 * i + j + 1)
                        c, ps = conv[:, 2 * s + j, :], k.bank(2 * s + j)
                        dve.scalar_tensor_tensor(c[:, 1:T], ps[:, 0:T - 1], col(w, 2 * FF_CHUNKS + 2 * n + j), c[:, 1:T],
                                                 ALU.mult, ALU.add).then_inc(own[s], 1)
                        dve.wait_ge(own[s], 2 * i + j + 1)
                        dve.scalar_tensor_tensor(c[:, 2:T], ps[:, 0:T - 2], col(w, 2 * n + j), c[:, 2:T],
                                                 ALU.mult, ALU.add).then_inc(tapped[s], 1)
                    dve.wait_ge(done[s], i)
                    dve.wait_ge(silued[s], i + 1)
                    dve.tensor_tensor(hidden[:, s, :], gate[:, s, :], conv[:, 2 * s, :], ALU.mult).then_inc(timed[s], 1)
                    dve.wait_ge(kept[s], i + 1)
                    rest_bits(dve, at(out.rest, n), hidden[:, s, :], at(out.leading, n)).then_inc(done[s], 1)

                for kk in range(KD):
                    leading_bits(dve, source.leading[:, kk, :], src[:, kk, :]).then_inc(source_masked, 1)
                for kk in range(KD):
                    dve.wait_ge(source_masked, kk + 1)
                    rest_bits(dve, source.rest[:, kk, :], src[:, kk, :], source.leading[:, kk, :]).then_inc(source_split, 1)
                split_unit(0, 0)
                pairs(dve, body)


def first_block(k):
    with ExitStack() as ctx:
        first_norm(k, k.x, k.h, "attn_norm", "attn_norm")
        with ExitStack() as mixers:
            def mx(what, shape):
                return mixers.enter_context(k.tensor(what, shape, F32))
            u = mx("sgu_u", [P, 4, T])
            v = mx("sgu_v", [P, TT, T])
            q = mx("nsa_q", [P, 4, T])
            raw = mx("nsa_raw", [P, 4, T])
            v_both = mx("nsa_v", [P, TT, 2 * P])
            gates = mx("nsa_gates", [P, TT, NSA_HEADS, 3])
            k_cmp = mx("nsa_k_cmp", [P, NSA_GROUPS, NCMP])
            v_cmp = mx("nsa_v_cmp", [NCMP, NSA_GROUPS, DH])
            k_slc = mx("nsa_k_slc", [P, NSA_GROUPS, T])
            k_win = mx("nsa_k_win", [P, NSA_GROUPS, T])

            def values_and_gates(eng, n, ps):
                return eng.tensor_copy(v_both[:, n, :], ps)

            def gate(eng, n, ps):
                return eng.activation(gates[:, n, :, :].rearrange("p h b -> p (h b)"), ps, ACT.Sigmoid)

            project(k, "proj1", [
                Section(k.dram["w_in_q"], 1, KD, k.h, copies_to(q), "vector"),
                Section(k.dram["w_in_k"], 1, KD, k.h, copies_to(raw), "vector"),
                Section(k.dram["w_in_v"], 1, KD, k.h, values_and_gates, "vector", chunks=TT, width=2 * P, by_tokens=True),
                Section(k.dram["w_in_g"], 1, KD, k.h, gate, "scalar", chunks=TT, width=3 * NSA_HEADS, by_tokens=True),
                Section(k.dram["w_in_u"], 1, KD, k.h, activates_to(u, ACT.Gelu_apprx_tanh), "scalar"),
                Section(k.dram["w_in_sv"], 1, KD, k.h, activates_to(v, ACT.Gelu_apprx_tanh), "scalar", chunks=TT,
                        by_tokens=True),
            ])
            spatial_gate(k, u, v, k.h[:, 4:8, :])
            compress(k, raw[:, 0, :], raw[:, 1, :], k_cmp, v_cmp)
            with k.stage("nsa_gains") as (sb2, sem):
                made = sem("gains_made")
                q_gain = mx("nsa_q_gain", [P, 1])
                with k.nc.Block() as block:
                    @block.vector
                    def _(dve):
                        dve.tensor_scalar(q_gain[:, :], k.p("q_norm"), DH ** -0.5, None, ALU.mult).then_inc(made, 1)
                        first = gates[:, 0, :, 0:1]
                        dve.tensor_scalar(first, first, k.c("any_cmp")[:, 0:1], None, ALU.mult).then_inc(made, 1)
                        dve.wait_ge(made, 2)
            cmp_flat = k_cmp[:, :, :].rearrange("p g n -> p (g n)")
            feature_norm(k, "nsa_norm",
                         [([q[:, n, :]], [q[:, n, :]], [q_gain[:, :]]) for n in range(4)]
                         + [([raw[:, 2, :]], [raw[:, 2, :]], [k.p("k_norm_slc")]),
                            ([raw[:, 3, :]], [raw[:, 3, :]], [k.p("k_norm_win")]),
                            ([cmp_flat], [cmp_flat], [k.p("k_norm_cmp")])],
                         k.c("halves"), 1.0 / DH, "eps")
            twice(k, "nsa_keys", [(dst[h * DH:(h + 1) * DH, g, :], raw[g * DH:(g + 1) * DH, n, :])
                                  for dst, n in ((k_slc, 2), (k_win, 3)) for g in range(2) for h in range(2)])
            strips = mx("nsa_strips", [P, NSA_HEADS, STRIP])
            bias_strips(k, strips)
            sparse_attention(k, q, k_cmp, v_cmp, k_slc, k_win, v_both, gates, strips, k.h)
        project(k, "out1", [Section(k.dram["w_out"], 2, KD, k.h, adds_to(k.x), "vector", spent=True)])
        first_norm(k, k.x, k.h, "ffn_norm", "ffn_norm")
        hidden = Parts(*(ctx.enter_context(k.tensor(f"ff_hidden_{x}", [P, FF_CHUNKS, T], F32R)) for x in ("leading", "rest")))
        feed_forward_up(k, k.h, hidden)
        project(k, "down1", [Section(k.dram["w_down"], KD, FF_CHUNKS, hidden, adds_to(k.x), "vector", chunks=1)])



def feature_center(k, name, srcs):
    n = len(srcs)
    with k.stage(name) as (sb, sem):
        summed, centered = sem("summed"), sem("centered")
        with k.nc.Block() as block:
            @block.tensor
            def _(pe):
                for m, s in enumerate(srcs):
                    last = pe.matmul(k.bank(0), k.c("ones"), s, start=(m == 0), stop=(m == n - 1))
                last.then_inc(summed, 1)

            @block.vector
            def _(dve):
                dve.wait_ge(summed, 1)
                for s in srcs:
                    dve.scalar_tensor_tensor(s, k.bank(0), -1.0 / (n * P), s, ALU.mult, ALU.add).then_inc(centered, 1)


def gated_products(k, name, weights, loops, kc_gate, source_gate, bias, kc, source, base, out):
    nc, N = k.nc, KD
    size = (kc_gate + kc) * P
    with k.stage(name) as (sb, sem):
        ring = sb("weights", [P, 2, size])
        leading = sb("leading", [P, 2, size], F32R)
        rest = k.over(f"{name}_rest", ring[:, :, :], [P, 2, size])
        gate_parts = Parts(*(sb(f"gate_source_{x}", [P, kc_gate, T], F32R) for x in ("leading", "rest")))
        parts = [Parts(sb(f"source{q}_leading", [P, kc, T], F32R), k.over(f"{name}_source{q}_rest", source(q)[:, :, :], [P, kc, T]))
                 for q in range(loops)]
        gate = sb("gate", [P, 2, T])
        part = sb("part", [P, 2, T])
        landed, masked, split, ready, opened, timed, added = ([sem(f"{x}{i}") for i in range(2)] for x in (
            "weights_landed", "weights_masked", "weights_split", "sums_ready", "gate_ready", "gated", "added"))
        source_masked, source_split = sem("source_masked"), sem("source_split")

        def each(eng, body, begin=None):
            for q in range(loops):
                if begin is not None:
                    begin(q)
                here = N // 2 - (q == loops - 1)
                with eng.Fori(0, here) as i:
                    for s in range(2):
                        body(q, s, 2 * i + s, i + q * (N // 2))
            for s in range(2):
                body(loops - 1, s, N - 2 + s, loops * N // 2 - 1)

        with nc.Block() as block:
            @block.sync
            def _(sp):
                def body(q, s, n, m):
                    sp.wait_ge(ready[s], 2 * m)
                    unit = weights[n + q * N, :, :] if isinstance(n, int) else \
                        weights[bass.ds(n + q * N, 1), :, :].rearrange("a p n -> p (a n)")
                    sp.dma_start(ring[:, s, :], unit).then_inc(landed[s], 16)
                each(sp, body)

            @block.tensor
            def _(pe):
                def body(q, s, n, m):
                    high, low = (w[:, s, :].rearrange("p (k n) -> p k n", n=P) for w in (leading, rest))
                    pe.wait_ge(split[s], m + 1)
                    pe.wait_ge(timed[s], m)
                    for j, (first, count, src) in enumerate(((0, kc_gate, gate_parts), (kc_gate, kc, parts[q]))):
                        for kk in range(count):
                            last = three_passes(pe, k.bank(2 * s + j), (high[:, first + kk, :], low[:, first + kk, :]),
                                                (src.leading[:, kk, :], src.rest[:, kk, :]), kk == 0, kk == count - 1)
                        last.then_inc(ready[s], 1)
                each(pe, body, lambda q: pe.wait_ge(source_split, kc_gate + (q + 1) * kc))

            @block.scalar
            def _(act):
                def body(q, s, n, m):
                    act.wait_ge(ready[s], 2 * m + 1)
                    act.wait_ge(timed[s], m)
                    act.activation(gate[:, s, :], k.bank(2 * s), ACT.Sigmoid, bias=col(bias, n + q * N)
                                   ).then_inc(opened[s], 1)
                each(act, body)

            @block.vector
            def _(dve):
                def split_unit(s, m):
                    dve.wait_ge(landed[s], 16 * m + 16)
                    leading_bits(dve, leading[:, s, :], ring[:, s, :]).then_inc(masked[s], 1)
                    dve.wait_ge(masked[s], m + 1)
                    rest_bits(dve, rest[:, s, :], ring[:, s, :], leading[:, s, :]).then_inc(split[s], 1)

                def split_source(src, into, chunks, before):
                    for kk in range(chunks):
                        leading_bits(dve, into.leading[:, kk, :], src[:, kk, :]).then_inc(source_masked, 1)
                    for kk in range(chunks):
                        dve.wait_ge(source_masked, before + kk + 1)
                        rest_bits(dve, into.rest[:, kk, :], src[:, kk, :], into.leading[:, kk, :]).then_inc(source_split, 1)

                def body(q, s, n, m):
                    if not (isinstance(n, int) and n == N - 1):
                        split_unit(1 - s, m + s)
                    dve.wait_ge(opened[s], m + 1)
                    dve.wait_ge(ready[s], 2 * m + 2)
                    dve.tensor_tensor(part[:, s, :], k.bank(2 * s + 1), gate[:, s, :], ALU.mult).then_inc(timed[s], 1)
                    dve.wait_ge(timed[s], m + 1)
                    dve.wait_ge(added[s], m)
                    dve.tensor_tensor(at(out, n), part[:, s, :], at(base, n), ALU.add).then_inc(added[s], 1)

                def begin(q):
                    if q + 1 < loops:
                        split_source(source(q + 1), parts[q + 1], kc, kc_gate + (q + 1) * kc)

                split_source(source_gate, gate_parts, kc_gate, 0)
                split_source(source(0), parts[0], kc, kc_gate)
                split_unit(0, 0)
                each(dve, body, begin)


def rates(k, raw, g, beta, log_f):
    nc = k.nc
    H, F = GDN_HEADS, 8
    W = H + F
    with k.stage("rates") as (sb, sem):
        bias = sb("bias", [P, 2 * H + F])
        y, mag, e, s, s2, p = (sb(x, [P, TT, W]) for x in ("y", "mag", "e", "s", "s2", "p"))
        rate = sb("rate", [P, H])
        landed, biased, exped, own, other = (sem(x) for x in (
            "biases_landed", "y_ready", "exp_ready", "vector_steps", "scalar_steps"))
        with nc.Block() as block:
            @block.sync
            def _(sp):
                sp.dma_start(bias[:, :], k.dram["rate_biases"][0:1, :].broadcast_to([P, 2 * H + F])).then_inc(landed, 16)

            @block.scalar
            def _(act):
                act.wait_ge(landed, 16)
                act.activation(rate[:, :], bias[:, W:W + H], ACT.Exp).then_inc(exped, 1)
                act.wait_ge(biased, 1)
                act.activation(mag[:, :, :], y[:, :, :], ACT.Abs).then_inc(other, 1)
                act.wait_ge(other, 1)
                act.activation(e[:, :, :], mag[:, :, :], ACT.Exp, scale=-1.0).then_inc(exped, 1)
                act.activation(beta[:, :, :], raw[:, :, H:2 * H], ACT.Sigmoid).then_inc(exped, 1)

            @block.vector
            def _(dve):
                step = Steps(dve, own)
                dve.wait_ge(landed, 16)
                step.then(dve.tensor_tensor(y[:, :, 0:H], raw[:, :, 0:H],
                                            bias[:, 0:H].unsqueeze(1).broadcast_to([P, TT, H]), ALU.add))
                step.do(dve.tensor_tensor(y[:, :, H:W], raw[:, :, 2 * H:2 * H + F],
                                          bias[:, H:W].unsqueeze(1).broadcast_to([P, TT, F]), ALU.add))
                dve.tensor_scalar(y[:, :, H:W], y[:, :, H:W], -1.0, None, ALU.mult).then_inc(biased, 1)
                dve.wait_ge(exped, 3)
                step.do(dve.tensor_scalar(s[:, :, :], e[:, :, :], 2.0, None, ALU.add))
                step.do(dve.reciprocal(s[:, :, :], s[:, :, :]))
                step.do(dve.tensor_tensor(s[:, :, :], s[:, :, :], e[:, :, :], ALU.mult))
                step.do(dve.tensor_tensor(s2[:, :, :], s[:, :, :], s[:, :, :], ALU.mult))
                step.do(dve.tensor_scalar(p[:, :, :], s2[:, :, :], 1.0 / 15, None, ALU.mult))
                for n in (13, 11, 9, 7, 5, 3):
                    step.do(dve.scalar_tensor_tensor(p[:, :, :], p[:, :, :], 1.0 / n, s2[:, :, :], ALU.add, ALU.mult))
                step.do(dve.scalar_tensor_tensor(p[:, :, :], p[:, :, :], 1.0, s[:, :, :], ALU.add, ALU.mult))
                step.do(dve.tensor_scalar(p[:, :, :], p[:, :, :], 2.0, None, ALU.mult))
                step.do(dve.scalar_tensor_tensor(p[:, :, :], y[:, :, :], 0.0, p[:, :, :], ALU.max, ALU.add))
                step.then(dve.tensor_scalar(log_f[:, :, :], p[:, :, H:W], -1.0, None, ALU.mult))
                step.do(dve.scalar_tensor_tensor(g[:, :, :], p[:, :, 0:H], -1.0,
                                                 rate[:, :].unsqueeze(1).broadcast_to([P, TT, H]), ALU.mult, ALU.mult))


def forget_rows(k, log_f, f_query, f_key):
    nc, H = k.nc, 8
    with k.stage("forget") as (sb, sem):
        row = sb("row", [H, 2, T])
        summed, copied, moved, filled = (sem(x) for x in ("sums_ready", "rows_copied", "rows_moved", "ones_filled"))
        with nc.Block() as block:
            @block.tensor
            def _(pe):
                for n in range(TT):
                    last = pe.matmul(k.psum[0:H, n * P:T], log_f[:, n, :], k.c("upto")[:, 0:T - n * P],
                                     start=(n == 0), stop=(n == TT - 1))
                last.then_inc(summed, 1)

            @block.vector
            def _(dve):
                dve.wait_ge(summed, 1)
                dve.tensor_copy(row[:, 0, :], k.psum[0:H, 0:T]).then_inc(copied, 1)
                dve.tensor_scalar(row[:, 1, :], k.psum[0:H, 0:T], -1.0, None, ALU.mult).then_inc(copied, 1)

            @block.gpsimd
            def _(pool):
                pool.memset(f_query[:, :, :], 1.0).then_inc(filled, 1)
                pool.memset(f_key[:, :, :], 1.0).then_inc(filled, 1)

            @block.sync
            def _(sp):
                sp.wait_ge(copied, 2)
                sp.wait_ge(filled, 2)
                for first in (0, DH):
                    sp.dma_start(f_query[first:first + 1, :, :], row[:, 0, :]).then_inc(moved, 16)
                    sp.dma_start(f_key[first + 1:first + 2, :, :], row[:, 1, :]).then_inc(moved, 16)
                sp.wait_ge(moved, 64)


def stick_breaking(k, q, keys, v, out):
    nc, pairs = k.nc, 4
    M = 4
    first = [0, BANK, 2 * BANK, BANK + 3 * P]
    order = [0, 1, 3, 2]
    width = [T - n * P for n in range(TT)]
    COLS = 2 * BANK + 2 * P
    with k.stage("stick") as (sb, sem):
        qs, ks, vs = sb("q", [P, 2, 2, T]), sb("k", [P, 2, T]), sb("v", [P, 2, TT, P])
        mag, soft, att = (sb(x, [P, 2, COLS]) for x in ("mag", "softplus", "att"))
        scored, absed, exped, logged, added, soft_ready, summed, weighed, valued, cleared = (sem(x) for x in (
            "scores_ready", "magnitudes", "exps", "logs", "softplus_added", "softplus_ready", "sums_ready",
            "weights_ready", "values_summed", "padding_cleared"))
        staged, taken = ([sem(f"{x}{slot}") for slot in range(2)] for x in ("operands_staged", "results_taken"))
        n_copies = 4

        def tile(ap, n, lo=0):
            return ap[:, first[n] + lo:first[n] + width[n]]

        def bank(m):
            return k.psum[:, (m % 2) * 3 * BANK:(m % 2) * 3 * BANK + COLS]

        def loop(eng, body):
            with eng.Fori(0, pairs // 2) as i:
                body(i)

        with nc.Block() as block:
            @block.gpsimd
            def _(pool):
                pool.memset(qs[:, :, :, :], 0.0).then_inc(cleared, 1)

            @block.sync
            def _(sp):
                sp.wait_ge(cleared, 1)

                def body(i):
                    for slot in range(2):
                        sp.wait_ge(valued, i * M)
                        pair = 2 * i + slot
                        for dst, src in head_copies(qs[:, slot, :, :], at(q, pair)) + [
                                (ks[:, slot, :], at(keys, pair)), (vs[:, slot, :, :], v[:, :, bass.ds(pair * P, P)])]:
                            sp.dma_start(dst, src).then_inc(staged[slot], 16)
                loop(sp, body)

            @block.tensor
            def _(pe):
                def body(i):
                    def scores(m):
                        slot, h = m // 2, m % 2
                        if h == 0:
                            pe.wait_ge(staged[slot], i * 16 * n_copies + 16 * n_copies)
                        if m >= 2:
                            pe.wait_ge(weighed, i * M + m - 1)
                        for n in order:
                            last = pe.matmul(tile(bank(m), n), ks[:, slot, n * P:(n + 1) * P], qs[:, slot, h, n * P:T],
                                             start=(n != 3), stop=True, skip_group_check=True)
                        last.then_inc(scored, 1)

                    def sums(m):
                        s = soft[:, m % 2, :]
                        pe.wait_ge(soft_ready, (i * M + m + 1) * TT)
                        for n in range(TT):
                            pe.matmul(tile(bank(m), n), k.c("minus_from"), tile(s, n), start=False, stop=False,
                                      skip_group_check=True)
                            for later in range(n + 1, TT):
                                pe.matmul(tile(bank(m), n, (later - n) * P), k.c("minus_ones"), tile(s, later), start=False,
                                          stop=False, skip_group_check=True)
                            last = pe.matmul(tile(bank(m), n)[:, 0:P], k.c("ident"), k.c("not_before"), start=False, stop=True,
                                             skip_group_check=True)
                        last.then_inc(summed, 1)

                    def values(m):
                        slot, h = m // 2, m % 2
                        half = slice(h * DH, (h + 1) * DH)
                        pe.wait_ge(weighed, i * M + m + 1)
                        if h == 0:
                            pe.wait_ge(taken[slot], i)
                        for n in range(TT):
                            last = pe.matmul(k.psum[half, (6 + slot) * BANK + n * P:(7 + slot) * BANK], vs[:, slot, n, half],
                                             tile(att[:, m % 2, :], n), start=(n == 0), stop=(n == TT - 1),
                                             skip_group_check=True)
                        last.then_inc(valued, 1)

                    scores(0)
                    for m in range(M):
                        if m + 1 < M:
                            scores(m + 1)
                        sums(m)
                        if m:
                            values(m - 1)
                    values(M - 1)
                loop(pe, body)

            @block.scalar
            def _(act):
                def body(i):
                    def logs(m):
                        x = mag[:, m % 2, :]
                        if m >= 2:
                            act.wait_ge(added, i * M + m - 1)
                        act.wait_ge(scored, i * M + m + 1)
                        act.activation(x, bank(m), ACT.Abs).then_inc(absed, 1)
                        act.wait_ge(absed, i * M + m + 1)
                        act.activation(x, x, ACT.Exp, scale=-1.0).then_inc(exped, 1)
                        act.wait_ge(exped, i * M + m + 1)
                        act.activation(x, x, ACT.Ln, bias=k.c("one")).then_inc(logged, 1)

                    logs(0)
                    for m in range(M):
                        if m + 1 < M:
                            logs(m + 1)
                        if m >= 2:
                            act.wait_ge(valued, i * M + m - 1)
                        act.wait_ge(summed, i * M + m + 1)
                        act.activation(att[:, m % 2, :], bank(m), ACT.Exp).then_inc(weighed, 1)
                loop(act, body)

            @block.vector
            def _(dve):
                def body(i):
                    def take(slot):
                        dve.wait_ge(valued, i * M + 2 * slot + 2)
                        dst = at(out, 2 * i + slot)
                        dve.tensor_tensor(dst, k.bank(6 + slot), dst, ALU.mult).then_inc(taken[slot], 1)

                    for m in range(M):
                        s = soft[:, m % 2, :]
                        if m >= 2:
                            dve.wait_ge(summed, i * M + m - 1)
                        dve.wait_ge(logged, i * M + m + 1)
                        dve.scalar_tensor_tensor(s, bank(m), 0.0, mag[:, m % 2, :], ALU.max, ALU.add).then_inc(added, 1)
                        dve.wait_ge(added, i * M + m + 1)
                        for n in range(TT):
                            dve.tensor_tensor(tile(s, n)[:, 0:P], tile(s, n)[:, 0:P], k.c("before")[:, 0:P],
                                              ALU.mult).then_inc(soft_ready, 1)
                    take(0)
                    take(1)
                loop(dve, body)


def forgetting(k, q, keys, v, f_query, f_key, out):
    with ExitStack() as ctx:
        def sb(what, shape):
            return ctx.enter_context(k.tensor(f"fox_{what}", shape, F32))

        qs, ks, vs = sb("q", [P, 2, 2, T]), sb("k", [P, 2, 2, T]), sb("v", [P, 2, TT, P])

        def copies(i, slot):
            pair = 2 * i + slot
            cols = slice(pair * P, (pair + 1) * P) if isinstance(i, int) else bass.ds(pair * P, P)
            found = [*head_copies(qs[:, slot, :, :], at(q, pair)), *head_copies(ks[:, slot, :, :], at(keys, pair)),
                     (vs[:, slot, :, :], v[:, :, cols])]
            for h in range(2):
                rows = slice(DH - h * DH, DH - h * DH + 2)
                found += [(qs[rows, slot, h, :], at(f_query, 2 * pair + h)[rows, :]),
                          (ks[rows, slot, h, :], at(f_key, 2 * pair + h)[rows, :])]
            return found

        def units(slot):
            found = []
            for t in range(TT):
                n = (t + 1) * P
                lo = 3 * P - t * P
                for h in range(2):
                    found.append(Unit([(qs[:, slot, h, t * P:(t + 1) * P], ks[:, slot, h, 0:n])], n,
                                      k.c("causal")[:, lo:lo + n], 1.0,
                                      [(m * P, P, vs[:, slot, m, h * DH:(h + 1) * DH]) for m in range(t + 1)],
                                      (h * DH, (h + 1) * DH), t, True, True))
            return found

        attention(k, "fox", 4, copies, units, lambda i, t: at(out, i)[:, t * P:(t + 1) * P],
                  padded=[qs[:, :, :, :], ks[:, :, :, :]], gating=True)


def delta_rule(k, qkv, g, beta, out):
    nc, H, C = k.nc, GDN_HEADS, GDN_CHUNK
    W = H * P
    with k.stage("delta_prepare") as (sb, sem):
        def kept(what, shape):
            return k.gdn.enter_context(k.tensor(f"delta_{what}", shape, F32))

        u = kept("u", [P, TT, W])
        wT = kept("w", [P, TT, W])
        q_dec = kept("q_dec", [P, H, T])
        k_dec = kept("k_dec", [P, TT, W])
        a_qk = kept("a_qk", [P, TT, W])
        g_end = kept("g_end", [P, H, T])
        with ExitStack() as inner:
            def tmp(what, shape):
                return inner.enter_context(k.tensor(f"delta_{what}", shape, F32))
            kv = tmp("kv", [P, 2, W])
            kb = tmp("kb", [P, W])
            vb = tmp("vb", [P, W])
            ga = tmp("ga", [P, W])
            gb = tmp("gb", [P, W])
            ex = tmp("ex", [P, 3, H])
            dec = tmp("decay", [P, 2, W])
            low = tmp("lower", [P, W])
            lev = tmp("level", [P, W])
            inv = tmp("inverse", [P, 2, W])
            mid = tmp("middle", [P, W])
            vs, ss, ps_ = sem("vector_steps"), sem("scalar_steps"), sem("tensor_steps")

            def heads(ap):
                return ap.rearrange("p (h c) -> p h c", h=H)

            def mask(name):
                return k.c(name)[:, 0:P].unsqueeze(1).broadcast_to([P, H, P])

            with nc.Block() as block:
                V_TILE, S_TILE, E_TILE = 31, 12, 21

                @block.tensor
                def _(pe):
                    for t in range(TT):
                        v0, s0 = V_TILE * t, S_TILE * t
                        here = slice(t * P, (t + 1) * P)
                        if t:
                            pe.wait_ge(vs, v0)
                            pe.wait_ge(ss, s0)
                        for n, first in ((0, GDN_HEADS), (1, 2 * GDN_HEADS)):
                            for h in range(H):
                                last = pe.transpose(k.bank(n)[:, h * P:(h + 1) * P], qkv[:, first + h, here], k.c("ident"))
                            last.then_inc(ps_, 1)
                        pe.matmul(k.psum[:, 2 * BANK:2 * BANK + H], k.c("g_upto"), g[:, t, :], start=True, stop=True)
                        pe.matmul(k.psum[:, 2 * BANK + H:2 * BANK + 2 * H], k.c("g_after"), g[:, t, :], start=True,
                                  stop=True).then_inc(ps_, 1)
                        pe.wait_ge(vs, v0 + 2)
                        for n, (left, right) in enumerate(((lambda h: k.c("g_upto"), lambda h: ga[:, h * P:(h + 1) * P]),
                                                           (lambda h: ga[:, h * P:(h + 1) * P], lambda h: k.c("g_upto")),
                                                           (lambda h: gb[:, h * P:(h + 1) * P], lambda h: k.c("g_upto")))):
                            for h in range(H):
                                last = pe.matmul(k.bank(3 + n)[:, h * P:(h + 1) * P], left(h), right(h), start=True, stop=True)
                            last.then_inc(ps_, 1)
                        for n, (left, right) in enumerate(((H, H), (H, 0))):
                            for h in range(H):
                                last = pe.matmul(k.bank(6 + n)[:, h * P:(h + 1) * P], qkv[:, left + h, here],
                                                 qkv[:, right + h, here], start=True, stop=True)
                            last.then_inc(ps_, 1)
                        for lv in range(6):
                            last_level = lv == 5
                            pe.wait_ge(vs, v0 + 13 + 3 * lv)
                            for h in range(H):
                                hs = slice(h * P, (h + 1) * P)
                                last = pe.matmul(k.bank(0)[:, hs], lev[:, hs], inv[:, 1, hs], start=True, stop=True)
                            last.then_inc(ps_, 1)
                            pe.wait_ge(ss, s0 + 7 + lv)
                            for h in range(H):
                                hs = slice(h * P, (h + 1) * P)
                                last = pe.matmul(k.bank(1)[:, hs], inv[:, 0, hs], mid[:, hs], start=True, stop=True)
                            if not last_level:
                                for h in range(H):
                                    hs = slice(h * P, (h + 1) * P)
                                    last = pe.matmul(k.bank(2)[:, hs], mid[:, hs], inv[:, 0, hs], start=True, stop=True)
                            last.then_inc(ps_, 1)
                        pe.wait_ge(vs, v0 + 29)
                        for n in range(2):
                            for h in range(H):
                                hs = slice(h * P, (h + 1) * P)
                                left, right = (inv[:, 1, hs], vb[:, hs]) if n == 0 else (kb[:, hs], inv[:, 1, hs])
                                last = pe.matmul(k.bank(3 + n)[:, hs], left, right, start=True, stop=True)
                        last.then_inc(ps_, 1)

                @block.scalar
                def _(act):
                    for t in range(TT):
                        s, e0, v0 = Steps(act, ss), E_TILE * t, V_TILE * t
                        s.n = S_TILE * t
                        if t:
                            act.wait_ge(vs, v0)
                        act.wait_ge(ps_, e0 + 3)
                        s.then(act.activation(ex[:, 0:2, :].rearrange("p a h -> p (a h)"),
                                              k.psum[:, 2 * BANK:2 * BANK + 2 * H], ACT.Exp))
                        for n in range(2):
                            act.wait_ge(ps_, e0 + 4 + n)
                            s.then(act.activation(dec[:, n, :], k.bank(3 + n), ACT.Exp))
                        act.wait_ge(ps_, e0 + 6)
                        s.then(act.activation(g_end[:, :, t * P:(t + 1) * P], heads(k.bank(5)), ACT.Exp))
                        act.wait_ge(ps_, e0 + 2)
                        s.then(act.copy(kv[:, 0, :], k.bank(0)))
                        s.then(act.copy(kv[:, 1, :], k.bank(1)))
                        for lv in range(6):
                            act.wait_ge(ps_, e0 + 9 + 2 * lv)
                            s.then(act.copy(mid[:, :], k.bank(0)))

                @block.vector
                def _(dve):
                    for t in range(TT):
                        v, e0, s0 = Steps(dve, vs), E_TILE * t, S_TILE * t
                        v.n = V_TILE * t
                        here = slice(t * P, (t + 1) * P)
                        if t:
                            dve.wait_ge(ps_, e0)
                        gt = g[:, t, :].unsqueeze(2).broadcast_to([P, H, P])
                        bt = beta[:, t, :].unsqueeze(2).broadcast_to([P, H, P])
                        v.then(dve.tensor_tensor(heads(ga[:, :]), mask("g_after"), gt, ALU.mult))
                        v.then(dve.tensor_tensor(heads(gb[:, :]), mask("ones"), gt, ALU.mult))
                        dve.wait_ge(ss, s0 + 1)
                        v.do(dve.tensor_tensor(ex[:, 2, :], ex[:, 0, :], beta[:, t, :], ALU.mult))
                        dve.wait_ge(ss, s0 + 6)
                        v.then(dve.tensor_tensor(heads(vb[:, :]), heads(kv[:, 1, :]), bt, ALU.mult))
                        v.then(dve.tensor_tensor(heads(kb[:, :]), heads(kv[:, 0, :]),
                                                 ex[:, 2, :].unsqueeze(2).broadcast_to([P, H, P]), ALU.mult))
                        v.then(dve.tensor_tensor(heads(k_dec[:, t, :]), heads(kv[:, 0, :]),
                                                 ex[:, 1, :].unsqueeze(2).broadcast_to([P, H, P]), ALU.mult))
                        v.then(dve.tensor_tensor(q_dec[:, :, here], qkv[:, 0:H, here], g_end[:, :, here], ALU.mult))
                        dve.wait_ge(ps_, e0 + 8)
                        v.do(dve.tensor_tensor(low[:, :], k.bank(6), dec[:, 0, :], ALU.mult))
                        v.then(dve.tensor_tensor(heads(low[:, :]), heads(low[:, :]), bt, ALU.mult))
                        v.do(dve.tensor_tensor(a_qk[:, t, :], k.bank(7), dec[:, 1, :], ALU.mult))
                        v.then(dve.tensor_tensor(heads(a_qk[:, t, :]), heads(a_qk[:, t, :]), mask("g_upto"), ALU.mult))
                        v.then(dve.tensor_copy(inv[:, :, :].rearrange("p a (h c) -> p (a h) c", h=H),
                                               k.c("ident").unsqueeze(1).broadcast_to([P, 2 * H, P])))
                        for lv in range(6):
                            v.settle()
                            v.then(dve.tensor_tensor(heads(lev[:, :]), heads(low[:, :]), mask(f"g_level{lv}"), ALU.mult))
                            dve.wait_ge(ps_, e0 + 10 + 2 * lv)
                            v.then(dve.tensor_tensor(inv[:, 1, :], inv[:, 1, :], k.bank(1), ALU.subtract))
                            if lv < 5:
                                v.then(dve.tensor_tensor(inv[:, 0, :], inv[:, 0, :], k.bank(2), ALU.subtract))
                        dve.wait_ge(ps_, e0 + 21)
                        v.then(dve.tensor_copy(u[:, t, :], k.bank(3)))
                        v.then(dve.tensor_copy(wT[:, t, :], k.bank(4)))
    with k.stage("delta_scan") as (sb, sem):
        state = sb("state", [P, H, P])
        fresh = sb("v_new", [P, 2, W])
        cleared, guessed, corrected, answered, learned, kept_, taken = (sem(x) for x in (
            "state_cleared", "predictions_ready", "v_new_ready", "answers_ready", "updates_ready", "state_updated",
            "answers_taken"))
        N = T // C
        with nc.Block() as block:
            @block.gpsimd
            def _(pool):
                pool.memset(state[:, :, :], 0.0).then_inc(cleared, 1)

            @block.tensor
            def _(pe):
                pe.wait_ge(cleared, 1)
                for n in range(N):
                    t, rows = n // 2, slice((n % 2) * C, (n % 2 + 1) * C)
                    tok = slice(n * C, (n + 1) * C)
                    pe.wait_ge(kept_, H * n)
                    for h in range(H):
                        hs = slice(h * P, (h + 1) * P)
                        last = pe.matmul(k.psum[rows, (n % 2) * BANK + h * P:(n % 2) * BANK + (h + 1) * P],
                                         wT[:, t, h * P + rows.start:h * P + rows.stop], state[:, h, :], start=True, stop=True)
                    last.then_inc(guessed, 1)
                    pe.wait_ge(corrected, n + 1)
                    if n >= 2:
                        pe.wait_ge(taken, n - 1)
                    for h in range(H):
                        hs = slice(h * P, (h + 1) * P)
                        o = k.psum[:, (2 + n % 2) * BANK + h * C:(2 + n % 2) * BANK + (h + 1) * C]
                        pe.matmul(o, state[:, h, :], q_dec[:, h, tok], start=True, stop=False)
                        last = pe.matmul(o, fresh[rows, n % 2, hs], a_qk[rows, t, h * P + rows.start:h * P + rows.stop],
                                         start=False, stop=True)
                    last.then_inc(answered, 1)
                    for h in range(H):
                        hs = slice(h * P, (h + 1) * P)
                        last = pe.matmul(k.bank(4 + n % 2)[:, hs], k_dec[rows, t, hs], fresh[rows, n % 2, hs],
                                         start=True, stop=True)
                    last.then_inc(learned, 1)

            @block.vector
            def _(dve):
                for n in range(N):
                    t, rows = n // 2, slice((n % 2) * C, (n % 2 + 1) * C)
                    dve.wait_ge(guessed, n + 1)
                    dve.tensor_tensor(fresh[rows, n % 2, :], u[rows, t, :], k.psum[rows, (n % 2) * BANK:(n % 2 + 1) * BANK],
                                      ALU.subtract).then_inc(corrected, 1)
                    dve.wait_ge(learned, n + 1)
                    if n:
                        dve.wait_ge(kept_, H * n)
                    for h in range(H):
                        end = (n + 1) * C - 1
                        dve.scalar_tensor_tensor(state[:, h, :], state[:, h, :], g_end[:, h, end:end + 1],
                                                 k.bank(4 + n % 2)[:, h * P:(h + 1) * P], ALU.mult, ALU.add).then_inc(kept_, 1)

            @block.scalar
            def _(act):
                for n in range(N):
                    act.wait_ge(answered, n + 1)
                    act.copy(out[:, :, n * C:(n + 1) * C],
                             k.psum[:, (2 + n % 2) * BANK:(2 + n % 2) * BANK + H * C].rearrange("p (h c) -> p h c", h=H)
                             ).then_inc(taken, 1)


def convolutions(k, qkv, wide, acc, short):
    def beside(dve, sem):
        step = Steps(dve, sem("convolution_steps"))
        w, b = k.p("conv_dw"), k.p("conv_dw_bias")
        for tap in range(CONV_K):
            step.settle()
            for n in range(4):
                x = wide[:, n, tap:tap + T]
                if tap == 0:
                    step.then(dve.tensor_scalar(acc[:, n, :], x, w[:, n:n + 1], b[:, n:n + 1], ALU.mult, ALU.add))
                else:
                    step.then(dve.scalar_tensor_tensor(acc[:, n, :], x, w[:, 4 * tap + n:4 * tap + n + 1], acc[:, n, :],
                                                       ALU.mult, ALU.add))
        w = k.p("conv_qkv")
        for tap in range(GDN_CONV):
            back = tap
            step.settle()
            for n in range(GDN_QKV):
                c = w[:, GDN_QKV * (GDN_CONV - 1 - tap) + n:GDN_QKV * (GDN_CONV - 1 - tap) + n + 1]
                if tap == 0:
                    step.then(dve.tensor_scalar(short[:, n, :], qkv[:, n, :], c, None, ALU.mult))
                else:
                    step.then(dve.scalar_tensor_tensor(short[:, n, back:T], qkv[:, n, 0:T - back], c, short[:, n, back:T],
                                                       ALU.mult, ALU.add))
        step.settle()
    return beside


def activate(k, name, func, pairs):
    with k.stage(name) as (sb, sem):
        done = sem("activated")
        with k.nc.Block() as block:
            @block.scalar
            def _(act):
                for out, src, bias in pairs:
                    if bias is None:
                        act.activation(out, src, func).then_inc(done, 1)
                    else:
                        act.activation(out, src, func, bias=bias).then_inc(done, 1)


def multiply(k, name, triples):
    with k.stage(name) as (sb, sem):
        done = sem("multiplied")
        with k.nc.Block() as block:
            @block.vector
            def _(dve):
                for out, a, b in triples:
                    dve.tensor_tensor(out, a, b, ALU.mult).then_inc(done, 1)


def second_block(k):
    nc = k.nc
    with ExitStack() as ctx:
        def sb(what, shape, stack=ctx):
            return stack.enter_context(k.tensor(f"second_{what}", shape, F32))

        y = sb("branches", [P, 4 * BRANCHES, T])
        g, beta, log_f = sb("g", [P, TT, GDN_HEADS]), sb("beta", [P, TT, GDN_HEADS]), sb("log_f", [P, TT, 8])
        with ExitStack() as branch_a:
            short = sb("qkv", [P, GDN_QKV, T], branch_a)
            with ExitStack() as branch_d:
                fox = sb("fox", [P, 12, T], branch_d)
                q_d, k_d, v_d = (fox[:, 4 * n:4 * n + 4, :] for n in range(3))
                with ExitStack() as branch_c:
                    q_c, k_c, v_c = (sb(f"{x}_stick", [P, 4, T], branch_c) for x in "qkv")
                    second_projections(k, y, short, fox, q_d, k_d, v_d, q_c, k_c, v_c, g, beta, log_f)
                    stick_breaking(k, q_c, k_c, v_c, y[:, 8:12, :])
                f_query, f_key = sb("f_query", [DH + 2, 8, T], branch_d), sb("f_key", [DH + 2, 8, T], branch_d)
                forget_rows(k, log_f, f_query, f_key)
                forgetting(k, q_d, k_d, v_d, f_query, f_key, y[:, 12:16, :])
            feature_norm(k, "delta_unit", [([short[:, n, :]], [short[:, n, :]], [k.c("gdn_scale")] if n < GDN_HEADS else None)
                                           for n in range(2 * GDN_HEADS)], k.c("ones"), 1.0, "eps")
            with ExitStack() as k.gdn:
                answers = k.h[:, 0:GDN_HEADS, :]
                delta_rule(k, short, g, beta, answers)
            feature_norm(k, "delta_norm", [([answers[:, n, :]], [answers[:, n, :]], [k.p("gdn_norm")])
                                           for n in range(GDN_HEADS)], k.c("ones"), 1.0 / P, "eps_2")
            multiply(k, "delta_gate", [(y[:, n, :], y[:, n, :], answers[:, n, :]) for n in range(GDN_HEADS)])
        merged = k.h
        with k.stage("merged") as (sb2, sem):
            cleared = sem("merged_cleared")
            with nc.Block() as block:
                @block.gpsimd
                def _(pool):
                    pool.memset(merged[:, :, :], 0.0).then_inc(cleared, 1)
        gated_products(k, "merge", k.dram["w_merge"], BRANCHES, KD, k.x, k.p("b_gate"), 4,
                       lambda q: y[:, 4 * q:4 * q + 4, :], merged, merged)

    def residual(eng, n, ps):
        return eng.scalar_tensor_tensor(at(k.x, n), at(k.x, n), ALPHA, ps, ALU.mult, ALU.add)

    project(k, "out2", [Section(k.dram["w_out_2"], 2, KD, k.h, residual, "vector", spent=True)])
    with k.stage("ple_in") as (sb, sem):
        per_layer = sb("p", [P, PLE // P, T])
        landed = sem("p_landed")
        with nc.Block() as block:
            @block.sync
            def _(sp):
                sp.dma_start(per_layer[:, :, :], k.dram["pT"].rearrange("(c p) t -> p c t", p=P)).then_inc(landed, 16)
                sp.wait_ge(landed, 16)
        gated_products(k, "ple", k.dram["w_ple"], 1, KD, k.x, k.p("b_ple_gate"), PLE // P, lambda q: per_layer, k.x, k.h)
    chunks = [k.h[:, n, :] for n in range(KD)]
    feature_center(k, "ln2_center", chunks)
    feature_norm(k, "ln2", [(chunks, [k.x[:, n, :] for n in range(KD)], [k.p("ln_g", n) for n in range(KD)])],
                 k.c("ones"), 1.0 / D, "eps_2", shift=[k.p("ln_b", n) for n in range(KD)])


def second_projections(k, y, short, fox, q_d, k_d, v_d, q_c, k_c, v_c, g, beta, log_f):
    nc = k.nc
    pad = CONV_K - 1
    acc = k.h[:, 0:4, :]
    with ExitStack() as ctx:
        def sb(what, shape):
            return ctx.enter_context(k.tensor(f"second_{what}", shape, F32))

        wide = sb("wide", [P, 4, pad + T])
        rate = sb("rates", [P, TT, 2 * GDN_HEADS + 8])
        lin = k.h[:, 4:8, :]

        def scaled(dst, scale):
            return lambda eng, n, ps: eng.activation(at(dst, n), ps, ACT.Copy, scale=scale)

        def plain(dst):
            return scaled(dst, 1.0)

        def silu_of(first):
            return activates_to(y[:, first:first + 4, :], ACT.Silu)

        def opened(eng, n, ps):
            return eng.activation(at(wide, n)[:, pad:pad + T], ps, ACT.Sigmoid)

        d = k.dram
        raw = [q_c, k_c, v_c]
        project(k, "proj2a", [
            Section(d["w2_glu_gate"], 1, KD, k.x, opened, "scalar"),
            Section(d["w2_glu_lin"], 1, KD, k.x, plain(lin), "scalar"),
            *[Section(d["w2_qkv_a"][n:n + 1], 1, KD, k.x, plain(raw[n]), "scalar") for n in range(3)],
        ], room={"leading": [a[:, 0:8, :].rearrange("p n t -> p (n t)") for a in (short, fox)], "parts": [y[:, 0:8, :], y[:, 8:16, :]]})
        with k.stage("glu") as (sb2, sem):
            opened_, cleared = sem("glu_opened"), sem("pad_cleared")
            with nc.Block() as block:
                @block.vector
                def _(dve):
                    for n in range(4):
                        dve.tensor_tensor(wide[:, n, pad:pad + T], wide[:, n, pad:pad + T], lin[:, n, :],
                                          ALU.mult).then_inc(opened_, 1)

                @block.gpsimd
                def _(pool):
                    pool.memset(wide[:, :, 0:pad], 0.0).then_inc(cleared, 1)

        def raw_chunk(n):
            return raw[n // 4][:, n % 4, :]

        class Raw:
            def __getitem__(self, key):
                return raw_chunk(key[1])[:, key[2]]

        project(k, "proj2b", [
            Section(d["w2_z_a"], 1, KD, k.x, silu_of(0), "scalar"),
            Section(d["w2_z_b"], 1, KD, k.x, silu_of(4), "scalar"),
            Section(d["w2_z_c"], 1, KD, k.x, silu_of(8), "scalar"),
            Section(d["w2_z_d"], 1, KD, k.x, silu_of(12), "scalar"),
            Section(d["w2_q_d"], 1, KD, k.x, scaled(q_d, DH ** -0.5), "scalar"),
            Section(d["w2_k_d"], 1, KD, k.x, plain(k_d), "scalar"),
            Section(d["w2_v_d"], 1, KD, k.x, plain(v_d), "scalar", by_tokens=True),
            Section(d["w2_rates"], 1, KD, k.x, lambda eng, n, ps: eng.activation(rate[:, n, :], ps, ACT.Copy), "scalar",
                    width=2 * GDN_HEADS + 8, by_tokens=True),
        ], beside=convolutions(k, Raw(), wide, acc, short))
        rates(k, rate, g, beta, log_f)
        activate(k, "qkv_silu", ACT.Silu, [(short[:, n, :], short[:, n, :], None) for n in range(GDN_QKV)])
        chunks = [acc[:, n, :] for n in range(4)]
        feature_center(k, "conv_center", chunks)
        feature_norm(k, "conv_ln", [(chunks, chunks, [k.p("conv_ln_g", n) for n in range(4)])], k.c("ones"), 1.0 / 512,
                     "eps_2")
        activate(k, "conv_silu", ACT.Silu, [(acc[:, n, :], acc[:, n, :], k.p("conv_ln_b", n)) for n in range(4)])
        multiply(k, "conv_gate", [(y[:, 4 + n, :], y[:, 4 + n, :], acc[:, n, :]) for n in range(4)])
    project(k, "proj2c", [
        Section(d["w2_q_c"], 2, KD, k.x, scaled(q_c, DH ** -0.5), "scalar", chunks=2),
        Section(d["w2_k_c"], 2, KD, k.x, plain(k_c), "scalar", chunks=2),
        Section(d["w2_v_c"], 2, KD, k.x, lambda eng, n, ps: eng.activation(
            v_c[:, n % TT, n // TT * 2 * P:(n // TT + 1) * 2 * P], ps, ACT.Copy), "scalar", width=2 * P, by_tokens=True),
    ], room={"parts": [k.h]})


def lay_out_second(i, a, p):
    w = i["w_in_2"][0]
    at_col = {"qkv_a": (0, 1536), "z_a": (1536, 512), "glu_lin": (2056, 512), "glu_gate": (2568, 512), "z_b": (3080, 512),
              "q_c": (3592, 512), "k_c": (4104, 512), "z_c": (5128, 512), "q_d": (5640, 512), "k_d": (6152, 512),
              "z_d": (7176, 512)}
    for n, (lo, width) in at_col.items():
        a[f"w2_{n}"] = units_of(w[:, lo:lo + width], 2 if n in ("q_c", "k_c") else 4)
    a["w2_v_c"], a["w2_v_d"] = units_of(w[:, 4616:5128], 2), whole(w[:, 6664:7176])
    a["w2_rates"] = whole(np.concatenate([w[:, 2048:2056], w[:, 7688:7696]], 1))
    a["rate_biases"] = np.concatenate([i["dt_bias_2"], i["forget_bias_2"], i["a_log_2"]], 1)
    gates = units_of(w[:, 7696:], 1)
    branch = np.concatenate([units_of(b, 1) for b in i["w_branch_2"][0]])
    a["w_merge"] = np.concatenate([gates, branch], 2)
    a["w_out_2"] = units_of(i["w_out_2"][0], 4)
    a["pT"] = i["p_2"][0, 0].T
    a["w_ple"] = np.concatenate([units_of(i["w_ple_gate_2"][0], 1), units_of(i["w_ple_2"][0], 1)], 2)
    for n in ("b_gate", "gdn_norm", "conv_dw_bias", "conv_ln_g", "conv_ln_b", "b_ple_gate", "ln_g", "ln_b"):
        p[n] = columns(i[n + "_2"][0])
    p["conv_qkv"] = columns(i["conv_qkv_2"][0].reshape(-1))
    p["conv_dw"] = columns(i["conv_dw_2"][0].reshape(-1))



def modulation(k, mod):
    nc = k.nc
    with ExitStack() as ctx:
        silu = ctx.enter_context(k.tensor("ada_silu", [P, KD, 2], F32))
        rows = ctx.enter_context(k.tensor("ada_rows", [2, 6 * D], F32))
        activate(k, "ada_silu_c", ACT.Silu, [(silu[:, :, :].rearrange("p a b -> p (a b)"), k.p("c"), None)])

        def row(eng, n, ps):
            at_n = slice(n * BANK, (n + 1) * BANK) if isinstance(n, int) else bass.ds(n * BANK, BANK)
            return eng.tensor_copy(rows[:, at_n], ps)

        project(k, "ada", [Section(k.dram["w_ada"], 12, KD, silu, row, "vector", chunks=1, by_tokens=True, rows=2, split=False)])
        with k.stage("ada_turn") as (sb, sem):
            turned, biased = sem("turned"), sem("biased")
            with nc.Block() as block:
                @block.tensor
                def _(pe):
                    for n in range(6 * KD):
                        last = pe.transpose(k.psum[:, 2 * n:2 * n + 2], rows[:, n * P:(n + 1) * P], k.c("ident")[0:2, 0:2])
                    last.then_inc(turned, 1)

                @block.vector
                def _(dve):
                    dve.wait_ge(turned, 1)
                    dve.tensor_tensor(mod[:, :, :], k.psum[:, 0:12 * KD].rearrange("p (n c) -> p n c", c=2),
                                      k.p("b_ada").unsqueeze(2).broadcast_to([P, 6 * KD, 2]), ALU.add).then_inc(biased, 1)


def third_columns(k, mod, gains, subln, minus_lam):
    nc = k.nc
    with k.stage("third_columns") as (sb, sem):
        prod, exps, diff = sb("products", [P, 2]), sb("exps", [P, 2]), sb("difference", [P, 1])
        own, summed, exped = sem("vector_steps"), sem("sums_ready"), sem("exps_ready")
        lam = k.p("lambdas")
        with nc.Block() as block:
            @block.vector
            def _(dve):
                step = Steps(dve, own)
                step.then(dve.tensor_tensor(prod[:, 0:1], lam[:, 0:1], lam[:, 1:2], ALU.mult))
                step.then(dve.tensor_tensor(prod[:, 1:2], lam[:, 2:3], lam[:, 3:4], ALU.mult))
                for n, (part, stream, weight) in enumerate(((1, 0, "attn_norm_w"), (1, 1, "attn_norm_w"), (4, 0, "ffn_norm_w"))):
                    step.then(dve.scalar_tensor_tensor(gains[:, n, :], mod[:, part * KD:(part + 1) * KD, stream], 1.0,
                                                       k.p(weight), ALU.add, ALU.mult))
                step.then(dve.tensor_scalar(subln[:, :], k.p("subln_w"), 1.0 - LAM_INIT, None, ALU.mult))
                dve.wait_ge(exped, 1)
                step.do(dve.tensor_tensor(diff[:, :], exps[:, 1:2], exps[:, 0:1], ALU.subtract))
                step.do(dve.tensor_scalar(minus_lam[:, :], diff[:, :], -LAM_INIT, None, ALU.add))

            @block.tensor
            def _(pe):
                pe.wait_ge(own, 2)
                pe.matmul(k.bank(0, 2), k.c("ones"), prod[:, :], start=True, stop=True).then_inc(summed, 1)

            @block.scalar
            def _(act):
                act.wait_ge(summed, 1)
                act.activation(exps[:, :], k.bank(0, 2), ACT.Exp).then_inc(exped, 1)


def rotate(k, name, pairs):
    nc = k.nc
    with k.stage(name) as (sb, sem):
        turn, keep = sb("turned", [P, 2, T]), sb("kept", [P, 2, T])
        swapped, own, done = sem("swapped"), sem("vector_steps"), sem("rotated")
        with nc.Block() as block:
            @block.tensor
            def _(pe):
                for n, (_, x) in enumerate(pairs):
                    if n >= 2:
                        pe.wait_ge(own, 2 * (n - 1))
                    pe.matmul(k.bank(n % 2), k.c("rope_swap"), x, start=True, stop=True).then_inc(swapped, 1)

            @block.vector
            def _(dve):
                for n, (out, x) in enumerate(pairs):
                    dve.wait_ge(swapped, n + 1)
                    if n >= 2:
                        dve.wait_ge(done, n - 1)
                    dve.tensor_tensor(turn[:, n % 2, :], k.bank(n % 2), k.c("rope_sin"), ALU.mult).then_inc(own, 1)
                    dve.tensor_tensor(keep[:, n % 2, :], x, k.c("rope_cos"), ALU.mult).then_inc(own, 1)
                    dve.wait_ge(own, 2 * n + 2)
                    dve.tensor_tensor(out, turn[:, n % 2, :], keep[:, n % 2, :], ALU.add).then_inc(done, 1)


def mixers(k, mod, gains, subln, minus_lam, mix):
    nc, d = k.nc, k.dram
    with ExitStack() as ctx:
        def sb(what, shape, stack=ctx):
            return stack.enter_context(k.tensor(f"third_{what}", shape, F32))

        dq, dk, dv = sb("dq", [P, 4, T]), sb("dk", [P, 4, TA]), sb("dv", [P, TA // P, 4 * P])
        cq, ckv, kr = sb("cq", [P, 2, T]), sb("ckv", [P, 1, TA]), sb("kr", [P, 1, TA])
        zeros = sb("zeros", [P, TA])
        with ExitStack() as inputs:
            hc = sb("ctx_normed", [P, KD, CTX], inputs)
            with ExitStack() as raw:
                cx = sb("ctx", [P, KD, CTX], raw)
                with k.stage("ctx_in") as (sb2, sem):
                    landed, cleared = sem("ctx_landed"), sem("zeros_cleared")
                    with nc.Block() as block:
                        @block.sync
                        def _(sp):
                            sp.dma_start(cx[:, :, :], d["ctxT"].rearrange("(k p) t -> p k t", p=P)).then_inc(landed, 16)
                            sp.wait_ge(landed, 16)

                        @block.gpsimd
                        def _(pool):
                            pool.memset(zeros[:, :], 0.0).then_inc(cleared, 1)
                for stream, (src, dst) in enumerate(((k.x, k.h), (cx, hc))):
                    feature_norm(k, f"third_norm{stream}",
                                 [([src[:, n, :] for n in range(KD)], [dst[:, n, :] for n in range(KD)],
                                   [gains[:, stream, n:n + 1] for n in range(KD)])], k.c("ones"), 1.0 / D, "eps",
                                 shift=[mod[:, n, stream:stream + 1] for n in range(KD)])

            def into(dst, lo, n_tokens, scale=1.0):
                return lambda eng, n, ps: eng.activation(at(dst, n)[:, lo:lo + n_tokens], ps, ACT.Copy, scale=scale)

            def tokens(dst, first):
                return lambda eng, n, ps: eng.activation(dst[:, first + n, :], ps, ACT.Copy)

            def misc(lo, n_tokens, first):
                def finish(eng, n, ps):
                    dst = [cq[:, 0, :], cq[:, 1, :], ckv[:, 0, lo:lo + n_tokens], kr[:, 0, lo:lo + n_tokens]][first + n]
                    return eng.activation(dst, ps, ACT.Copy)
                return finish

            project(k, "proj3", [
                Section(d["w3_dq"], 1, KD, k.h, into(dq, 0, T, DH ** -0.5), "scalar", spent=True),
                Section(d["w3_dk"], 1, KD, k.h, into(dk, CTX, T), "scalar", spent=True),
                Section(d["w3_dk"], 1, KD, hc, into(dk, 0, CTX), "scalar", width=CTX, spent=True),
                Section(d["w3_dv"], 1, KD, k.h, tokens(dv, CTX // P), "scalar", by_tokens=True, spent=True),
                Section(d["w3_dv"], 1, KD, hc, tokens(dv, 0), "scalar", chunks=CTX // P, by_tokens=True, spent=True),
                Section(d["w3_misc"], 1, KD, k.h, misc(CTX, T, 0), "scalar", spent=True),
                Section(d["w3_misc_ctx"], 1, KD, hc, misc(0, CTX, 2), "scalar", chunks=2, width=CTX, spent=True),
            ], room={"parts": [mix]})
        rotate(k, "rope_diff", [(dq[:, n, :], dq[:, n, :]) for n in range(4)]
               + [(dk[:, n, CTX:TA], dk[:, n, CTX:TA]) for n in range(4)] + [(kr[:, 0, CTX:TA], kr[:, 0, CTX:TA])])
        halves = [(0, BANK), (BANK, TA)]
        feature_norm(k, "latent_norm", [([cq[:, n, :] for n in range(2)], [cq[:, n, :] for n in range(2)],
                                         [k.p("q_norm_w", n) for n in range(2)])], k.c("ones"), 1.0 / 256, "eps")
        feature_norm(k, "latent_kv_norm", [([ckv[:, 0, a:b]], [ckv[:, 0, a:b]], [k.p("kv_norm_w")]) for a, b in halves],
                     k.c("ones"), 1.0 / P, "eps")

        with ExitStack() as heads:
            qs, ks, vs = sb("diff_q", [P, 2, 2, T], heads), sb("diff_k", [P, 2, TA], heads), sb("diff_v", [P, 2, TA // P, P], heads)

            def copies(i, slot):
                head = 2 * i + slot
                cols = slice(head * P, (head + 1) * P) if isinstance(i, int) else bass.ds(head * P, P)
                return [*head_copies(qs[:, slot, :, :], at(dq, head)), (ks[:, slot, :], at(dk, head)),
                        (vs[:, slot, :, :], dv[:, :, cols])]

            def units(slot):
                return [Unit([(qs[:, slot, m, t * P:(t + 1) * P], ks[:, slot, :])], TA, zeros[:, :],
                             minus_lam[:, :] if m else 1.0, [(n * P, P, vs[:, slot, n, :]) for n in range(TA // P)],
                             (0, P), t, m == 0, m == 1) for t in range(TT) for m in range(2)]

            attention(k, "diff", DIFF_HEADS, copies, units, lambda i, t: at(mix, i)[:, t * P:(t + 1) * P],
                      padded=[qs[:, :, :, :]])
        feature_norm(k, "diff_norm", [([mix[:, n, :]], [mix[:, n, :]], [subln[:, :]]) for n in range(DIFF_HEADS)],
                     k.c("ones"), 1.0 / P, "eps")

        scale = (P + DH) ** -0.5
        qn, qr = sb("mla_qn", [P, 4, T]), sb("mla_qr", [P, 2, T])
        kn, mv = dk, dv

        def queries(eng, n, ps):
            return eng.activation(qn[:, n, :] if n < 4 else qr[:, n - 4, :], ps, ACT.Copy, scale=scale)

        def shifted(finish, first):
            return lambda eng, n, ps: finish(eng, n + first, ps)

        project(k, "proj3b", [
            Section(d["w3_uq"][0:1], 1, 2, cq, shifted(queries, 0), "scalar", chunks=3),
            Section(d["w3_uq"][1:2], 1, 2, cq, shifted(queries, 3), "scalar", chunks=3),
            Section(d["w3_uk"], 1, 1, ckv[:, :, 0:CTX], lambda eng, n, ps: eng.activation(kn[:, n, 0:CTX], ps, ACT.Copy),
                    "scalar", width=CTX),
            Section(d["w3_uk"], 1, 1, ckv[:, :, CTX:TA], lambda eng, n, ps: eng.activation(kn[:, n, CTX:TA], ps, ACT.Copy),
                    "scalar"),
            Section(d["w3_uv"], 1, 1, ckv, lambda eng, n, ps: eng.activation(mv[:, n, :], ps, ACT.Copy), "scalar",
                    chunks=3, by_tokens=True),
            Section(d["w3_uv"], 1, 1, ckv[:, :, 3 * P:TA], lambda eng, n, ps: eng.activation(mv[:, 3 + n, :], ps, ACT.Copy),
                    "scalar", chunks=3, by_tokens=True),
        ])
        rotate(k, "rope_mla", [(qr[:, n, :], qr[:, n, :]) for n in range(2)])
        with ExitStack() as heads:
            qrs = sb("mla_qrs", [P, 2, 2, T], heads)

            def copies(i, slot):
                return head_copies(qrs[:, slot, :, :], qr[:, slot, :])

            def units(slot):
                found = []
                for t in range(TT):
                    here = slice(t * P, (t + 1) * P)
                    for h in range(2):
                        head = 2 * slot + h
                        found.append(Unit([(qn[:, head, here], kn[:, head, :]), (qrs[:, slot, h, here], kr[:, 0, :])], TA,
                                          zeros[:, :], 1.0, [(n * P, P, mv[:, n, head * P:(head + 1) * P]) for n in range(TA // P)],
                                          (0, P), 2 * t + h, True, True))
                return found

            attention(k, "mla", 2, copies, units,
                      lambda i, g: at(mix, 4 + 2 * i + g % 2)[:, (g // 2) * P:(g // 2 + 1) * P], padded=[qrs[:, :, :, :]])


def route(k, logits, gate, dest, row_of, block_expert, gate_by_expert):
    nc, E, K, B = k.nc, EXPERTS, TOP_K, SLOTS_MAX + 1
    table = nc.dram_tensor("row_tokens", (B * P, 1), I32, kind="Internal").ap()
    with k.stage("route") as (sb, sem):
        top, ids = sb("top", [P, TT, 8]), sb("ids", [P, TT, 8], U32)
        idf, neg = sb("ids_f", [P, TT, 8]), sb("neg", [P, TT])
        ex, total, inv = sb("exps", [P, TT, K]), sb("total", [P, TT]), sb("inverse", [P, TT])
        hot, part = sb("hot", [P, TT, K, E]), sb("part", [P, K, E])
        chosen, slot, spread = sb("chosen", [P, TT, E]), sb("slots", [P, TT, E]), sb("spread", [P, TT, E])
        start, blocks, ends = sb("start", [P, E]), sb("blocks", [E, P]), sb("ends", [E, 1])
        past, count_t = sb("past", [E, B]), sb("counts", [E, P])
        dest_f, toks, fill = sb("dest_f", [P, TT, K]), sb("tokens", [P, TT], I32), sb("fill", [B, P], I32)
        row_i, row_f = sb("row_i", [B, P], I32), sb("row_f", [B, P])
        own, exped, ranked, started, ended, mapped, filled, scattered, loaded, cast, turned = (sem(x) for x in (
            "vector_steps", "exps_ready", "ranks_ready", "starts_ready", "ends_ready", "map_ready", "table_filled",
            "tokens_scattered", "table_loaded", "table_cast", "table_turned"))
        with nc.Block() as block:
            @block.vector
            def _(dve):
                v = Steps(dve, own)
                for t in range(TT):
                    v.do(dve.max(top[:, t, :], logits[:, t, :]))
                    v.then(dve.max_index(ids[:, t, :], top[:, t, :], logits[:, t, :]))
                v.settle()
                v.then(dve.tensor_copy(idf[:, :, :], ids[:, :, :]))
                v.then(dve.tensor_copy(toks[:, :], k.c("lanes_on")))
                v.then(dve.memset(fill[:, :], T))
                v.do(dve.tensor_scalar(neg[:, :], top[:, :, 0], -1.0, None, ALU.mult))
                for t in range(TT):
                    v.do(dve.tensor_tensor(hot[:, t, :, :], k.c("experts").unsqueeze(1).broadcast_to([P, K, E]),
                                           idf[:, t, 0:K].unsqueeze(2).broadcast_to([P, K, E]), ALU.is_equal))
                    v.then(dve.tensor_reduce(chosen[:, t, :], hot[:, t, :, :].rearrange("p k e -> p e k"), AX_X, ALU.add))
                v.settle()
                dve.wait_ge(ranked, 3)
                v.do(dve.tensor_copy(count_t[:, :], k.psum[0:E, 2 * BANK:2 * BANK + P]))
                v.do(dve.tensor_scalar(blocks[:, :], count_t[:, :], 0.0, None, ALU.is_gt))
                for n in range(1, T // P):
                    v.do(dve.scalar_tensor_tensor(blocks[:, :], count_t[:, :], float(n * P), blocks[:, :], ALU.is_gt, ALU.add))
                dve.wait_ge(started, 1)
                v.do(dve.tensor_scalar(start[:, :], k.bank(3, E), float(P), None, ALU.mult))
                v.do(dve.tensor_tensor(slot[:, :, :], k.psum[:, 0:TT * E].rearrange("p (t e) -> p t e", e=E),
                                       start[:, :].unsqueeze(1).broadcast_to([P, TT, E]), ALU.add))
                for t in range(TT):
                    v.do(dve.tensor_tensor(part[:, :, :], hot[:, t, :, :], slot[:, t, :].unsqueeze(1).broadcast_to([P, K, E]),
                                           ALU.mult))
                    v.do(dve.tensor_reduce(dest_f[:, t, :], part[:, :, :], AX_X, ALU.add))
                v.do(dve.tensor_copy(dest[:, :, :], dest_f[:, :, :]))
                dve.wait_ge(ended, 1)
                v.do(dve.tensor_copy(ends[:, :], k.psum[0:E, 4 * BANK:4 * BANK + 1]))
                v.then(dve.tensor_scalar(past[:, :], k.c("blocks")[0:E, :], ends[:, 0:1], None, ALU.is_ge))
                dve.wait_ge(mapped, 1)
                v.then(dve.tensor_copy(block_expert[:, 0:B + 1], k.psum[0:1, 5 * BANK:5 * BANK + B + 1]))
                v.then(dve.tensor_scalar(block_expert[:, B + 1:B + 2], k.psum[0:1, 5 * BANK + B:5 * BANK + B + 1], -1.0, float(B),
                                         ALU.mult, ALU.add))
                dve.wait_ge(exped, TT)
                v.do(dve.reciprocal(inv[:, :], total[:, :]))
                v.do(dve.tensor_tensor(gate[:, :, :], ex[:, :, :], inv[:, :].unsqueeze(2).broadcast_to([P, TT, K]), ALU.mult))
                for t in range(TT):
                    v.do(dve.tensor_tensor(part[:, :, :], hot[:, t, :, :], gate[:, t, :].unsqueeze(2).broadcast_to([P, K, E]),
                                           ALU.mult))
                    v.do(dve.tensor_reduce(spread[:, t, :], part[:, :, :].rearrange("p k e -> p e k"), AX_X, ALU.add))
                dve.wait_ge(loaded, 16)
                dve.tensor_copy(row_f[:, :], row_i[:, :]).then_inc(cast, 1)
                dve.wait_ge(turned, 1)
                v.then(dve.tensor_copy(row_of[:, 0:B], k.psum[:, 6 * BANK:6 * BANK + B]))
                v.then(dve.tensor_copy(gate_by_expert[:, :], k.psum[0:E, 7 * BANK:7 * BANK + T]))

            @block.scalar
            def _(act):
                act.wait_ge(own, 12)
                for t in range(TT):
                    act.activation(ex[:, t, :], top[:, t, 0:K], ACT.Exp, bias=neg[:, t:t + 1],
                                   accum_out=total[:, t:t + 1]).then_inc(exped, 1)

            @block.tensor
            def _(pe):
                pe.wait_ge(own, 20)
                for t in range(TT):
                    out = k.psum[:, t * E:(t + 1) * E]
                    for n in range(t + 1):
                        last = pe.matmul(out, k.c("before")[:, 0:P] if n == t else k.c("ones"), chosen[:, n, :],
                                         start=(n == 0), stop=(n == t))
                last.then_inc(ranked, 2)
                for n in range(TT):
                    last = pe.matmul(k.psum[0:E, 2 * BANK:2 * BANK + P], chosen[:, n, :], k.c("ones"), start=(n == 0),
                                     stop=(n == TT - 1))
                last.then_inc(ranked, 1)
                pe.wait_ge(own, 25)
                pe.matmul(k.bank(3, E), blocks[:, :], k.c("before")[0:E, 0:E], start=True, stop=True).then_inc(started, 1)
                pe.matmul(k.psum[0:E, 4 * BANK:4 * BANK + P], k.c("upto")[0:E, 0:E], blocks[:, :], start=True,
                          stop=True).then_inc(ended, 1)
                pe.wait_ge(own, 38)
                pe.matmul(k.psum[0:1, 5 * BANK:5 * BANK + B], k.c("one")[0:E, :], past[:, :], start=True, stop=True)
                pe.matmul(k.psum[0:1, 5 * BANK + B:5 * BANK + B + 1], blocks[:, 0:1], k.c("one")[0:E, :], start=True,
                          stop=True).then_inc(mapped, 1)
                pe.wait_ge(own, 50)
                for t in range(TT):
                    pe.transpose(k.psum[0:E, 7 * BANK + t * P:7 * BANK + (t + 1) * P], spread[:, t, :], k.c("ident"))
                pe.wait_ge(cast, 1)
                pe.transpose(k.psum[:, 6 * BANK:6 * BANK + B], row_f[:, :], k.c("ident")[0:B, 0:B]).then_inc(turned, 1)

            @block.gpsimd
            def _(pool):
                pool.wait_ge(own, 36)
                pool.wait_ge(filled, 16)
                for t in range(TT):
                    for n in range(K):
                        pool.indirect_dma_start(out=table, out_offset=bass.IndirectOffsetOnAxis(ap=dest[:, t, n:n + 1], axis=0),
                                                in_=toks[:, t:t + 1], in_offset=None).then_inc(scattered, 16)

            @block.sync
            def _(sp):
                sp.wait_ge(own, 12)
                sp.dma_start(table.rearrange("(b p) one -> b (p one)", p=P), fill[:, :]).then_inc(filled, 16)
                sp.wait_ge(scattered, 16 * TT * K)
                sp.dma_start(row_i[:, :], table.rearrange("(b p) one -> b (p one)", p=P)).then_inc(loaded, 16)


def experts(k, rows, row_of, block_expert, results):
    nc, d = k.nc, k.dram
    UP, DOWN, CH = 4, 2, 4
    HALF = 2 * P
    with k.stage("experts") as (sb, sem):
        ring_up = sb("up", [P, UP, KD * CH * P + CH])
        ring_down = sb("down", [P, DOWN, KD * BANK])
        index = sb("index", [P, 2], I32)
        x_rows, x_t = sb("x", [P, 2, D]), sb("xT", [P, 2, KD, P])
        gate, lin, sig = sb("gate", [P, 2, HALF]), sb("lin", [P, 2, HALF]), sb("sig", [P, 2, HALF])
        product, y = sb("product", [P, 2, HALF]), sb("y", [P, DOWN, BANK])
        hidden = Parts(*(sb(f"hidden_{x}", [P, KD, P], F32R) for x in ("leading", "rest")))
        leading = [k.over("experts_leading0", k.h[:, :, :], [P, KD * BANK]), sb("leading1", [P, KD * BANK], F32R)]
        rest = [k.over(f"experts_rest{u}", ring_down[:, u, :], [P, KD * BANK]) for u in range(DOWN)]

        def sems(what, n):
            return [sem(f"{what}{i}") for i in range(n)]

        up_landed, down_landed, up_ready, gated, sigged, hid_done = (sems(x, UP) for x in (
            "up_landed", "down_landed", "up_ready", "gate_ready", "sigmoid_ready", "hidden_done"))
        down_masked, down_split, down_ready, y_copied, y_stored = (sems(x, DOWN) for x in (
            "down_masked", "down_split", "down_ready", "y_copied", "y_stored"))
        indexed, gathered, x_turned, x_copied = (sems(x, 2) for x in ("indexed", "gathered", "x_turned", "x_copied"))
        own, cleared, zeroed, passed = (sem(x) for x in ("vector_steps", "zero_cleared", "empty_blocks_zeroed", "waits_passed"))
        zero = sb("zero", [P, D])
        OWN = 6

        def blocks(eng, body, empty=None):
            with eng.Fori(0, (SLOTS_MAX + 1) // 2) as i:
                for s in range(2):
                    b = 2 * i + s
                    e = eng.value_load(block_expert[0:1, bass.ds(b, 1)], min_val=0, max_val=EXPERTS)
                    with eng.If(e < EXPERTS):
                        body(i, s, b, nc.s_assert_within(
                            e, 0, EXPERTS - 1, skip_runtime_bounds_check_because="inside the branch for e < EXPERTS"))
                    if empty:
                        with eng.Else():
                            empty(b)

        with nc.Block() as block:
            @block.sync
            def _(sp):
                def body(i, s, b, e):
                    for u in range(UP):
                        sp.wait_ge(hid_done[u], b)
                        sp.dma_start(ring_up[:, u, :], d["w_up_3"][bass.ds(e, 1), u, :, :].rearrange("a p n -> p (a n)")
                                     ).then_inc(up_landed[u], 16)
                    for u in range(DOWN):
                        sp.wait_ge(y_copied[u], b)
                        sp.dma_start(ring_down[:, u, :], d["w_down_3"][bass.ds(e, 1), u, :, :].rearrange("a p n -> p (a n)")
                                     ).then_inc(down_landed[u], 16)

                def empty(b):
                    sp.dma_start(results[bass.ds(b * P, P), :], zero[:, :]).then_inc(zeroed, 16)

                sp.wait_ge(cleared, 1)
                blocks(sp, body, empty)
                count = SLOTS_MAX + 1
                empties = sp.value_load(block_expert[0:1, count + 1:count + 2], min_val=0, max_val=count)
                wait_apart(sp, zeroed, empties * 16, passed)

            @block.gpsimd
            def _(pool):
                pool.memset(zero[:, :], 0.0).then_inc(cleared, 1)

                def gather(s, i, b):
                    if not isinstance(i, int):
                        pool.wait_ge(gathered[s], i * 16)
                        pool.wait_ge(x_turned[s], i)
                    pool.tensor_copy(index[:, s:s + 1], row_of[:, b:b + 1] if isinstance(b, int) else row_of[:, bass.ds(b, 1)]
                                     ).then_inc(indexed[s], 1)
                    wait_apart(pool, indexed[s], i + 1, passed)
                    pool.indirect_dma_start(out=x_rows[:, s, :], out_offset=None, in_=rows,
                                            in_offset=bass.IndirectOffsetOnAxis(ap=index[:, s:s + 1], axis=0)
                                            ).then_inc(gathered[s], 16)

                gather(0, 0, 0)
                blocks(pool, lambda i, s, b, e: gather(1 - s, i + s, b + 1))

            @block.tensor
            def _(pe):
                def turn(s, i):
                    pe.wait_ge(gathered[s], i * 16 + 16)
                    for n in range(KD):
                        last = pe.transpose(k.psum[:, 6 * BANK + n * P:6 * BANK + (n + 1) * P], x_rows[:, s, n * P:(n + 1) * P],
                                            k.c("ident"))
                    last.then_inc(x_turned[s], 1)

                def body(i, s, b, e):
                    pe.wait_ge(x_copied[s], i + 1)
                    for u in range(UP):
                        w = ring_up[:, u, 0:KD * CH * P].rearrange("p (k n) -> p k n", k=KD)
                        pe.wait_ge(up_landed[u], b * 16 + 16)
                        pe.wait_ge(hid_done[(u + 2) % UP], b + 1 if u >= 2 else b)
                        for c in range(CH):
                            for kk in range(KD):
                                last = pe.matmul(k.bank(u % 2)[:, c * P:(c + 1) * P], w[:, kk, c * P:(c + 1) * P],
                                                 x_t[:, s, kk, :], start=(kk == 0), stop=(kk == KD - 1))
                        last.then_inc(up_ready[u], 1)
                    turn(1 - s, i + s)
                    for u in range(DOWN):
                        high, low = (x[u].rearrange("p (k n) -> p k n", k=KD) for x in (leading, rest))
                        pe.wait_ge(down_split[u], b + 1)
                        pe.wait_ge(y_copied[u], b)
                        for kk in range(KD):
                            if u == 0 and kk % 2 == 0:
                                pe.wait_ge(hid_done[kk // 2], b + 1)
                            last = three_passes(pe, k.bank(2 + u), (hidden.leading[:, kk, :], hidden.rest[:, kk, :]),
                                                (high[:, kk, :], low[:, kk, :]), kk == 0, kk == KD - 1)
                        last.then_inc(down_ready[u], 1)
                turn(0, 0)
                blocks(pe, body)

            @block.scalar
            def _(act):
                def keep_x(s, i):
                    act.wait_ge(x_turned[s], i + 1)
                    act.copy(x_t[:, s, :, :].rearrange("p k n -> p (k n)"), k.psum[:, 6 * BANK:8 * BANK]
                             ).then_inc(x_copied[s], 1)

                def body(i, s, b, e):
                    for u in range(UP):
                        act.wait_ge(gated[u], 2 * b + 2)
                        act.activation(sig[:, u % 2, :], gate[:, u % 2, :], ACT.Sigmoid, scale=SWIGLU_ALPHA
                                       ).then_inc(sigged[u], 1)
                        if u < DOWN:
                            act.wait_ge(down_ready[u], b)
                            act.wait_ge(down_landed[u], b * 16 + 16)
                            act.copy(leading[u][:, :], ring_down[:, u, :]).then_inc(down_masked[u], 1)
                    keep_x(1 - s, i + s)
                    for u in range(DOWN):
                        act.wait_ge(down_ready[u], b + 1)
                        act.wait_ge(y_stored[u], b * 16)
                        act.copy(y[:, u, :], k.bank(2 + u)).then_inc(y_copied[u], 1)
                        act.wait_ge(y_copied[u], b + 1)
                        act.dma_start(results[bass.ds(b * P, P), u * BANK:(u + 1) * BANK], y[:, u, :]).then_inc(y_stored[u], 16)
                keep_x(0, 0)
                blocks(act, body)
                filled = act.value_load(block_expert[0:1, SLOTS_MAX + 1:SLOTS_MAX + 2], min_val=1, max_val=SLOTS_MAX + 1)
                for u in range(DOWN):
                    wait_apart(act, y_stored[u], filled * 16, passed)

            @block.vector
            def _(dve):
                def body(i, s, b, e):
                    dve.wait_ge(down_ready[DOWN - 1], b)
                    for u in range(UP):
                        n = u % 2
                        bias = ring_up[:, u, KD * CH * P:KD * CH * P + CH]
                        v = Steps(dve, own)
                        v.n = b * (OWN * UP) + u * OWN
                        ps = k.bank(u % 2)
                        dve.wait_ge(up_ready[u], b + 1)
                        for c in range(2):
                            dve.tensor_scalar(gate[:, n, c * P:(c + 1) * P], ps[:, c * P:(c + 1) * P], bias[:, c:c + 1], LIMIT,
                                              ALU.add, ALU.min).then_inc(gated[u], 1)
                        for c in range(2):
                            v.then(dve.tensor_scalar(lin[:, n, c * P:(c + 1) * P], ps[:, (2 + c) * P:(3 + c) * P],
                                                     bias[:, 2 + c:3 + c], -LIMIT, ALU.add, ALU.max))
                        v.settle()
                        v.do(dve.tensor_scalar(lin[:, n, :], lin[:, n, :], LIMIT, 1.0, ALU.min, ALU.add))
                        dve.wait_ge(gated[u], 2 * b + 2)
                        v.do(dve.tensor_tensor(lin[:, n, :], lin[:, n, :], gate[:, n, :], ALU.mult))
                        dve.wait_ge(sigged[u], b + 1)
                        v.do(dve.tensor_tensor(product[:, n, :], lin[:, n, :], sig[:, n, :], ALU.mult))
                        high, low = (x[:, 2 * u:2 * u + 2, :].rearrange("p k n -> p (k n)") for x in (hidden.leading, hidden.rest))
                        v.do(leading_bits(dve, high, product[:, n, :]))
                        rest_bits(dve, low, product[:, n, :], high).then_inc(hid_done[u], 1)
                        if u < DOWN:
                            dve.wait_ge(down_masked[u], b + 1)
                            rest_bits(dve, rest[u][:, :], ring_down[:, u, :], leading[u][:, :]
                                      ).then_inc(down_split[u], 1)
                blocks(dve, body)


def third_block(k):
    nc, d = k.nc, k.dram
    with ExitStack() as ctx:
        def sb(what, shape, dtype=F32, stack=ctx):
            return stack.enter_context(k.tensor(f"third_{what}", shape, dtype))

        mod, gains = sb("mod", [P, 6 * KD, 2]), sb("gains", [P, 3, KD])
        subln, minus_lam = sb("subln", [P, 1]), sb("minus_lam", [P, 1])
        modulation(k, mod)
        third_columns(k, mod, gains, subln, minus_lam)
        with ExitStack() as attend:
            mix = sb("mix", [P, KD, T], F32, attend)
            mixers(k, mod, gains, subln, minus_lam, mix)

            def gated_residual(first):
                def finish(eng, n, ps):
                    g = mod[:, first + n, 0:1] if isinstance(n, int) else \
                        mod[:, bass.ds(n + first, 1), 0:1].rearrange("p a b -> p (a b)")
                    return eng.scalar_tensor_tensor(at(k.x, n), ps, g, at(k.x, n), ALU.mult, ALU.add)
                return finish

            project(k, "out3", [Section(d["w_out_3"], 2, KD, mix, gated_residual(2 * KD), "vector", spent=True)])
        feature_norm(k, "moe_norm", [([k.x[:, n, :] for n in range(KD)], [k.h[:, n, :] for n in range(KD)],
                                      [gains[:, 2, n:n + 1] for n in range(KD)])], k.c("ones"), 1.0 / D, "eps",
                     shift=[mod[:, 3 * KD + n, 0:1] for n in range(KD)])
        gate = sb("gate", [P, TT, TOP_K])
        dest = sb("dest", [P, TT, TOP_K], I32)
        by_expert = sb("gate_by_expert", [EXPERTS, T])
        rows = nc.dram_tensor("token_rows", (T + 1, D), F32, kind="Internal").ap()
        results = nc.dram_tensor("expert_rows", ((SLOTS_MAX + 1) * P, D), F32, kind="Internal").ap()
        with ExitStack() as routing:
            row_of = sb("row_of", [P, SLOTS_MAX + 2], I32, routing)
            block_expert = sb("block_expert", [1, SLOTS_MAX + 3], I32, routing)
            with ExitStack() as deciding:
                logits, bias = sb("logits", [P, TT, EXPERTS], F32, deciding), sb("router_b", [P, EXPERTS], F32, deciding)
                token_rows(k, rows, bias)
                project(k, "router", [Section(d["router_w"], 1, KD, k.h,
                                              lambda eng, n, ps: eng.tensor_tensor(logits[:, n, :], ps, bias[:, :], ALU.add),
                                              "vector", width=EXPERTS, by_tokens=True)])
                route(k, logits, gate, dest, row_of, block_expert, by_expert)
            experts(k, rows, row_of, block_expert, results)
        combine(k, results, gate, dest, by_expert, mod)
    chunks = [k.x[:, n, :] for n in range(KD)]
    feature_norm(k, "final_norm", [(chunks, chunks, [k.p("final_norm_w", n) for n in range(KD)])], k.c("ones"), 1.0 / D, "eps")
    store_stream(k)


def token_rows(k, rows, bias):
    nc = k.nc
    with k.stage("token_rows") as (sb, sem):
        by_token, zero = sb("by_token", [P, TT, D]), sb("zero", [1, D])
        turned, copied, cleared, stored = (sem(x) for x in ("turned", "copied", "zero_cleared", "rows_stored"))
        with nc.Block() as block:
            @block.tensor
            def _(pe):
                for t in range(TT):
                    for half in range(2):
                        for n in range(4):
                            last = pe.transpose(k.bank(2 * t + half)[:, n * P:(n + 1) * P],
                                                k.h[:, 4 * half + n, t * P:(t + 1) * P], k.c("ident"))
                        last.then_inc(turned, 1)

            @block.vector
            def _(dve):
                dve.memset(zero[:, :], 0.0).then_inc(cleared, 1)
                for n in range(2 * TT):
                    dve.wait_ge(turned, n + 1)
                    dve.tensor_copy(by_token[:, n // 2, (n % 2) * BANK:(n % 2 + 1) * BANK], k.bank(n)).then_inc(copied, 1)

            @block.sync
            def _(sp):
                sp.dma_start(bias[:, :], k.dram["router_b"][0:1, :].broadcast_to([P, EXPERTS])).then_inc(stored, 16)
                sp.wait_ge(cleared, 1)
                sp.dma_start(rows[T:T + 1, :], zero[:, :]).then_inc(stored, 16)
                for t in range(TT):
                    sp.wait_ge(copied, 2 * t + 2)
                    sp.dma_start(rows[t * P:(t + 1) * P, :], by_token[:, t, :]).then_inc(stored, 16)
                sp.wait_ge(stored, 16 * (TT + 2))


def combine(k, results, gate, dest, by_expert, mod):
    nc = k.nc
    with k.stage("combine") as (sb, sem):
        b2 = sb("b2", [EXPERTS, D])
        got, acc = sb("got", [P, 4, D]), sb("acc", [P, TT, D])
        landed, gathered, weighed, summed, added = sem("b2_landed"), [sem(f"rows{i}_gathered") for i in range(4)], sem("rows_weighed"), \
            sem("sums_ready"), sem("residual_added")
        N = TT * TOP_K
        with nc.Block() as block:
            @block.sync
            def _(sp):
                sp.dma_start(b2[:, :], k.dram["b2_3"]).then_inc(landed, 16)

            @block.gpsimd
            def _(pool):
                for n in range(N):
                    t, c = n // TOP_K, n % TOP_K
                    if n >= 4:
                        pool.wait_ge(weighed, n - 3)
                    pool.indirect_dma_start(out=got[:, n % 4, :], out_offset=None, in_=results,
                                            in_offset=bass.IndirectOffsetOnAxis(ap=dest[:, t, c:c + 1], axis=0)
                                            ).then_inc(gathered[n % 4], 16)

            @block.vector
            def _(dve):
                for n in range(N):
                    t, c = n // TOP_K, n % TOP_K
                    dve.wait_ge(gathered[n % 4], 16 * (n // 4) + 16)
                    g = gate[:, t, c:c + 1]
                    if c == 0:
                        dve.tensor_scalar(acc[:, t, :], got[:, n % 4, :], g, None, ALU.mult).then_inc(weighed, 1)
                    else:
                        dve.wait_ge(weighed, n)
                        dve.scalar_tensor_tensor(acc[:, t, :], got[:, n % 4, :], g, acc[:, t, :], ALU.mult,
                                                 ALU.add).then_inc(weighed, 1)
                for n in range(KD):
                    dve.wait_ge(summed, n + 1)
                    dve.scalar_tensor_tensor(k.x[:, n, :], k.bank(n), mod[:, 5 * KD + n, 0:1], k.x[:, n, :], ALU.mult,
                                             ALU.add).then_inc(added, 1)

            @block.tensor
            def _(pe):
                pe.wait_ge(landed, 16)
                pe.wait_ge(weighed, N)
                for n in range(KD):
                    pe.matmul(k.bank(n), b2[:, n * P:(n + 1) * P], by_expert[:, :], start=True, stop=False)
                    for t in range(TT):
                        last = pe.matmul(k.bank(n)[:, t * P:(t + 1) * P], acc[:, t, n * P:(n + 1) * P], k.c("ident"),
                                         start=False, stop=(t == TT - 1))
                    last.then_inc(summed, 1)


def lay_out_third(i, a, p):
    a["ctxT"] = i["ctx_3"][0].T
    p["c"] = np.stack([columns(i["c_3"][0]), columns(i["c_ctx_3"])], 2).reshape(P, -1)
    for n in ("b_ada", "attn_norm_w", "q_norm_w", "kv_norm_w", "subln_w", "ffn_norm_w"):
        p[n] = columns(i[n + "_3"][0])
    p["final_norm_w"] = columns(i["final_norm_w_3"])
    lam = np.zeros((P, 4), np.float32)
    for n, name in enumerate(("q1", "k1", "q2", "k2")):
        lam[0:DH, n] = i[f"lambda_{name}_3"][0]
    p["lambdas"] = lam
    a["w_ada"] = units_of(i["w_ada_3"][0], 4)
    w = i["w_in_3"][0]
    kr = np.concatenate([w[:, 1920:1984]] * 2, 1)
    a["w3_dq"], a["w3_dk"], a["w3_dv"] = units_of(w[:, 0:512], 4), units_of(w[:, 512:1024], 4), whole(w[:, 1024:1536])
    a["w3_misc"] = units_of(np.concatenate([w[:, 1536:1920], kr], 1), 4)
    a["w3_misc_ctx"] = units_of(np.concatenate([w[:, 1792:1920], kr], 1), 2)
    uq = i["w_uq_3"][0].reshape(256, MLA_HEADS, P + DH)
    a["w3_uq"] = units_of(np.concatenate([uq[:, :, 0:P].reshape(256, -1), uq[:, :, P:].reshape(256, -1)], 1), 3)
    ukv = i["w_ukv_3"][0].reshape(P, MLA_HEADS, 2, P)
    a["w3_uk"], a["w3_uv"] = units_of(ukv[:, :, 0].reshape(P, -1), 4), whole(ukv[:, :, 1].reshape(P, -1))
    a["w_out_3"] = units_of(i["w_out_3"][0], 4)
    a["router_w"], a["router_b"] = whole(i["router_w_3"][0]), i["router_b_3"]
    w1 = i["w1_3"][0].reshape(EXPERTS, KD, P, 2, 4, 2 * P).transpose(0, 4, 2, 1, 3, 5).reshape(EXPERTS, 4, P, -1)
    b1 = i["b1_3"][0].reshape(EXPERTS, 2, 4, 2, P).transpose(0, 2, 4, 1, 3).reshape(EXPERTS, 4, P, 4)
    a["w_up_3"] = np.concatenate([w1, b1], 3)
    a["w_down_3"] = i["w2_3"][0].reshape(EXPERTS, KD, P, 2, BANK).transpose(0, 3, 2, 1, 4).reshape(EXPERTS, 2, P, -1)
    a["b2_3"] = i["b2_3"][0]



def program(nc, dram):
    with ExitStack() as ctx:
        k = Core(nc, ctx, dram)
        k.x = k.keep("residual", [P, KD, T])
        k.h = k.keep("normed", [P, KD, T])
        k.const = k.keep("constants", [P, CONST_N])
        k.param = k.keep("parameters", [P, PARAM_N])
        load_inputs(k)
        first_block(k)
        second_block(k)
        third_block(k)


def store_stream(k):
    with k.stage("store") as (sb, sem):
        stored = sem("result_stored")
        with k.nc.Block() as block:
            @block.sync
            def _(sp):
                sp.dma_start(k.dram["out"].rearrange("(k p) t -> p k t", p=P), k.x[:, :, :]).then_inc(stored, 16)
                sp.wait_ge(stored, 16)


def units_of(w, chunks):
    kc = w.shape[0] // P
    return w.reshape(kc, P, -1, chunks * P).transpose(2, 1, 0, 3).reshape(-1, P, kc * chunks * P)


def whole(w):
    return w.reshape(w.shape[0] // P, P, -1).transpose(1, 0, 2).reshape(1, P, -1)


def columns(v):
    return v.reshape(-1, P).T


def lay_out(i):
    a = {"consts": np.concatenate(list(constants().values()), 1), "buckets": bucket_rows()}
    a["xT"] = i["x"][0].T
    a["rel_bias"] = i["rel_bias"]
    w = i["w_in"][0]
    a["w_in_q"] = units_of(w[:, 0:512], 4)
    a["w_in_k"] = units_of(np.concatenate([w[:, 512:640], w[:, 640:768], w[:, 768:896], w[:, 1024:1152]], 1), 4)
    a["w_in_v"] = whole(np.concatenate([w[:, 896:1024], w[:, 1152:1280]], 1))
    a["w_in_g"] = whole(w[:, 1280:1304])
    a["w_in_u"] = units_of(w[:, 1304:1816], 4)
    a["w_in_sv"] = whole(w[:, 1816:2328])
    for x in "kv":
        a[f"cmp_w1_{x}"] = i[f"cmp_w1_{x}"][0]
    a["cmp_w2_k"] = np.concatenate([i["cmp_w2_k"][0]] * 2, 1)
    a["cmp_w2_v"] = i["cmp_w2_v"][0]
    a["sgu_wT"] = i["sgu_w"][0].transpose(2, 0, 1).reshape(P, -1)
    a["sgu_norm"] = i["sgu_norm"]
    a["sgu_b"] = i["sgu_b"][0]
    a["w_out"] = units_of(i["w_out"][0], 4)
    up = units_of(i["w_up"][0], 1).reshape(2, FF_CHUNKS, P, KD, P)
    a["w_up"] = up.transpose(1, 2, 3, 0, 4).reshape(FF_CHUNKS, P, KD * 2 * P)
    a["w_down"] = units_of(i["w_down"][0], 1)

    def interleaved(v):
        return v.reshape(-1, 2, FF_CHUNKS, P).transpose(0, 2, 1, 3).reshape(-1)

    p = {n: columns(i[n][0]) for n in ("attn_norm", "ffn_norm", "cmp_b1_k", "cmp_b1_v")}
    p["cmp_pe_k"], p["cmp_pe_v"] = columns(i["cmp_pe_k"][0].reshape(-1)), columns(i["cmp_pe_v"][0].reshape(-1))
    for n in ("q_norm", "k_norm_cmp", "k_norm_slc", "k_norm_win"):
        p[n] = columns(np.concatenate([i[n][0]] * 2))
    p["conv_w"], p["conv_b"] = columns(interleaved(i["conv_w"][0])), columns(interleaved(i["conv_b"][0]))
    lay_out_second(i, a, p)
    lay_out_third(i, a, p)
    a["params"] = np.concatenate([p[n] for n in PARAM_COLUMNS], 1)
    return {n: np.ascontiguousarray(v) for n, v in a.items()}


def kernel(**inputs):
    from concourse import bacc
    from concourse.bass_utils import run_bass_kernel_spmd

    arrays = lay_out({n: np.asarray(v) for n, v in inputs.items()})
    nc = bacc.Bacc("TRN2", target_bir_lowering=False, num_devices=1)
    dram = {n: nc.dram_tensor(f"in_{n}", v.shape, F32, kind="ExternalInput").ap() for n, v in arrays.items()}
    dram["out"] = nc.dram_tensor("out", (D, T), F32, kind="ExternalOutput").ap()
    program(nc, dram)
    run = run_bass_kernel_spmd(nc, [{f"in_{n}": v for n, v in arrays.items()}], core_ids=[0])
    return run.results[0]["out"].T[None]
```

```python
import math
from contextlib import ExitStack, contextmanager

import numpy as np

import concourse.bass as bass
from concourse import mybir

F32 = mybir.dt.float32
F32R = mybir.dt.float32r
I32 = mybir.dt.int32
U32 = mybir.dt.uint32
ALU = mybir.AluOpType
ACT = mybir.ActivationFunctionType
AX_X = mybir.AxisListType.X

P = 128
T = 512
TT = T // P
D = 1024
KD = D // P
BANK = 512
NEG = -1e30
EPS = 1e-6
EPS_2 = 1e-5

NSA_HEADS, NSA_GROUPS, DH = 8, 2, 64
CMP_BLOCK, CMP_STRIDE, CMP_HIDDEN = 32, 16, 256
NCMP = (T - CMP_BLOCK) // CMP_STRIDE + 1
CMP_PAIRS = CMP_BLOCK * DH // P
REL_BUCKETS, REL_MAX_DIST = 32, 128
STRIP = T + 3 * P
SKEW = STRIP + P
D_FF = 2816
FF_CHUNKS = D_FF // P
GDN_HEADS, GDN_CHUNK, GDN_CONV = 4, 64, 4
GDN_QKV = 3 * GDN_HEADS
CONV_K = 31
BRANCHES = 4
PLE = 256
ALPHA = 2 ** 0.25
CTX = 256
TA = T + CTX
DIFF_HEADS, MLA_HEADS = 4, 4
LAM_INIT = 0.8 - 0.6 * math.exp(0.0)
EXPERTS, TOP_K, D_FF_3 = 32, 4, 1024
LIMIT, SWIGLU_ALPHA = 7.0, 1.702
SLOTS_MAX = T * TOP_K // P + EXPERTS - 1


class Core:

    def __init__(self, nc, ctx, dram):
        self.nc, self.ctx, self.dram = nc, ctx, dram
        self.psum = ctx.enter_context(nc.psum_tensor("psum", [P, 8 * BANK], F32))
        self.byte_of = {}

    @contextmanager
    def tensor(self, name, shape, dtype=F32):
        with self.nc.sbuf_tensor(name, shape, dtype) as t:
            self.byte_of[t.name] = self.nc.sbuf_base - 4 * math.prod(shape[1:])
            yield t

    def keep(self, name, shape, dtype=F32):
        return self.ctx.enter_context(self.tensor(name, shape, dtype))

    def over(self, name, ap, shape):
        at = self.byte_of[ap.tensor.name] + 4 * ap.offset
        return self.nc.alloc_sbuf_tensor_at(name, shape, F32R, offset=at)

    def bank(self, n, width=BANK):
        return self.psum[:, n * BANK:n * BANK + width]

    def c(self, name):
        at, n = CONST_AT[name]
        return self.const[:, at:at + n]

    def p(self, name, n=None):
        at, width = PARAM_AT[name]
        return self.param[:, at:at + width] if n is None else self.param[:, at + n:at + n + 1]

    @contextmanager
    def stage(self, name):
        nc, sems = self.nc, []
        with ExitStack() as ctx:
            def sb(what, shape, dtype=F32):
                return ctx.enter_context(self.tensor(f"{name}_{what}", shape, dtype))

            def sem(what):
                sems.append(nc.alloc_semaphore(f"{name}_{what}"))
                return sems[-1]

            yield sb, sem
        nc.clear_and_free_semaphores(sems)
        nc.all_engine_barrier()


class Steps:

    def __init__(self, eng, sem):
        self.eng, self.sem, self.n = eng, sem, 0

    def then(self, instruction):
        self.n = self.n + 1
        instruction.then_inc(self.sem, 1)

    def settle(self):
        self.eng.wait_ge(self.sem, self.n)

    def do(self, instruction):
        self.then(instruction)
        self.settle()


def wait_apart(eng, sem, count, passed):
    eng.wait_ge(sem, count)
    eng.sem_inc(passed, 1)


def at(ap, n):
    if isinstance(n, int):
        return ap[:, n, :]
    return ap[:, bass.ds(n, 1), :].rearrange("p a n -> p (a n)")


def col(ap, n):
    return ap[:, n:n + 1] if isinstance(n, int) else ap[:, bass.ds(n, 1)]



def constants():
    i = np.arange(P)
    row, colm = i[:, None], i[None, :]
    same = row // GDN_CHUNK == colm // GDN_CHUNK
    c = {
        "ident": np.eye(P),
        "ones": np.ones((P, P)),
        "halves": row // DH == colm // DH,
        "upto": np.concatenate([row <= colm, np.ones((P, 3 * P))], 1),
        "before": np.concatenate([row < colm, np.ones((P, 3 * P))], 1),
        "minus_from": -1.0 * (row >= colm),
        "minus_ones": -np.ones((P, P)),
        "not_before": np.where(row >= colm, NEG, 0.0),
        "pick1": np.arange(15)[None, :] == np.full((P, 1), 7),
        "pick2": np.arange(30)[None, :] == 14 + row // DH,
        "g_upto": same & (row <= colm),
        "g_after": same & (row > colm),
    }
    for n in range(6):
        k = 1 << n
        c[f"g_level{n}"] = (row // (2 * k) == colm // (2 * k)) & (row % (2 * k) >= k) & (colm % (2 * k) < k)
    m = np.arange(T)
    c["causal"] = np.where(row - m[None, :] + 3 * P >= 0, 0.0, NEG)
    pairs, grid = DH // 4, 64
    inv = 10000.0 ** (-np.arange(pairs, dtype=np.float32) / np.float32(pairs)).astype(np.float32)
    tok = np.arange(T)
    spot = np.stack([tok // grid, tok % grid]).astype(np.float32)
    feat = i % DH
    ang = spot[feat // 32] * inv.astype(np.float32)[feat % pairs][:, None]
    c["rope_cos"], c["rope_sin"] = np.cos(ang), np.sin(ang)
    swap = np.zeros((P, P))
    for f in range(P):
        other = f + pairs if f % 32 < pairs else f - pairs
        swap[other, f] = -1.0 if f % 32 < pairs else 1.0
    c["rope_swap"] = swap
    c["any_cmp"] = (row + P * np.arange(TT)[None, :]) >= CMP_BLOCK - 1
    c["gdn_scale"] = np.full((P, 1), float(P) ** -0.5)
    c["eps"] = np.full((P, 1), EPS)
    c["eps_2"] = np.full((P, 1), EPS_2)
    c["lane"] = row
    c["lanes_on"] = row + P * np.arange(TT)[None, :]
    c["experts"] = np.broadcast_to(np.arange(EXPERTS), (P, EXPERTS))
    c["blocks"] = np.broadcast_to(np.arange(SLOTS_MAX + 1), (P, SLOTS_MAX + 1))
    c["one"] = np.ones((P, 1))
    return {k: np.ascontiguousarray(v, dtype=np.float32) for k, v in c.items()}


def bucket_rows():
    dist = 3 * P + P - 1 - np.arange(SKEW)
    half = REL_BUCKETS // 2
    d = np.maximum(dist, 1).astype(np.float32)
    log_b = half + (np.log(d / np.float32(half)) / np.float32(math.log(REL_MAX_DIST / half))
                    * np.float32(REL_BUCKETS - half)).astype(np.int32)
    bucket = np.where(dist < half, np.maximum(dist, 0), np.clip(log_b, half, REL_BUCKETS - 1))
    rows = np.zeros((P, SKEW), np.float32)
    rows[bucket, np.arange(SKEW)] = dist >= 0
    rows[REL_BUCKETS] = dist < 0
    return rows


def places(named):
    found, n = {}, 0
    for name, a in named.items():
        found[name] = (n, a.shape[1])
        n += a.shape[1]
    return found, n


CONST_AT, CONST_N = places(constants())
PARAM_COLUMNS = {
    "attn_norm": 8, "ffn_norm": 8, "q_norm": 1, "k_norm_cmp": 1, "k_norm_slc": 1, "k_norm_win": 1,
    "cmp_pe_k": CMP_PAIRS, "cmp_b1_k": 2, "cmp_pe_v": CMP_PAIRS, "cmp_b1_v": 2,
    "conv_w": 3 * 2 * FF_CHUNKS, "conv_b": 2 * FF_CHUNKS,
    "b_gate": 32, "conv_qkv": GDN_CONV * GDN_QKV, "gdn_norm": 1, "conv_dw": CONV_K * 4,
    "conv_dw_bias": 4, "conv_ln_g": 4, "conv_ln_b": 4, "b_ple_gate": 8, "ln_g": 8, "ln_b": 8,
    "c": 16, "b_ada": 48, "attn_norm_w": 8, "q_norm_w": 2, "kv_norm_w": 1, "subln_w": 1,
    "ffn_norm_w": 8, "final_norm_w": 8, "lambdas": 4,
}
PARAM_AT, PARAM_N = {}, 0
for _name, _n in PARAM_COLUMNS.items():
    PARAM_AT[_name] = (PARAM_N, _n)
    PARAM_N += _n



def feature_norm(k, name, groups, matrix, scale, eps, shift=None, memory=()):
    nc = k.nc
    results = [o for _, out, _ in groups for o in out]
    flat = [(g, n) for g, (src, _, _) in enumerate(groups) for n in range(len(src))]
    width = [src[0].shape[-1] for src, _, _ in groups]
    with k.stage(name) as (sb, sem):
        sq = sb("sq", [P, 3, T])
        std = sb("std", [P, 2, T])
        rstd = sb("rstd", [P, 2, T])
        squared, summed, rooted, turned, scaled, shifted, stored = (
            sem(x) for x in ("squared", "summed", "rooted", "turned", "scaled", "shifted", "results_stored"))
        with nc.Block() as block:
            if memory:
                @block.sync
                def _(sp):
                    for n, place in enumerate(memory):
                        sp.wait_ge(scaled, n + 1)
                        sp.dma_start(place, results[n]).then_inc(stored, 16)
                    sp.wait_ge(stored, 16 * len(memory))

            @block.scalar
            def _(act):
                done = 0
                for g, (src, _, _) in enumerate(groups):
                    for s in src:
                        if done >= 3:
                            act.wait_ge(summed, done - 2)
                        act.activation(sq[:, done % 3, 0:width[g]], s, ACT.Square).then_inc(squared, 1)
                        done += 1
                    act.wait_ge(summed, done)
                    if g >= 2:
                        act.wait_ge(turned, g - 1)
                    act.activation(std[:, g % 2, 0:width[g]], k.bank(g % 2, width[g]), ACT.Sqrt,
                                   bias=k.c(eps), scale=scale).then_inc(rooted, 1)
                for n, o in enumerate(results if shift else []):
                    act.wait_ge(scaled, n + 1)
                    act.activation(o, o, ACT.Identity, bias=shift[n]).then_inc(shifted, 1)

            @block.tensor
            def _(pe):
                for n, (g, s) in enumerate(flat):
                    pe.wait_ge(squared, n + 1)
                    if s == 0 and g >= 2:
                        pe.wait_ge(rooted, g - 1)
                    pe.matmul(k.bank(g % 2, width[g]), matrix, sq[:, n % 3, 0:width[g]], start=(s == 0),
                              stop=(s == len(groups[g][0]) - 1)).then_inc(summed, 1)

            @block.vector
            def _(dve):
                for g, (src, out, gain) in enumerate(groups):
                    dve.wait_ge(rooted, g + 1)
                    r = rstd[:, g % 2, 0:width[g]]
                    dve.reciprocal(r, std[:, g % 2, 0:width[g]]).then_inc(turned, 1)
                    dve.wait_ge(turned, g + 1)
                    for n, s in enumerate(src):
                        if gain is None:
                            dve.tensor_tensor(out[n], s, r, ALU.mult).then_inc(scaled, 1)
                        else:
                            dve.scalar_tensor_tensor(out[n], s, gain[n], r, ALU.mult,
                                                     ALU.mult).then_inc(scaled, 1)


def chunk_norms(k, name, chunks, parts, scale, eps):
    nc = k.nc
    G = len(chunks)
    rows = G * parts
    picks = 8
    width = [src.shape[-1] for src, _, _ in chunks]
    with k.stage(name) as (sb, sem):
        sq = sb("sq", [P, 3, T])
        std, rstd = sb("std", [rows, T]), sb("rstd", [P, T])
        column = sb("column", [P, G * P])
        squared, summed, rooted, cleared, picked, turned, spread, scaled = (sem(x) for x in (
            "squared", "summed", "rooted", "rows_cleared", "columns_picked", "turned", "spread", "scaled"))
        with nc.Block() as block:
            @block.gpsimd
            def _(pool):
                pool.memset(rstd[:, :], 0.0).then_inc(cleared, 1)
                pool.tensor_copy(column[:, :].rearrange("p (n m) -> p n m", n=rows),
                                 k.c("ident")[:, 0:rows].unsqueeze(2).broadcast_to([P, rows, P // parts])).then_inc(picked, 1)

            @block.scalar
            def _(act):
                for n, (src, _, _) in enumerate(chunks):
                    if n >= 3:
                        act.wait_ge(summed, n - 2)
                    act.activation(sq[:, n % 3, 0:width[n]], src, ACT.Square).then_inc(squared, 1)
                act.wait_ge(summed, G)
                act.activation(std[:, :], k.psum[0:rows, 0:T], ACT.Sqrt, bias=k.c(eps)[0:rows, :], scale=scale
                               ).then_inc(rooted, 1)

            @block.tensor
            def _(pe):
                for n in range(G):
                    first = parts * (picks - 1 - n)
                    pe.wait_ge(squared, n + 1)
                    pe.matmul(k.psum[0:rows, 0:width[n]], k.c(f"pick{parts}")[:, first:first + rows], sq[:, n % 3, 0:width[n]],
                              start=(n == 0), stop=(n == G - 1)).then_inc(summed, 1)
                pe.wait_ge(picked, 1)
                pe.wait_ge(turned, 1)
                for n in range(G):
                    if n >= 4:
                        pe.wait_ge(scaled, n - 3)
                    pe.matmul(k.bank(1 + n % 4, width[n]), column[:, n * P:(n + 1) * P], rstd[:, 0:width[n]], start=True, stop=True).then_inc(spread, 1)

            @block.vector
            def _(dve):
                dve.wait_ge(cleared, 1)
                dve.wait_ge(rooted, 1)
                dve.reciprocal(rstd[0:rows, :], std[:, :]).then_inc(turned, 1)
                for n, (src, out, gain) in enumerate(chunks):
                    dve.wait_ge(spread, n + 1)
                    dve.scalar_tensor_tensor(out, src, gain, k.bank(1 + n % 4, width[n]), ALU.mult, ALU.mult).then_inc(scaled, 1)



def leading_bits(dve, out, src):
    return dve.tensor_copy(out, src)


def rest_bits(dve, out, src, leading):
    return dve.tensor_tensor(out, src, leading.bitcast(F32), ALU.subtract)


def three_passes(pe, out, left, right, start, stop):
    (lh, ll), (rh, rl) = left, right
    pe.matmul(out, lh, rh, start=start, stop=False)
    pe.matmul(out, lh, rl, start=False, stop=False)
    return pe.matmul(out, ll, rh, start=False, stop=stop)


class Parts:

    def __init__(self, leading, rest):
        self.leading, self.rest = leading, rest


class Section:

    def __init__(self, weights, units, kc, source, finish, engine, chunks=4, width=T, by_tokens=False, rows=P, spent=False, split=True):
        self.weights, self.units, self.kc, self.source = weights, units, kc, source
        self.finish, self.engine, self.chunks = finish, engine, chunks
        self.width, self.by_tokens, self.rows, self.spent = width, by_tokens, rows, spent
        self.columns = width if by_tokens else chunks * P
        self.split = split and width >= 2 * P
        self.set_cuts()

    def set_cuts(self):
        kc, self.first_chunk = self.kc, self.split and not self.by_tokens and self.chunks > 1
        if self.first_chunk:
            self.cuts = [(0, 1), (1, self.chunks)]
        else:
            self.cuts = [(0, kc)] if kc == 1 else [(0, kc // 2), (kc // 2, kc)]

    def cut(self, unit, c):
        lo, hi = self.cuts[c]
        if self.first_chunk:
            return unit[:, 0:self.kc * self.columns].rearrange("p (k n) -> p k n", k=self.kc)[:, :, lo * P:hi * P]
        return unit[:, lo * self.columns:hi * self.columns]


def run_units(eng, units, start, body):
    pairs = (units - 1) // 2
    if pairs >= 2:
        with eng.Fori(0, pairs) as i:
            for s in range(2):
                body(2 * i + s, (start + s) % 2, i)
    else:
        pairs = 0
    for u in range(2 * pairs, units):
        body(u, (start + u) % 2, u // 2)


def project(k, name, sections, beside=None, room={}):
    nc = k.nc
    starts, landed0, done0, split0 = [], [], [], []
    n, lands, dones, splits = 0, [[0, 0], [0, 0]], [0, 0], [0, 0]
    for s in sections:
        if beside is not None:
            s.split = False
            s.set_cuts()
        starts.append(n)
        landed0.append([list(x) for x in lands])
        done0.append(list(dones))
        split0.append(list(splits))
        for u in range(s.units):
            for c in range(len(s.cuts)):
                lands[(n + u) % 2][c] += 1
            dones[(n + u) % 2] += s.chunks
            splits[(n + u) % 2] += len(s.cuts) * s.split
        n += s.units
    size = max(s.kc * s.columns for s in sections)
    with k.stage(name) as (sb, sem):
        ring = sb("weights", [P, 2, size])
        landed = [[sem(f"weights{i}_half{c}_landed") for c in range(2)] for i in range(2)]
        ready = [sem(f"sums{i}_ready") for i in range(2)]
        emptied = [sem(f"banks{i}_emptied") for i in range(2)]
        apart = {}
        if any(s.split for s in sections):
            widest = max(s.kc * s.columns for s in sections if s.split)
            if "leading" in room:
                leading = [k.over(f"{name}_leading{i}", a, [P, widest]) for i, a in enumerate(room["leading"])]
            else:
                leading = [sb(f"leading{i}", [P, widest], F32R) for i in range(2)]
            rest = [k.over(f"{name}_rest{i}", ring[:, i, :], [P, widest]) for i in range(2)]
            masked = [sem(f"weights{i}_masked") for i in range(2)]
            split = [sem(f"weights{i}_split") for i in range(2)]
            source_masked, source_split = sem("source_masked"), sem("source_split")
        to_split = []
        for s in sections:
            if s.split and isinstance(s.source, Parts):
                apart[id(s.source)] = (s.source, 0)
            elif s.split and id(s.source) not in apart:
                shape = [P, s.kc, s.source.shape[-1]]
                free = list(room.get("parts", [])) if not apart else []
                places = [free.pop(0) if free else None, s.source if s.spent else free.pop(0) if free else None]
                high, low = (k.over(f"{name}_{x}{len(apart)}", a[:, :, :], shape) if a is not None else sb(f"{x}{len(apart)}", shape, F32R)
                             for x, a in zip(("source_leading", "source_rest"), places))
                apart[id(s.source)] = (Parts(high, low), sum(x.kc for x, _ in to_split) + s.kc)
                to_split.append((s, apart[id(s.source)][0]))

        with nc.Block() as block:
            @block.sync
            def _(sp):
                for q, s in enumerate(sections):
                    def load(u, slot, turn, q=q, s=s):
                        sp.wait_ge(emptied[slot], turn * s.chunks + done0[q][slot])
                        src = s.weights[u, :, :] if isinstance(u, int) else \
                            s.weights[bass.ds(u, 1), :, :].rearrange("a p n -> p (a n)")
                        for c in range(len(s.cuts)):
                            sp.dma_start(s.cut(ring[:, slot, :], c), s.cut(src, c)).then_inc(landed[slot][c], 16)
                    run_units(sp, s.units, starts[q], load)

            @block.tensor
            def _(pe):
                for q, s in enumerate(sections):
                    def products(u, slot, turn, q=q, s=s):
                        w = ring[:, slot, 0:s.kc * s.columns].rearrange("p (k n) -> p k n", k=s.kc)
                        cuts = len(s.cuts)
                        if s.split:
                            high, low = (x[slot][:, 0:s.kc * s.columns].rearrange("p (k n) -> p k n", k=s.kc)
                                         for x in (leading, rest))
                            source, source_chunks = apart[id(s.source)]
                        pe.wait_ge(emptied[slot], turn * s.chunks + done0[q][slot])

                        def wait_for_cut(c):
                            if s.split:
                                pe.wait_ge(split[slot], turn * cuts + split0[q][slot] + c + 1)
                            else:
                                pe.wait_ge(landed[slot][c], (turn + landed0[q][slot][c] + 1) * 16)

                        for j in range(s.chunks):
                            out = k.bank(4 * slot + j, s.width)[0:s.rows, :]
                            for kk in range(s.kc):
                                for c, (lo, _) in enumerate(s.cuts):
                                    if (j, kk) == ((lo, 0) if s.first_chunk else (0, lo)):
                                        wait_for_cut(c)
                                half = s.kc // 2 or s.kc
                                if j == 0 and s.split and source_chunks and kk in (0, half):
                                    pe.wait_ge(source_split, source_chunks - s.kc + (s.kc if kk else half))

                                def both(x):
                                    tok = x[:, kk, j * P:j * P + s.rows] if s.by_tokens else x[:, kk, 0:s.width]
                                    return tok

                                def of(x):
                                    return x[:, kk, :] if s.by_tokens else x[:, kk, j * P:(j + 1) * P]
                                ends = {"start": kk == 0, "stop": kk == s.kc - 1}
                                if s.split:
                                    pair = (both(source.leading), both(source.rest)), (of(high), of(low))
                                    left, right = pair if s.by_tokens else pair[::-1]
                                    last = three_passes(pe, out, left, right, **ends)
                                else:
                                    left, right = (both(s.source), of(w)) if s.by_tokens else (of(w), both(s.source))
                                    last = pe.matmul(out, left, right, **ends)
                            last.then_inc(ready[slot], 1)
                    run_units(pe, s.units, starts[q], products)

            def take(eng, q, s, u, slot, turn):
                for j in range(s.chunks):
                    eng.wait_ge(ready[slot], turn * s.chunks + done0[q][slot] + j + 1)
                    s.finish(eng, u * s.chunks + j, k.bank(4 * slot + j, s.width)[0:s.rows, :]).then_inc(emptied[slot], 1)

            @block.scalar
            def _(act):
                for s, parts in to_split:
                    for kk in range(s.kc):
                        act.activation(parts.leading[:, kk, :], s.source[:, kk, :], ACT.Copy).then_inc(source_masked, 1)
                for q, s in enumerate(sections):
                    if s.engine == "scalar":
                        run_units(act, s.units, starts[q], lambda u, slot, turn, q=q, s=s: take(act, q, s, u, slot, turn))

            @block.vector
            def _(dve):
                def split_unit(q, u, slot, turn, only=None):
                    s = sections[q]
                    if not s.split:
                        return
                    for c in range(len(s.cuts)) if only is None else [only]:
                        raw, high, low = (s.cut(x, c) for x in (ring[:, slot, :], leading[slot], rest[slot]))
                        n = turn * len(s.cuts) + c + 1
                        dve.wait_ge(landed[slot][c], (turn + landed0[q][slot][c] + 1) * 16)
                        leading_bits(dve, high, raw).then_inc(masked[slot], 1)
                        dve.wait_ge(masked[slot], n + split0[q][slot])
                        rest_bits(dve, low, raw, high).then_inc(split[slot], 1)

                def split_source(chunks):
                    for n in chunks:
                        parts, kk, source = flat[n]
                        dve.wait_ge(source_masked, n + 1)
                        rest_bits(dve, parts.rest[:, kk, :], source[:, kk, :], parts.leading[:, kk, :]).then_inc(source_split, 1)

                flat = [(parts, kk, s.source) for s, parts in to_split for kk in range(s.kc)]
                first = sections[0]
                own = first.kc if first.split and not isinstance(first.source, Parts) else 0
                split_source(range(own // 2))
                split_unit(0, 0, starts[0] % 2, 0, only=0)
                split_source(range(own // 2, own))
                for c in range(1, len(first.cuts)):
                    split_unit(0, 0, starts[0] % 2, 0, only=c)
                split_source(range(own, len(flat)))
                for q, s in enumerate(sections):
                    def step(u, slot, turn, q=q, s=s):
                        if isinstance(u, int) and u + 1 == s.units:
                            if q + 1 < len(sections):
                                split_unit(q + 1, 0, starts[q + 1] % 2, 0)
                        else:
                            split_unit(q, u + 1, 1 - slot, turn + (slot != starts[q] % 2))
                        if s.engine == "vector":
                            take(dve, q, s, u, slot, turn)
                    if s.split or s.engine == "vector" or q + 1 < len(sections):
                        run_units(dve, s.units, starts[q], step)
                if beside is not None:
                    beside(dve, sem)


def copies_to(dst):
    return lambda eng, n, ps: eng.tensor_copy(at(dst, n), ps)


def adds_to(dst):
    return lambda eng, n, ps: eng.tensor_tensor(at(dst, n), ps, at(dst, n), ALU.add)


def activates_to(dst, func, bias=None):
    def finish(eng, n, ps):
        if bias is None:
            return eng.activation(at(dst, n), ps, func)
        return eng.activation(at(dst, n), ps, func, bias=col(bias, n))
    return finish


def head_copies(dst, src):
    return [(dst[h * DH:(h + 1) * DH, h, :], src[h * DH:(h + 1) * DH, :]) for h in range(2)]


class Unit:

    def __init__(self, products, keys, bias, gate, tiles, out, group, opens, closes):
        self.products, self.keys, self.bias, self.gate = products, keys, bias, gate
        self.tiles, self.out, self.group, self.opens, self.closes = tiles, out, group, opens, closes


def attention(k, name, rounds, copies, units, results, padded=(), gating=False, joined=False):
    nc = k.nc
    sequence = [u for slot in range(2) for u in units(slot)]
    N = len(sequence)
    U = N // 2
    wide = max(u.keys for u in sequence) > BANK
    score_buffers, turn_buffers = (2, 1) if wide else (4, 2)
    keys_max = max(u.keys for u in sequence)
    G = max(u.group for u in sequence) + 1
    n_copies = len(copies(0, 0))
    LAG = 2 if wide else 3
    AHEAD = LAG + 1

    def group(n):
        return (n // U) * G + sequence[n].group

    closing = {group(n): n for n in range(N)}
    copied_units = [n for n in range(N) if closing[group(n)] == n or not joined]
    C = len(copied_units)

    def copy_of(n):
        return group(n) if joined else n

    with k.stage(name) as (sb, sem):
        masked_sb = sb("masked", [P, AHEAD, keys_max])
        probs = sb("probs", [P, AHEAD, keys_max])
        top, total, inverse = (sb(x, [P, AHEAD]) for x in ("top", "total", "inverse"))
        diag = sb("diag", [P, AHEAD, P])
        turned_sb = sb("turned", [P, 2, -(-keys_max // P) * P])
        scored, masked, exped, inverted, weighed, turned, copied, taken, passed, cleared = (sem(x) for x in (
            "scores_ready", "scores_masked", "probs_ready", "sums_inverted", "weights_ready",
            "probs_turned", "probs_copied", "results_taken", "waits_passed", "padding_cleared"))
        staged, summed = ([sem(f"{x}{slot}") for slot in range(2)] for x in ("operands_staged", "values_summed"))

        def scores_bank(n, keys):
            at = n % score_buffers * (4 // score_buffers) * BANK
            return k.psum[:, at:at + keys]

        def turned_bank(n):
            at = copy_of(n) % turn_buffers
            return k.psum[:, (4 + at) * BANK:(6 if wide else 5 + at) * BANK]

        def out_bank(g):
            return k.psum[:, (6 + g % 2) * BANK:(6 + g % 2) * BANK + P]

        def loop(eng, body):
            if rounds == 2:
                body(0)
            else:
                with eng.Fori(0, rounds // 2) as i:
                    body(i)

        with nc.Block() as block:
            @block.gpsimd
            def _(pool):
                for place in padded:
                    pool.memset(place, 0.0).then_inc(cleared, 1)

            @block.sync
            def _(sp):
                if padded:
                    sp.wait_ge(cleared, len(padded))

                def body(i):
                    for slot in range(2):
                        if rounds > 2:
                            sp.wait_ge(summed[slot], i * (C // 2))
                        for dst, src in copies(i, slot):
                            sp.dma_start(dst, src).then_inc(staged[slot], 16)
                loop(sp, body)

            @block.tensor
            def _(pe):
                def body(i):
                    for step in range(N + LAG + 1):
                        if step < N:
                            u = sequence[step]
                            if step % U == 0:
                                pe.wait_ge(staged[step // U], i * 16 * n_copies + 16 * n_copies)
                            if step >= score_buffers:
                                pe.wait_ge(masked, i * N + step - score_buffers + 1)
                            for lo in range(0, u.keys, BANK):
                                hi = min(lo + BANK, u.keys)
                                for m, (left, right) in enumerate(u.products):
                                    last = pe.matmul(scores_bank(step, u.keys)[:, lo:hi], left, right[:, lo:hi],
                                                     start=(m == 0), stop=(m == len(u.products) - 1))
                            last.then_inc(scored, 1)
                        v = step - LAG
                        if 0 <= v < N:
                            u = sequence[v]
                            pe.wait_ge(weighed, i * N + v + 1)
                            c = copy_of(v)
                            if c >= turn_buffers and (u.opens or not joined):
                                pe.wait_ge(copied, i * C + c + 1 - turn_buffers)
                            for n, (lo, keys, _) in enumerate(u.tiles):
                                last = pe.matmul(turned_bank(v)[0:keys, n * P:(n + 1) * P],
                                                 probs[:, v % AHEAD, lo:lo + keys], diag[:, v % AHEAD, :],
                                                 start=(not joined or (u.opens and n % (BANK // P) == 0)),
                                                 stop=(u.closes or not joined),
                                                 skip_group_check=joined)
                            last.then_inc(turned, 1)
                        w = step - LAG - 1
                        if w in copied_units:
                            u, c = sequence[w], copy_of(w)
                            pe.wait_ge(copied, i * C + c + 1)
                            if (u.opens or joined) and group(w) >= 2:
                                pe.wait_ge(taken, i * 2 * G + group(w) - 1)
                            for n, (_, keys, values) in enumerate(u.tiles):
                                last = pe.matmul(out_bank(group(w))[u.out[0]:u.out[1], :], values,
                                                 turned_sb[0:keys, c % 2, n * P:(n + 1) * P],
                                                 start=((u.opens or joined) and n == 0), stop=(u.closes and n == len(u.tiles) - 1))
                            last.then_inc(summed[w // U], 1)
                loop(pe, body)

            @block.vector
            def _(dve):
                def body(i):
                    for step in range(N + LAG + 2):
                        if step < N:
                            u, b = sequence[step], step % AHEAD
                            if step % U == 0:
                                dve.wait_ge(staged[step // U], i * 16 * n_copies + 16 * n_copies)
                            if step >= AHEAD:
                                dve.wait_ge(exped, i * N + step - AHEAD + 1)
                            wait_apart(dve, scored, i * N + step + 1, passed)
                            dve.tensor_tensor_reduce(masked_sb[:, b, 0:u.keys], scores_bank(step, u.keys), u.bias,
                                                     -1.0, 3.0e38, ALU.add, ALU.min, top[:, b:b + 1]).then_inc(masked, 1)
                        v = step - 1
                        if 0 <= v < N:
                            u, b = sequence[v], v % AHEAD
                            dve.wait_ge(exped, i * N + v + 1)
                            dve.reciprocal(inverse[:, b:b + 1], total[:, b:b + 1]).then_inc(inverted, 1)
                            if v >= AHEAD:
                                dve.wait_ge(turned, i * N + v - AHEAD + 1)
                            dve.wait_ge(inverted, i * N + v + 1)
                            dve.tensor_scalar(diag[:, b, :], k.c("ident"), inverse[:, b:b + 1], u.gate,
                                              ALU.mult, ALU.mult).then_inc(weighed, 1)
                        w = step - LAG - 2
                        if 0 <= w < N and closing[group(w)] == w:
                            dve.wait_ge(summed[w // U], i * (C // 2) + copy_of(w) % (C // 2) + 1)
                            g = group(w)
                            dst = results(2 * i + g // G, g % G)
                            if gating:
                                dve.tensor_tensor(dst, out_bank(g), dst, ALU.mult).then_inc(taken, 1)
                            else:
                                dve.tensor_copy(dst, out_bank(g)).then_inc(taken, 1)
                loop(dve, body)

            @block.scalar
            def _(act):
                def body(i):
                    for step in range(N + LAG):
                        if step < N:
                            u, b = sequence[step], step % AHEAD
                            if step >= AHEAD:
                                act.wait_ge(turned, i * N + step - AHEAD + 1)
                            act.wait_ge(masked, i * N + step + 1)
                            act.activation(probs[:, b, 0:u.keys], masked_sb[:, b, 0:u.keys], ACT.Exp, scale=-1.0,
                                           bias=top[:, b:b + 1], accum_out=total[:, b:b + 1]).then_inc(exped, 1)
                        v = step - LAG
                        if v in copied_units:
                            u, c = sequence[v], copy_of(v)
                            b = c % 2
                            if c >= 2:
                                act.wait_ge(summed[(c - 2) // (C // 2)], i * (C // 2) + (c - 2) % (C // 2) + 1)
                            act.wait_ge(turned, i * N + v + 1)
                            rows = max(keys for _, keys, _ in u.tiles)
                            act.copy(turned_sb[0:rows, b, 0:len(u.tiles) * P],
                                     turned_bank(v)[0:rows, 0:len(u.tiles) * P]).then_inc(copied, 1)
                loop(act, body)



def load_inputs(k):
    nc = k.nc
    with k.stage("inputs") as (sb, sem):
        landed = sem("inputs_landed")
        with nc.Block() as block:
            @block.sync
            def _(sp):
                sp.dma_start(k.x[:, :, :], k.dram["xT"].rearrange("(k p) t -> p k t", p=P)).then_inc(landed, 16)
                sp.dma_start(k.param[:, :], k.dram["params"]).then_inc(landed, 16)
                sp.wait_ge(landed, 48)

            @block.scalar
            def _(act):
                act.dma_start(k.const[:, :], k.dram["consts"]).then_inc(landed, 16)


def bias_strips(k, strips):
    nc = k.nc
    rows = P
    skewed = nc.dram_tensor("bias_skewed", (NSA_HEADS, P * (SKEW + 1)), F32, kind="Internal").ap()
    with k.stage("strips") as (sb, sem):
        bias = sb("rel_bias", [rows, NSA_HEADS])
        hot = sb("buckets", [rows, SKEW])
        spread = sb("spread", [rows, NSA_HEADS, P])
        line = sb("line", [P, 2, SKEW])
        landed, filled, spreaded, ready, copied, back = (sem(x) for x in (
            "inputs_landed", "mask_row_set", "bias_spread", "lines_ready", "lines_copied", "strips_landed"))
        written = [sem(f"lines{i}_written") for i in range(2)]
        with nc.Block() as block:
            @block.sync
            def _(sp):
                sp.dma_start(hot[:, :], k.dram["buckets"]).then_inc(landed, 16)
                sp.wait_ge(filled, 1)
                sp.dma_start(bias[0:REL_BUCKETS, :], k.dram["rel_bias"]).then_inc(landed, 16)
                for h in range(NSA_HEADS):
                    sp.wait_ge(copied, 2 * h + 2)
                    sp.dma_start(skewed[h].rearrange("(p w) -> p w", w=SKEW + 1)[:, 0:SKEW],
                                 line[:, h % 2, :]).then_inc(written[h % 2], 16)

            @block.scalar
            def _(act):
                for h in range(NSA_HEADS):
                    act.wait_ge(written[h % 2], 16 * (h // 2) + 16)
                    act.dma_start(strips[:, h, :], skewed[h, P - 1:P - 1 + P * SKEW].rearrange("(p w) -> p w", w=SKEW)
                                  [:, 0:STRIP]).then_inc(back, 16)
                act.wait_ge(back, 16 * NSA_HEADS)

            @block.vector
            def _(dve):
                dve.memset(bias[:, :], 0.0).then_inc(filled, 1)
                dve.wait_ge(filled, 1)
                dve.memset(bias[REL_BUCKETS:REL_BUCKETS + 1, :], NEG).then_inc(filled, 1)
                dve.wait_ge(filled, 2)
                dve.wait_ge(landed, 32)
                for h in range(NSA_HEADS):
                    dve.tensor_scalar(spread[:, h, :], k.c("ones")[0:rows, :], bias[:, h:h + 1], None,
                                      ALU.mult).then_inc(spreaded, 1)
                for h in range(NSA_HEADS):
                    if h >= 2:
                        dve.wait_ge(written[h % 2], 16 * (h // 2))
                    for half in range(2):
                        dve.wait_ge(ready, 2 * h + half + 1)
                        dve.tensor_copy(line[:, h % 2, half * BANK:(half + 1) * BANK],
                                        k.bank(2 * (h % 2) + half)).then_inc(copied, 1)

            @block.tensor
            def _(pe):
                for h in range(NSA_HEADS):
                    pe.wait_ge(spreaded, h + 1)
                    if h >= 2:
                        pe.wait_ge(copied, 2 * h - 2)
                    for half in range(2):
                        pe.matmul(k.bank(2 * (h % 2) + half), spread[:, h, :], hot[:, half * BANK:(half + 1) * BANK],
                                  start=True, stop=True).then_inc(ready, 1)


def first_norm(k, src, out, gain, name, eps="eps"):
    feature_norm(k, name, [([src[:, n, :] for n in range(KD)], [out[:, n, :] for n in range(KD)],
                            [k.p(gain, n) for n in range(KD)])], k.c("ones"), 1.0 / D, eps)


def twice(k, name, pairs):
    with k.stage(name) as (sb, sem):
        moved = sem("copies_moved")
        with k.nc.Block() as block:
            @block.sync
            def _(sp):
                for dst, src in pairs:
                    sp.dma_start(dst, src).then_inc(moved, 16)
                sp.wait_ge(moved, 16 * len(pairs))


def compress(k, raw_kc, raw_vc, k_cmp, v_cmp):
    nc = k.nc
    N = NSA_GROUPS * NCMP
    with k.stage("compress") as (sb, sem):
        pairs = [sb(f"pairs_{x}", [P, NSA_GROUPS, T]) for x in "kv"]
        w1 = [sb(f"w1_{x}", [P, CMP_PAIRS, CMP_HIDDEN]) for x in "kv"]
        w2k = sb("w2_k", [P, 2, P])
        w2v = sb("w2_v", [P, 2, DH])
        blocks = [sb(f"blocks_{x}", [P, CMP_PAIRS, N]) for x in "kv"]
        by_block = [sb(f"by_block_{x}", [N, CMP_HIDDEN]) for x in "kv"]
        hid = [sb(f"hidden_{x}", [P, 2, N]) for x in "kv"]
        cleared, placed, hidden, kept, turned, gelued, outs, copied, last_landed = (sem(x) for x in (
            "ends_cleared", "blocks_ready", "hidden_ready", "hidden_kept", "hidden_turned", "hidden_gelued", "outputs_ready",
            "outputs_copied", "second_weights_landed"))
        raw_landed, landed = ([sem(f"{x}_{y}_landed") for y in "kv"] for x in ("pairs", "weights"))
        raws = (raw_kc, raw_vc)
        with nc.Block() as block:
            @block.sync
            def _(sp):
                sp.wait_ge(cleared, 2)
                for n in range(2):
                    for g in range(NSA_GROUPS):
                        sp.dma_start(pairs[n][0:DH, g, :], raws[n][g * DH:(g + 1) * DH, :]).then_inc(raw_landed[n], 16)
                        sp.dma_start(pairs[n][DH:P, g, 0:T - 1],
                                     raws[n][g * DH:(g + 1) * DH, 1:T]).then_inc(raw_landed[n], 16)
                    sp.dma_start(w1[n][:, :, :], k.dram[f"cmp_w1_{'kv'[n]}"].rearrange("(j p) n -> p j n", p=P)
                                 ).then_inc(landed[n], 16)
                sp.dma_start(w2k[:, :, :], k.dram["cmp_w2_k"].rearrange("(c p) n -> p c n", p=P)).then_inc(last_landed, 16)
                sp.dma_start(w2v[:, :, :], k.dram["cmp_w2_v"].rearrange("(c p) n -> p c n", p=P)).then_inc(last_landed, 16)

            @block.gpsimd
            def _(pool):
                for n in range(2):
                    pool.memset(pairs[n][:, :, T - 1:T], 0.0).then_inc(cleared, 1)

            @block.tensor
            def _(pe):
                for n in range(2):
                    pe.wait_ge(landed[n], 16)
                    for j in range(CMP_PAIRS):
                        pe.wait_ge(placed, n * CMP_PAIRS + j + 1)
                        last = pe.matmul(k.psum[0:N, n * BANK:n * BANK + CMP_HIDDEN], blocks[n][:, j, :], w1[n][:, j, :],
                                         start=(j == 0), stop=(j == CMP_PAIRS - 1))
                    last.then_inc(hidden, 1)
                for n in range(2):
                    pe.wait_ge(kept, n + 1)
                    for c in range(2):
                        pe.transpose(k.psum[:, (2 + 2 * n + c) * BANK:(2 + 2 * n + c) * BANK + N], by_block[n][:, c * P:(c + 1) * P],
                                     k.c("ident")[0:N, 0:N]).then_inc(turned, 1)
                pe.wait_ge(last_landed, 32)
                pe.wait_ge(gelued, 4)
                for c in range(2):
                    last = pe.matmul(k.bank(0, N), w2k[:, c, :], hid[0][:, c, :], start=(c == 0), stop=(c == 1))
                last.then_inc(outs, 1)
                for g in range(NSA_GROUPS):
                    for c in range(2):
                        last = pe.matmul(k.psum[0:NCMP, (1 + g) * BANK:(1 + g) * BANK + DH],
                                         hid[1][:, c, g * NCMP:(g + 1) * NCMP], w2v[:, c, :],
                                         start=(c == 0), stop=(c == 1))
                    last.then_inc(outs, 1)

            @block.vector
            def _(dve):
                for n in range(2):
                    dve.wait_ge(raw_landed[n], 16 * 2 * NSA_GROUPS)
                    for j in range(CMP_PAIRS):
                        dve.tensor_scalar(blocks[n][:, j, :].rearrange("p (g n) -> p g n", g=NSA_GROUPS),
                                          pairs[n][:, :, 2 * j:2 * j + CMP_STRIDE * (NCMP - 1) + 1:CMP_STRIDE],
                                          k.p(f"cmp_pe_{'kv'[n]}")[:, j:j + 1], None, ALU.add).then_inc(placed, 1)
                for n in range(2):
                    dve.wait_ge(hidden, n + 1)
                    dve.tensor_copy(by_block[n][:, :], k.psum[0:N, n * BANK:n * BANK + CMP_HIDDEN]).then_inc(kept, 1)
                dve.wait_ge(outs, 1)
                dve.tensor_copy(k_cmp[:, :, :].rearrange("p g n -> p (g n)"), k.bank(0, N)).then_inc(copied, 1)
                for g in range(NSA_GROUPS):
                    dve.wait_ge(outs, 2 + g)
                    dve.tensor_copy(v_cmp[0:NCMP, g, :], k.psum[0:NCMP, (1 + g) * BANK:(1 + g) * BANK + DH]
                                    ).then_inc(copied, 1)

            @block.scalar
            def _(act):
                for n in range(2):
                    for c in range(2):
                        b = 2 * n + c
                        act.wait_ge(turned, b + 1)
                        act.activation(hid[n][:, c, :], k.bank(2 + b, N), ACT.Gelu_apprx_tanh,
                                       bias=k.p(f"cmp_b1_{'kv'[n]}", c)).then_inc(gelued, 1)


def sparse_attention(k, q, k_cmp, v_cmp, k_slc, k_win, v_both, gates, strips, out):
    for g in range(NSA_GROUPS):
        with ExitStack() as ctx:
            def sb(what, shape):
                return ctx.enter_context(k.tensor(f"nsa{g}_{what}", shape, F32))

            qs = sb("q", [P, 2, 2, T])
            strip = sb("strip", [P, 2, 2, STRIP])

            def copies(i, slot, g=g):
                pair, h = 2 * g + slot, 4 * g + 2 * slot
                return [*head_copies(qs[:, slot, :, :], at(q, pair)), (strip[:, slot, :, :], strips[:, h:h + 2, :])]

            def units(slot, g=g):
                found = []
                for t in range(TT):
                    keys = (t + 1) * P
                    lo = 3 * P - t * P
                    for h in range(2):
                        query = qs[:, slot, h, t * P:(t + 1) * P]
                        gate = gates[:, t, 4 * g + 2 * slot + h, :]
                        first = lo + CMP_BLOCK - 1
                        found.append(Unit([(query, k_cmp[:, g, :])], NCMP,
                                          strip[:, slot, h, first:first + CMP_STRIDE * (NCMP - 1) + 1:CMP_STRIDE],
                                          gate[:, 0:1], [(0, NCMP, v_cmp[0:NCMP, g, :])],
                                          (h * DH, (h + 1) * DH), t, True, False))
                        for b, keys_of in ((1, k_slc), (2, k_win)):
                            found.append(Unit([(query, keys_of[:, g, 0:keys])], keys, strip[:, slot, h, lo:lo + keys],
                                              gate[:, b:b + 1],
                                              [(n * P, P, v_both[:, n, (b - 1) * P + g * DH:(b - 1) * P + (g + 1) * DH])
                                               for n in range(t + 1)],
                                              (h * DH, (h + 1) * DH), t, False, b == 2))
                return found

            def results(i, t, g=g):
                return at(out, 2 * g + i)[:, t * P:(t + 1) * P]

            attention(k, f"nsa{g}", 2, copies, units, results, padded=[qs[:, :, :, :]])


def spatial_gate(k, u, v, out):
    nc = k.nc
    G, chunks = 8, T // P
    with k.stage("sgu") as (sb, sem):
        w = sb("w", [P, G, P])
        gain = sb("gain", [P, T])
        b = sb("b", [P, G // 2, P])
        junk = sb("squares", [P, T])
        mean = sb("mean", [P, chunks])
        root = sb("root", [P, chunks])
        rstd = sb("rstd", [P, chunks])
        z = sb("z", [P, 2, T])
        landed, masked, squared, rooted, turned, scaled, mixed, biased, gated = (sem(x) for x in (
            "inputs_landed", "w_masked", "v_squared", "v_rooted", "rstd_ready", "v_scaled", "z_ready", "z_biased",
            "results_ready"))
        with nc.Block() as block:
            @block.sync
            def _(sp):
                sp.dma_start(w[:, :, :], k.dram["sgu_wT"].rearrange("j (g i) -> j g i", g=G)).then_inc(landed, 16)
                sp.dma_start(gain[:, :], k.dram["sgu_norm"][0:1, :].broadcast_to([P, T])).then_inc(landed, 16)
                for g in range(G):
                    sp.dma_start(b[(g % 2) * DH:(g % 2 + 1) * DH, g // 2, :],
                                 k.dram["sgu_b"][g:g + 1, :].broadcast_to([DH, P])).then_inc(landed, 16)

            @block.scalar
            def _(act):
                for c in range(chunks):
                    if c:
                        act.wait_ge(squared, c)
                    act.activation(junk[:, :], v[:, c, :], ACT.Square, accum_out=mean[:, c:c + 1]).then_inc(squared, 1)
                act.wait_ge(squared, chunks)
                act.activation(root[:, :], mean[:, :], ACT.Sqrt, bias=k.c("eps"), scale=1.0 / T).then_inc(rooted, 1)

            @block.vector
            def _(dve):
                dve.wait_ge(landed, 16 * (2 + G))
                for g in range(G):
                    dve.tensor_tensor(w[:, g, :], w[:, g, :], k.c("upto")[:, 0:P], ALU.mult).then_inc(masked, 1)
                dve.wait_ge(rooted, 1)
                dve.reciprocal(rstd[:, :], root[:, :]).then_inc(turned, 1)
                dve.wait_ge(turned, 1)
                for c in range(chunks):
                    dve.scalar_tensor_tensor(v[:, c, :], v[:, c, :], rstd[:, c:c + 1], gain[:, :], ALU.mult,
                                             ALU.mult).then_inc(scaled, 1)
                for n in range(G // 2):
                    dve.wait_ge(mixed, n + 1)
                    zn = z[:, n % 2, :]
                    if n >= 2:
                        dve.wait_ge(gated, n - 1)
                    dve.tensor_tensor(zn.rearrange("p (c i) -> p c i", c=chunks),
                                      k.bank(n).rearrange("p (c i) -> p c i", c=chunks),
                                      b[:, n:n + 1, :].broadcast_to([P, chunks, P]), ALU.add).then_inc(biased, 1)
                    dve.wait_ge(biased, n + 1)
                    dve.tensor_tensor(out[:, n, :], zn, u[:, n, :], ALU.mult).then_inc(gated, 1)

            @block.tensor
            def _(pe):
                pe.wait_ge(masked, G)
                pe.wait_ge(scaled, chunks)
                for n in range(G // 2):
                    for h in range(2):
                        g = 2 * n + h
                        for c in range(chunks):
                            last = pe.matmul(k.psum[h * DH:(h + 1) * DH, n * BANK + c * P:n * BANK + (c + 1) * P],
                                             v[:, c, g * DH:(g + 1) * DH], w[:, g, :], start=True, stop=True)
                    last.then_inc(mixed, 1)


def feed_forward_up(k, src, out):
    nc = k.nc
    units = FF_CHUNKS
    width = KD * 2 * P
    with k.stage("ff_up") as (sb, sem):
        ring = sb("weights", [P, 2, width])
        leading = sb("leading", [P, 2, width], F32R)
        rest = k.over("ff_up_rest", ring[:, :, :], [P, 2, width])
        source = Parts(sb("source_leading", [P, KD, T], F32R), k.over("ff_up_source_rest", src[:, :, :], [P, KD, T]))
        conv = sb("conv", [P, 4, T])
        gate = sb("gate", [P, 2, T])
        hidden = sb("hidden", [P, 2, T])
        landed, masked, split, ready, based, tapped, silued, timed, kept, done = ([sem(f"{x}{i}") for i in range(2)] for x in (
            "weights_landed", "weights_masked", "weights_split", "sums_ready", "last_tap", "taps_added", "gate_ready",
            "hidden_ready", "hidden_masked", "unit_done"))
        own = [sem(f"tap_written{i}") for i in range(2)]
        source_masked, source_split = sem("source_masked"), sem("source_split")

        def pairs(eng, body):
            with eng.Fori(0, units // 2 - 1) as i:
                for s in range(2):
                    body(i, s, 2 * i + s)
            for s in range(2):
                body(units // 2 - 1, s, units - 2 + s)

        with nc.Block() as block:
            @block.sync
            def _(sp):
                def body(i, s, n):
                    sp.wait_ge(ready[s], 2 * i)
                    unit = k.dram["w_up"][n, :, :] if isinstance(n, int) else \
                        k.dram["w_up"][bass.ds(n, 1), :, :].rearrange("a p n -> p (a n)")
                    sp.dma_start(ring[:, s, :], unit).then_inc(landed[s], 16)
                pairs(sp, body)

            @block.tensor
            def _(pe):
                def body(i, s, n):
                    high, low = (w[:, s, :].rearrange("p (k n) -> p k n", k=KD) for w in (leading, rest))
                    pe.wait_ge(split[s], i + 1)
                    pe.wait_ge(tapped[s], 2 * i)
                    for j in range(2):
                        here = slice(j * P, (j + 1) * P)
                        for kk in range(KD):
                            if j == 0 and kk in (0, KD // 2):
                                pe.wait_ge(source_split, KD if kk else KD // 2)
                            last = three_passes(pe, k.bank(2 * s + j), (high[:, kk, here], low[:, kk, here]),
                                                (source.leading[:, kk, :], source.rest[:, kk, :]), kk == 0, kk == KD - 1)
                        last.then_inc(ready[s], 1)
                pairs(pe, body)

            @block.scalar
            def _(act):
                w, b = k.p("conv_w"), k.p("conv_b")

                def body(i, s, n):
                    act.wait_ge(timed[s], i)
                    for j in range(2):
                        act.wait_ge(ready[s], 2 * i + j + 1)
                        act.activation(conv[:, 2 * s + j, :], k.bank(2 * s + j), ACT.Identity,
                                       bias=col(b, 2 * n + j), scale=col(w, 2 * 2 * FF_CHUNKS + 2 * n + j)
                                       ).then_inc(based[s], 1)
                    act.wait_ge(tapped[s], 2 * i + 2)
                    act.activation(gate[:, s, :], conv[:, 2 * s + 1, :], ACT.Silu).then_inc(silued[s], 1)
                    act.wait_ge(timed[s], i + 1)
                    act.activation(at(out.leading, n), hidden[:, s, :], ACT.Copy).then_inc(kept[s], 1)

                for kk in range(KD):
                    act.activation(source.leading[:, kk, :], src[:, kk, :], ACT.Copy).then_inc(source_masked, 1)
                pairs(act, body)

            @block.vector
            def _(dve):
                w = k.p("conv_w")

                def split_unit(s, i):
                    dve.wait_ge(landed[s], 16 * i + 16)
                    leading_bits(dve, leading[:, s, :], ring[:, s, :]).then_inc(masked[s], 1)
                    dve.wait_ge(masked[s], i + 1)
                    rest_bits(dve, rest[:, s, :], ring[:, s, :], leading[:, s, :]).then_inc(split[s], 1)

                def body(i, s, n):
                    if not (isinstance(n, int) and n == units - 1):
                        split_unit(1 - s, i + s)
                    for j in range(2):
                        dve.wait_ge(based[s], 2 * i + j + 1)
                        c, ps = conv[:, 2 * s + j, :], k.bank(2 * s + j)
                        dve.scalar_tensor_tensor(c[:, 1:T], ps[:, 0:T - 1], col(w, 2 * FF_CHUNKS + 2 * n + j), c[:, 1:T],
                                                 ALU.mult, ALU.add).then_inc(own[s], 1)
                        dve.wait_ge(own[s], 2 * i + j + 1)
                        dve.scalar_tensor_tensor(c[:, 2:T], ps[:, 0:T - 2], col(w, 2 * n + j), c[:, 2:T],
                                                 ALU.mult, ALU.add).then_inc(tapped[s], 1)
                    dve.wait_ge(done[s], i)
                    dve.wait_ge(silued[s], i + 1)
                    dve.tensor_tensor(hidden[:, s, :], gate[:, s, :], conv[:, 2 * s, :], ALU.mult).then_inc(timed[s], 1)
                    dve.wait_ge(kept[s], i + 1)
                    rest_bits(dve, at(out.rest, n), hidden[:, s, :], at(out.leading, n)).then_inc(done[s], 1)

                for kk in range(KD):
                    if kk == KD // 2:
                        split_unit(0, 0)
                    dve.wait_ge(source_masked, kk + 1)
                    rest_bits(dve, source.rest[:, kk, :], src[:, kk, :], source.leading[:, kk, :]).then_inc(source_split, 1)
                pairs(dve, body)


def first_block(k):
    with ExitStack() as ctx:
        first_norm(k, k.x, k.h, "attn_norm", "attn_norm")
        with ExitStack() as mixers:
            def mx(what, shape):
                return mixers.enter_context(k.tensor(what, shape, F32))
            u = mx("sgu_u", [P, 4, T])
            v = mx("sgu_v", [P, TT, T])
            q = mx("nsa_q", [P, 4, T])
            raw = mx("nsa_raw", [P, 4, T])
            v_both = mx("nsa_v", [P, TT, 2 * P])
            gates = mx("nsa_gates", [P, TT, NSA_HEADS, 3])
            k_cmp = mx("nsa_k_cmp", [P, NSA_GROUPS, NCMP])
            v_cmp = mx("nsa_v_cmp", [NCMP, NSA_GROUPS, DH])
            k_slc = mx("nsa_k_slc", [P, NSA_GROUPS, T])
            k_win = mx("nsa_k_win", [P, NSA_GROUPS, T])

            def values_and_gates(eng, n, ps):
                return eng.tensor_copy(v_both[:, n, :], ps)

            def gate(eng, n, ps):
                return eng.activation(gates[:, n, :, :].rearrange("p h b -> p (h b)"), ps, ACT.Sigmoid)

            project(k, "proj1", [
                Section(k.dram["w_in_q"], 1, KD, k.h, copies_to(q), "vector"),
                Section(k.dram["w_in_k"], 1, KD, k.h, copies_to(raw), "vector"),
                Section(k.dram["w_in_v"], 1, KD, k.h, values_and_gates, "vector", chunks=TT, width=2 * P, by_tokens=True),
                Section(k.dram["w_in_g"], 1, KD, k.h, gate, "scalar", chunks=TT, width=3 * NSA_HEADS, by_tokens=True),
                Section(k.dram["w_in_u"], 1, KD, k.h, activates_to(u, ACT.Gelu_apprx_tanh), "scalar"),
                Section(k.dram["w_in_sv"], 1, KD, k.h, activates_to(v, ACT.Gelu_apprx_tanh), "scalar", chunks=TT,
                        by_tokens=True),
            ])
            spatial_gate(k, u, v, k.h[:, 4:8, :])
            compress(k, raw[:, 0, :], raw[:, 1, :], k_cmp, v_cmp)
            with k.stage("nsa_gains") as (sb2, sem):
                made = sem("gains_made")
                q_gain = mx("nsa_q_gain", [P, 1])
                with k.nc.Block() as block:
                    @block.vector
                    def _(dve):
                        dve.tensor_scalar(q_gain[:, :], k.p("q_norm"), DH ** -0.5, None, ALU.mult).then_inc(made, 1)
                        first = gates[:, 0, :, 0:1]
                        dve.tensor_scalar(first, first, k.c("any_cmp")[:, 0:1], None, ALU.mult).then_inc(made, 1)
                        dve.wait_ge(made, 2)
            cmp_flat = k_cmp[:, :, :].rearrange("p g n -> p (g n)")
            chunk_norms(k, "nsa_norm",
                        [(q[:, n, :], q[:, n, :], q_gain[:, :]) for n in range(4)]
                        + [(raw[:, 2, :], raw[:, 2, :], k.p("k_norm_slc")), (raw[:, 3, :], raw[:, 3, :], k.p("k_norm_win")),
                           (cmp_flat, cmp_flat, k.p("k_norm_cmp"))], 2, 1.0 / DH, "eps")
            twice(k, "nsa_keys", [(dst[h * DH:(h + 1) * DH, g, :], raw[g * DH:(g + 1) * DH, n, :])
                                  for dst, n in ((k_slc, 2), (k_win, 3)) for g in range(2) for h in range(2)])
            strips = mx("nsa_strips", [P, NSA_HEADS, STRIP])
            bias_strips(k, strips)
            sparse_attention(k, q, k_cmp, v_cmp, k_slc, k_win, v_both, gates, strips, k.h)
        project(k, "out1", [Section(k.dram["w_out"], 2, KD, k.h, adds_to(k.x), "vector", spent=True)])
        first_norm(k, k.x, k.h, "ffn_norm", "ffn_norm")
        hidden = Parts(*(ctx.enter_context(k.tensor(f"ff_hidden_{x}", [P, FF_CHUNKS, T], F32R)) for x in ("leading", "rest")))
        feed_forward_up(k, k.h, hidden)
        project(k, "down1", [Section(k.dram["w_down"], KD, FF_CHUNKS, hidden, adds_to(k.x), "vector", chunks=1)])



def feature_center(k, name, srcs):
    n = len(srcs)
    with k.stage(name) as (sb, sem):
        summed, centered = sem("summed"), sem("centered")
        with k.nc.Block() as block:
            @block.tensor
            def _(pe):
                for m, s in enumerate(srcs):
                    last = pe.matmul(k.bank(0), k.c("ones"), s, start=(m == 0), stop=(m == n - 1))
                last.then_inc(summed, 1)

            @block.vector
            def _(dve):
                dve.wait_ge(summed, 1)
                for s in srcs:
                    dve.scalar_tensor_tensor(s, k.bank(0), -1.0 / (n * P), s, ALU.mult, ALU.add).then_inc(centered, 1)


def gated_products(k, name, weights, loops, kc_gate, source_gate, bias, kc, source, base, out):
    nc, N = k.nc, KD
    size = (kc_gate + kc) * P
    with k.stage(name) as (sb, sem):
        ring = sb("weights", [P, 2, size])
        leading = sb("leading", [P, 2, size], F32R)
        rest = k.over(f"{name}_rest", ring[:, :, :], [P, 2, size])
        gate_parts = Parts(*(sb(f"gate_source_{x}", [P, kc_gate, T], F32R) for x in ("leading", "rest")))
        parts = [Parts(sb(f"source{q}_leading", [P, kc, T], F32R), k.over(f"{name}_source{q}_rest", source(q)[:, :, :], [P, kc, T]))
                 for q in range(loops)]
        gate = sb("gate", [P, 2, T])
        part = sb("part", [P, 2, T])
        landed, masked, split, ready, opened, timed, added = ([sem(f"{x}{i}") for i in range(2)] for x in (
            "weights_landed", "weights_masked", "weights_split", "sums_ready", "gate_ready", "gated", "added"))
        source_masked, source_split = sem("source_masked"), sem("source_split")

        def each(eng, body, begin=None):
            for q in range(loops):
                if begin is not None:
                    begin(q)
                here = N // 2 - (q == loops - 1)
                with eng.Fori(0, here) as i:
                    for s in range(2):
                        body(q, s, 2 * i + s, i + q * (N // 2))
            for s in range(2):
                body(loops - 1, s, N - 2 + s, loops * N // 2 - 1)

        with nc.Block() as block:
            @block.sync
            def _(sp):
                def body(q, s, n, m):
                    sp.wait_ge(ready[s], 2 * m)
                    unit = weights[n + q * N, :, :] if isinstance(n, int) else \
                        weights[bass.ds(n + q * N, 1), :, :].rearrange("a p n -> p (a n)")
                    sp.dma_start(ring[:, s, :], unit).then_inc(landed[s], 16)
                each(sp, body)

            @block.tensor
            def _(pe):
                def body(q, s, n, m):
                    high, low = (w[:, s, :].rearrange("p (k n) -> p k n", n=P) for w in (leading, rest))
                    pe.wait_ge(split[s], m + 1)
                    pe.wait_ge(timed[s], m)
                    for j, (first, count, src) in enumerate(((0, kc_gate, gate_parts), (kc_gate, kc, parts[q]))):
                        for kk in range(count):
                            if q == 0 and (j, kk) in ((0, 0), (0, kc_gate // 2), (1, 0)):
                                pe.wait_ge(source_split, (kc_gate // 2 if kk == 0 else kc_gate) if j == 0 else kc_gate + kc)
                            last = three_passes(pe, k.bank(2 * s + j), (high[:, first + kk, :], low[:, first + kk, :]),
                                                (src.leading[:, kk, :], src.rest[:, kk, :]), kk == 0, kk == count - 1)
                        last.then_inc(ready[s], 1)
                each(pe, body, lambda q: pe.wait_ge(source_split, kc_gate + (q + 1) * kc) if q else None)

            @block.scalar
            def _(act):
                for src, into, chunks in ((source_gate, gate_parts, kc_gate), (source(0), parts[0], kc)):
                    for kk in range(chunks):
                        act.activation(into.leading[:, kk, :], src[:, kk, :], ACT.Copy).then_inc(source_masked, 1)

                def body(q, s, n, m):
                    act.wait_ge(ready[s], 2 * m + 1)
                    act.wait_ge(timed[s], m)
                    act.activation(gate[:, s, :], k.bank(2 * s), ACT.Sigmoid, bias=col(bias, n + q * N)
                                   ).then_inc(opened[s], 1)
                each(act, body)

            @block.vector
            def _(dve):
                def split_unit(s, m):
                    dve.wait_ge(landed[s], 16 * m + 16)
                    leading_bits(dve, leading[:, s, :], ring[:, s, :]).then_inc(masked[s], 1)
                    dve.wait_ge(masked[s], m + 1)
                    rest_bits(dve, rest[:, s, :], ring[:, s, :], leading[:, s, :]).then_inc(split[s], 1)

                def split_source(src, into, chunks, before, lo=0):
                    for kk in range(lo, chunks):
                        dve.wait_ge(source_masked, before + kk + 1)
                        rest_bits(dve, into.rest[:, kk, :], src[:, kk, :], into.leading[:, kk, :]).then_inc(source_split, 1)

                def body(q, s, n, m):
                    if not (isinstance(n, int) and n == N - 1):
                        split_unit(1 - s, m + s)
                    dve.wait_ge(opened[s], m + 1)
                    dve.wait_ge(ready[s], 2 * m + 2)
                    if q == 0 and base is None:
                        dve.tensor_tensor(at(out, n), k.bank(2 * s + 1), gate[:, s, :], ALU.mult).then_inc(timed[s], 1)
                        return
                    before = N // 2 if base is None else 0
                    dve.tensor_tensor(part[:, s, :], k.bank(2 * s + 1), gate[:, s, :], ALU.mult).then_inc(timed[s], 1)
                    dve.wait_ge(timed[s], m + 1)
                    if loops > 1:
                        dve.wait_ge(added[s], m - before)
                    dve.tensor_tensor(at(out, n), part[:, s, :], at(out if base is None else base, n), ALU.add
                                      ).then_inc(added[s], 1)

                def begin(q):
                    if q + 1 < loops:
                        for kk in range(kc):
                            leading_bits(dve, parts[q + 1].leading[:, kk, :], source(q + 1)[:, kk, :]).then_inc(source_masked, 1)
                        split_source(source(q + 1), parts[q + 1], kc, kc_gate + (q + 1) * kc)

                split_source(source_gate, gate_parts, kc_gate // 2, 0)
                split_unit(0, 0)
                split_source(source_gate, gate_parts, kc_gate, 0, lo=kc_gate // 2)
                split_source(source(0), parts[0], kc, kc_gate)
                each(dve, body, begin)


def rates(k, raw, g, beta, log_f):
    nc = k.nc
    H, F = GDN_HEADS, 8
    W = H + F
    with k.stage("rates") as (sb, sem):
        bias = sb("bias", [P, 2 * H + F])
        y, mag, e, s, s2, p = (sb(x, [P, TT, W]) for x in ("y", "mag", "e", "s", "s2", "p"))
        rate = sb("rate", [P, H])
        landed, biased, exped, own, other = (sem(x) for x in (
            "biases_landed", "y_ready", "exp_ready", "vector_steps", "scalar_steps"))
        with nc.Block() as block:
            @block.sync
            def _(sp):
                sp.dma_start(bias[:, :], k.dram["rate_biases"][0:1, :].broadcast_to([P, 2 * H + F])).then_inc(landed, 16)

            @block.scalar
            def _(act):
                act.wait_ge(landed, 16)
                act.activation(rate[:, :], bias[:, W:W + H], ACT.Exp).then_inc(exped, 1)
                act.wait_ge(biased, 1)
                act.activation(mag[:, :, :], y[:, :, :], ACT.Abs).then_inc(other, 1)
                act.wait_ge(other, 1)
                act.activation(e[:, :, :], mag[:, :, :], ACT.Exp, scale=-1.0).then_inc(exped, 1)
                act.activation(beta[:, :, :], raw[:, :, H:2 * H], ACT.Sigmoid).then_inc(exped, 1)

            @block.vector
            def _(dve):
                step = Steps(dve, own)
                dve.wait_ge(landed, 16)
                step.then(dve.tensor_tensor(y[:, :, 0:H], raw[:, :, 0:H],
                                            bias[:, 0:H].unsqueeze(1).broadcast_to([P, TT, H]), ALU.add))
                step.do(dve.tensor_tensor(y[:, :, H:W], raw[:, :, 2 * H:2 * H + F],
                                          bias[:, H:W].unsqueeze(1).broadcast_to([P, TT, F]), ALU.add))
                dve.tensor_scalar(y[:, :, H:W], y[:, :, H:W], -1.0, None, ALU.mult).then_inc(biased, 1)
                dve.wait_ge(exped, 3)
                step.do(dve.tensor_scalar(s[:, :, :], e[:, :, :], 2.0, None, ALU.add))
                step.do(dve.reciprocal(s[:, :, :], s[:, :, :]))
                step.do(dve.tensor_tensor(s[:, :, :], s[:, :, :], e[:, :, :], ALU.mult))
                step.do(dve.tensor_tensor(s2[:, :, :], s[:, :, :], s[:, :, :], ALU.mult))
                step.do(dve.tensor_scalar(p[:, :, :], s2[:, :, :], 1.0 / 15, None, ALU.mult))
                for n in (13, 11, 9, 7, 5, 3):
                    step.do(dve.scalar_tensor_tensor(p[:, :, :], p[:, :, :], 1.0 / n, s2[:, :, :], ALU.add, ALU.mult))
                step.do(dve.scalar_tensor_tensor(p[:, :, :], p[:, :, :], 1.0, s[:, :, :], ALU.add, ALU.mult))
                step.do(dve.tensor_scalar(p[:, :, :], p[:, :, :], 2.0, None, ALU.mult))
                step.do(dve.scalar_tensor_tensor(p[:, :, :], y[:, :, :], 0.0, p[:, :, :], ALU.max, ALU.add))
                step.then(dve.tensor_scalar(log_f[:, :, :], p[:, :, H:W], -1.0, None, ALU.mult))
                step.do(dve.scalar_tensor_tensor(g[:, :, :], p[:, :, 0:H], -1.0,
                                                 rate[:, :].unsqueeze(1).broadcast_to([P, TT, H]), ALU.mult, ALU.mult))


def forget_rows(k, log_f, f_query, f_key):
    nc, H = k.nc, 8
    with k.stage("forget") as (sb, sem):
        row = sb("row", [H, 2, T])
        summed, copied, moved, filled = (sem(x) for x in ("sums_ready", "rows_copied", "rows_moved", "ones_filled"))
        with nc.Block() as block:
            @block.tensor
            def _(pe):
                for n in range(TT):
                    last = pe.matmul(k.psum[0:H, n * P:T], log_f[:, n, :], k.c("upto")[:, 0:T - n * P],
                                     start=(n == 0), stop=(n == TT - 1))
                last.then_inc(summed, 1)

            @block.vector
            def _(dve):
                dve.wait_ge(summed, 1)
                dve.tensor_copy(row[:, 0, :], k.psum[0:H, 0:T]).then_inc(copied, 1)
                dve.tensor_scalar(row[:, 1, :], k.psum[0:H, 0:T], -1.0, None, ALU.mult).then_inc(copied, 1)

            @block.gpsimd
            def _(pool):
                pool.memset(f_query[:, :, :], 1.0).then_inc(filled, 1)
                pool.memset(f_key[:, :, :], 1.0).then_inc(filled, 1)

            @block.sync
            def _(sp):
                sp.wait_ge(copied, 2)
                sp.wait_ge(filled, 2)
                for first in (0, DH):
                    sp.dma_start(f_query[first:first + 1, :, :], row[:, 0, :]).then_inc(moved, 16)
                    sp.dma_start(f_key[first + 1:first + 2, :, :], row[:, 1, :]).then_inc(moved, 16)
                sp.wait_ge(moved, 64)


def stick_breaking(k, q, keys, v, out):
    nc, pairs = k.nc, 4
    M = 4
    first = [0, BANK, 2 * BANK, BANK + 3 * P]
    order = [0, 1, 3, 2]
    width = [T - n * P for n in range(TT)]
    COLS = 2 * BANK + 2 * P
    with k.stage("stick") as (sb, sem):
        qs, ks, vs = sb("q", [P, 2, 2, T]), sb("k", [P, 2, T]), sb("v", [P, 2, TT, P])
        mag, soft, att = (sb(x, [P, 2, COLS]) for x in ("mag", "softplus", "att"))
        scored, absed, exped, logged, added, soft_ready, summed, weighed, valued, cleared = (sem(x) for x in (
            "scores_ready", "magnitudes", "exps", "logs", "softplus_added", "softplus_ready", "sums_ready",
            "weights_ready", "values_summed", "padding_cleared"))
        staged, taken = ([sem(f"{x}{slot}") for slot in range(2)] for x in ("operands_staged", "results_taken"))
        n_copies = 4

        def tile(ap, n, lo=0):
            return ap[:, first[n] + lo:first[n] + width[n]]

        def bank(m):
            return k.psum[:, (m % 2) * 3 * BANK:(m % 2) * 3 * BANK + COLS]

        def loop(eng, body):
            with eng.Fori(0, pairs // 2) as i:
                body(i)

        with nc.Block() as block:
            @block.gpsimd
            def _(pool):
                pool.memset(qs[:, :, :, :], 0.0).then_inc(cleared, 1)

            @block.sync
            def _(sp):
                sp.wait_ge(cleared, 1)

                def body(i):
                    for slot in range(2):
                        sp.wait_ge(valued, i * M)
                        pair = 2 * i + slot
                        for dst, src in head_copies(qs[:, slot, :, :], at(q, pair)) + [
                                (ks[:, slot, :], at(keys, pair)), (vs[:, slot, :, :], v[:, :, bass.ds(pair * P, P)])]:
                            sp.dma_start(dst, src).then_inc(staged[slot], 16)
                loop(sp, body)

            @block.tensor
            def _(pe):
                def body(i):
                    def scores(m):
                        slot, h = m // 2, m % 2
                        if h == 0:
                            pe.wait_ge(staged[slot], i * 16 * n_copies + 16 * n_copies)
                        if m >= 2:
                            pe.wait_ge(weighed, i * M + m - 1)
                        for n in order:
                            last = pe.matmul(tile(bank(m), n), ks[:, slot, n * P:(n + 1) * P], qs[:, slot, h, n * P:T],
                                             start=(n != 3), stop=True, skip_group_check=True)
                        last.then_inc(scored, 1)

                    def sums(m):
                        s = soft[:, m % 2, :]
                        pe.wait_ge(soft_ready, (i * M + m + 1) * TT)
                        for n in range(TT):
                            pe.matmul(tile(bank(m), n), k.c("minus_from"), tile(s, n), start=False, stop=False,
                                      skip_group_check=True)
                            for later in range(n + 1, TT):
                                pe.matmul(tile(bank(m), n, (later - n) * P), k.c("minus_ones"), tile(s, later), start=False,
                                          stop=False, skip_group_check=True)
                            last = pe.matmul(tile(bank(m), n)[:, 0:P], k.c("ident"), k.c("not_before"), start=False, stop=True,
                                             skip_group_check=True)
                        last.then_inc(summed, 1)

                    def values(m):
                        slot, h = m // 2, m % 2
                        half = slice(h * DH, (h + 1) * DH)
                        pe.wait_ge(weighed, i * M + m + 1)
                        if h == 0:
                            pe.wait_ge(taken[slot], i)
                        for n in range(TT):
                            last = pe.matmul(k.psum[half, (6 + slot) * BANK + n * P:(7 + slot) * BANK], vs[:, slot, n, half],
                                             tile(att[:, m % 2, :], n), start=(n == 0), stop=(n == TT - 1),
                                             skip_group_check=True)
                        last.then_inc(valued, 1)

                    scores(0)
                    for m in range(M):
                        if m + 1 < M:
                            scores(m + 1)
                        sums(m)
                        if m:
                            values(m - 1)
                    values(M - 1)
                loop(pe, body)

            @block.scalar
            def _(act):
                def body(i):
                    def logs(m):
                        x = mag[:, m % 2, :]
                        if m >= 2:
                            act.wait_ge(added, i * M + m - 1)
                        act.wait_ge(scored, i * M + m + 1)
                        act.activation(x, bank(m), ACT.Abs).then_inc(absed, 1)
                        act.wait_ge(absed, i * M + m + 1)
                        act.activation(x, x, ACT.Exp, scale=-1.0).then_inc(exped, 1)
                        act.wait_ge(exped, i * M + m + 1)
                        act.activation(x, x, ACT.Ln, bias=k.c("one")).then_inc(logged, 1)

                    logs(0)
                    for m in range(M):
                        if m + 1 < M:
                            logs(m + 1)
                        if m >= 2:
                            act.wait_ge(valued, i * M + m - 1)
                        act.wait_ge(summed, i * M + m + 1)
                        act.activation(att[:, m % 2, :], bank(m), ACT.Exp).then_inc(weighed, 1)
                loop(act, body)

            @block.vector
            def _(dve):
                def body(i):
                    def take(slot):
                        dve.wait_ge(valued, i * M + 2 * slot + 2)
                        dst = at(out, 2 * i + slot)
                        dve.tensor_tensor(dst, k.bank(6 + slot), dst, ALU.mult).then_inc(taken[slot], 1)

                    for m in range(M):
                        s = soft[:, m % 2, :]
                        if m >= 2:
                            dve.wait_ge(summed, i * M + m - 1)
                        dve.wait_ge(logged, i * M + m + 1)
                        dve.scalar_tensor_tensor(s, bank(m), 0.0, mag[:, m % 2, :], ALU.max, ALU.add).then_inc(added, 1)
                        dve.wait_ge(added, i * M + m + 1)
                        for n in range(TT):
                            dve.tensor_tensor(tile(s, n)[:, 0:P], tile(s, n)[:, 0:P], k.c("before")[:, 0:P],
                                              ALU.mult).then_inc(soft_ready, 1)
                    take(0)
                    take(1)
                loop(dve, body)


def forgetting(k, q, keys, v, f_query, f_key, out):
    with ExitStack() as ctx:
        def sb(what, shape):
            return ctx.enter_context(k.tensor(f"fox_{what}", shape, F32))

        qs, ks, vs = sb("q", [P, 2, 2, T]), sb("k", [P, 2, 2, T]), sb("v", [P, 2, TT, P])

        def copies(i, slot):
            pair = 2 * i + slot
            cols = slice(pair * P, (pair + 1) * P) if isinstance(i, int) else bass.ds(pair * P, P)
            found = [*head_copies(qs[:, slot, :, :], at(q, pair)), *head_copies(ks[:, slot, :, :], at(keys, pair)),
                     (vs[:, slot, :, :], v[:, :, cols])]
            for h in range(2):
                rows = slice(DH - h * DH, DH - h * DH + 2)
                found += [(qs[rows, slot, h, :], at(f_query, 2 * pair + h)[rows, :]),
                          (ks[rows, slot, h, :], at(f_key, 2 * pair + h)[rows, :])]
            return found

        def units(slot):
            found = []
            for t in range(TT):
                n = (t + 1) * P
                lo = 3 * P - t * P
                for h in range(2):
                    found.append(Unit([(qs[:, slot, h, t * P:(t + 1) * P], ks[:, slot, h, 0:n])], n,
                                      k.c("causal")[:, lo:lo + n], 1.0,
                                      [(m * P, P, vs[:, slot, m, h * DH:(h + 1) * DH]) for m in range(t + 1)],
                                      (h * DH, (h + 1) * DH), t, True, True))
            return found

        attention(k, "fox", 4, copies, units, lambda i, t: at(out, i)[:, t * P:(t + 1) * P],
                  padded=[qs[:, :, :, :], ks[:, :, :, :]], gating=True)


def delta_rule(k, qkv, g, beta, out):
    nc, H, C = k.nc, GDN_HEADS, GDN_CHUNK
    W = H * P
    with k.stage("delta_prepare") as (sb, sem):
        def kept(what, shape):
            return k.gdn.enter_context(k.tensor(f"delta_{what}", shape, F32))

        u = kept("u", [P, TT, W])
        wT = kept("w", [P, TT, W])
        q_dec = kept("q_dec", [P, H, T])
        k_dec = kept("k_dec", [P, TT, W])
        a_qk = kept("a_qk", [P, TT, W])
        g_end = kept("g_end", [P, H, T])
        with ExitStack() as inner:
            def tmp(what, shape):
                return inner.enter_context(k.tensor(f"delta_{what}", shape, F32))
            kv = tmp("kv", [P, 2, 2, W])
            kb = tmp("kb", [P, 2, W])
            vb = tmp("vb", [P, 2, W])
            ga = tmp("ga", [P, 2, W])
            gb = tmp("gb", [P, W])
            ex = tmp("ex", [P, 2, 3, H])
            dec = tmp("decay", [P, 2, 2, W])
            low = tmp("lower", [P, 2, W])
            lev = tmp("level", [P, 2, W])
            inv = tmp("inverse", [P, 2, 2, W])
            mid = tmp("middle", [P, 2, W])
            vs, ss, ps_ = ([sem(f"{x}_steps{p}") for p in range(2)] for x in ("vector", "scalar", "tensor"))
            V_TILE, S_TILE, E_TILE = 31, 12, 21
            LEVELS = 6

            def heads(ap):
                return ap.rearrange("p (h c) -> p h c", h=H)

            def mask(name):
                return k.c(name)[:, 0:P].unsqueeze(1).broadcast_to([P, H, P])

            def counts(t):
                return t % 2, V_TILE * (t // 2), S_TILE * (t // 2), E_TILE * (t // 2)

            with nc.Block() as block:
                @block.tensor
                def _(pe):
                    def before(t):
                        p, v0, s0, _ = counts(t)
                        here = slice(t * P, (t + 1) * P)

                        def free(scalar, vector):
                            if p == 1:
                                if scalar:
                                    pe.wait_ge(ss[0], s0 + scalar)
                                if vector:
                                    pe.wait_ge(vs[0], v0 + vector)

                        if p == 0 and t:
                            for other in range(2):
                                pe.wait_ge(vs[other], v0)
                                pe.wait_ge(ss[other], s0)
                        free(6, 0)
                        for n, first in ((0, GDN_HEADS), (1, 2 * GDN_HEADS)):
                            for h in range(H):
                                last = pe.transpose(k.bank(n)[:, h * P:(h + 1) * P], qkv[:, first + h, here], k.c("ident"))
                            last.then_inc(ps_[p], 1)
                        pe.matmul(k.psum[:, 2 * BANK:2 * BANK + H], k.c("g_upto"), g[:, t, :], start=True, stop=True)
                        pe.matmul(k.psum[:, 2 * BANK + H:2 * BANK + 2 * H], k.c("g_after"), g[:, t, :], start=True,
                                  stop=True).then_inc(ps_[p], 1)
                        pe.wait_ge(vs[p], v0 + 2)
                        a = ga[:, p, :]
                        for n, (left, right) in enumerate(((lambda h: k.c("g_upto"), lambda h: a[:, h * P:(h + 1) * P]),
                                                           (lambda h: a[:, h * P:(h + 1) * P], lambda h: k.c("g_upto")),
                                                           (lambda h: gb[:, h * P:(h + 1) * P], lambda h: k.c("g_upto")))):
                            for h in range(H):
                                last = pe.matmul(k.bank(3 + n)[:, h * P:(h + 1) * P], left(h), right(h), start=True, stop=True)
                            last.then_inc(ps_[p], 1)
                        free(0, 10)
                        for n, (left, right) in enumerate(((H, H), (H, 0))):
                            for h in range(H):
                                last = pe.matmul(k.bank(6 + n)[:, h * P:(h + 1) * P], qkv[:, left + h, here],
                                                 qkv[:, right + h, here], start=True, stop=True)
                            last.then_inc(ps_[p], 1)

                    def middle(t, lv):
                        p, v0, s0, _ = counts(t)
                        pe.wait_ge(vs[p], v0 + (12 + 3 * lv if lv else 13))
                        if lv == 0:
                            pe.wait_ge(ss[1], s0 + 6)
                        for h in range(H):
                            hs = slice(h * P, (h + 1) * P)
                            last = pe.matmul(k.bank(3 * p)[:, hs], lev[:, p, hs], inv[:, p, 1, hs], start=True, stop=True)
                        last.then_inc(ps_[p], 1)

                    def change(t, lv):
                        p, v0, s0, _ = counts(t)
                        if lv:
                            pe.wait_ge(vs[p], v0 + 13 + 3 * lv)
                        pe.wait_ge(ss[p], s0 + 7 + lv)
                        for h in range(H):
                            hs = slice(h * P, (h + 1) * P)
                            last = pe.matmul(k.bank(3 * p + 1)[:, hs], inv[:, p, 0, hs], mid[:, p, hs], start=True, stop=True)
                        if lv < LEVELS - 1:
                            for h in range(H):
                                hs = slice(h * P, (h + 1) * P)
                                last = pe.matmul(k.bank(3 * p + 2)[:, hs], mid[:, p, hs], inv[:, p, 0, hs], start=True, stop=True)
                        last.then_inc(ps_[p], 1)

                    def after(t):
                        p, v0, _, _ = counts(t)
                        pe.wait_ge(vs[p], v0 + 29)
                        if p == 1:
                            pe.wait_ge(vs[0], v0 + 31)
                        for n in range(2):
                            for h in range(H):
                                hs = slice(h * P, (h + 1) * P)
                                left, right = (inv[:, p, 1, hs], vb[:, p, hs]) if n == 0 else (kb[:, p, hs], inv[:, p, 1, hs])
                                last = pe.matmul(k.bank(6 + n)[:, hs], left, right, start=True, stop=True)
                        last.then_inc(ps_[p], 1)

                    for t in range(0, TT, 2):
                        before(t)
                        before(t + 1)
                        for lv in range(LEVELS):
                            middle(t, lv)
                            middle(t + 1, lv)
                            change(t, lv)
                            change(t + 1, lv)
                        after(t)
                        after(t + 1)

                @block.scalar
                def _(act):
                    def before(t):
                        p, v0, s0, e0 = counts(t)
                        s = Steps(act, ss[p])
                        s.n = s0
                        if t >= 2:
                            act.wait_ge(vs[p], v0)
                        act.wait_ge(ps_[p], e0 + 3)
                        s.then(act.activation(ex[:, p, 0:2, :].rearrange("p a h -> p (a h)"),
                                              k.psum[:, 2 * BANK:2 * BANK + 2 * H], ACT.Exp))
                        for n in range(2):
                            act.wait_ge(ps_[p], e0 + 4 + n)
                            s.then(act.activation(dec[:, p, n, :], k.bank(3 + n), ACT.Exp))
                        act.wait_ge(ps_[p], e0 + 6)
                        s.then(act.activation(g_end[:, :, t * P:(t + 1) * P], heads(k.bank(5)), ACT.Exp))
                        act.wait_ge(ps_[p], e0 + 2)
                        s.then(act.copy(kv[:, p, 0, :], k.bank(0)))
                        s.then(act.copy(kv[:, p, 1, :], k.bank(1)))

                    for t in range(0, TT, 2):
                        before(t)
                        before(t + 1)
                        for lv in range(LEVELS):
                            for p in range(2):
                                act.wait_ge(ps_[p], counts(t)[3] + 9 + 2 * lv)
                                act.copy(mid[:, p, :], k.bank(3 * p)).then_inc(ss[p], 1)

                @block.vector
                def _(dve):
                    def before(t, v):
                        p, _, s0, e0 = counts(t)
                        here = slice(t * P, (t + 1) * P)
                        if t:
                            dve.wait_ge(ps_[p], e0)
                            dve.wait_ge(ps_[1 - p], e0 + (6 if p else 0))
                        gt = g[:, t, :].unsqueeze(2).broadcast_to([P, H, P])
                        bt = beta[:, t, :].unsqueeze(2).broadcast_to([P, H, P])
                        l, x = low[:, p, :], ex[:, p, :, :]
                        v.then(dve.tensor_tensor(heads(ga[:, p, :]), mask("g_after"), gt, ALU.mult))
                        v.then(dve.tensor_tensor(heads(gb[:, :]), mask("ones"), gt, ALU.mult))
                        dve.wait_ge(ss[p], s0 + 1)
                        v.do(dve.tensor_tensor(x[:, 2, :], x[:, 0, :], beta[:, t, :], ALU.mult))
                        dve.wait_ge(ss[p], s0 + 6)
                        v.then(dve.tensor_tensor(heads(vb[:, p, :]), heads(kv[:, p, 1, :]), bt, ALU.mult))
                        v.then(dve.tensor_tensor(heads(kb[:, p, :]), heads(kv[:, p, 0, :]),
                                                 x[:, 2, :].unsqueeze(2).broadcast_to([P, H, P]), ALU.mult))
                        v.then(dve.tensor_tensor(heads(k_dec[:, t, :]), heads(kv[:, p, 0, :]),
                                                 x[:, 1, :].unsqueeze(2).broadcast_to([P, H, P]), ALU.mult))
                        v.then(dve.tensor_tensor(q_dec[:, :, here], qkv[:, 0:H, here], g_end[:, :, here], ALU.mult))
                        dve.wait_ge(ps_[p], e0 + 8)
                        v.do(dve.tensor_tensor(l, k.bank(6), dec[:, p, 0, :], ALU.mult))
                        v.then(dve.tensor_tensor(heads(l), heads(l), bt, ALU.mult))
                        v.do(dve.tensor_tensor(a_qk[:, t, :], k.bank(7), dec[:, p, 1, :], ALU.mult))
                        v.then(dve.tensor_tensor(heads(a_qk[:, t, :]), heads(a_qk[:, t, :]), mask("g_upto"), ALU.mult))
                        v.then(dve.tensor_copy(inv[:, p, :, :].rearrange("p a (h c) -> p (a h) c", h=H),
                                               k.c("ident").unsqueeze(1).broadcast_to([P, 2 * H, P])))
                        level(t, v, 0)

                    def level(t, v, lv):
                        p = t % 2
                        v.settle()
                        if lv:
                            dve.wait_ge(ps_[p], counts(t)[3] + 7 + 2 * lv)
                        v.then(dve.tensor_tensor(heads(lev[:, p, :]), heads(low[:, p, :]), mask(f"g_level{lv}"), ALU.mult))

                    for t in range(0, TT, 2):
                        v = [Steps(dve, vs[p]) for p in range(2)]
                        for p in range(2):
                            v[p].n = counts(t)[1]
                            before(t + p, v[p])
                        for lv in range(LEVELS):
                            for p in range(2):
                                if lv < LEVELS - 1:
                                    level(t + p, v[p], lv + 1)
                            for p in range(2):
                                v[p].settle()
                                dve.wait_ge(ps_[p], counts(t)[3] + 10 + 2 * lv)
                                v[p].then(dve.tensor_tensor(inv[:, p, 1, :], inv[:, p, 1, :], k.bank(3 * p + 1), ALU.subtract))
                                if lv < LEVELS - 1:
                                    v[p].then(dve.tensor_tensor(inv[:, p, 0, :], inv[:, p, 0, :], k.bank(3 * p + 2), ALU.subtract))
                        for p in range(2):
                            dve.wait_ge(ps_[p], counts(t)[3] + 21)
                            v[p].then(dve.tensor_copy(u[:, t + p, :], k.bank(6)))
                            v[p].then(dve.tensor_copy(wT[:, t + p, :], k.bank(7)))
    with k.stage("delta_scan") as (sb, sem):
        state = sb("state", [P, 2, H, P])
        fresh = sb("v_new", [P, 2, W])
        cleared, guessed, corrected, answered, learned, kept_, taken = (sem(x) for x in (
            "state_cleared", "predictions_ready", "v_new_ready", "answers_ready", "updates_ready", "state_updated",
            "answers_taken"))
        N = T // C
        with nc.Block() as block:
            @block.gpsimd
            def _(pool):
                pool.memset(state[:, 0, :, :], 0.0).then_inc(cleared, 1)

            @block.tensor
            def _(pe):
                pe.wait_ge(cleared, 1)
                for n in range(N):
                    t, rows = n // 2, slice((n % 2) * C, (n % 2 + 1) * C)
                    tok = slice(n * C, (n + 1) * C)
                    for h in range(H):
                        if n:
                            pe.wait_ge(kept_, H * (n - 1) + h + 1)
                        last = pe.matmul(k.psum[rows, (n % 2) * BANK + h * P:(n % 2) * BANK + (h + 1) * P],
                                         wT[:, t, h * P + rows.start:h * P + rows.stop], state[:, n % 2, h, :], start=True, stop=True)
                    last.then_inc(guessed, 1)
                    pe.wait_ge(corrected, n + 1)
                    for h in range(H):
                        hs = slice(h * P, (h + 1) * P)
                        last = pe.matmul(k.bank(4 + n % 2)[:, hs], k_dec[rows, t, hs], fresh[rows, n % 2, hs],
                                         start=True, stop=True)
                    last.then_inc(learned, 1)
                    if n >= 2:
                        pe.wait_ge(taken, n - 1)
                    for h in range(H):
                        hs = slice(h * P, (h + 1) * P)
                        o = k.psum[:, (2 + n % 2) * BANK + h * C:(2 + n % 2) * BANK + (h + 1) * C]
                        pe.matmul(o, state[:, n % 2, h, :], q_dec[:, h, tok], start=True, stop=False)
                        last = pe.matmul(o, fresh[rows, n % 2, hs], a_qk[rows, t, h * P + rows.start:h * P + rows.stop],
                                         start=False, stop=True)
                    last.then_inc(answered, 1)

            @block.vector
            def _(dve):
                for n in range(N):
                    t, rows = n // 2, slice((n % 2) * C, (n % 2 + 1) * C)
                    dve.wait_ge(guessed, n + 1)
                    dve.tensor_tensor(fresh[rows, n % 2, :], u[rows, t, :], k.psum[rows, (n % 2) * BANK:(n % 2 + 1) * BANK],
                                      ALU.subtract).then_inc(corrected, 1)
                    dve.wait_ge(learned, n + 1)
                    if n:
                        dve.wait_ge(answered, n)
                        dve.wait_ge(kept_, H * n)
                    for h in range(H):
                        end = (n + 1) * C - 1
                        dve.scalar_tensor_tensor(state[:, 1 - n % 2, h, :], state[:, n % 2, h, :], g_end[:, h, end:end + 1],
                                                 k.bank(4 + n % 2)[:, h * P:(h + 1) * P], ALU.mult, ALU.add).then_inc(kept_, 1)

            @block.scalar
            def _(act):
                for n in range(N):
                    act.wait_ge(answered, n + 1)
                    act.copy(out[:, :, n * C:(n + 1) * C],
                             k.psum[:, (2 + n % 2) * BANK:(2 + n % 2) * BANK + H * C].rearrange("p (h c) -> p h c", h=H)
                             ).then_inc(taken, 1)


def convolutions(k, qkv, wide, acc, short):
    def beside(dve, sem):
        step = Steps(dve, sem("convolution_steps"))
        w, b = k.p("conv_dw"), k.p("conv_dw_bias")
        for tap in range(CONV_K):
            step.settle()
            for n in range(4):
                x = wide[:, n, tap:tap + T]
                if tap == 0:
                    step.then(dve.tensor_scalar(acc[:, n, :], x, w[:, n:n + 1], b[:, n:n + 1], ALU.mult, ALU.add))
                else:
                    step.then(dve.scalar_tensor_tensor(acc[:, n, :], x, w[:, 4 * tap + n:4 * tap + n + 1], acc[:, n, :],
                                                       ALU.mult, ALU.add))
        w = k.p("conv_qkv")
        for tap in range(GDN_CONV):
            back = tap
            step.settle()
            for n in range(GDN_QKV):
                c = w[:, GDN_QKV * (GDN_CONV - 1 - tap) + n:GDN_QKV * (GDN_CONV - 1 - tap) + n + 1]
                if tap == 0:
                    step.then(dve.tensor_scalar(short[:, n, :], qkv[:, n, :], c, None, ALU.mult))
                else:
                    step.then(dve.scalar_tensor_tensor(short[:, n, back:T], qkv[:, n, 0:T - back], c, short[:, n, back:T],
                                                       ALU.mult, ALU.add))
        step.settle()
    return beside


def activate(k, name, func, pairs):
    with k.stage(name) as (sb, sem):
        done = sem("activated")
        with k.nc.Block() as block:
            @block.scalar
            def _(act):
                for out, src, bias in pairs:
                    if bias is None:
                        act.activation(out, src, func).then_inc(done, 1)
                    else:
                        act.activation(out, src, func, bias=bias).then_inc(done, 1)


def multiply(k, name, triples):
    with k.stage(name) as (sb, sem):
        done = sem("multiplied")
        with k.nc.Block() as block:
            @block.vector
            def _(dve):
                for out, a, b in triples:
                    dve.tensor_tensor(out, a, b, ALU.mult).then_inc(done, 1)


def second_block(k):
    nc = k.nc
    with ExitStack() as ctx:
        def sb(what, shape, stack=ctx):
            return stack.enter_context(k.tensor(f"second_{what}", shape, F32))

        y = sb("branches", [P, 4 * BRANCHES, T])
        g, beta, log_f = sb("g", [P, TT, GDN_HEADS]), sb("beta", [P, TT, GDN_HEADS]), sb("log_f", [P, TT, 8])
        with ExitStack() as branch_a:
            short = sb("qkv", [P, GDN_QKV, T], branch_a)
            with ExitStack() as branch_d:
                fox = sb("fox", [P, 12, T], branch_d)
                q_d, k_d, v_d = (fox[:, 4 * n:4 * n + 4, :] for n in range(3))
                with ExitStack() as branch_c:
                    q_c, k_c, v_c = (sb(f"{x}_stick", [P, 4, T], branch_c) for x in "qkv")
                    second_projections(k, y, short, fox, q_d, k_d, v_d, q_c, k_c, v_c, g, beta, log_f)
                    stick_breaking(k, q_c, k_c, v_c, y[:, 8:12, :])
                f_query, f_key = sb("f_query", [DH + 2, 8, T], branch_d), sb("f_key", [DH + 2, 8, T], branch_d)
                forget_rows(k, log_f, f_query, f_key)
                forgetting(k, q_d, k_d, v_d, f_query, f_key, y[:, 12:16, :])
            chunk_norms(k, "delta_unit", [(short[:, n, :], short[:, n, :], k.c("gdn_scale") if n < GDN_HEADS else 1.0)
                                          for n in range(2 * GDN_HEADS)], 1, 1.0, "eps")
            with ExitStack() as k.gdn:
                answers = k.h[:, 0:GDN_HEADS, :]
                delta_rule(k, short, g, beta, answers)
            chunk_norms(k, "delta_norm", [(answers[:, n, :], answers[:, n, :], k.p("gdn_norm")) for n in range(GDN_HEADS)],
                        1, 1.0 / P, "eps_2")
            multiply(k, "delta_gate", [(y[:, n, :], y[:, n, :], answers[:, n, :]) for n in range(GDN_HEADS)])
        merged = k.h
        gated_products(k, "merge", k.dram["w_merge"], BRANCHES, KD, k.x, k.p("b_gate"), 4,
                       lambda q: y[:, 4 * q:4 * q + 4, :], None, merged)

    def residual(eng, n, ps):
        return eng.scalar_tensor_tensor(at(k.x, n), at(k.x, n), ALPHA, ps, ALU.mult, ALU.add)

    project(k, "out2", [Section(k.dram["w_out_2"], 2, KD, k.h, residual, "vector", spent=True)])
    with k.stage("ple_in") as (sb, sem):
        per_layer = sb("p", [P, PLE // P, T])
        landed = sem("p_landed")
        with nc.Block() as block:
            @block.sync
            def _(sp):
                sp.dma_start(per_layer[:, :, :], k.dram["pT"].rearrange("(c p) t -> p c t", p=P)).then_inc(landed, 16)
                sp.wait_ge(landed, 16)
        gated_products(k, "ple", k.dram["w_ple"], 1, KD, k.x, k.p("b_ple_gate"), PLE // P, lambda q: per_layer, k.x, k.h)
    chunks = [k.h[:, n, :] for n in range(KD)]
    feature_center(k, "ln2_center", chunks)
    feature_norm(k, "ln2", [(chunks, [k.x[:, n, :] for n in range(KD)], [k.p("ln_g", n) for n in range(KD)])],
                 k.c("ones"), 1.0 / D, "eps_2", shift=[k.p("ln_b", n) for n in range(KD)])


def second_projections(k, y, short, fox, q_d, k_d, v_d, q_c, k_c, v_c, g, beta, log_f):
    nc = k.nc
    pad = CONV_K - 1
    acc = k.h[:, 0:4, :]
    with ExitStack() as ctx:
        def sb(what, shape):
            return ctx.enter_context(k.tensor(f"second_{what}", shape, F32))

        wide = sb("wide", [P, 4, pad + T])
        rate = sb("rates", [P, TT, 2 * GDN_HEADS + 8])
        lin = k.h[:, 4:8, :]

        def scaled(dst, scale):
            return lambda eng, n, ps: eng.activation(at(dst, n), ps, ACT.Copy, scale=scale)

        def plain(dst):
            return scaled(dst, 1.0)

        def silu_of(first):
            return activates_to(y[:, first:first + 4, :], ACT.Silu)

        def opened(eng, n, ps):
            return eng.activation(at(wide, n)[:, pad:pad + T], ps, ACT.Sigmoid)

        d = k.dram
        raw = [q_c, k_c, v_c]
        project(k, "proj2a", [
            Section(d["w2_glu_gate"], 1, KD, k.x, opened, "scalar"),
            Section(d["w2_glu_lin"], 1, KD, k.x, plain(lin), "scalar"),
            *[Section(d["w2_qkv_a"][n:n + 1], 1, KD, k.x, plain(raw[n]), "scalar") for n in range(3)],
        ], room={"leading": [a[:, 0:8, :].rearrange("p n t -> p (n t)") for a in (short, fox)], "parts": [y[:, 0:8, :], y[:, 8:16, :]]})
        with k.stage("glu") as (sb2, sem):
            opened_, cleared = sem("glu_opened"), sem("pad_cleared")
            with nc.Block() as block:
                @block.vector
                def _(dve):
                    for n in range(4):
                        dve.tensor_tensor(wide[:, n, pad:pad + T], wide[:, n, pad:pad + T], lin[:, n, :],
                                          ALU.mult).then_inc(opened_, 1)

                @block.gpsimd
                def _(pool):
                    pool.memset(wide[:, :, 0:pad], 0.0).then_inc(cleared, 1)

        def raw_chunk(n):
            return raw[n // 4][:, n % 4, :]

        class Raw:
            def __getitem__(self, key):
                return raw_chunk(key[1])[:, key[2]]

        project(k, "proj2b", [
            Section(d["w2_z_a"], 1, KD, k.x, silu_of(0), "scalar"),
            Section(d["w2_z_b"], 1, KD, k.x, silu_of(4), "scalar"),
            Section(d["w2_z_c"], 1, KD, k.x, silu_of(8), "scalar"),
            Section(d["w2_z_d"], 1, KD, k.x, silu_of(12), "scalar"),
            Section(d["w2_q_d"], 1, KD, k.x, scaled(q_d, DH ** -0.5), "scalar"),
            Section(d["w2_k_d"], 1, KD, k.x, plain(k_d), "scalar"),
            Section(d["w2_v_d"], 1, KD, k.x, plain(v_d), "scalar", by_tokens=True),
            Section(d["w2_rates"], 1, KD, k.x, lambda eng, n, ps: eng.activation(rate[:, n, :], ps, ACT.Copy), "scalar",
                    width=2 * GDN_HEADS + 8, by_tokens=True),
        ], beside=convolutions(k, Raw(), wide, acc, short))
        rates(k, rate, g, beta, log_f)
        activate(k, "qkv_silu", ACT.Silu, [(short[:, n, :], short[:, n, :], None) for n in range(GDN_QKV)])
        chunks = [acc[:, n, :] for n in range(4)]
        feature_center(k, "conv_center", chunks)
        feature_norm(k, "conv_ln", [(chunks, chunks, [k.p("conv_ln_g", n) for n in range(4)])], k.c("ones"), 1.0 / 512,
                     "eps_2")
        activate(k, "conv_silu", ACT.Silu, [(acc[:, n, :], acc[:, n, :], k.p("conv_ln_b", n)) for n in range(4)])
        multiply(k, "conv_gate", [(y[:, 4 + n, :], y[:, 4 + n, :], acc[:, n, :]) for n in range(4)])
    project(k, "proj2c", [
        Section(d["w2_q_c"], 2, KD, k.x, scaled(q_c, DH ** -0.5), "scalar", chunks=2),
        Section(d["w2_k_c"], 2, KD, k.x, plain(k_c), "scalar", chunks=2),
        Section(d["w2_v_c"], 2, KD, k.x, lambda eng, n, ps: eng.activation(
            v_c[:, n % TT, n // TT * 2 * P:(n // TT + 1) * 2 * P], ps, ACT.Copy), "scalar", width=2 * P, by_tokens=True),
    ], room={"parts": [k.h]})


def lay_out_second(i, a, p):
    w = i["w_in_2"][0]
    at_col = {"qkv_a": (0, 1536), "z_a": (1536, 512), "glu_lin": (2056, 512), "glu_gate": (2568, 512), "z_b": (3080, 512),
              "q_c": (3592, 512), "k_c": (4104, 512), "z_c": (5128, 512), "q_d": (5640, 512), "k_d": (6152, 512),
              "z_d": (7176, 512)}
    for n, (lo, width) in at_col.items():
        a[f"w2_{n}"] = units_of(w[:, lo:lo + width], 2 if n in ("q_c", "k_c") else 4)
    a["w2_v_c"], a["w2_v_d"] = units_of(w[:, 4616:5128], 2), whole(w[:, 6664:7176])
    a["w2_rates"] = whole(np.concatenate([w[:, 2048:2056], w[:, 7688:7696]], 1))
    a["rate_biases"] = np.concatenate([i["dt_bias_2"], i["forget_bias_2"], i["a_log_2"]], 1)
    gates = units_of(w[:, 7696:], 1)
    branch = np.concatenate([units_of(b, 1) for b in i["w_branch_2"][0]])
    a["w_merge"] = np.concatenate([gates, branch], 2)
    a["w_out_2"] = units_of(i["w_out_2"][0], 4)
    a["pT"] = i["p_2"][0, 0].T
    a["w_ple"] = np.concatenate([units_of(i["w_ple_gate_2"][0], 1), units_of(i["w_ple_2"][0], 1)], 2)
    for n in ("b_gate", "gdn_norm", "conv_dw_bias", "conv_ln_g", "conv_ln_b", "b_ple_gate", "ln_g", "ln_b"):
        p[n] = columns(i[n + "_2"][0])
    p["conv_qkv"] = columns(i["conv_qkv_2"][0].reshape(-1))
    p["conv_dw"] = columns(i["conv_dw_2"][0].reshape(-1))



def modulation(k, mod):
    nc = k.nc
    with ExitStack() as ctx:
        silu = ctx.enter_context(k.tensor("ada_silu", [P, KD, 2], F32))
        rows = ctx.enter_context(k.tensor("ada_rows", [2, 6 * D], F32))
        activate(k, "ada_silu_c", ACT.Silu, [(silu[:, :, :].rearrange("p a b -> p (a b)"), k.p("c"), None)])

        def row(eng, n, ps):
            at_n = slice(n * BANK, (n + 1) * BANK) if isinstance(n, int) else bass.ds(n * BANK, BANK)
            return eng.tensor_copy(rows[:, at_n], ps)

        project(k, "ada", [Section(k.dram["w_ada"], 12, KD, silu, row, "vector", chunks=1, by_tokens=True, rows=2, split=False)])
        with k.stage("ada_turn") as (sb, sem):
            turned, biased = sem("turned"), sem("biased")
            with nc.Block() as block:
                @block.tensor
                def _(pe):
                    for n in range(6 * KD):
                        last = pe.transpose(k.psum[:, 2 * n:2 * n + 2], rows[:, n * P:(n + 1) * P], k.c("ident")[0:2, 0:2])
                    last.then_inc(turned, 1)

                @block.vector
                def _(dve):
                    dve.wait_ge(turned, 1)
                    dve.tensor_tensor(mod[:, :, :], k.psum[:, 0:12 * KD].rearrange("p (n c) -> p n c", c=2),
                                      k.p("b_ada").unsqueeze(2).broadcast_to([P, 6 * KD, 2]), ALU.add).then_inc(biased, 1)


def third_columns(k, mod, gains, subln, minus_lam):
    nc = k.nc
    with k.stage("third_columns") as (sb, sem):
        prod, exps, diff = sb("products", [P, 2]), sb("exps", [P, 2]), sb("difference", [P, 1])
        own, summed, exped = sem("vector_steps"), sem("sums_ready"), sem("exps_ready")
        lam = k.p("lambdas")
        with nc.Block() as block:
            @block.vector
            def _(dve):
                step = Steps(dve, own)
                step.then(dve.tensor_tensor(prod[:, 0:1], lam[:, 0:1], lam[:, 1:2], ALU.mult))
                step.then(dve.tensor_tensor(prod[:, 1:2], lam[:, 2:3], lam[:, 3:4], ALU.mult))
                for n, (part, stream, weight) in enumerate(((1, 0, "attn_norm_w"), (1, 1, "attn_norm_w"), (4, 0, "ffn_norm_w"))):
                    step.then(dve.scalar_tensor_tensor(gains[:, n, :], mod[:, part * KD:(part + 1) * KD, stream], 1.0,
                                                       k.p(weight), ALU.add, ALU.mult))
                step.then(dve.tensor_scalar(subln[:, :], k.p("subln_w"), 1.0 - LAM_INIT, None, ALU.mult))
                dve.wait_ge(exped, 1)
                step.do(dve.tensor_tensor(diff[:, :], exps[:, 1:2], exps[:, 0:1], ALU.subtract))
                step.do(dve.tensor_scalar(minus_lam[:, :], diff[:, :], -LAM_INIT, None, ALU.add))

            @block.tensor
            def _(pe):
                pe.wait_ge(own, 2)
                pe.matmul(k.bank(0, 2), k.c("ones"), prod[:, :], start=True, stop=True).then_inc(summed, 1)

            @block.scalar
            def _(act):
                act.wait_ge(summed, 1)
                act.activation(exps[:, :], k.bank(0, 2), ACT.Exp).then_inc(exped, 1)


def rotate(k, name, pairs):
    nc = k.nc
    with k.stage(name) as (sb, sem):
        turn, keep = sb("turned", [P, 2, T]), sb("kept", [P, 2, T])
        swapped, own, done = sem("swapped"), sem("vector_steps"), sem("rotated")
        with nc.Block() as block:
            @block.tensor
            def _(pe):
                for n, (_, x) in enumerate(pairs):
                    if n >= 2:
                        pe.wait_ge(own, 2 * (n - 1))
                    pe.matmul(k.bank(n % 2), k.c("rope_swap"), x, start=True, stop=True).then_inc(swapped, 1)

            @block.vector
            def _(dve):
                for n, (out, x) in enumerate(pairs):
                    dve.wait_ge(swapped, n + 1)
                    if n >= 2:
                        dve.wait_ge(done, n - 1)
                    dve.tensor_tensor(turn[:, n % 2, :], k.bank(n % 2), k.c("rope_sin"), ALU.mult).then_inc(own, 1)
                    dve.tensor_tensor(keep[:, n % 2, :], x, k.c("rope_cos"), ALU.mult).then_inc(own, 1)
                    dve.wait_ge(own, 2 * n + 2)
                    dve.tensor_tensor(out, turn[:, n % 2, :], keep[:, n % 2, :], ALU.add).then_inc(done, 1)


def mixers(k, mod, gains, subln, minus_lam, mix):
    nc, d = k.nc, k.dram
    with ExitStack() as ctx:
        def sb(what, shape, stack=ctx):
            return stack.enter_context(k.tensor(f"third_{what}", shape, F32))

        dq, dk, dv = sb("dq", [P, 4, T]), sb("dk", [P, 4, TA]), sb("dv", [P, TA // P, 4 * P])
        cq, ckv, kr = sb("cq", [P, 2, T]), sb("ckv", [P, 1, TA]), sb("kr", [P, 1, TA])
        zeros = sb("zeros", [P, TA])
        with ExitStack() as inputs:
            hc = sb("ctx_normed", [P, KD, CTX], inputs)
            with ExitStack() as raw:
                cx = sb("ctx", [P, KD, CTX], raw)
                with k.stage("ctx_in") as (sb2, sem):
                    landed, cleared = sem("ctx_landed"), sem("zeros_cleared")
                    with nc.Block() as block:
                        @block.sync
                        def _(sp):
                            sp.dma_start(cx[:, :, :], d["ctxT"].rearrange("(k p) t -> p k t", p=P)).then_inc(landed, 16)
                            sp.wait_ge(landed, 16)

                        @block.gpsimd
                        def _(pool):
                            pool.memset(zeros[:, :], 0.0).then_inc(cleared, 1)
                for stream, (src, dst) in enumerate(((k.x, k.h), (cx, hc))):
                    feature_norm(k, f"third_norm{stream}",
                                 [([src[:, n, :] for n in range(KD)], [dst[:, n, :] for n in range(KD)],
                                   [gains[:, stream, n:n + 1] for n in range(KD)])], k.c("ones"), 1.0 / D, "eps",
                                 shift=[mod[:, n, stream:stream + 1] for n in range(KD)])

            def into(dst, lo, n_tokens, scale=1.0):
                return lambda eng, n, ps: eng.activation(at(dst, n)[:, lo:lo + n_tokens], ps, ACT.Copy, scale=scale)

            def tokens(dst, first):
                return lambda eng, n, ps: eng.activation(dst[:, first + n, :], ps, ACT.Copy)

            def misc(lo, n_tokens, first):
                def finish(eng, n, ps):
                    dst = [cq[:, 0, :], cq[:, 1, :], ckv[:, 0, lo:lo + n_tokens], kr[:, 0, lo:lo + n_tokens]][first + n]
                    return eng.activation(dst, ps, ACT.Copy)
                return finish

            project(k, "proj3", [
                Section(d["w3_dq"], 1, KD, k.h, into(dq, 0, T, DH ** -0.5), "scalar", spent=True),
                Section(d["w3_dk"], 1, KD, k.h, into(dk, CTX, T), "scalar", spent=True),
                Section(d["w3_dk"], 1, KD, hc, into(dk, 0, CTX), "scalar", width=CTX, spent=True),
                Section(d["w3_dv"], 1, KD, k.h, tokens(dv, CTX // P), "scalar", by_tokens=True, spent=True),
                Section(d["w3_dv"], 1, KD, hc, tokens(dv, 0), "scalar", chunks=CTX // P, by_tokens=True, spent=True),
                Section(d["w3_misc"], 1, KD, k.h, misc(CTX, T, 0), "scalar", spent=True),
                Section(d["w3_misc_ctx"], 1, KD, hc, misc(0, CTX, 2), "scalar", chunks=2, width=CTX, spent=True),
            ], room={"parts": [mix]})
        rotate(k, "rope_diff", [(dq[:, n, :], dq[:, n, :]) for n in range(4)]
               + [(dk[:, n, CTX:TA], dk[:, n, CTX:TA]) for n in range(4)] + [(kr[:, 0, CTX:TA], kr[:, 0, CTX:TA])])
        halves = [(0, BANK), (BANK, TA)]
        feature_norm(k, "latent_norm", [([cq[:, n, :] for n in range(2)], [cq[:, n, :] for n in range(2)],
                                         [k.p("q_norm_w", n) for n in range(2)])], k.c("ones"), 1.0 / 256, "eps")
        feature_norm(k, "latent_kv_norm", [([ckv[:, 0, a:b]], [ckv[:, 0, a:b]], [k.p("kv_norm_w")]) for a, b in halves],
                     k.c("ones"), 1.0 / P, "eps")

        with ExitStack() as heads:
            qs, ks, vs = sb("diff_q", [P, 2, 2, T], heads), sb("diff_k", [P, 2, TA], heads), sb("diff_v", [P, 2, TA // P, P], heads)

            def copies(i, slot):
                head = 2 * i + slot
                cols = slice(head * P, (head + 1) * P) if isinstance(i, int) else bass.ds(head * P, P)
                return [*head_copies(qs[:, slot, :, :], at(dq, head)), (ks[:, slot, :], at(dk, head)),
                        (vs[:, slot, :, :], dv[:, :, cols])]

            def units(slot):
                return [Unit([(qs[:, slot, m, t * P:(t + 1) * P], ks[:, slot, :])], TA, zeros[:, :],
                             minus_lam[:, :] if m else 1.0, [(n * P, P, vs[:, slot, n, :]) for n in range(TA // P)],
                             (0, P), t, m == 0, m == 1) for t in range(TT) for m in range(2)]

            attention(k, "diff", DIFF_HEADS, copies, units, lambda i, t: at(mix, i)[:, t * P:(t + 1) * P],
                      padded=[qs[:, :, :, :]], joined=True)
        chunk_norms(k, "diff_norm", [(mix[:, n, :], mix[:, n, :], subln[:, :]) for n in range(DIFF_HEADS)], 1, 1.0 / P, "eps")

        scale = (P + DH) ** -0.5
        qn, qr = sb("mla_qn", [P, 4, T]), sb("mla_qr", [P, 2, T])
        kn, mv = dk, dv

        def queries(eng, n, ps):
            return eng.activation(qn[:, n, :] if n < 4 else qr[:, n - 4, :], ps, ACT.Copy, scale=scale)

        def shifted(finish, first):
            return lambda eng, n, ps: finish(eng, n + first, ps)

        project(k, "proj3b", [
            Section(d["w3_uq"][0:1], 1, 2, cq, shifted(queries, 0), "scalar", chunks=3),
            Section(d["w3_uq"][1:2], 1, 2, cq, shifted(queries, 3), "scalar", chunks=3),
            Section(d["w3_uk"], 1, 1, ckv[:, :, 0:CTX], lambda eng, n, ps: eng.activation(kn[:, n, 0:CTX], ps, ACT.Copy),
                    "scalar", width=CTX),
            Section(d["w3_uk"], 1, 1, ckv[:, :, CTX:TA], lambda eng, n, ps: eng.activation(kn[:, n, CTX:TA], ps, ACT.Copy),
                    "scalar"),
            Section(d["w3_uv"], 1, 1, ckv, lambda eng, n, ps: eng.activation(mv[:, n, :], ps, ACT.Copy), "scalar",
                    chunks=3, by_tokens=True),
            Section(d["w3_uv"], 1, 1, ckv[:, :, 3 * P:TA], lambda eng, n, ps: eng.activation(mv[:, 3 + n, :], ps, ACT.Copy),
                    "scalar", chunks=3, by_tokens=True),
        ])
        rotate(k, "rope_mla", [(qr[:, n, :], qr[:, n, :]) for n in range(2)])
        with ExitStack() as heads:
            qrs = sb("mla_qrs", [P, 2, 2, T], heads)

            def copies(i, slot):
                return head_copies(qrs[:, slot, :, :], qr[:, slot, :])

            def units(slot):
                found = []
                for t in range(TT):
                    here = slice(t * P, (t + 1) * P)
                    for h in range(2):
                        head = 2 * slot + h
                        found.append(Unit([(qn[:, head, here], kn[:, head, :]), (qrs[:, slot, h, here], kr[:, 0, :])], TA,
                                          zeros[:, :], 1.0, [(n * P, P, mv[:, n, head * P:(head + 1) * P]) for n in range(TA // P)],
                                          (0, P), 2 * t + h, True, True))
                return found

            attention(k, "mla", 2, copies, units,
                      lambda i, g: at(mix, 4 + 2 * i + g % 2)[:, (g // 2) * P:(g // 2 + 1) * P], padded=[qrs[:, :, :, :]])


def route(k, logits, gate, dest, row_of, block_expert, gate_by_expert):
    nc, E, K, B = k.nc, EXPERTS, TOP_K, SLOTS_MAX + 1
    table = nc.dram_tensor("row_tokens", (B * P, 1), I32, kind="Internal").ap()
    with k.stage("route") as (sb, sem):
        top, ids = sb("top", [P, TT, 8]), sb("ids", [P, TT, 8], U32)
        idf, neg = sb("ids_f", [P, TT, 8]), sb("neg", [P, TT])
        ex, total, inv = sb("exps", [P, TT, K]), sb("total", [P, TT]), sb("inverse", [P, TT])
        hot, part = sb("hot", [P, TT, K, E]), sb("part", [P, K, E])
        chosen, slot, spread = sb("chosen", [P, TT, E]), sb("slots", [P, TT, E]), sb("spread", [P, TT, E])
        start, blocks, ends = sb("start", [P, E]), sb("blocks", [E, P]), sb("ends", [E, 1])
        past, count_t = sb("past", [E, B]), sb("counts", [E, P])
        dest_f, toks, fill = sb("dest_f", [P, TT, K]), sb("tokens", [P, TT], I32), sb("fill", [B, P], I32)
        row_i, row_f = sb("row_i", [B, P], I32), sb("row_f", [B, P])
        own, exped, ranked, started, ended, mapped, filled, scattered, loaded, cast, turned = (sem(x) for x in (
            "vector_steps", "exps_ready", "ranks_ready", "starts_ready", "ends_ready", "map_ready", "table_filled",
            "tokens_scattered", "table_loaded", "table_cast", "table_turned"))
        with nc.Block() as block:
            @block.vector
            def _(dve):
                v = Steps(dve, own)
                for t in range(TT):
                    v.do(dve.max(top[:, t, :], logits[:, t, :]))
                    v.then(dve.max_index(ids[:, t, :], top[:, t, :], logits[:, t, :]))
                v.settle()
                v.then(dve.tensor_copy(idf[:, :, :], ids[:, :, :]))
                v.then(dve.tensor_copy(toks[:, :], k.c("lanes_on")))
                v.then(dve.memset(fill[:, :], T))
                v.do(dve.tensor_scalar(neg[:, :], top[:, :, 0], -1.0, None, ALU.mult))
                for t in range(TT):
                    v.do(dve.tensor_tensor(hot[:, t, :, :], k.c("experts").unsqueeze(1).broadcast_to([P, K, E]),
                                           idf[:, t, 0:K].unsqueeze(2).broadcast_to([P, K, E]), ALU.is_equal))
                    v.then(dve.tensor_reduce(chosen[:, t, :], hot[:, t, :, :].rearrange("p k e -> p e k"), AX_X, ALU.add))
                v.settle()
                dve.wait_ge(ranked, 3)
                v.do(dve.tensor_copy(count_t[:, :], k.psum[0:E, 2 * BANK:2 * BANK + P]))
                v.do(dve.tensor_scalar(blocks[:, :], count_t[:, :], 0.0, None, ALU.is_gt))
                for n in range(1, T // P):
                    v.do(dve.scalar_tensor_tensor(blocks[:, :], count_t[:, :], float(n * P), blocks[:, :], ALU.is_gt, ALU.add))
                dve.wait_ge(started, 1)
                v.do(dve.tensor_scalar(start[:, :], k.bank(3, E), float(P), None, ALU.mult))
                v.do(dve.tensor_tensor(slot[:, :, :], k.psum[:, 0:TT * E].rearrange("p (t e) -> p t e", e=E),
                                       start[:, :].unsqueeze(1).broadcast_to([P, TT, E]), ALU.add))
                for t in range(TT):
                    v.do(dve.tensor_tensor(part[:, :, :], hot[:, t, :, :], slot[:, t, :].unsqueeze(1).broadcast_to([P, K, E]),
                                           ALU.mult))
                    v.do(dve.tensor_reduce(dest_f[:, t, :], part[:, :, :], AX_X, ALU.add))
                v.do(dve.tensor_copy(dest[:, :, :], dest_f[:, :, :]))
                dve.wait_ge(ended, 1)
                v.do(dve.tensor_copy(ends[:, :], k.psum[0:E, 4 * BANK:4 * BANK + 1]))
                v.then(dve.tensor_scalar(past[:, :], k.c("blocks")[0:E, :], ends[:, 0:1], None, ALU.is_ge))
                dve.wait_ge(mapped, 1)
                v.then(dve.tensor_copy(block_expert[:, 0:B + 1], k.psum[0:1, 5 * BANK:5 * BANK + B + 1]))
                v.then(dve.tensor_scalar(block_expert[:, B + 1:B + 2], k.psum[0:1, 5 * BANK + B:5 * BANK + B + 1], -1.0, float(B),
                                         ALU.mult, ALU.add))
                dve.wait_ge(exped, TT)
                v.do(dve.reciprocal(inv[:, :], total[:, :]))
                v.do(dve.tensor_tensor(gate[:, :, :], ex[:, :, :], inv[:, :].unsqueeze(2).broadcast_to([P, TT, K]), ALU.mult))
                for t in range(TT):
                    v.do(dve.tensor_tensor(part[:, :, :], hot[:, t, :, :], gate[:, t, :].unsqueeze(2).broadcast_to([P, K, E]),
                                           ALU.mult))
                    v.do(dve.tensor_reduce(spread[:, t, :], part[:, :, :].rearrange("p k e -> p e k"), AX_X, ALU.add))
                dve.wait_ge(loaded, 16)
                dve.tensor_copy(row_f[:, :], row_i[:, :]).then_inc(cast, 1)
                dve.wait_ge(turned, 1)
                v.then(dve.tensor_copy(row_of[:, 0:B], k.psum[:, 6 * BANK:6 * BANK + B]))
                v.then(dve.tensor_copy(gate_by_expert[:, :], k.psum[0:E, 7 * BANK:7 * BANK + T]))

            @block.scalar
            def _(act):
                act.wait_ge(own, 12)
                for t in range(TT):
                    act.activation(ex[:, t, :], top[:, t, 0:K], ACT.Exp, bias=neg[:, t:t + 1],
                                   accum_out=total[:, t:t + 1]).then_inc(exped, 1)

            @block.tensor
            def _(pe):
                pe.wait_ge(own, 20)
                for t in range(TT):
                    out = k.psum[:, t * E:(t + 1) * E]
                    for n in range(t + 1):
                        last = pe.matmul(out, k.c("before")[:, 0:P] if n == t else k.c("ones"), chosen[:, n, :],
                                         start=(n == 0), stop=(n == t))
                last.then_inc(ranked, 2)
                for n in range(TT):
                    last = pe.matmul(k.psum[0:E, 2 * BANK:2 * BANK + P], chosen[:, n, :], k.c("ones"), start=(n == 0),
                                     stop=(n == TT - 1))
                last.then_inc(ranked, 1)
                pe.wait_ge(own, 25)
                pe.matmul(k.bank(3, E), blocks[:, :], k.c("before")[0:E, 0:E], start=True, stop=True).then_inc(started, 1)
                pe.matmul(k.psum[0:E, 4 * BANK:4 * BANK + P], k.c("upto")[0:E, 0:E], blocks[:, :], start=True,
                          stop=True).then_inc(ended, 1)
                pe.wait_ge(own, 38)
                pe.matmul(k.psum[0:1, 5 * BANK:5 * BANK + B], k.c("one")[0:E, :], past[:, :], start=True, stop=True)
                pe.matmul(k.psum[0:1, 5 * BANK + B:5 * BANK + B + 1], blocks[:, 0:1], k.c("one")[0:E, :], start=True,
                          stop=True).then_inc(mapped, 1)
                pe.wait_ge(own, 50)
                for t in range(TT):
                    pe.transpose(k.psum[0:E, 7 * BANK + t * P:7 * BANK + (t + 1) * P], spread[:, t, :], k.c("ident"))
                pe.wait_ge(cast, 1)
                pe.transpose(k.psum[:, 6 * BANK:6 * BANK + B], row_f[:, :], k.c("ident")[0:B, 0:B]).then_inc(turned, 1)

            @block.gpsimd
            def _(pool):
                pool.wait_ge(own, 36)
                pool.wait_ge(filled, 16)
                for t in range(TT):
                    for n in range(K):
                        pool.indirect_dma_start(out=table, out_offset=bass.IndirectOffsetOnAxis(ap=dest[:, t, n:n + 1], axis=0),
                                                in_=toks[:, t:t + 1], in_offset=None).then_inc(scattered, 16)

            @block.sync
            def _(sp):
                sp.wait_ge(own, 12)
                sp.dma_start(table.rearrange("(b p) one -> b (p one)", p=P), fill[:, :]).then_inc(filled, 16)
                sp.wait_ge(scattered, 16 * TT * K)
                sp.dma_start(row_i[:, :], table.rearrange("(b p) one -> b (p one)", p=P)).then_inc(loaded, 16)


def experts(k, rows, row_of, block_expert, results):
    nc, d = k.nc, k.dram
    UP, DOWN, CH = 4, 2, 4
    HALF = 2 * P
    with k.stage("experts") as (sb, sem):
        ring_up = sb("up", [P, UP, KD * CH * P + CH])
        ring_down = sb("down", [P, DOWN, KD * BANK])
        index = sb("index", [P, 2], I32)
        x_rows, x_t = sb("x", [P, 2, D]), sb("xT", [P, 2, KD, P])
        gate, lin, sig = sb("gate", [P, 2, HALF]), sb("lin", [P, 2, HALF]), sb("sig", [P, 2, HALF])
        product, y = sb("product", [P, 2, HALF]), sb("y", [P, DOWN, BANK])
        hidden = Parts(*(sb(f"hidden_{x}", [P, KD, P], F32R) for x in ("leading", "rest")))
        leading = [k.over("experts_leading0", k.h[:, :, :], [P, KD * BANK]), sb("leading1", [P, KD * BANK], F32R)]
        rest = [k.over(f"experts_rest{u}", ring_down[:, u, :], [P, KD * BANK]) for u in range(DOWN)]

        def sems(what, n):
            return [sem(f"{what}{i}") for i in range(n)]

        up_landed, down_landed, up_ready, gated, sigged, hid_done = (sems(x, UP) for x in (
            "up_landed", "down_landed", "up_ready", "gate_ready", "sigmoid_ready", "hidden_done"))
        down_masked, down_split, down_ready, y_copied, y_stored = (sems(x, DOWN) for x in (
            "down_masked", "down_split", "down_ready", "y_copied", "y_stored"))
        indexed, gathered, x_turned, x_copied = (sems(x, 2) for x in ("indexed", "gathered", "x_turned", "x_copied"))
        own, cleared, zeroed, passed = (sem(x) for x in ("vector_steps", "zero_cleared", "empty_blocks_zeroed", "waits_passed"))
        zero = sb("zero", [P, D])
        OWN = 6

        def blocks(eng, body, empty=None):
            def block_of(i, s, otherwise, then=None):
                b = 2 * i + s
                e = eng.value_load(block_expert[0:1, bass.ds(b, 1)], min_val=0, max_val=EXPERTS)
                with eng.If(e < EXPERTS):
                    body(i, s, b, nc.s_assert_within(
                        e, 0, EXPERTS - 1, skip_runtime_bounds_check_because="inside the branch for e < EXPERTS"))
                    if then:
                        then()
                if empty:
                    with eng.Else():
                        for n in otherwise:
                            empty(2 * i + n)

            with eng.Fori(0, (SLOTS_MAX + 1) // 2) as i:
                block_of(i, 0, (0, 1), lambda: block_of(i, 1, (1,)))

        with nc.Block() as block:
            @block.sync
            def _(sp):
                def body(i, s, b, e):
                    for u in range(UP):
                        sp.wait_ge(hid_done[u], b)
                        sp.dma_start(ring_up[:, u, :], d["w_up_3"][bass.ds(e, 1), u, :, :].rearrange("a p n -> p (a n)")
                                     ).then_inc(up_landed[u], 16)
                    for u in range(DOWN):
                        sp.wait_ge(y_copied[u], b)
                        sp.dma_start(ring_down[:, u, :], d["w_down_3"][bass.ds(e, 1), u, :, :].rearrange("a p n -> p (a n)")
                                     ).then_inc(down_landed[u], 16)

                def empty(b):
                    sp.dma_start(results[bass.ds(b * P, P), :], zero[:, :]).then_inc(zeroed, 16)

                sp.wait_ge(cleared, 1)
                blocks(sp, body, empty)
                count = SLOTS_MAX + 1
                empties = sp.value_load(block_expert[0:1, count + 1:count + 2], min_val=0, max_val=count)
                wait_apart(sp, zeroed, empties * 16, passed)

            @block.gpsimd
            def _(pool):
                pool.memset(zero[:, :], 0.0).then_inc(cleared, 1)

                def gather(s, i, b):
                    if not isinstance(i, int):
                        pool.wait_ge(gathered[s], i * 16)
                        pool.wait_ge(x_turned[s], i)
                    pool.tensor_copy(index[:, s:s + 1], row_of[:, b:b + 1] if isinstance(b, int) else row_of[:, bass.ds(b, 1)]
                                     ).then_inc(indexed[s], 1)
                    wait_apart(pool, indexed[s], i + 1, passed)
                    pool.indirect_dma_start(out=x_rows[:, s, :], out_offset=None, in_=rows,
                                            in_offset=bass.IndirectOffsetOnAxis(ap=index[:, s:s + 1], axis=0)
                                            ).then_inc(gathered[s], 16)

                gather(0, 0, 0)
                blocks(pool, lambda i, s, b, e: gather(1 - s, i + s, b + 1))

            @block.tensor
            def _(pe):
                def turn(s, i):
                    pe.wait_ge(gathered[s], i * 16 + 16)
                    for n in range(KD):
                        last = pe.transpose(k.psum[:, 6 * BANK + n * P:6 * BANK + (n + 1) * P], x_rows[:, s, n * P:(n + 1) * P],
                                            k.c("ident"))
                    last.then_inc(x_turned[s], 1)

                def body(i, s, b, e):
                    pe.wait_ge(x_copied[s], i + 1)
                    for u in range(UP):
                        w = ring_up[:, u, 0:KD * CH * P].rearrange("p (k n) -> p k n", k=KD)
                        pe.wait_ge(up_landed[u], b * 16 + 16)
                        pe.wait_ge(hid_done[(u + 2) % UP], b + 1 if u >= 2 else b)
                        for c in range(CH):
                            for kk in range(KD):
                                last = pe.matmul(k.bank(u % 2)[:, c * P:(c + 1) * P], w[:, kk, c * P:(c + 1) * P],
                                                 x_t[:, s, kk, :], start=(kk == 0), stop=(kk == KD - 1))
                        last.then_inc(up_ready[u], 1)
                    turn(1 - s, i + s)
                    for u in range(DOWN):
                        high, low = (x[u].rearrange("p (k n) -> p k n", k=KD) for x in (leading, rest))
                        pe.wait_ge(down_split[u], b + 1)
                        pe.wait_ge(y_copied[u], b)
                        for kk in range(KD):
                            if u == 0 and kk % 2 == 0:
                                pe.wait_ge(hid_done[kk // 2], b + 1)
                            last = three_passes(pe, k.bank(2 + u), (hidden.leading[:, kk, :], hidden.rest[:, kk, :]),
                                                (high[:, kk, :], low[:, kk, :]), kk == 0, kk == KD - 1)
                        last.then_inc(down_ready[u], 1)
                turn(0, 0)
                blocks(pe, body)

            @block.scalar
            def _(act):
                def keep_x(s, i):
                    act.wait_ge(x_turned[s], i + 1)
                    act.copy(x_t[:, s, :, :].rearrange("p k n -> p (k n)"), k.psum[:, 6 * BANK:8 * BANK]
                             ).then_inc(x_copied[s], 1)

                def body(i, s, b, e):
                    for u in range(UP):
                        act.wait_ge(gated[u], 2 * b + 2)
                        act.activation(sig[:, u % 2, :], gate[:, u % 2, :], ACT.Sigmoid, scale=SWIGLU_ALPHA
                                       ).then_inc(sigged[u], 1)
                        if u < DOWN:
                            act.wait_ge(down_ready[u], b)
                            act.wait_ge(down_landed[u], b * 16 + 16)
                            act.copy(leading[u][:, :], ring_down[:, u, :]).then_inc(down_masked[u], 1)
                    keep_x(1 - s, i + s)
                    for u in range(DOWN):
                        act.wait_ge(down_ready[u], b + 1)
                        act.wait_ge(y_stored[u], b * 16)
                        act.copy(y[:, u, :], k.bank(2 + u)).then_inc(y_copied[u], 1)
                        act.wait_ge(y_copied[u], b + 1)
                        act.dma_start(results[bass.ds(b * P, P), u * BANK:(u + 1) * BANK], y[:, u, :]).then_inc(y_stored[u], 16)
                keep_x(0, 0)
                blocks(act, body)
                filled = act.value_load(block_expert[0:1, SLOTS_MAX + 1:SLOTS_MAX + 2], min_val=1, max_val=SLOTS_MAX + 1)
                for u in range(DOWN):
                    wait_apart(act, y_stored[u], filled * 16, passed)

            @block.vector
            def _(dve):
                def body(i, s, b, e):
                    dve.wait_ge(down_ready[DOWN - 1], b)
                    for u in range(UP):
                        n = u % 2
                        bias = ring_up[:, u, KD * CH * P:KD * CH * P + CH]
                        v = Steps(dve, own)
                        v.n = b * (OWN * UP) + u * OWN
                        ps = k.bank(u % 2)
                        dve.wait_ge(up_ready[u], b + 1)
                        for c in range(2):
                            dve.tensor_scalar(gate[:, n, c * P:(c + 1) * P], ps[:, c * P:(c + 1) * P], bias[:, c:c + 1], LIMIT,
                                              ALU.add, ALU.min).then_inc(gated[u], 1)
                        for c in range(2):
                            v.then(dve.tensor_scalar(lin[:, n, c * P:(c + 1) * P], ps[:, (2 + c) * P:(3 + c) * P],
                                                     bias[:, 2 + c:3 + c], -LIMIT, ALU.add, ALU.max))
                        v.settle()
                        v.do(dve.tensor_scalar(lin[:, n, :], lin[:, n, :], LIMIT, 1.0, ALU.min, ALU.add))
                        dve.wait_ge(gated[u], 2 * b + 2)
                        v.do(dve.tensor_tensor(lin[:, n, :], lin[:, n, :], gate[:, n, :], ALU.mult))
                        dve.wait_ge(sigged[u], b + 1)
                        v.do(dve.tensor_tensor(product[:, n, :], lin[:, n, :], sig[:, n, :], ALU.mult))
                        high, low = (x[:, 2 * u:2 * u + 2, :].rearrange("p k n -> p (k n)") for x in (hidden.leading, hidden.rest))
                        v.do(leading_bits(dve, high, product[:, n, :]))
                        rest_bits(dve, low, product[:, n, :], high).then_inc(hid_done[u], 1)
                        if u < DOWN:
                            dve.wait_ge(down_masked[u], b + 1)
                            rest_bits(dve, rest[u][:, :], ring_down[:, u, :], leading[u][:, :]
                                      ).then_inc(down_split[u], 1)
                blocks(dve, body)


def third_block(k):
    nc, d = k.nc, k.dram
    with ExitStack() as ctx:
        def sb(what, shape, dtype=F32, stack=ctx):
            return stack.enter_context(k.tensor(f"third_{what}", shape, dtype))

        mod, gains = sb("mod", [P, 6 * KD, 2]), sb("gains", [P, 3, KD])
        subln, minus_lam = sb("subln", [P, 1]), sb("minus_lam", [P, 1])
        modulation(k, mod)
        third_columns(k, mod, gains, subln, minus_lam)
        with ExitStack() as attend:
            mix = sb("mix", [P, KD, T], F32, attend)
            mixers(k, mod, gains, subln, minus_lam, mix)

            def gated_residual(first):
                def finish(eng, n, ps):
                    g = mod[:, first + n, 0:1] if isinstance(n, int) else \
                        mod[:, bass.ds(n + first, 1), 0:1].rearrange("p a b -> p (a b)")
                    return eng.scalar_tensor_tensor(at(k.x, n), ps, g, at(k.x, n), ALU.mult, ALU.add)
                return finish

            project(k, "out3", [Section(d["w_out_3"], 2, KD, mix, gated_residual(2 * KD), "vector", spent=True)])
        feature_norm(k, "moe_norm", [([k.x[:, n, :] for n in range(KD)], [k.h[:, n, :] for n in range(KD)],
                                      [gains[:, 2, n:n + 1] for n in range(KD)])], k.c("ones"), 1.0 / D, "eps",
                     shift=[mod[:, 3 * KD + n, 0:1] for n in range(KD)])
        gate = sb("gate", [P, TT, TOP_K])
        dest = sb("dest", [P, TT, TOP_K], I32)
        by_expert = sb("gate_by_expert", [EXPERTS, T])
        rows = nc.dram_tensor("token_rows", (T + 1, D), F32, kind="Internal").ap()
        results = nc.dram_tensor("expert_rows", ((SLOTS_MAX + 1) * P, D), F32, kind="Internal").ap()
        with ExitStack() as routing:
            row_of = sb("row_of", [P, SLOTS_MAX + 2], I32, routing)
            block_expert = sb("block_expert", [1, SLOTS_MAX + 3], I32, routing)
            with ExitStack() as deciding:
                logits, bias = sb("logits", [P, TT, EXPERTS], F32, deciding), sb("router_b", [P, EXPERTS], F32, deciding)
                token_rows(k, rows, bias)
                project(k, "router", [Section(d["router_w"], 1, KD, k.h,
                                              lambda eng, n, ps: eng.tensor_tensor(logits[:, n, :], ps, bias[:, :], ALU.add),
                                              "vector", width=EXPERTS, by_tokens=True)])
                route(k, logits, gate, dest, row_of, block_expert, by_expert)
            experts(k, rows, row_of, block_expert, results)
        combine(k, results, gate, dest, by_expert, mod)
    chunks = [k.x[:, n, :] for n in range(KD)]
    feature_norm(k, "final_norm", [(chunks, chunks, [k.p("final_norm_w", n) for n in range(KD)])], k.c("ones"), 1.0 / D, "eps",
                 memory=[k.dram["out"][n * P:(n + 1) * P, :] for n in range(KD)])


def token_rows(k, rows, bias):
    nc = k.nc
    with k.stage("token_rows") as (sb, sem):
        by_token, zero = sb("by_token", [P, TT, D]), sb("zero", [1, D])
        turned, copied, cleared, stored = (sem(x) for x in ("turned", "copied", "zero_cleared", "rows_stored"))
        with nc.Block() as block:
            @block.tensor
            def _(pe):
                for t in range(TT):
                    for half in range(2):
                        for n in range(4):
                            last = pe.transpose(k.bank(2 * t + half)[:, n * P:(n + 1) * P],
                                                k.h[:, 4 * half + n, t * P:(t + 1) * P], k.c("ident"))
                        last.then_inc(turned, 1)

            @block.vector
            def _(dve):
                dve.memset(zero[:, :], 0.0).then_inc(cleared, 1)
                for n in range(2 * TT):
                    dve.wait_ge(turned, n + 1)
                    dve.tensor_copy(by_token[:, n // 2, (n % 2) * BANK:(n % 2 + 1) * BANK], k.bank(n)).then_inc(copied, 1)

            @block.sync
            def _(sp):
                sp.dma_start(bias[:, :], k.dram["router_b"][0:1, :].broadcast_to([P, EXPERTS])).then_inc(stored, 16)
                sp.wait_ge(cleared, 1)
                sp.dma_start(rows[T:T + 1, :], zero[:, :]).then_inc(stored, 16)
                for t in range(TT):
                    sp.wait_ge(copied, 2 * t + 2)
                    sp.dma_start(rows[t * P:(t + 1) * P, :], by_token[:, t, :]).then_inc(stored, 16)
                sp.wait_ge(stored, 16 * (TT + 2))


def combine(k, results, gate, dest, by_expert, mod):
    nc = k.nc
    with k.stage("combine") as (sb, sem):
        b2 = sb("b2", [EXPERTS, D])
        got, acc = sb("got", [P, 4, D]), sb("acc", [P, TT, D])
        landed, gathered, weighed, summed, added = sem("b2_landed"), [sem(f"rows{i}_gathered") for i in range(4)], sem("rows_weighed"), \
            sem("sums_ready"), sem("residual_added")
        N = TT * TOP_K
        with nc.Block() as block:
            @block.sync
            def _(sp):
                sp.dma_start(b2[:, :], k.dram["b2_3"]).then_inc(landed, 16)

            @block.gpsimd
            def _(pool):
                for n in range(N):
                    t, c = n // TOP_K, n % TOP_K
                    if n >= 4:
                        pool.wait_ge(weighed, n - 3)
                    pool.indirect_dma_start(out=got[:, n % 4, :], out_offset=None, in_=results,
                                            in_offset=bass.IndirectOffsetOnAxis(ap=dest[:, t, c:c + 1], axis=0)
                                            ).then_inc(gathered[n % 4], 16)

            @block.vector
            def _(dve):
                for n in range(N):
                    t, c = n // TOP_K, n % TOP_K
                    dve.wait_ge(gathered[n % 4], 16 * (n // 4) + 16)
                    g = gate[:, t, c:c + 1]
                    if c == 0:
                        dve.tensor_scalar(acc[:, t, :], got[:, n % 4, :], g, None, ALU.mult).then_inc(weighed, 1)
                    else:
                        dve.wait_ge(weighed, n)
                        dve.scalar_tensor_tensor(acc[:, t, :], got[:, n % 4, :], g, acc[:, t, :], ALU.mult,
                                                 ALU.add).then_inc(weighed, 1)
                for n in range(KD):
                    dve.wait_ge(summed, n + 1)
                    dve.scalar_tensor_tensor(k.x[:, n, :], k.bank(n), mod[:, 5 * KD + n, 0:1], k.x[:, n, :], ALU.mult,
                                             ALU.add).then_inc(added, 1)

            @block.tensor
            def _(pe):
                pe.wait_ge(landed, 16)
                for n in range(KD):
                    pe.matmul(k.bank(n), b2[:, n * P:(n + 1) * P], by_expert[:, :], start=True, stop=False, skip_group_check=True)
                for t in range(TT):
                    pe.wait_ge(weighed, TOP_K * (t + 1))
                    for n in range(KD):
                        last = pe.matmul(k.bank(n)[:, t * P:(t + 1) * P], acc[:, t, n * P:(n + 1) * P], k.c("ident"),
                                         start=False, stop=(t == TT - 1), skip_group_check=True)
                        if t == TT - 1:
                            last.then_inc(summed, 1)


def lay_out_third(i, a, p):
    a["ctxT"] = i["ctx_3"][0].T
    p["c"] = np.stack([columns(i["c_3"][0]), columns(i["c_ctx_3"])], 2).reshape(P, -1)
    for n in ("b_ada", "attn_norm_w", "q_norm_w", "kv_norm_w", "subln_w", "ffn_norm_w"):
        p[n] = columns(i[n + "_3"][0])
    p["final_norm_w"] = columns(i["final_norm_w_3"])
    lam = np.zeros((P, 4), np.float32)
    for n, name in enumerate(("q1", "k1", "q2", "k2")):
        lam[0:DH, n] = i[f"lambda_{name}_3"][0]
    p["lambdas"] = lam
    a["w_ada"] = units_of(i["w_ada_3"][0], 4)
    w = i["w_in_3"][0]
    kr = np.concatenate([w[:, 1920:1984]] * 2, 1)
    a["w3_dq"], a["w3_dk"], a["w3_dv"] = units_of(w[:, 0:512], 4), units_of(w[:, 512:1024], 4), whole(w[:, 1024:1536])
    a["w3_misc"] = units_of(np.concatenate([w[:, 1536:1920], kr], 1), 4)
    a["w3_misc_ctx"] = units_of(np.concatenate([w[:, 1792:1920], kr], 1), 2)
    uq = i["w_uq_3"][0].reshape(256, MLA_HEADS, P + DH)
    a["w3_uq"] = units_of(np.concatenate([uq[:, :, 0:P].reshape(256, -1), uq[:, :, P:].reshape(256, -1)], 1), 3)
    ukv = i["w_ukv_3"][0].reshape(P, MLA_HEADS, 2, P)
    a["w3_uk"], a["w3_uv"] = units_of(ukv[:, :, 0].reshape(P, -1), 4), whole(ukv[:, :, 1].reshape(P, -1))
    a["w_out_3"] = units_of(i["w_out_3"][0], 4)
    a["router_w"], a["router_b"] = whole(i["router_w_3"][0]), i["router_b_3"]
    w1 = i["w1_3"][0].reshape(EXPERTS, KD, P, 2, 4, 2 * P).transpose(0, 4, 2, 1, 3, 5).reshape(EXPERTS, 4, P, -1)
    b1 = i["b1_3"][0].reshape(EXPERTS, 2, 4, 2, P).transpose(0, 2, 4, 1, 3).reshape(EXPERTS, 4, P, 4)
    a["w_up_3"] = np.concatenate([w1, b1], 3)
    a["w_down_3"] = i["w2_3"][0].reshape(EXPERTS, KD, P, 2, BANK).transpose(0, 3, 2, 1, 4).reshape(EXPERTS, 2, P, -1)
    a["b2_3"] = i["b2_3"][0]



def program(nc, dram):
    with ExitStack() as ctx:
        k = Core(nc, ctx, dram)
        k.x = k.keep("residual", [P, KD, T])
        k.h = k.keep("normed", [P, KD, T])
        k.const = k.keep("constants", [P, CONST_N])
        k.param = k.keep("parameters", [P, PARAM_N])
        load_inputs(k)
        first_block(k)
        second_block(k)
        third_block(k)


def units_of(w, chunks):
    kc = w.shape[0] // P
    return w.reshape(kc, P, -1, chunks * P).transpose(2, 1, 0, 3).reshape(-1, P, kc * chunks * P)


def whole(w):
    return w.reshape(w.shape[0] // P, P, -1).transpose(1, 0, 2).reshape(1, P, -1)


def columns(v):
    return v.reshape(-1, P).T


def lay_out(i):
    a = {"consts": np.concatenate(list(constants().values()), 1), "buckets": bucket_rows()}
    a["xT"] = i["x"][0].T
    a["rel_bias"] = i["rel_bias"]
    w = i["w_in"][0]
    a["w_in_q"] = units_of(w[:, 0:512], 4)
    a["w_in_k"] = units_of(np.concatenate([w[:, 512:640], w[:, 640:768], w[:, 768:896], w[:, 1024:1152]], 1), 4)
    a["w_in_v"] = whole(np.concatenate([w[:, 896:1024], w[:, 1152:1280]], 1))
    a["w_in_g"] = whole(w[:, 1280:1304])
    a["w_in_u"] = units_of(w[:, 1304:1816], 4)
    a["w_in_sv"] = whole(w[:, 1816:2328])
    for x in "kv":
        a[f"cmp_w1_{x}"] = i[f"cmp_w1_{x}"][0]
    a["cmp_w2_k"] = np.concatenate([i["cmp_w2_k"][0]] * 2, 1)
    a["cmp_w2_v"] = i["cmp_w2_v"][0]
    a["sgu_wT"] = i["sgu_w"][0].transpose(2, 0, 1).reshape(P, -1)
    a["sgu_norm"] = i["sgu_norm"]
    a["sgu_b"] = i["sgu_b"][0]
    a["w_out"] = units_of(i["w_out"][0], 4)
    up = units_of(i["w_up"][0], 1).reshape(2, FF_CHUNKS, P, KD, P)
    a["w_up"] = up.transpose(1, 2, 3, 0, 4).reshape(FF_CHUNKS, P, KD * 2 * P)
    a["w_down"] = units_of(i["w_down"][0], 1)

    def interleaved(v):
        return v.reshape(-1, 2, FF_CHUNKS, P).transpose(0, 2, 1, 3).reshape(-1)

    p = {n: columns(i[n][0]) for n in ("attn_norm", "ffn_norm", "cmp_b1_k", "cmp_b1_v")}
    p["cmp_pe_k"], p["cmp_pe_v"] = columns(i["cmp_pe_k"][0].reshape(-1)), columns(i["cmp_pe_v"][0].reshape(-1))
    for n in ("q_norm", "k_norm_cmp", "k_norm_slc", "k_norm_win"):
        p[n] = columns(np.concatenate([i[n][0]] * 2))
    p["conv_w"], p["conv_b"] = columns(interleaved(i["conv_w"][0])), columns(interleaved(i["conv_b"][0]))
    lay_out_second(i, a, p)
    lay_out_third(i, a, p)
    a["params"] = np.concatenate([p[n] for n in PARAM_COLUMNS], 1)
    return {n: np.ascontiguousarray(v) for n, v in a.items()}


def kernel(**inputs):
    from concourse import bacc
    from concourse.bass_utils import run_bass_kernel_spmd

    arrays = lay_out({n: np.asarray(v) for n, v in inputs.items()})
    nc = bacc.Bacc("TRN2", target_bir_lowering=False, num_devices=1)
    dram = {n: nc.dram_tensor(f"in_{n}", v.shape, F32, kind="ExternalInput").ap() for n, v in arrays.items()}
    dram["out"] = nc.dram_tensor("out", (D, T), F32, kind="ExternalOutput").ap()
    program(nc, dram)
    run = run_bass_kernel_spmd(nc, [{f"in_{n}": v for n, v in arrays.items()}], core_ids=[0])
    return run.results[0]["out"].T[None]
```
